# Optimizing a Trainium2 kernel written in Bass

```python
import jax, jax.numpy as jnp
from jax import lax
import numpy as np

D_MODEL = 1024
BATCH = 1
SEQ = 256
DEPTH = 2

N_EVEN = (DEPTH + 1) // 2
N_ODD = DEPTH // 2

N_Q_HEADS = 8
N_KV_HEADS = 2
HEAD_DIM = 64
Q_GROUP = N_Q_HEADS // N_KV_HEADS
WINDOW = 128
ATTN_BLOCK = 128
ALIBI_MAX = 8.0
CONV_WIDTH_B = D_MODEL // 2
CONV_GROUPS_B = 8
CONV_K_B = 3
Q_DIM = N_Q_HEADS * HEAD_DIM
KV_DIM = N_KV_HEADS * HEAD_DIM
EVEN_IN = Q_DIM + 2 * KV_DIM + 3 * CONV_WIDTH_B
EVEN_MIX = Q_DIM + CONV_WIDTH_B
EVEN_SPLITS = (Q_DIM, Q_DIM + KV_DIM, Q_DIM + 2 * KV_DIM, Q_DIM + 2 * KV_DIM + CONV_WIDTH_B, Q_DIM + 2 * KV_DIM + 2 * CONV_WIDTH_B)
LRU_WIDTH = D_MODEL
LRU_HEADS = 8
LRU_HEAD_DIM = LRU_WIDTH // LRU_HEADS
CONV_K_C = 4
LRU_C = 8.0
D_FF = (D_MODEL * 7) // 2
N_EXPERTS = 8
TOP_K = 2
MOE_BLOCK = 128
NORM_EPS = 1e-6
NEG_INF = -1e30


def rms_norm(x, g):
    xf = x.astype(jnp.float32)
    y = xf * lax.rsqrt(jnp.mean(xf * xf, axis=-1, keepdims=True) + NORM_EPS)
    return (y * g.astype(jnp.float32)).astype(x.dtype)

def causal_depthwise_conv(x, w):
    K = w.shape[0]
    S = x.shape[1]
    xp = jnp.pad(x, ((0, 0), (K - 1, 0), (0, 0)))
    return sum(xp[:, k:k + S] * w[k] for k in range(K))

def alibi_slopes():
    h = jnp.arange(1, N_Q_HEADS + 1, dtype=jnp.float32)
    return jnp.exp2(-ALIBI_MAX * h / N_Q_HEADS)

def sliding_window_attention(q, k, v, sinks):
    B, S = q.shape[0], q.shape[1]
    L = ATTN_BLOCK
    nb = S // L
    qb = q.reshape(B, nb, L, N_KV_HEADS, Q_GROUP, HEAD_DIM)

    def band(t):
        cur = t.reshape(B, nb, L, N_KV_HEADS, HEAD_DIM)
        prev = jnp.pad(cur, ((0, 0), (1, 0), (0, 0), (0, 0), (0, 0)))[:, :-1]
        return jnp.concatenate([prev, cur], axis=2)

    kb, vb = band(k), band(v)
    scores = jnp.einsum('bnqkgd,bnskd->bnkgqs', qb, kb, preferred_element_type=jnp.float32) * (HEAD_DIM ** -0.5)
    qi = jnp.arange(L)[:, None]
    sj = jnp.arange(2 * L)[None, :]
    diff = L + qi - sj
    s_abs = (jnp.arange(nb)[:, None] - 1) * L + jnp.arange(2 * L)[None, :]
    valid = (diff >= 0)[None] & (diff < WINDOW)[None] & (s_abs >= 0)[:, None, :]
    slopes = alibi_slopes().reshape(N_KV_HEADS, Q_GROUP)
    bias = -slopes[:, :, None, None] * diff.astype(jnp.float32)
    scores = jnp.where(valid[None, :, None, None], scores + bias, NEG_INF)
    sink = jnp.broadcast_to(sinks.astype(jnp.float32).reshape(N_KV_HEADS, Q_GROUP)[None, None, :, :, None, None], scores.shape[:-1] + (1,))
    probs = jax.nn.softmax(jnp.concatenate([scores, sink], axis=-1), axis=-1)[..., :-1]
    out = jnp.einsum('bnkgqs,bnskd->bnqkgd', probs.astype(v.dtype), vb)
    return out.reshape(B, S, Q_DIM)

def attn_conv_mixer(h, w_in, q_gain, k_gain, sinks, conv_w, w_out):
    B, S, _ = h.shape
    q, k, v, gate_b, gate_c, u = jnp.split(h @ w_in, EVEN_SPLITS, axis=-1)
    q = rms_norm(q.reshape(B, S, N_Q_HEADS, HEAD_DIM), q_gain)
    k = rms_norm(k.reshape(B, S, N_KV_HEADS, HEAD_DIM), k_gain)
    v = v.reshape(B, S, N_KV_HEADS, HEAD_DIM)
    attn = sliding_window_attention(q, k, v, sinks)
    conv = gate_b * causal_depthwise_conv(gate_c * u, conv_w)
    return jnp.concatenate([attn, conv], axis=-1) @ w_out

def recurrent_mixer(h, w_in, conv_w, conv_b, ga_w, ga_b, gx_w, gx_b, lam, w_out):
    B, S, _ = h.shape
    y_branch, x_branch = jnp.split(h @ w_in, 2, axis=-1)
    y_branch = jax.nn.gelu(y_branch)
    xc = causal_depthwise_conv(x_branch, conv_w) + conv_b
    xh = xc.reshape(B, S, LRU_HEADS, LRU_HEAD_DIM)
    r = jax.nn.sigmoid(jnp.einsum('bshi,hij->bshj', xh, ga_w).reshape(B, S, LRU_WIDTH) + ga_b)
    i = jax.nn.sigmoid(jnp.einsum('bshi,hij->bshj', xh, gx_w).reshape(B, S, LRU_WIDTH) + gx_b)
    log_a = -LRU_C * r.astype(jnp.float32) * jax.nn.softplus(-lam.astype(jnp.float32))
    a = jnp.exp(log_a)
    mult = jnp.sqrt(jnp.maximum(-jnp.expm1(2.0 * log_a), 0.0))
    mult = jnp.where(jnp.arange(S)[None, :, None] == 0, 1.0, mult)
    b = mult * (i * xc).astype(jnp.float32)

    def combine(c1, c2):
        a1, b1 = c1
        a2, b2 = c2
        return a1 * a2, a2 * b1 + b2

    _, hs = lax.associative_scan(combine, (a, b), axis=1)
    return (y_branch * hs.astype(h.dtype)) @ w_out

def swiglu(h, w_gate, w_up, w_down):
    return (jax.nn.silu(h @ w_gate) * (h @ w_up)) @ w_down

def moe_swiglu(h, w_router, w_gate, w_up, w_down):
    B, S, D = h.shape
    T = B * S
    xf = h.reshape(T, D)
    logits = (xf @ w_router).astype(jnp.float32)
    top_logits, top_idx = lax.top_k(logits, TOP_K)
    gates = jax.nn.softmax(top_logits, axis=-1)
    n_assign = T * TOP_K
    e_flat = top_idx.reshape(-1).astype(jnp.int32)
    tok_flat = jnp.repeat(jnp.arange(T, dtype=jnp.int32), TOP_K)
    g_flat = gates.reshape(-1)
    order = jnp.argsort(e_flat)
    e_sorted = e_flat[order]
    counts = jnp.zeros((N_EXPERTS,), jnp.int32).at[e_flat].add(1)
    padded = (counts + MOE_BLOCK - 1) // MOE_BLOCK * MOE_BLOCK
    pad_end = jnp.cumsum(padded)
    pad_start = pad_end - padded
    start = jnp.cumsum(counts) - counts
    dest = pad_start[e_sorted] + jnp.arange(n_assign, dtype=jnp.int32) - start[e_sorted]
    n_rows = n_assign + N_EXPERTS * MOE_BLOCK
    n_blocks = n_rows // MOE_BLOCK
    row_tok = jnp.zeros((n_rows,), jnp.int32).at[dest].set(tok_flat[order])
    row_gate = jnp.zeros((n_rows,), jnp.float32).at[dest].set(g_flat[order])
    blk_start = jnp.arange(n_blocks, dtype=jnp.int32) * MOE_BLOCK
    blk_expert = jnp.minimum(jnp.searchsorted(pad_end, blk_start, side='right'), N_EXPERTS - 1)

    def expert_block(args):
        tok, e = args
        xb = xf[tok]
        hb = jax.nn.silu(xb @ w_gate[e]) * (xb @ w_up[e])
        return hb @ w_down[e]

    yb = lax.map(expert_block, (row_tok.reshape(n_blocks, MOE_BLOCK), blk_expert))
    y = yb.reshape(n_rows, D).astype(jnp.float32) * row_gate[:, None]
    out = jnp.zeros((T, D), jnp.float32).at[row_tok].add(y)
    return out.astype(h.dtype).reshape(B, S, D)

def first_inputs(seed: int = 0) -> dict:
    key = jax.random.key(seed)
    ks = iter(jax.random.split(key, 32))
    f32 = jnp.float32
    res_scale = (2 * DEPTH) ** -0.5

    def nrm(shape, scale):
        return jax.random.normal(next(ks), shape, f32) * scale

    x = nrm((BATCH, SEQ, D_MODEL), 1.0)
    norm_mix = 1.0 + nrm((DEPTH, D_MODEL), 0.02)
    norm_ffn = 1.0 + nrm((DEPTH, D_MODEL), 0.02)
    hy_w_in = nrm((N_EVEN, D_MODEL, EVEN_IN), D_MODEL ** -0.5)
    hy_q_gain = 1.0 + nrm((N_EVEN, HEAD_DIM), 0.02)
    hy_k_gain = 1.0 + nrm((N_EVEN, HEAD_DIM), 0.02)
    hy_sinks = nrm((N_EVEN, N_Q_HEADS), 0.5)
    hy_conv_w = nrm((N_EVEN, CONV_K_B, CONV_WIDTH_B), CONV_K_B ** -0.5)
    hy_w_out = nrm((N_EVEN, EVEN_MIX, D_MODEL), EVEN_MIX ** -0.5 * res_scale)
    rg_w_in = nrm((N_ODD, D_MODEL, 2 * LRU_WIDTH), D_MODEL ** -0.5)
    rg_conv_w = nrm((N_ODD, CONV_K_C, LRU_WIDTH), CONV_K_C ** -0.5)
    rg_conv_b = nrm((N_ODD, LRU_WIDTH), 0.01)
    rg_gate_a_w = nrm((N_ODD, LRU_HEADS, LRU_HEAD_DIM, LRU_HEAD_DIM), LRU_HEAD_DIM ** -0.5)
    rg_gate_a_b = nrm((N_ODD, LRU_WIDTH), 0.01)
    rg_gate_x_w = nrm((N_ODD, LRU_HEADS, LRU_HEAD_DIM, LRU_HEAD_DIM), LRU_HEAD_DIM ** -0.5)
    rg_gate_x_b = nrm((N_ODD, LRU_WIDTH), 0.01)
    a_pow_c = jax.random.uniform(next(ks), (N_ODD, LRU_WIDTH), f32, minval=0.9, maxval=0.999)
    a0 = a_pow_c ** (1.0 / LRU_C)
    rg_lambda = jnp.log(a0) - jnp.log1p(-a0)
    rg_w_out = nrm((N_ODD, LRU_WIDTH, D_MODEL), LRU_WIDTH ** -0.5 * res_scale)
    ffn_w_gate = nrm((N_EVEN, D_MODEL, D_FF), D_MODEL ** -0.5)
    ffn_w_up = nrm((N_EVEN, D_MODEL, D_FF), D_MODEL ** -0.5)
    ffn_w_down = nrm((N_EVEN, D_FF, D_MODEL), D_FF ** -0.5 * res_scale)
    moe_router = nrm((N_ODD, D_MODEL, N_EXPERTS), D_MODEL ** -0.5)
    moe_w_gate = nrm((N_ODD, N_EXPERTS, D_MODEL, D_FF), D_MODEL ** -0.5)
    moe_w_up = nrm((N_ODD, N_EXPERTS, D_MODEL, D_FF), D_MODEL ** -0.5)
    moe_w_down = nrm((N_ODD, N_EXPERTS, D_FF, D_MODEL), D_FF ** -0.5 * res_scale)
    return {'x': x, 'norm_mix': norm_mix, 'norm_ffn': norm_ffn,
            'hy_w_in': hy_w_in, 'hy_q_gain': hy_q_gain, 'hy_k_gain': hy_k_gain, 'hy_sinks': hy_sinks,
            'hy_conv_w': hy_conv_w, 'hy_w_out': hy_w_out,
            'rg_w_in': rg_w_in, 'rg_conv_w': rg_conv_w, 'rg_conv_b': rg_conv_b,
            'rg_gate_a_w': rg_gate_a_w, 'rg_gate_a_b': rg_gate_a_b, 'rg_gate_x_w': rg_gate_x_w,
            'rg_gate_x_b': rg_gate_x_b, 'rg_lambda': rg_lambda, 'rg_w_out': rg_w_out,
            'ffn_w_gate': ffn_w_gate, 'ffn_w_up': ffn_w_up, 'ffn_w_down': ffn_w_down,
            'moe_router': moe_router, 'moe_w_gate': moe_w_gate, 'moe_w_up': moe_w_up, 'moe_w_down': moe_w_down}

def first_block(x, norm_mix, norm_ffn, hy_w_in, hy_q_gain, hy_k_gain, hy_sinks, hy_conv_w, hy_w_out,
              rg_w_in, rg_conv_w, rg_conv_b, rg_gate_a_w, rg_gate_a_b, rg_gate_x_w, rg_gate_x_b, rg_lambda, rg_w_out,
              ffn_w_gate, ffn_w_up, ffn_w_down, moe_router, moe_w_gate, moe_w_up, moe_w_down):
    for layer in range(DEPTH):
        j = layer // 2
        h = rms_norm(x, norm_mix[layer])
        if layer % 2 == 0:
            x = x + attn_conv_mixer(h, hy_w_in[j], hy_q_gain[j], hy_k_gain[j], hy_sinks[j], hy_conv_w[j], hy_w_out[j])
            h = rms_norm(x, norm_ffn[layer])
            x = x + swiglu(h, ffn_w_gate[j], ffn_w_up[j], ffn_w_down[j])
        else:
            x = x + recurrent_mixer(h, rg_w_in[j], rg_conv_w[j], rg_conv_b[j], rg_gate_a_w[j], rg_gate_a_b[j],
                                    rg_gate_x_w[j], rg_gate_x_b[j], rg_lambda[j], rg_w_out[j])
            h = rms_norm(x, norm_ffn[layer])
            x = x + moe_swiglu(h, moe_router[j], moe_w_gate[j], moe_w_up[j], moe_w_down[j])
    return x


MIX_WIDTH = D_MODEL
FOX_HEADS = MIX_WIDTH // (4 * HEAD_DIM)
MOBA_HEADS = MIX_WIDTH // (4 * HEAD_DIM)
RWKV_HEADS = MIX_WIDTH // (2 * HEAD_DIM)
FOX_WIDTH = FOX_HEADS * HEAD_DIM
MOBA_WIDTH = MOBA_HEADS * HEAD_DIM
RWKV_WIDTH = RWKV_HEADS * HEAD_DIM
RWKV_DECAY_LORA = 64
RWKV_ICLR_LORA = 64
RWKV_GATE_LORA = 160
RWKV_GN_EPS = 64e-5
FOX_IN = 3 * FOX_WIDTH + FOX_HEADS
MOBA_IN = 3 * MOBA_WIDTH
RWKV_IN = 3 * RWKV_WIDTH + RWKV_DECAY_LORA + RWKV_ICLR_LORA + RWKV_GATE_LORA
IN_WIDTH = FOX_IN + MOBA_IN + RWKV_IN
FOX_QBLOCK = 128
MOBA_BLOCK = 256
MOBA_TOPK = 3
MOBA_QCHUNK = 32
ROPE_THETA = 500000.0
ROPE_DIM = HEAD_DIM // 4
FFN_DIM = 2816
MEM_LEN = 256
XATTN_HEADS = 4
XATTN_HEAD_DIM = 128
XATTN_WIDTH = XATTN_HEADS * XATTN_HEAD_DIM


def rms_norm_2(t, g):
    tf = t.astype(jnp.float32)
    y = tf * lax.rsqrt(jnp.mean(tf * tf, axis=-1, keepdims=True) + NORM_EPS)
    return (y * g).astype(t.dtype)

def swiglu_2(h, w_in, w_out):
    gate, up = jnp.split(h @ w_in, 2, axis=-1)
    return (jax.nn.silu(gate) * up) @ w_out

def split_heads(t, n_heads):
    B, S, _ = t.shape
    return t.reshape(B, S, n_heads, HEAD_DIM).transpose(0, 2, 1, 3)

def merge_heads(t):
    B, H, S, d = t.shape
    return t.transpose(0, 2, 1, 3).reshape(B, S, H * d)

def rope_tables(positions):
    inv_freq = ROPE_THETA ** (-jnp.arange(0, ROPE_DIM, 2, dtype=jnp.float32) / ROPE_DIM)
    ang = positions.astype(jnp.float32)[..., None] * inv_freq
    return jnp.cos(ang), jnp.sin(ang)

def apply_partial_rope(t, cos, sin):
    half = ROPE_DIM // 2
    x1, x2, rest = t[..., :half], t[..., half:ROPE_DIM], t[..., ROPE_DIM:]
    c, s = cos[:, None], sin[:, None]
    out = jnp.concatenate([x1 * c - x2 * s, x2 * c + x1 * s, rest.astype(jnp.float32)], axis=-1)
    return out.astype(t.dtype)

def forgetting_attention(q, k, v, log_f):
    B, H, S, d = q.shape
    c = jnp.cumsum(log_f, axis=-1)
    n_qb = S // FOX_QBLOCK
    q_blocks = q.reshape(B, H, n_qb, FOX_QBLOCK, d).transpose(2, 0, 1, 3, 4)
    c_blocks = c.reshape(B, H, n_qb, FOX_QBLOCK).transpose(2, 0, 1, 3)
    k_pos = jnp.arange(S)
    scale = d ** -0.5

    def block(args):
        i, q_i, c_i = args
        s = jnp.einsum('bhqd,bhkd->bhqk', q_i, k).astype(jnp.float32) * scale
        s = s + c_i[..., None] - c[:, :, None, :]
        q_pos = i * FOX_QBLOCK + jnp.arange(FOX_QBLOCK)
        s = jnp.where(k_pos[None, :] <= q_pos[:, None], s, -jnp.inf)
        p = jax.nn.softmax(s, axis=-1).astype(v.dtype)
        return jnp.einsum('bhqk,bhkd->bhqd', p, v)

    out = lax.map(block, (jnp.arange(n_qb), q_blocks, c_blocks))
    return out.transpose(1, 2, 0, 3, 4).reshape(B, H, S, d)

def fox_mixer(z, f_bias, q_gain, k_gain):
    q, k, v, f = jnp.split(z, [FOX_WIDTH, 2 * FOX_WIDTH, 3 * FOX_WIDTH], axis=-1)
    q = rms_norm_2(split_heads(q, FOX_HEADS), q_gain)
    k = rms_norm_2(split_heads(k, FOX_HEADS), k_gain)
    v = split_heads(v, FOX_HEADS)
    log_f = jax.nn.log_sigmoid(f.astype(jnp.float32) + f_bias).transpose(0, 2, 1)
    return merge_heads(forgetting_attention(q, k, v, log_f))

def moba_attention(q, k, v):
    B, H, S, d = q.shape
    s_pad = -(-S // MOBA_BLOCK) * MOBA_BLOCK
    pad = ((0, 0), (0, 0), (0, s_pad - S), (0, 0))
    k_pad = jnp.pad(k, pad)
    v_pad = jnp.pad(v, pad)
    n_blk = s_pad // MOBA_BLOCK
    top_k = min(MOBA_TOPK, n_blk)
    k_blk = k_pad.reshape(B, H, n_blk, MOBA_BLOCK, d)
    v_blk = v_pad.reshape(B, H, n_blk, MOBA_BLOCK, d)
    k_mean = jnp.mean(k_blk.astype(jnp.float32), axis=3)
    n_chunk = S // MOBA_QCHUNK
    q_chunks = q.reshape(B, H, n_chunk, MOBA_QCHUNK, d).transpose(2, 0, 1, 3, 4)
    b_idx = jnp.arange(B)[:, None, None, None]
    h_idx = jnp.arange(H)[None, :, None, None]
    blk_ids = jnp.arange(n_blk)
    scale = d ** -0.5

    def chunk(args):
        i, q_i = args
        q_start = i * MOBA_QCHUNK
        q_blk = q_start // MOBA_BLOCK
        gate = jnp.einsum('bhqd,bhnd->bhqn', q_i.astype(jnp.float32), k_mean)
        gate = jnp.where(blk_ids < q_blk, gate, -jnp.inf)
        _, sel = lax.top_k(gate, top_k)
        valid = sel < q_blk
        k_sel = k_blk[b_idx, h_idx, sel]
        v_sel = v_blk[b_idx, h_idx, sel]
        s_sel = jnp.einsum('bhqd,bhqnkd->bhqnk', q_i, k_sel).astype(jnp.float32) * scale
        s_sel = jnp.where(valid[..., None], s_sel, -jnp.inf)
        s_sel = s_sel.reshape(B, H, MOBA_QCHUNK, top_k * MOBA_BLOCK)
        blk_start = q_blk * MOBA_BLOCK
        k_own = lax.dynamic_slice_in_dim(k_pad, blk_start, MOBA_BLOCK, axis=2)
        v_own = lax.dynamic_slice_in_dim(v_pad, blk_start, MOBA_BLOCK, axis=2)
        s_own = jnp.einsum('bhqd,bhkd->bhqk', q_i, k_own).astype(jnp.float32) * scale
        q_pos = q_start + jnp.arange(MOBA_QCHUNK)
        k_pos = blk_start + jnp.arange(MOBA_BLOCK)
        s_own = jnp.where(k_pos[None, :] <= q_pos[:, None], s_own, -jnp.inf)
        p = jax.nn.softmax(jnp.concatenate([s_sel, s_own], axis=-1), axis=-1).astype(v.dtype)
        p_sel = p[..., :top_k * MOBA_BLOCK].reshape(B, H, MOBA_QCHUNK, top_k, MOBA_BLOCK)
        p_own = p[..., top_k * MOBA_BLOCK:]
        return (jnp.einsum('bhqnk,bhqnkd->bhqd', p_sel, v_sel)
                + jnp.einsum('bhqk,bhkd->bhqd', p_own, v_own))

    out = lax.map(chunk, (jnp.arange(n_chunk), q_chunks))
    return out.transpose(1, 2, 0, 3, 4).reshape(B, H, S, d)

def moba_mixer(z, cos, sin, q_gain, k_gain):
    q, k, v = jnp.split(z, [MOBA_WIDTH, 2 * MOBA_WIDTH], axis=-1)
    q = apply_partial_rope(rms_norm_2(split_heads(q, MOBA_HEADS), q_gain), cos, sin)
    k = apply_partial_rope(rms_norm_2(split_heads(k, MOBA_HEADS), k_gain), cos, sin)
    v = split_heads(v, MOBA_HEADS)
    return merge_heads(moba_attention(q, k, v))

def rwkv7_mixer(z, mu, w0, w2, a0, a2, g2, k_k, k_a, r_k, ln_w, ln_b):
    B, S, _ = z.shape
    zf = z.astype(jnp.float32)
    z_prev = jnp.pad(zf, ((0, 0), (1, 0), (0, 0)))[:, :S]
    zf = zf + (z_prev - zf) * mu
    W = RWKV_WIDTH
    r, k, v, w_lo, a_lo, g_lo = jnp.split(
        zf, [W, 2 * W, 3 * W, 3 * W + RWKV_DECAY_LORA, 3 * W + RWKV_DECAY_LORA + RWKV_ICLR_LORA], axis=-1)
    w_raw = w0 + jnp.tanh(w_lo) @ w2
    decay = jnp.exp(-jnp.exp(-jax.nn.softplus(-w_raw) - 0.5))
    a = jax.nn.sigmoid(a0 + a_lo @ a2)
    g = jax.nn.sigmoid(g_lo) @ g2
    kk = k * k_k
    k = k * (1.0 + (a - 1.0) * k_a)

    def hd(t):
        return t.reshape(B, S, RWKV_HEADS, HEAD_DIM)

    r, k, v, decay, a, kk = hd(r), hd(k), hd(v), hd(decay), hd(a), hd(kk)
    kk = kk / jnp.maximum(jnp.sqrt(jnp.sum(kk * kk, axis=-1, keepdims=True)), 1e-12)

    def step(state, inp):
        r_t, w_t, k_t, v_t, kk_t, a_t = inp
        sa = jnp.einsum('bhij,bhj->bhi', state, -kk_t)
        state = (state * w_t[:, :, None, :] + sa[..., None] * (kk_t * a_t)[:, :, None, :]
                 + v_t[..., None] * k_t[:, :, None, :])
        return state, jnp.einsum('bhij,bhj->bhi', state, r_t)

    xs = tuple(t.transpose(1, 0, 2, 3) for t in (r, decay, k, v, kk, a))
    state0 = jnp.zeros((B, RWKV_HEADS, HEAD_DIM, HEAD_DIM), jnp.float32)
    _, ys = lax.scan(step, state0, xs)
    y = ys.transpose(1, 0, 2, 3)
    mean = jnp.mean(y, axis=-1, keepdims=True)
    var = jnp.mean(jnp.square(y - mean), axis=-1, keepdims=True)
    y = ((y - mean) * lax.rsqrt(var + RWKV_GN_EPS)).reshape(B, S, W) * ln_w + ln_b
    bonus = (jnp.sum(r * k * r_k, axis=-1, keepdims=True) * v).reshape(B, S, W)
    return ((y + bonus) * g).astype(z.dtype)

def memory_cross_attention(h, m, w_q, w_kv, q_gain, k_gain, w_o):
    B, S, _ = h.shape
    M = m.shape[1]
    q = rms_norm_2((h @ w_q).reshape(B, S, XATTN_HEADS, XATTN_HEAD_DIM), q_gain)
    kv = (m @ w_kv).reshape(B, M, 2, XATTN_HEADS, XATTN_HEAD_DIM)
    k = rms_norm_2(kv[:, :, 0], k_gain)
    v = kv[:, :, 1]
    s = jnp.einsum('bqhd,bkhd->bhqk', q, k).astype(jnp.float32) * (XATTN_HEAD_DIM ** -0.5)
    p = jax.nn.softmax(s, axis=-1).astype(v.dtype)
    o = jnp.einsum('bhqk,bkhd->bqhd', p, v).reshape(B, S, XATTN_WIDTH)
    return o @ w_o

def second_inputs(seed: int = 0) -> dict:
    key = jax.random.key(seed)
    ks = iter(jax.random.split(key, 64))
    L, D = DEPTH, D_MODEL

    def nrm(shape, scale):
        return jax.random.normal(next(ks), shape, jnp.float32) * scale

    def gain(shape):
        return 1.0 + nrm(shape, 0.02)

    x = nrm((BATCH, SEQ, D), 1.0)
    mem = nrm((BATCH, MEM_LEN, D), 1.0)
    offset = jax.random.randint(next(ks), (BATCH, 1), 0, SEQ, dtype=jnp.int32)
    positions = (offset + jnp.arange(SEQ, dtype=jnp.int32)[None, :]).astype(jnp.int32)
    return {
        'x': x, 'mem': mem, 'positions': positions,
        'ffn1_norm': gain((L, D)),
        'ffn1_w_in': nrm((L, D, 2 * FFN_DIM), D ** -0.5),
        'ffn1_w_out': nrm((L, FFN_DIM, D), FFN_DIM ** -0.5),
        'mix_norm': gain((L, D)),
        'mix_w_in': nrm((L, D, IN_WIDTH), D ** -0.5),
        'mix_w_out': nrm((L, MIX_WIDTH, D), MIX_WIDTH ** -0.5),
        'fox_f_bias': 3.0 + nrm((L, FOX_HEADS), 0.5),
        'fox_q_gain': gain((L, HEAD_DIM)),
        'fox_k_gain': gain((L, HEAD_DIM)),
        'moba_q_gain': gain((L, HEAD_DIM)),
        'moba_k_gain': gain((L, HEAD_DIM)),
        'rwkv_mu': jax.random.uniform(next(ks), (L, RWKV_IN), jnp.float32, 0.0, 1.0),
        'rwkv_w0': nrm((L, RWKV_WIDTH), 1.0) - 1.0,
        'rwkv_w2': nrm((L, RWKV_DECAY_LORA, RWKV_WIDTH), RWKV_DECAY_LORA ** -0.5),
        'rwkv_a0': nrm((L, RWKV_WIDTH), 0.5),
        'rwkv_a2': nrm((L, RWKV_ICLR_LORA, RWKV_WIDTH), RWKV_ICLR_LORA ** -0.5),
        'rwkv_g2': nrm((L, RWKV_GATE_LORA, RWKV_WIDTH), RWKV_GATE_LORA ** -0.5),
        'rwkv_k_k': 0.85 + nrm((L, RWKV_WIDTH), 0.05),
        'rwkv_k_a': 1.0 + nrm((L, RWKV_WIDTH), 0.05),
        'rwkv_r_k': nrm((L, RWKV_HEADS, HEAD_DIM), 0.1),
        'rwkv_ln_w': gain((L, RWKV_WIDTH)),
        'rwkv_ln_b': nrm((L, RWKV_WIDTH), 0.02),
        'xattn_norm': gain((L, D)),
        'xattn_mem_norm': gain((L, D)),
        'xattn_w_q': nrm((L, D, XATTN_WIDTH), D ** -0.5),
        'xattn_w_kv': nrm((L, D, 2 * XATTN_WIDTH), D ** -0.5),
        'xattn_q_gain': gain((L, XATTN_HEAD_DIM)),
        'xattn_k_gain': gain((L, XATTN_HEAD_DIM)),
        'xattn_w_out': nrm((L, XATTN_WIDTH, D), XATTN_WIDTH ** -0.5),
        'ffn2_norm': gain((L, D)),
        'ffn2_w_in': nrm((L, D, 2 * FFN_DIM), D ** -0.5),
        'ffn2_w_out': nrm((L, FFN_DIM, D), FFN_DIM ** -0.5),
    }

def second_block(x, mem, positions, ffn1_norm, ffn1_w_in, ffn1_w_out, mix_norm, mix_w_in, mix_w_out,
              fox_f_bias, fox_q_gain, fox_k_gain, moba_q_gain, moba_k_gain,
              rwkv_mu, rwkv_w0, rwkv_w2, rwkv_a0, rwkv_a2, rwkv_g2, rwkv_k_k, rwkv_k_a, rwkv_r_k,
              rwkv_ln_w, rwkv_ln_b, xattn_norm, xattn_mem_norm, xattn_w_q, xattn_w_kv,
              xattn_q_gain, xattn_k_gain, xattn_w_out, ffn2_norm, ffn2_w_in, ffn2_w_out):
    cos, sin = rope_tables(positions)
    for l in range(DEPTH):
        x = x + 0.5 * swiglu_2(rms_norm_2(x, ffn1_norm[l]), ffn1_w_in[l], ffn1_w_out[l]).astype(x.dtype)
        z = rms_norm_2(x, mix_norm[l]) @ mix_w_in[l]
        z_fox, z_moba, z_rwkv = jnp.split(z, [FOX_IN, FOX_IN + MOBA_IN], axis=-1)
        y_fox = fox_mixer(z_fox, fox_f_bias[l], fox_q_gain[l], fox_k_gain[l])
        y_rwkv = rwkv7_mixer(z_rwkv, rwkv_mu[l], rwkv_w0[l], rwkv_w2[l], rwkv_a0[l], rwkv_a2[l],
                             rwkv_g2[l], rwkv_k_k[l], rwkv_k_a[l], rwkv_r_k[l], rwkv_ln_w[l], rwkv_ln_b[l])
        y_moba = moba_mixer(z_moba, cos, sin, moba_q_gain[l], moba_k_gain[l])
        y = jnp.concatenate([y_fox, y_rwkv, y_moba], axis=-1) @ mix_w_out[l]
        x = x + y.astype(x.dtype)
        x = x + memory_cross_attention(rms_norm_2(x, xattn_norm[l]), rms_norm_2(mem, xattn_mem_norm[l]),
                                       xattn_w_q[l], xattn_w_kv[l], xattn_q_gain[l], xattn_k_gain[l],
                                       xattn_w_out[l]).astype(x.dtype)
        x = x + 0.5 * swiglu_2(rms_norm_2(x, ffn2_norm[l]), ffn2_w_in[l], ffn2_w_out[l]).astype(x.dtype)
    return x


def setup_inputs(seed=0):
    out = dict(first_inputs(seed))
    for name, value in second_inputs(seed + 1).items():
        if name != "x":
            out[name + "_2"] = value
    return out


def reference(
    x, norm_mix, norm_ffn, hy_w_in, hy_q_gain, hy_k_gain, hy_sinks, hy_conv_w, hy_w_out,
    rg_w_in, rg_conv_w, rg_conv_b, rg_gate_a_w, rg_gate_a_b, rg_gate_x_w, rg_gate_x_b,
    rg_lambda, rg_w_out, ffn_w_gate, ffn_w_up, ffn_w_down, moe_router, moe_w_gate, moe_w_up,
    moe_w_down, mem_2, positions_2, ffn1_norm_2, ffn1_w_in_2, ffn1_w_out_2, mix_norm_2,
    mix_w_in_2, mix_w_out_2, fox_f_bias_2, fox_q_gain_2, fox_k_gain_2, moba_q_gain_2,
    moba_k_gain_2, rwkv_mu_2, rwkv_w0_2, rwkv_w2_2, rwkv_a0_2, rwkv_a2_2, rwkv_g2_2, rwkv_k_k_2,
    rwkv_k_a_2, rwkv_r_k_2, rwkv_ln_w_2, rwkv_ln_b_2, xattn_norm_2, xattn_mem_norm_2,
    xattn_w_q_2, xattn_w_kv_2, xattn_q_gain_2, xattn_k_gain_2, xattn_w_out_2, ffn2_norm_2,
    ffn2_w_in_2, ffn2_w_out_2,
):
    x = first_block(
        x, norm_mix, norm_ffn, hy_w_in, hy_q_gain, hy_k_gain, hy_sinks, hy_conv_w, hy_w_out,
        rg_w_in, rg_conv_w, rg_conv_b, rg_gate_a_w, rg_gate_a_b, rg_gate_x_w, rg_gate_x_b,
        rg_lambda, rg_w_out, ffn_w_gate, ffn_w_up, ffn_w_down, moe_router, moe_w_gate, moe_w_up,
        moe_w_down,
    )
    return second_block(
        x, mem_2, positions_2, ffn1_norm_2, ffn1_w_in_2, ffn1_w_out_2, mix_norm_2, mix_w_in_2,
        mix_w_out_2, fox_f_bias_2, fox_q_gain_2, fox_k_gain_2, moba_q_gain_2, moba_k_gain_2,
        rwkv_mu_2, rwkv_w0_2, rwkv_w2_2, rwkv_a0_2, rwkv_a2_2, rwkv_g2_2, rwkv_k_k_2,
        rwkv_k_a_2, rwkv_r_k_2, rwkv_ln_w_2, rwkv_ln_b_2, xattn_norm_2, xattn_mem_norm_2,
        xattn_w_q_2, xattn_w_kv_2, xattn_q_gain_2, xattn_k_gain_2, xattn_w_out_2, ffn2_norm_2,
        ffn2_w_in_2, ffn2_w_out_2,
    )


_drawn_inputs = setup_inputs


def setup_inputs(seed=0):
    import zlib

    import numpy as np

    out = dict(_drawn_inputs(seed))
    spreads = {}
    factors = {'hy_q_gain': 6.197,
     'hy_k_gain': 3.004,
     'rg_gate_a_b': 6.388,
     'rg_gate_x_b': 8.0,
     'ffn1_norm_2': 4.118,
     'mix_norm_2': 2.913,
     'fox_q_gain_2': 8.0,
     'fox_k_gain_2': 8.0,
     'moba_q_gain_2': 8.0,
     'moba_k_gain_2': 8.0,
     'rwkv_k_k_2': 7.026,
     'rwkv_ln_w_2': 6.002,
     'rwkv_ln_b_2': 5.882,
     'xattn_norm_2': 8.0,
     'xattn_mem_norm_2': 8.0,
     'xattn_q_gain_2': 8.0,
     'xattn_k_gain_2': 8.0,
     'ffn2_norm_2': 5.72}
    for name, (base, spread) in spreads.items():
        noise = np.random.default_rng([zlib.crc32(name.encode()), seed]).standard_normal(out[name].shape)
        drawn = base * np.exp(spread * noise) if base else spread * noise
        out[name] = __import__('jax').numpy.asarray(drawn.astype(out[name].dtype))
    for name, factor in factors.items():
        out[name] = (out[name] * factor).astype(out[name].dtype)
    return out
```

```python
from contextlib import ExitStack, contextmanager

import concourse.bass as bass
from concourse import mybir

F32 = mybir.dt.float32
I32 = mybir.dt.int32
U32 = mybir.dt.uint32
ALU = mybir.AluOpType
ACT = mybir.ActivationFunctionType
AX = mybir.AxisListType

P = 128
D = 1024
DC = D // P
S = 256
TT = S // P
HALF = 512
BIG = 1e30
EPS = 1e-6
GN_EPS = 64e-5
NSLOT = 6
CH = 256
D_FF = 3584
FFN_DIM = 2816
N_EXP = 8
CAP = 128
HD = 64
RW = 64
NRW = S // RW
LEVELS = (1, 2, 4, 8, 16, 32)
DEPTH2 = 2


class Turns:

    def __init__(self, eng, sem):
        self.eng, self.sem = eng, sem
        self.n, self.loops = {}, []

    def now(self, name):
        v = self.n[name]
        for i, per in self.loops:
            if per.get(name):
                v = i * per[name] + v
        return v

    def next(self, name, count=1):
        self.n[name] = self.n.get(name, 0) + count
        return self.now(name)

    def mark(self, name):
        self.n[name] = self.n.get(name, 0) + 1
        return 1

    @contextmanager
    def loop(self, n, per):
        with self.eng.Fori(0, n) as i:
            start = dict(self.n)
            self.loops.append((i, per))
            yield i
            self.loops.pop()
        got = {k: v - start.get(k, 0) for k, v in self.n.items() if v != start.get(k, 0)}
        assert got == {k: v for k, v in per.items() if v}, got
        for k, v in got.items():
            self.n[k] = start.get(k, 0) + n * v


class Slots:

    def __init__(self):
        self.at, self.used = 0, set()

    def next(self):
        s = self.at % NSLOT
        self.at += 1
        return s

def seq(*sizes):
    out, at = [], 0
    for n in sizes:
        out.append((at, at + n))
        at += n
    return out


V1 = dict(zip(
    ("mix", "ffn", "rconv", "rconvb", "gab", "gxb", "lam", "hconv", "qg", "kg"),
    seq(2 * DC, 2 * DC, 4 * DC, DC, DC, DC, DC, 12, 1, 1)))
N1 = V1["kg"][1]
V2 = dict(zip(
    ("ffn1", "mix", "xat", "mem", "ffn2", "w0", "a0", "k_k", "k_a", "r_k", "ln_w", "ln_b", "mu",
     "fqg", "fkg", "mqg", "mkg", "xqg", "xkg", "fb"),
    seq(DC, DC, DC, DC, DC, 4, 4, 4, 4, 4, 4, 4, 15, 1, 1, 1, 1, 1, 1, 1)))
N2 = V2["fb"][1]

FOX_IN, MOBA_IN = 772, 768
RW0 = FOX_IN + MOBA_IN
MIX0_LOADS = [(k * CH, CH) for k in range(9)]
MIX1_LOADS = [(k * CH, CH) for k in range(8)]
MIX2_LOADS = ([(0, CH), (CH, CH), (2 * CH, CH), (3 * CH, 4)]
              + [(FOX_IN + k * CH, CH) for k in range(3)]
              + [(RW0 + k * CH, CH) for k in range(7)] + [(RW0 + 7 * CH, 32)])
XKV_LOADS = [(k * CH, CH) for k in range(4)]
XQ_LOADS = [(k * CH, CH) for k in range(2)]
SKIP2 = 2


SEMAPHORES = (
    "x_loaded", "out_stored",
    "hT_psum_act", "hT_psum_dve", "proj_psum", "out_psum", "scores_psum", "probsT_psum", "attn_psum",
    "sumsq_psum", "cols_psum", "gates_psum", "logits_psum", "ranks_psum", "rope_psum", "lora_psum",
    "bonus_psum", "tokens_psum", "gram_psum", "akv_psum", "inv_a_psum", "inv_x_psum", "inv_y_psum",
    "removal_psum", "state_psum", "y_psum", "yT_psum", "ffn_psum", "carry_psum", "carry_y_psum",
    "rows_loaded", "sinks_loaded", "pos_loaded", "router_loaded", "mem_loaded", "act_done", "rms_ready", "hT_act",
    "proj_copied", "root_ready", "squares_ready", "exp_ready", "probsT_ready", "attn_copied", "rope_tables",
    "lam_exp", "xc_started", "tanh_ready", "decay_ready", "mult_ready", "gate_exp", "forget_exp",
    "lora_ready", "decays_ready", "tokens_copied", "akv_ready", "inv_x_ready", "carry_y_ready",
    "removal_ready", "y_root", "yT_ready",
    "dve_done", "xn_ready", "hT_dve", "qk_ready", "maxima_ready", "probs_ready", "x_ready", "cols_ready",
    "angles_ready", "lam_abs", "conv_ready", "xc_ready", "log_a_ready", "mult_sq_ready", "lru_ready",
    "tail_shifted", "top_ready", "chosen_ready", "ranks_ready", "count_ready", "forget_abs", "rope_ready", "forget_ready",
    "sums_ready", "removal_keys", "sumsq_read", "bonus_in", "tokens_in", "gram_in", "bonus_ready",
    "gram_ready", "inv_ready", "removal_in", "state_ready", "y_var", "y_normed", "rwkv_ready", "out_ready",
    "rows_zeroed", "pool_done", "eps_ready", "consts_ready",
)
PASS_SEMAPHORES = tuple(f"slot{s}_{what}" for s in range(NSLOT) for what in ("full", "free")) + (
    "gate_up_psum", "hidden_ready", "silu_ready", "sel_ready", "selT_psum", "selT_ready", "chosen_h_psum",
    "chosen_h_ready", "expert_ffn_psum", "expert_out", "expert_psum", "expert_added")


ROW_DMAS = 8 + 4 + DEPTH2 * 25
LAYER_SP = {
    "slot0_free": 15, "slot1_free": 15, "slot2_free": 16, "slot3_free": 16, "slot4_free": 16,
    "slot5_free": 16}
LAYER_PE = {
    "xn_ready": 10, "hT_act": 10, "hT_dve": 10, "slot0_full": 240, "slot1_full": 240, "slot2_full":
    304, "proj_copied": 33, "slot3_full": 256, "slot4_full": 256, "slot5_full": 256,
    "squares_ready": 10, "qk_ready": 8, "probs_ready": 12, "probsT_ready": 12, "attn_copied": 12,
    "hidden_ready": 44, "forget_ready": 1, "rope_ready": 2, "lora_ready": 1, "bonus_in": 2,
    "tokens_in": 3, "sumsq_read": 2, "tokens_copied": 6, "gram_in": 1, "bonus_ready": 1,
    "gram_ready": 16, "inv_ready": 24, "inv_x_ready": 20, "akv_ready": 2, "removal_ready": 4,
    "state_ready": 3, "removal_in": 3, "y_normed": 2, "rwkv_ready": 1}
LAYER_ACT = {
    "act_done": 10, "hT_psum_act": 10, "proj_psum": 21, "proj_copied": 33, "sumsq_psum": 10,
    "qk_ready": 8, "maxima_ready": 12, "probsT_psum": 12, "attn_psum": 12, "x_ready": 4,
    "gate_up_psum": 44, "forget_abs": 1, "tail_shifted": 1, "lora_psum": 12, "removal_keys": 1,
    "sums_ready": 1, "tokens_psum": 6, "akv_psum": 2, "inv_x_psum": 20, "removal_psum": 4,
    "carry_y_psum": 3, "y_var": 2, "yT_psum": 2}
LAYER_DVE = {
    "dve_done": 87, "rms_ready": 5, "hT_psum_dve": 10, "proj_copied": 33, "root_ready": 10,
    "scores_psum": 12, "exp_ready": 12, "out_psum": 2, "silu_ready": 44, "ffn_psum": 2, "rope_psum":
    2, "forget_exp": 1, "tail_shifted": 1, "tokens_in": 3, "sumsq_read": 2, "decays_ready": 4,
    "bonus_psum": 2, "gram_psum": 16, "inv_a_psum": 4, "inv_y_psum": 20, "state_psum": 3,
    "carry_psum": 3, "akv_ready": 2, "y_psum": 2, "carry_y_ready": 3, "y_root": 2, "yT_ready": 2}


def run_layers(w, layer, per):
    if per is None:
        for l in range(DEPTH2):
            layer(l)
        return
    with w.loop(DEPTH2, per) as l:
        layer(l)


def build(nc, A, out):
    ctx = ExitStack()

    def sb(name, shape, dt=F32):
        return ctx.enter_context(nc.sbuf_tensor(name, shape, dt))

    with ctx:
        sem = {name: ctx.enter_context(nc.semaphore(name)) for name in SEMAPHORES + PASS_SEMAPHORES}
        sem_over = {name: ctx.enter_context(nc.semaphore(name + "_over")) for name in PASS_SEMAPHORES + ("dve_done",)}

        banks = ctx.enter_context(nc.psum_tensor("banks", [P, 8, HALF], F32))
        gu = [banks[:, i, :] for i in range(2)]
        tr = [banks[:, 2 + i, :] for i in range(2)]
        acc = [banks[:, 4 + i, :] for i in range(4)]
        sbank = [banks[:, 0:2, :], banks[:, 6:8, :]]

        ring = sb("ring", [P, NSLOT, DC * CH])
        x = sb("x", [P, TT, D])
        xn = sb("xn", [P, TT, D])
        hT = sb("hT", [P, DC, S])
        mixT = sb("mixT", [P, DC, S])
        hid = sb("hid", [P, 2, S])
        sg = sb("sg", [P, 2, S])
        sc = sb("sc", [P, 2, 2, S])
        pT = sb("pT", [P, 2, 2, S])
        negmx = sb("negmx", [P, 2, 2])
        rsum = sb("rsum", [P, 2, 2])
        snk = sb("snk", [P, 2, 2])
        ident = sb("ident", [P, P])
        blk64 = sb("blk64", [P, P])
        ones = sb("ones", [P, P])
        upper = sb("upper", [P, P])
        iota_s = sb("iota_s", [P, P])
        cmask = sb("cmask", [P, S])
        awin = sb("awin", [P, S])
        rmask = sb("rmask", [P, 4, P])
        lvl = sb("lvl", [P, 2, len(LEVELS), P], mybir.dt.uint8)
        sel4 = sb("sel4", [P, 4, P])
        rope = sb("rope", [P, P])
        cosT = sb("cosT", [P, S])
        sinT = sb("sinT", [P, S])
        frow = sb("frow", [1, P])
        fcol = sb("fcol", [P, 1])
        epsc = sb("epsc", [P, 4])
        keep = sb("keep", [P, 4 * S], mybir.dt.bfloat16)
        pv1 = sb("pv1", [P, N1])
        pv2 = sb("pv2", [P, DEPTH2, N2])
        pv = sb("pv", [P, N2])
        sinks = sb("sinks", [P, 16])
        ss = sb("ss", [P, 2, 2])
        rt = sb("rt", [P, DC, N_EXP])
        lg = sb("lg", [P, TT, N_EXP])
        top = sb("top", [P, TT, 8])
        topi = sb("topi", [P, TT, 8], U32)
        topf = sb("topf", [P, TT, 8])
        gt = sb("gt", [P, TT, 4])
        hot = sb("hot", [P, 2, TT, N_EXP])
        route = sb("route", [P, 3, TT, N_EXP])
        cur = sb("cur", [P, 3, TT])
        cnt_f = sb("cnt_f", [P, 2])
        took = sb("took", [P, 24])
        cnt = sb("cnt", [P, 1], I32)
        lamb = sb("lamb", [P, 5, DC])
        gnst = sb("gnst", [P, 4, 8])
        mem = sb("mem", [P, TT, D])
        arena = sb("arena", [P, 22528])

        def region(at, *shape, dt=None):
            n = 1
            for k in shape:
                n *= k
            v = arena[:, at:at + n]
            if dt is not None:
                v = v.bitcast(dt)
            if len(shape) == 2:
                return v.rearrange("p (a b) -> p a b", a=shape[0])
            if len(shape) == 3:
                return v.rearrange("p (a b c) -> p a b c", a=shape[0], b=shape[1])
            if len(shape) == 4:
                return v.rearrange("p (a b c d) -> p a b c d", a=shape[0], b=shape[1], c=shape[2])
            return v

        rows = region(0, 3, P)
        part_i, col_i = region(512, P, dt=I32), region(640, P, dt=I32)
        lv_a, lv_b, lv_c = (region(768 + P * i, P, dt=I32) for i in range(3))
        awin_i = region(1280, S, dt=I32)
        pos_i = region(1536, S, dt=I32)
        ang = region(1792, 4, S)
        z0 = region(0, 19, S)
        gcu = region(19 * S, 4, S + 2)
        cv = region(19 * S + 4 * (S + 2), 4, S)
        g_y, g_x, g_xc = region(0, DC, S), region(2048, DC, S + 3), region(4128, DC, S)
        g_r, g_i, g_t = region(6176, DC, S), region(8224, DC, S), region(10272, DC, S)
        g_m = region(12320, DC, S)
        sel, selg, selT = region(0, TT, P), region(256, TT, P), region(512, TT, P)
        hTe, ye = region(1024, DC, P), region(2048, D)
        rg, bon = region(0, 4, S), region(1024, 4, S)
        Bh, Kh, AR = region(2048, 4, S), region(3072, 4, S), region(4096, 4, TT, 2, P)
        Bt, Kt, Vt = (region(6144 + 1024 * i, TT, HALF) for i in range(3))
        q2, v2 = region(4096, 8, S), region(6144, 2, TT, S)
        zf, fsc = region(7168, S), region(7424, 6, S)
        zr, zd = region(9216, 15, S + 1), region(13072, 4, S)
        lw, ra, kk = (region(14096 + 1024 * i, 4, S) for i in range(3))
        cw, ew, et = (region(17168 + 1024 * i, 4, S) for i in range(3))
        Bb, Kb = region(20240, 4, S), region(21264, 4, S)
        ep, ei = lw, zd
        G = arena[:, 9216:17408].rearrange("p (t h k s) -> p t h k s", t=TT, h=8, k=4)
        Xb = region(17408, 2, HALF)
        SA, AkV, yS = (region(18432 + 1024 * i, TT, HALF) for i in range(3))
        Sbd, sdec = region(21504, 4, P), region(22016, 4, P)
        Tm = xn[:, :, :].rearrange("p t (u s) -> p (t u) s", s=P)
        Um = hT[:, :, :].rearrange("p c (u s) -> p (c u) s", s=P)
        xk, xv, xq = region(2048, 4, S), region(3072, TT, HALF), region(4096, 4, S)

        sqb = [sc[:, i, :, :].rearrange("p a b -> p (a b)") for i in range(2)]
        rtb = [pT[:, i, :, :].rearrange("p a b -> p (a b)") for i in range(2)]

        def col(name, i=0):
            return pv1[:, V1[name][0] + i:V1[name][0] + i + 1]

        def col2(name, i=0):
            return pv[:, V2[name][0] + i:V2[name][0] + i + 1]

        def wcols(s, w):
            return ring[:, s, 0:DC * w].rearrange("p (c n) -> p c n", c=DC)

        def wrows(s):
            return ring[:, s, :].rearrange("p (k n) -> p k n", k=2)

        def units_mix0():
            return [dict(q=[z0[64 * h:64 * h + 64, hp, t * P:t * P + P] for h in range(2)],
                         k=[z0[64 * h:64 * h + 64, 4 + hp // 2, 0:P * (t + 1)] for h in range(2)],
                         nk=P * (t + 1),
                         slope=[2.0 ** -(2 * hp + h + 1) for h in range(2)], t=t,
                         sink=2 * hp,
                         v=[[z0[:, 6, kt * P + 64 * (hp // 2):kt * P + 64 * (hp // 2) + 64]
                             for kt in range(t + 1)] for h in range(2)],
                         dst=mixT[:, hp, t * P:t * P + P], wide=False)
                    for t in range(TT) for hp in range(4)]

        def units_causal(m):
            return [dict(q=[q2[64 * h:64 * h + 64, 4 * m + hp, t * P:t * P + P] for h in range(2)],
                         k=[q2[64 * h:64 * h + 64, 4 * m + 2 + hp, 0:P * (t + 1)] for h in range(2)],
                         nk=P * (t + 1), t=t, causal=True,
                         forget=[2 * hp + h for h in range(2)] if m == 0 else None,
                         v=[[v2[:, m, kt, (2 * hp + h) * 64:(2 * hp + h) * 64 + 64]
                             for kt in range(t + 1)] for h in range(2)],
                         dst=mixT[:, (0 if m == 0 else 6) + hp, t * P:t * P + P], wide=False)
                    for t in range(TT) for hp in range(2)]

        def units_mem():
            return [dict(q=[xq[:, 2 * hp + h, t * P:t * P + P] for h in range(2)],
                         k=[xk[:, 2 * hp + h, :] for h in range(2)], nk=S, t=t,
                         v=[[xv[:, kt, (2 * hp + h) * P:(2 * hp + h) * P + P]
                             for kt in range(TT)] for h in range(2)],
                         dst=mixT[:, 2 * hp:2 * hp + 2, t * P:t * P + P], wide=True)
                    for t in range(TT) for hp in range(2)]

        block = ctx.enter_context(nc.Block())

        @block.sync
        def _(sp):
            w = Turns(sp, sem)
            slots = Slots()

            def load(parts, w=w, slots=slots):
                s = slots.next()
                if s in slots.used:
                    sp.wait_ge(w.sem[f"slot{s}_free"], w.next(f"slot{s}_free"))
                slots.used.add(s)
                for dst, src in parts(s):
                    sp.dma_start(dst, src).then_inc(w.sem[f"slot{s}_full"], 16)

            def load_cols(W, l, c0, n, w=w, slots=slots):
                load(lambda s: [(wcols(s, n), W[bass.ds(l, 1), :, bass.ds(c0, n)].rearrange(
                    "o (c p) n -> p (o c) n", p=P))], w, slots)

            def load_rows(W, l, r0, w=w, slots=slots):
                load(lambda s: [(wrows(s), W[bass.ds(l, 1), bass.ds(r0, 2 * P), :].rearrange(
                    "o (k p) n -> p (o k) n", p=P))], w, slots)

            def load_chunk(Wg, Wu, up0, Wd, l, k, w=w, slots=slots):
                load_cols(Wg, l, k * CH, CH, w, slots)
                load_cols(Wu, l, k * CH + up0, CH, w, slots)
                load_rows(Wd, l, k * CH, w, slots)

            def load_ffn(Wg, Wu, up0, Wd, l, n, w=w, slots=slots):
                if n % 2:
                    load_chunk(Wg, Wu, up0, Wd, l, 0, w, slots)
                with w.loop(n // 2, {f"slot{s}_free": 1 for s in range(NSLOT)}) as i:
                    for j in range(2):
                        load_chunk(Wg, Wu, up0, Wd, l, i * 2 + (n % 2 + j), w, slots)

            def load_experts(w, slots):
                one = {n: A[n][0] for n in ("moe_w_gate", "moe_w_up", "moe_w_down")}
                with w.loop(N_EXP, {f"slot{s}_free": 7 for s in range(NSLOT)}) as e:
                    load_ffn(one["moe_w_gate"], one["moe_w_up"], 0, one["moe_w_down"], e, D_FF // CH,
                             w, slots)

            sp.dma_start(x[:, :, :], A["x"][0].rearrange("(t p) d -> p t d", p=P)).then_inc(sem["x_loaded"], 16)
            for c0, n in MIX0_LOADS:
                load_cols(A["hy_w_in"], 0, c0, n)
            for k in range(4):
                load_rows(A["hy_w_out"], 0, k * CH)
            load_ffn(A["ffn_w_gate"], A["ffn_w_up"], 0, A["ffn_w_down"], 0, D_FF // CH)
            for c0, n in MIX1_LOADS:
                load_cols(A["rg_w_in"], 0, c0, n)
            load(lambda s: [(ring[:, s, g * D:g * D + D].rearrange("p (h j) -> p h j", h=DC),
                             A[n][0].rearrange("h i j -> i h j"))
                            for g, n in enumerate(("rg_gate_a_w", "rg_gate_x_w"))])
            for k in range(4):
                load_rows(A["rg_w_out"], 0, k * CH)
            load_experts(w, slots)
            sp.wait_ge(sem["count_ready"], 1)
            n_max = sp.value_load(cnt[0:1, 0:1], min_val=0, max_val=S)
            with sp.If(n_max > CAP):
                w_over = Turns(sp, sem_over)
                over = Slots()
                over.used = set(range(NSLOT))
                for s in range(NSLOT):
                    sp.wait_ge(sem[f"slot{s}_free"], w.n[f"slot{s}_free"] + 1)
                    sp.sem_inc(w_over.sem[f"slot{s}_free"], 1)
                load_experts(w_over, over)
                for s in range(NSLOT):
                    sp.wait_ge(w_over.sem[f"slot{s}_free"], w_over.next(f"slot{s}_free"))

            def layer(l):
                load_ffn(A["ffn1_w_in_2"], A["ffn1_w_in_2"], FFN_DIM, A["ffn1_w_out_2"], l, FFN_DIM // CH)
                for c0, n in MIX2_LOADS:
                    load_cols(A["mix_w_in_2"], l, c0, n)
                load(lambda s: [
                    (ring[0:64, s, 0:HALF], A["rwkv_w2_2"][bass.ds(l, 1), :, :].rearrange("o k n -> (o k) n")),
                    (ring[64:P, s, 0:HALF], A["rwkv_a2_2"][bass.ds(l, 1), :, :].rearrange("o k n -> (o k) n")),
                    (ring[:, s, HALF:D], A["rwkv_g2_2"][bass.ds(l, 1), 0:P, :].rearrange("o k n -> (o k) n")),
                    (ring[0:32, s, D:D + HALF],
                     A["rwkv_g2_2"][bass.ds(l, 1), P:P + 32, :].rearrange("o k n -> (o k) n"))])
                for k in range(4):
                    load_rows(A["mix_w_out_2"], l, k * CH)
                for c0, n in XKV_LOADS:
                    load_cols(A["xattn_w_kv_2"], l, c0, n)
                for c0, n in XQ_LOADS:
                    load_cols(A["xattn_w_q_2"], l, c0, n)
                for k in range(2):
                    load_rows(A["xattn_w_out_2"], l, k * CH)
                load_ffn(A["ffn2_w_in_2"], A["ffn2_w_in_2"], FFN_DIM, A["ffn2_w_out_2"], l, FFN_DIM // CH)
                slots.at += SKIP2

            run_layers(w, layer, LAYER_SP)
            sp.wait_ge(sem["out_ready"], 1)
            sp.dma_start(out[0].rearrange("(t p) d -> p t d", p=P), x[:, :, :]).then_inc(sem["out_stored"], 16)
            sp.wait_ge(sem["out_stored"], 16)

        @block.tensor
        def _(pe):
            w = Turns(pe, sem)
            slots = Slots()
            mm = nc.tensor.matmul

            def take(ndma=1, w=w, slots=slots):
                s = slots.next()
                pe.wait_ge(w.sem[f"slot{s}_full"], w.next(f"slot{s}_full", 16 * ndma))
                return s

            def turn(dst, src):
                return nc.tensor.transpose(dst, src, ident[0:src.shape[0], 0:src.shape[0]])

            def transpose_h():
                pe.wait_ge(sem["xn_ready"], w.next("xn_ready", TT))
                for cp in range(DC // 2):
                    if cp == 2:
                        pe.wait_ge(sem["hT_act"], w.next("hT_act"))
                    if cp == 3:
                        pe.wait_ge(sem["hT_dve"], w.next("hT_dve"))
                    for i in range(2):
                        for t in range(TT):
                            c = 2 * cp + i
                            ins = turn(tr[cp % 2][:, i * S + t * P:i * S + t * P + P],
                                       xn[:, t, c * P:c * P + P])
                    ins.then_inc(sem["hT_psum_act" if cp % 2 == 0 else "hT_psum_dve"], 1)
                pe.wait_ge(sem["hT_act"], w.next("hT_act"))
                pe.wait_ge(sem["hT_dve"], w.next("hT_dve"))

            fills = [0]

            def begin_fill():
                n = fills[0]
                fills[0] += 1
                if n >= 2:
                    pe.wait_ge(sem["proj_copied"], w.next("proj_copied"))
                return gu[n % 2]

            def end_fills():
                pe.wait_ge(sem["proj_copied"], w.next("proj_copied", min(2, fills[0])))
                fills[0] = 0

            def tiles_out(s, width, tiles):
                b = begin_fill()
                wv = wcols(s, width)
                for co, m, oc, po in tiles:
                    for c in range(DC):
                        ins = mm(b[po:po + m, oc:oc + S], wv[:, c, co:co + m], hT[:, c, :],
                                 start=(c == 0), stop=(c == DC - 1))
                ins.then_inc(sem["proj_psum"], 1)

            def tokens_out(s, width, co, n):
                b = begin_fill()
                wv = wcols(s, width)
                for t in range(TT):
                    for c in range(DC):
                        ins = mm(b[:, t * n:t * n + n], hT[:, c, t * P:t * P + P], wv[:, c, co:co + n],
                                 start=(c == 0), stop=(c == DC - 1))
                ins.then_inc(sem["proj_psum"], 1)

            def two_tiles(width=CH):
                s = take()
                tiles_out(s, width, [(0, P, 0, 0), (P, P, S, 0)])

            def out_proj(nslots):
                for k in range(nslots):
                    s = take()
                    wv = wrows(s)
                    for j in range(2):
                        c = 2 * k + j
                        for t in range(TT):
                            for h in range(2):
                                ins = mm(acc[2 * t + h][:, :], mixT[:, c, t * P:t * P + P],
                                         wv[:, j, h * HALF:h * HALF + HALF],
                                         start=(c == 0), stop=(c == 2 * nslots - 1))
                    ins.then_inc(sem["out_psum" if k == nslots - 1 else f"slot{s}_free"], 1)

            def ffn(n, rhs, nt, done="ffn_psum", w=w, slots=slots):
                N = nt * P
                base = slots.at
                slots.at += 3 * n

                def slot(k, j):
                    return (base + 3 * k + j) % NSLOT

                def gate_up(k, f):
                    g, u = slot(k, 0), slot(k, 1)
                    if f == 0:
                        pe.wait_ge(w.sem[f"slot{g}_full"], w.next(f"slot{g}_full", 16))
                        pe.wait_ge(w.sem[f"slot{u}_full"], w.next(f"slot{u}_full", 16))
                    for c in range(DC):
                        ins = mm(gu[f][:, 0:N], wcols(g, CH)[:, c, f * P:f * P + P], rhs[:, c, :],
                                 start=(c == 0), stop=(c == DC - 1))
                    if f == 1:
                        ins.then_inc(w.sem[f"slot{g}_free"], 1)
                    for c in range(DC):
                        ins = mm(gu[f][:, S:S + N], wcols(u, CH)[:, c, f * P:f * P + P], rhs[:, c, :],
                                 start=(c == 0), stop=(c == DC - 1))
                    ins.then_inc(w.sem["gate_up_psum"], 1)

                def down(k, f, first=False, last=False):
                    u, d = slot(k, 1), slot(k, 2)
                    if f == 0:
                        pe.wait_ge(w.sem[f"slot{d}_full"], w.next(f"slot{d}_full", 16))
                    pe.wait_ge(w.sem["hidden_ready"], w.next("hidden_ready"))
                    for i in range(2 * nt):
                        t, h = i // 2, i % 2
                        ins = mm(acc[i][:, :], hid[:, f, t * P:t * P + P],
                                 wrows(d)[:, f, h * HALF:h * HALF + HALF], start=first, stop=last)
                        if f == 0 and i == 0:
                            ins.then_inc(w.sem[f"slot{u}_free"], 1)
                    if f == 1:
                        ins.then_inc(w.sem[done if last else f"slot{d}_free"], 1)

                def step(k):
                    gate_up(k, 0)
                    down(k - 1, 1)
                    gate_up(k, 1)
                    down(k, 0)

                gate_up(0, 0)
                gate_up(0, 1)
                down(0, 0, first=True)
                loops = (n - 1) // 2
                per = {f"slot{s}_full": 16 for s in range(NSLOT)} | {"hidden_ready": 4}
                with w.loop(loops, per):
                    step(1)
                    step(2)
                if n % 2 == 0:
                    step(n - 1)
                down(n - 1, 1, last=True)

            def attention(units):
                n = len(units)
                for i in range(n + 2):
                    if i < n:
                        u = units[i]
                        for h in range(2):
                            o = sbank[i % 2][:, h, 0:u["nk"]]
                            fg = u.get("forget")
                            ins = mm(o, u["q"][h], u["k"][h], start=True, stop=fg is None)
                            if fg is not None:
                                t0, nk, r = u["t"] * P, u["nk"], slice(64 * h, 64 * h + 4)
                                mm(o, fsc[r, 4, t0:t0 + P],
                                   sel4[r, fg[h]:fg[h] + 1, :].to_broadcast([4, nk // P, P]),
                                   start=False, stop=False)
                                ins = mm(o, sel4[r, fg[h], :], fsc[r, 5, 0:nk], start=False, stop=True)
                        ins.then_inc(sem["scores_psum"], 1)
                    if 1 <= i <= n:
                        u = units[i - 1]
                        pe.wait_ge(sem["probs_ready"], w.next("probs_ready"))
                        for h in range(2):
                            for kt in range(u["nk"] // P):
                                o = h * S + kt * P
                                ins = turn(tr[(i - 1) % 2][:, o:o + P],
                                           sc[:, (i - 1) % 2, h, kt * P:kt * P + P])
                        ins.then_inc(sem["probsT_psum"], 1)
                    if i >= 2:
                        u = units[i - 2]
                        pe.wait_ge(sem["probsT_ready"], w.next("probsT_ready"))
                        b = acc[i % 2]
                        for h in range(2):
                            o = b[:, h * P:h * P + P] if u["wide"] else b[64 * h:64 * h + 64, 0:P]
                            kts = u["nk"] // P
                            for kt in range(kts):
                                ins = mm(o, u["v"][h][kt], pT[:, i % 2, h, kt * P:kt * P + P],
                                         start=(kt == 0), stop=(kt == kts - 1))
                        ins.then_inc(sem["attn_psum"], 1)
                pe.wait_ge(sem["attn_copied"], w.next("attn_copied", n))

            def head_norms(n, block):
                for i in range(n):
                    pe.wait_ge(sem["squares_ready"], w.next("squares_ready"))
                    mm(tr[i % 2][:, :], block[:, :], sqb[i % 2], start=True,
                       stop=True).then_inc(sem["sumsq_psum"], 1)

            pe.wait_ge(sem["consts_ready"], w.next("consts_ready"))
            pe.wait_ge(sem["rows_loaded"], w.next("rows_loaded", 16 * ROW_DMAS))
            turn(tr[0][:, 0:N1], rows[0:N1, 0, :])
            for l in range(DEPTH2):
                turn(tr[0][:, P + l * N2:P + l * N2 + N2], rows[0:N2, 1 + l, :])
            ins = mm(tr[1][:, 0:1], frow[0:1, :], ones[0:1, 0:1], start=True, stop=True)
            ins.then_inc(sem["cols_psum"], 1)
            pe.wait_ge(sem["cols_ready"], w.next("cols_ready"))

            transpose_h()
            for k in range(9):
                if k == 2:
                    s = take()
                    tiles_out(s, CH, [(64 * g, 64, g * S, po) for g in range(2) for po in (0, 64)])
                    tokens_out(s, CH, P, P)
                else:
                    two_tiles()
            end_fills()
            head_norms(3, blk64)
            pe.wait_ge(sem["qk_ready"], w.next("qk_ready", 3))
            attention(units_mix0())
            pe.wait_ge(sem["conv_ready"], w.next("conv_ready"))
            out_proj(4)
            transpose_h()
            ffn(D_FF // CH, hT, TT)

            transpose_h()
            for k in range(8):
                two_tiles()
            end_fills()
            s = take(2)
            for h in range(DC):
                pe.wait_ge(sem["xc_ready"], w.next("xc_ready"))
                b = begin_fill()
                for g in range(2):
                    ins = mm(b[:, g * S:g * S + S], ring[:, s, g * D + h * P:g * D + h * P + P],
                             g_xc[:, h, :], start=True, stop=True)
                ins.then_inc(sem["gates_psum"], 1)
            end_fills()
            pe.wait_ge(sem["lru_ready"], w.next("lru_ready"))
            out_proj(4)

            transpose_h()
            pe.wait_ge(sem["router_loaded"], w.next("router_loaded", 16))
            for t in range(TT):
                for c in range(DC):
                    ins = mm(tr[0][:, t * N_EXP:t * N_EXP + N_EXP], hT[:, c, t * P:t * P + P],
                             rt[:, c, :], start=(c == 0), stop=(c == DC - 1))
            ins.then_inc(sem["logits_psum"], 1)
            pe.wait_ge(sem["chosen_ready"], w.next("chosen_ready"))
            for t in range(TT):
                for tt in range(t + 1):
                    mm(tr[1][:, t * N_EXP:t * N_EXP + N_EXP], (upper if tt == t else ones)[:, :],
                       route[:, 2, tt, :], start=(tt == 0), stop=(tt == t))
            for t in range(TT):
                ins = mm(tr[1][:, 32:32 + N_EXP], ones[:, :], route[:, 2, t, :],
                         start=(t == 0), stop=(t == TT - 1))
            ins.then_inc(sem["ranks_psum"], 1)

            def experts(w, slots):
                per = ({f"slot{s}_full": 16 * 7 for s in range(NSLOT)}
                       | {"hidden_ready": 28, "sel_ready": 1, "selT_ready": 1, "chosen_h_ready": 2,
                          "expert_out": 1, "expert_added": 1})
                with w.loop(N_EXP, per):
                    pe.wait_ge(w.sem["sel_ready"], w.next("sel_ready"))
                    for c in range(DC):
                        for t in range(TT):
                            ins = mm(tr[c // 4][:, (c % 4) * P:(c % 4) * P + P],
                                     xn[:, t, c * P:c * P + P], sel[:, t, :],
                                     start=(t == 0), stop=(t == TT - 1))
                        if c % 4 == 3:
                            ins.then_inc(w.sem["chosen_h_psum"], 1)
                    for t in range(TT):
                        ins = turn(acc[2][:, t * P:t * P + P], selg[:, t, :])
                    ins.then_inc(w.sem["selT_psum"], 1)
                    pe.wait_ge(w.sem["chosen_h_ready"], w.next("chosen_h_ready", 2))
                    ffn(D_FF // CH, hTe, 1, "expert_ffn_psum", w, slots)
                    pe.wait_ge(w.sem["selT_ready"], w.next("selT_ready"))
                    pe.wait_ge(w.sem["expert_out"], w.next("expert_out"))
                    for t in range(TT):
                        for h in range(2):
                            ins = mm((acc[2], acc[3], tr[0], tr[1])[2 * t + h][:, :], selT[:, t, :],
                                     ye[:, h * HALF:h * HALF + HALF], start=True, stop=True)
                    ins.then_inc(w.sem["expert_psum"], 1)
                    pe.wait_ge(w.sem["expert_added"], w.next("expert_added"))

            pe.wait_ge(sem["ranks_ready"], w.next("ranks_ready"))
            experts(w, slots)
            pe.wait_ge(sem["count_ready"], w.next("count_ready"))
            n_max = pe.value_load(cnt[0:1, 0:1], min_val=0, max_val=S)
            with pe.If(n_max > CAP):
                experts(Turns(pe, sem_over), Slots())

            def layer(l):
                transpose_h()
                ffn(FFN_DIM // CH, hT, TT)
                transpose_h()
                for m in range(2):
                    two_tiles()
                    two_tiles()
                    s = take()
                    tokens_out(s, CH, 0, CH)
                    if m == 0:
                        s = take()
                        tiles_out(s, 4, [(0, 4, 0, 0), (0, 4, 0, 64)])
                for k in range(7):
                    two_tiles()
                s = take()
                tiles_out(s, 32, [(0, 32, 0, 0)])
                end_fills()
                head_norms(4, blk64)
                pe.wait_ge(sem["qk_ready"], w.next("qk_ready", 4))
                for i in range(2):
                    for j in range(2):
                        ins = mm(gu[i][:, j * S:j * S + S], rope[:, :], q2[:, 4 + 2 * i + j, :],
                                 start=True, stop=True)
                    ins.then_inc(sem["rope_psum"], 1)
                pe.wait_ge(sem["forget_ready"], w.next("forget_ready"))
                pe.wait_ge(sem["rope_ready"], w.next("rope_ready", 2))
                attention(units_causal(0) + units_causal(1))
                rwkv()
                out_proj(4)
                transpose_h()
                for k in range(2):
                    two_tiles()
                for k in range(2):
                    s = take()
                    tokens_out(s, CH, 0, CH)
                transpose_h()
                for k in range(2):
                    two_tiles()
                end_fills()
                head_norms(4, ones)
                pe.wait_ge(sem["qk_ready"], w.next("qk_ready", 4))
                attention(units_mem())
                out_proj(2)
                transpose_h()
                ffn(FFN_DIM // CH, hT, TT)
                slots.at += SKIP2

            def rwkv():
                s = take(4)
                pe.wait_ge(sem["lora_ready"], w.next("lora_ready"))
                for j in range(3):
                    for p in range(4):
                        b = begin_fill()
                        cs = slice(p * P, p * P + P)
                        if j == 0:
                            ins = mm(b[:, 0:S], ring[0:64, s, cs], zr[0:64, 12, 1:S + 1], start=True, stop=True)
                        elif j == 1:
                            ins = mm(b[:, 0:S], ring[64:P, s, cs], zr[64:P, 12, 1:S + 1], start=True, stop=True)
                        else:
                            mm(b[:, 0:S], ring[:, s, HALF + p * P:HALF + p * P + P], zr[:, 13, 1:S + 1],
                               start=True, stop=False)
                            ins = mm(b[:, 0:S], ring[0:32, s, D + p * P:D + p * P + P],
                                     zr[0:32, 14, 1:S + 1], start=False, stop=True)
                        ins.then_inc(sem["lora_psum"], 1)
                end_fills()
                for i in range(2):
                    pe.wait_ge(sem["squares_ready"], w.next("squares_ready"))
                    mm(tr[i][:, :], blk64[:, :], sqb[i], start=True, stop=True).then_inc(sem["sumsq_psum"], 1)
                for i in range(2):
                    pe.wait_ge(sem["bonus_in"], w.next("bonus_in"))
                    mm(gu[i][:, :], blk64[:, :], rtb[i], start=True, stop=True).then_inc(sem["bonus_psum"], 1)
                for n, (src, off) in enumerate(((zr, 1), (Bb, 0), (Kb, 0))):
                    pe.wait_ge(sem["tokens_in"], w.next("tokens_in"))
                    for t in range(TT):
                        b = tr[t]
                        if n:
                            pe.wait_ge(sem["tokens_copied"], w.next("tokens_copied"))
                        else:
                            pe.wait_ge(sem["sumsq_read"], w.next("sumsq_read"))
                        for p in range(4):
                            v = src[:, 8 + p, off + t * P:off + t * P + P] if n == 0 else src[:, p, t * P:t * P + P]
                            ins = turn(b[:, p * P:p * P + P], v)
                        ins.then_inc(sem["tokens_psum"], 1)
                pe.wait_ge(sem["gram_in"], w.next("gram_in"))
                pe.wait_ge(sem["bonus_ready"], w.next("bonus_ready"))
                for u in range(2 * 8):
                    t, h = u // 8, u % 8
                    p, r = h // 2, slice(64 * (h % 2), 64 * (h % 2) + 64)
                    if u >= 2:
                        pe.wait_ge(sem["gram_ready"], w.next("gram_ready"))
                    b = gu[u % 2]
                    mm(b[:, 0:S], Bh[r, p, t * P:t * P + P], AR[r, p, t, :, :].rearrange("p a s -> p (a s)"),
                       start=True, stop=True)
                    mm(b[:, S:2 * S], Kh[r, p, t * P:t * P + P], AR[r, p, t, :, :].rearrange("p a s -> p (a s)"),
                       start=True, stop=True).then_inc(sem["gram_psum"], 1)
                pe.wait_ge(sem["gram_ready"], w.next("gram_ready", 2))
                pe.wait_ge(sem["tokens_copied"], w.next("tokens_copied", 2))
                for t in range(TT):
                    for h in range(8):
                        ins = mm(tr[t][:, h * 64:h * 64 + 64], G[:, t, h, 2, :], Vt[:, t, h * 64:h * 64 + 64],
                                 start=True, stop=True)
                    ins.then_inc(sem["akv_psum"], 1)
                for q in range(4):
                    if q >= 2:
                        pe.wait_ge(sem["inv_ready"], w.next("inv_ready"))
                    for j in range(4):
                        ins = mm(gu[q % 2][:, j * P:j * P + P], G[:, q // 2, 4 * (q % 2) + j, 0, :],
                                 ident[:, :], start=True, stop=True)
                    ins.then_inc(sem["inv_a_psum"], 1)
                steps = 4 * (len(LEVELS) - 1)
                for i in range(steps + 1):
                    if i < steps:
                        q = i % 4
                        if i < 2:
                            pe.wait_ge(sem["inv_ready"], w.next("inv_ready"))
                        for j in range(4):
                            ins = mm(gu[i % 2][:, j * P:j * P + P], G[:, q // 2, 4 * (q % 2) + j, 0, :],
                                     Tm[:, 4 * q + j, :], start=True, stop=True)
                        ins.then_inc(sem["inv_x_psum"], 1)
                    if i >= 1:
                        k = i - 1
                        q = k % 4
                        pe.wait_ge(sem["inv_x_ready"], w.next("inv_x_ready"))
                        if k >= 2:
                            pe.wait_ge(sem["inv_ready"], w.next("inv_ready"))
                        for j in range(4):
                            o = slice(j * P, j * P + P)
                            if k < steps - 4:
                                mm(tr[k % 2][:, o], Um[:, 4 * q + j, :], Xb[:, k % 2, o], start=True, stop=True)
                            ins = mm(acc[k % 2][:, o], Xb[:, k % 2, o], Um[:, 4 * q + j, :],
                                     start=True, stop=True)
                        ins.then_inc(sem["inv_y_psum"], 1)
                pe.wait_ge(sem["inv_ready"], w.next("inv_ready", 2))
                pe.wait_ge(sem["akv_ready"], w.next("akv_ready", TT))
                for c in range(NRW):
                    t, r = c // 2, slice(RW * (c % 2), RW * (c % 2) + RW)
                    if c:
                        pe.wait_ge(sem["state_ready"], w.next("state_ready"))
                        for k, name in enumerate(("carry_psum", "carry_y_psum")):
                            for p in range(4):
                                ins = mm(gu[k][:, p * P:p * P + P], AR[:, p, t, k, :], Sbd[:, p, :],
                                         start=True, stop=True)
                            ins.then_inc(sem[name], 1)
                        pe.wait_ge(sem["removal_in"], w.next("removal_in"))
                    for h in range(8):
                        ins = mm(tr[0][:, h * 64:h * 64 + 64], Um[:, 8 * t + h, :],
                                 AkV[:, t, h * 64:h * 64 + 64], start=True, stop=True)
                    ins.then_inc(sem["removal_psum"], 1)
                    pe.wait_ge(sem["removal_ready"], w.next("removal_ready"))
                    if c < NRW - 1:
                        for p in range(4):
                            o = slice(p * P, p * P + P)
                            mm(tr[1][:, o], Bt[r, t, o], SA[r, t, o], start=True, stop=False)
                            ins = mm(tr[1][:, o], Kt[r, t, o], Vt[r, t, o], start=False, stop=True)
                        ins.then_inc(sem["state_psum"], 1)
                    if c % 2:
                        for h in range(8):
                            o = slice(h * 64, h * 64 + 64)
                            mm(acc[t][:, o], G[:, t, h, 1, :], SA[:, t, o], start=True, stop=False)
                            ins = mm(acc[t][:, o], G[:, t, h, 3, :], Vt[:, t, o], start=False, stop=True)
                        ins.then_inc(sem["y_psum"], 1)
                for t in range(TT):
                    pe.wait_ge(sem["y_normed"], w.next("y_normed"))
                    for p in range(4):
                        ins = turn(acc[2 + t][:, p * P:p * P + P], yS[:, t, p * P:p * P + P])
                    ins.then_inc(sem["yT_psum"], 1)
                pe.wait_ge(sem["rwkv_ready"], w.next("rwkv_ready"))

            run_layers(w, layer, LAYER_PE)

        @block.scalar
        def _(act):
            w = Turns(act, sem)
            slots = Slots()
            f = nc.scalar.activation

            def load_rows_table(i, name, at, src, n, last=P):
                full = n if last == P else n - 1
                if full:
                    act.dma_start(rows[at:at + full, i, :], src[0:full * P].rearrange(
                        "(r k) -> r k", k=P)).then_inc(sem["rows_loaded"], 16)
                if last != P:
                    act.dma_start(rows[at + full:at + n, i, 0:last],
                                  src[full * P:full * P + last].rearrange("(r k) -> r k", r=1)
                                  ).then_inc(sem["rows_loaded"], 16)

            act.wait_ge(sem["rows_zeroed"], w.next("rows_zeroed"))
            flat1 = [("mix", A["norm_mix"].rearrange("l d -> (l d)"), 16),
                     ("ffn", A["norm_ffn"].rearrange("l d -> (l d)"), 16),
                     ("rconv", A["rg_conv_w"][0].rearrange("k d -> (k d)"), 32),
                     ("rconvb", A["rg_conv_b"][0], 8), ("gab", A["rg_gate_a_b"][0], 8),
                     ("gxb", A["rg_gate_x_b"][0], 8), ("lam", A["rg_lambda"][0], 8),
                     ("hconv", A["hy_conv_w"][0].rearrange("k d -> (k d)"), 12)]
            for name, src, n in flat1:
                load_rows_table(0, name, V1[name][0], src, n)
            for name, src in (("qg", A["hy_q_gain"][0]), ("kg", A["hy_k_gain"][0])):
                for h in range(2):
                    act.dma_start(rows[V1[name][0]:V1[name][1], 0, h * HD:h * HD + HD],
                                  src.rearrange("(r k) -> r k", r=1)).then_inc(sem["rows_loaded"], 16)
            for l in range(DEPTH2):
                for name, key, n, last in (
                        ("ffn1", "ffn1_norm_2", 8, P), ("mix", "mix_norm_2", 8, P), ("xat", "xattn_norm_2", 8, P),
                        ("mem", "xattn_mem_norm_2", 8, P), ("ffn2", "ffn2_norm_2", 8, P),
                        ("w0", "rwkv_w0_2", 4, P), ("a0", "rwkv_a0_2", 4, P), ("k_k", "rwkv_k_k_2", 4, P),
                        ("k_a", "rwkv_k_a_2", 4, P), ("ln_w", "rwkv_ln_w_2", 4, P), ("ln_b", "rwkv_ln_b_2", 4, P),
                        ("mu", "rwkv_mu_2", 15, 32), ("xqg", "xattn_q_gain_2", 1, P),
                        ("xkg", "xattn_k_gain_2", 1, P)):
                    load_rows_table(1 + l, name, V2[name][0], A[key][l], n, last)
                act.dma_start(rows[V2["fb"][0]:V2["fb"][1], 1 + l, :].rearrange("o (r k) -> o r k", k=4),
                              A["fox_f_bias_2"][l:l + 1, None, :].to_broadcast([1, P // 4, 4])
                              ).then_inc(sem["rows_loaded"], 16)
                load_rows_table(1 + l, "r_k", V2["r_k"][0], A["rwkv_r_k_2"][l].rearrange("h k -> (h k)"), 4)
                for name, key in (("fqg", "fox_q_gain_2"), ("fkg", "fox_k_gain_2"),
                                  ("mqg", "moba_q_gain_2"), ("mkg", "moba_k_gain_2")):
                    for h in range(2):
                        act.dma_start(rows[V2[name][0]:V2[name][1], 1 + l, h * HD:h * HD + HD],
                                      A[key][l].rearrange("(r k) -> r k", r=1)).then_inc(sem["rows_loaded"], 16)
            act.dma_start(sinks[:, 0:8], A["hy_sinks"][0:1, :].to_broadcast([P, 8])).then_inc(sem["sinks_loaded"], 16)
            act.dma_start(pos_i[:, :], A["positions_2"][0:1, :].to_broadcast([P, S])).then_inc(sem["pos_loaded"], 16)
            act.dma_start(rt[:, :, :], A["moe_router"][0].rearrange("(c p) e -> p c e", p=P)
                          ).then_inc(sem["router_loaded"], 16)

            act.dma_start(mem[:, :, :], A["mem_2"][0].rearrange("(t p) d -> p t d", p=P)
                          ).then_inc(sem["mem_loaded"], 16)

            def square_sum(src, ready):
                for t in range(TT):
                    act.wait_ge(w.sem[ready[t]], w.next(ready[t])) if ready[t] else None
                    f(mixT[:, :, :].rearrange("p c s -> p (c s)")[:, t * D:t * D + D], src[:, t, :], ACT.Square,
                            accum_out=ss[:, 0, t:t + 1]).then_inc(sem["act_done"], w.mark("act_done"))
                act.wait_ge(sem["act_done"], w.now("act_done"))
                f(ss[:, 1, :], ss[:, 0, :], ACT.Sqrt, scale=1.0 / D, bias=epsc[:, 0:1]).then_inc(sem["rms_ready"], 1)

            def finish_h(gain):
                for cp in (0, 2):
                    act.wait_ge(sem["hT_psum_act"], w.next("hT_psum_act"))
                    for i in range(2):
                        c = 2 * cp + i
                        ins = f(hT[:, c, :], tr[0][:, i * S:i * S + S], ACT.Copy, scale=gain(c))
                        if i:
                            ins.then_inc(sem["hT_act"], 1)

            def copy_fill(n, parts, freed=None):
                act.wait_ge(sem["proj_psum"], w.next("proj_psum"))
                for j, (dst, src, fn, kw) in enumerate(parts):
                    ins = f(dst, src, fn, **kw)
                    if j == 0 and freed is not None:
                        ins.then_inc(sem[f"slot{freed}_free"], 1)
                    elif j == len(parts) - 1:
                        ins.then_inc(sem["proj_copied"], w.mark("proj_copied"))

            def two(n, d0, d1, freed, fn=ACT.Copy, rows_=P):
                b = gu[n % 2]
                copy_fill(n, [(d0, b[0:rows_, 0:S], fn, {}), (d1, b[0:rows_, S:2 * S], fn, {})], freed)

            def halves(n, dst, rows_, freed):
                b = gu[n % 2]
                copy_fill(n, [(dst[0:rows_, i * P:i * P + P], b[0:rows_, i * P:i * P + P], ACT.Copy, {})
                              for i in range(2)], freed)

            def ffn(n, nt, w=w, slots=slots):
                N = nt * P
                slots.at += 3 * n
                with w.loop(n, {"gate_up_psum": 2}):
                    for j in range(2):
                        act.wait_ge(w.sem["gate_up_psum"], w.next("gate_up_psum"))
                        f(sg[:, j, 0:N], gu[j][:, 0:N], ACT.Silu).then_inc(w.sem["silu_ready"], 1)

            def head_norms(pairs, inv):
                n = len(pairs)

                def root(i):
                    act.wait_ge(sem["sumsq_psum"], w.next("sumsq_psum"))
                    if i >= 2:
                        act.wait_ge(sem["qk_ready"], w.next("qk_ready"))
                    f(rtb[i % 2], tr[i % 2][:, :], ACT.Sqrt, scale=inv, bias=epsc[:, 0:1]).then_inc(sem["root_ready"], 1)

                for i in range(n):
                    if i >= 2:
                        root(i - 2)
                    f(sqb[i % 2].rearrange("p (a b) -> p a b", a=2), pairs[i], ACT.Square).then_inc(sem["squares_ready"], 1)
                for i in range(max(0, n - 2), n):
                    root(i)
                act.wait_ge(sem["qk_ready"], w.next("qk_ready", min(2, n)))

            def attention(units):
                n = len(units)
                for i in range(n + 2):
                    if i < n:
                        u, b = units[i], i % 2
                        act.wait_ge(sem["maxima_ready"], w.next("maxima_ready"))
                        src = sc[:, b, :, :] if ("slope" in u or "causal" in u) else sbank[b][:, :, 0:S]
                        nk = u["nk"]
                        if "sink" in u:
                            f(snk[:, b, :], snk[:, b, :], ACT.Exp)
                        for h in range(2):
                            ins = f(sc[:, b, h, 0:nk], src[:, h, 0:nk], ACT.Exp, bias=negmx[:, b, h:h + 1],
                                    accum_out=rsum[:, b, h:h + 1])
                        ins.then_inc(sem["exp_ready"], 1)
                    if 1 <= i <= n:
                        u, b = units[i - 1], (i - 1) % 2
                        act.wait_ge(sem["probsT_psum"], w.next("probsT_psum"))
                        nk = u["nk"]
                        f(pT[:, b, :, 0:nk], tr[b][:, :].rearrange("p (h k) -> p h k", h=2)[:, :, 0:nk],
                                ACT.Copy).then_inc(sem["probsT_ready"], 1)
                    if i >= 2:
                        u, b = units[i - 2], acc[i % 2]
                        act.wait_ge(sem["attn_psum"], w.next("attn_psum"))
                        src = b[:, 0:2 * P].rearrange("p (h s) -> p h s", h=2) if u["wide"] else b[:, 0:P]
                        f(u["dst"], src, ACT.Copy).then_inc(sem["attn_copied"], 1)

            act.wait_ge(sem["angles_ready"], w.next("angles_ready"))
            f(sinT[:, :], ang[:, 0, :], ACT.Sin)
            f(cosT[:, :], ang[:, 1, :], ACT.Sin).then_inc(sem["rope_tables"], 1)
            act.wait_ge(sem["lam_abs"], w.next("lam_abs"))
            f(lamb[:, 1, :], lamb[:, 1, :], ACT.Exp, scale=-1.0).then_inc(sem["lam_exp"], 1)

            act.wait_ge(sem["x_loaded"], w.next("x_loaded", 16))
            act.wait_ge(sem["eps_ready"], w.next("eps_ready"))
            square_sum(x, (None, None))
            finish_h(lambda c: col("mix", c))
            n = 0
            for k in range(9):
                s = slots.next()
                if k == 2:
                    two(n, z0[:, 4, :], z0[:, 5, :], None)
                    halves(n + 1, z0[:, 6, :], P, s)
                    n += 2
                else:
                    j = (0, 2, None, 7, 9, 11, 13, 15, 17)[k]
                    two(n, z0[:, j, :], z0[:, j + 1, :], s)
                    n += 1
            head_norms([z0[:, 2 * i:2 * i + 2, :] for i in range(3)], 1.0 / HD)
            attention(units_mix0())
            slots.at += 4
            act.wait_ge(sem["x_ready"], w.next("x_ready"))
            square_sum(x, (None, None))
            finish_h(lambda c: col("ffn", c))
            ffn(D_FF // CH, TT)

            act.wait_ge(sem["x_ready"], w.next("x_ready"))
            square_sum(x, (None, None))
            finish_h(lambda c: col("mix", DC + c))
            for k in range(8):
                s = slots.next()
                if k < 4:
                    two(k, g_y[:, 2 * k, :], g_y[:, 2 * k + 1, :], s, ACT.Gelu_apprx_tanh)
                else:
                    j = 2 * (k - 4)
                    two(k, g_x[:, j, 3:S + 3], g_x[:, j + 1, 3:S + 3], s)
            act.wait_ge(sem["proj_copied"], w.now("proj_copied"))
            for c in range(DC):
                f(g_xc[:, c, :], g_x[:, c, 3:S + 3], ACT.Identity, scale=col("rconv", 3 * DC + c),
                        bias=col("rconvb", c)).then_inc(sem["xc_started"], 1)
            s = slots.next()
            for h in range(DC):
                act.wait_ge(sem["gates_psum"], w.next("gates_psum"))
                b = gu[h % 2]
                ins = f(g_r[:, h, :], b[:, 0:S], ACT.Sigmoid, bias=col("gab", h))
                if h == DC - 1:
                    ins.then_inc(sem[f"slot{s}_free"], 1)
                f(g_i[:, h, :], b[:, S:2 * S], ACT.Sigmoid, bias=col("gxb", h)).then_inc(sem["proj_copied"], w.mark("proj_copied"))
            act.wait_ge(sem["log_a_ready"], w.next("log_a_ready"))
            f(g_t[:, :, :], g_r[:, :, :], ACT.Tanh).then_inc(sem["tanh_ready"], 1)
            f(g_r[:, :, :], g_r[:, :, :], ACT.Exp).then_inc(sem["decay_ready"], 1)
            act.wait_ge(sem["mult_sq_ready"], w.next("mult_sq_ready"))
            f(g_m[:, :, :], g_m[:, :, :], ACT.Sqrt, scale=-2.0).then_inc(sem["mult_ready"], 1)
            slots.at += 4
            act.wait_ge(sem["x_ready"], w.next("x_ready"))
            square_sum(x, (None, None))
            finish_h(lambda c: col("ffn", DC + c))
            act.wait_ge(sem["top_ready"], w.next("top_ready"))
            f(gt[:, :, 1], gt[:, :, 0], ACT.Exp).then_inc(sem["gate_exp"], 1)

            def experts(w, slots):
                with w.loop(N_EXP, {"selT_psum": 1, "gate_up_psum": 28, "expert_ffn_psum": 1}):
                    act.wait_ge(w.sem["selT_psum"], w.next("selT_psum"))
                    f(selT[:, :, :], acc[2][:, 0:S].rearrange("p (t s) -> p t s", t=TT), ACT.Copy).then_inc(w.sem["selT_ready"], 1)
                    ffn(D_FF // CH, 1, w, slots)
                    act.wait_ge(w.sem["expert_ffn_psum"], w.next("expert_ffn_psum"))
                    f(ye[:, 0:HALF], acc[0][:, :], ACT.Copy).then_inc(w.sem[f"slot{(slots.at - 1) % NSLOT}_free"], 1)
                    f(ye[:, HALF:D], acc[1][:, :], ACT.Copy).then_inc(w.sem["expert_out"], 1)

            experts(w, slots)
            act.wait_ge(sem["count_ready"], w.next("count_ready"))
            n_max = act.value_load(cnt[0:1, 0:1], min_val=0, max_val=S)
            with act.If(n_max > CAP):
                experts(Turns(act, sem_over), Slots())

            def layer(l):
                act.wait_ge(sem["x_ready"], w.next("x_ready"))
                square_sum(x, (None, None))
                finish_h(lambda c: col2("ffn1", c))
                ffn(FFN_DIM // CH, TT)
                act.wait_ge(sem["x_ready"], w.next("x_ready"))
                square_sum(x, (None, None))
                finish_h(lambda c: col2("mix", c))
                n = 0
                for m in range(2):
                    for j in (0, 2):
                        s = slots.next()
                        two(n, q2[:, 4 * m + j, :], q2[:, 4 * m + j + 1, :], s)
                        n += 1
                    s = slots.next()
                    two(n, v2[:, m, 0, :], v2[:, m, 1, :], s)
                    n += 1
                    if m == 0:
                        s = slots.next()
                        copy_fill(n, [(zf[r:r + 4, :], gu[n % 2][r:r + 4, 0:S], ACT.Copy, {}) for r in (0, 64)], s)
                        n += 1
                for k in range(7):
                    s = slots.next()
                    two(n, zr[:, 2 * k, 1:S + 1], zr[:, 2 * k + 1, 1:S + 1], s)
                    n += 1
                s = slots.next()
                halves(n, zr[:, 14, 1:S + 1], 32, s)
                head_norms([q2[:, 2 * i:2 * i + 2, :] for i in range(4)], 1.0 / HD)
                act.wait_ge(sem["forget_abs"], w.next("forget_abs"))
                f(fsc[:, 2, :], fsc[:, 1, :], ACT.Exp, scale=-1.0).then_inc(sem["forget_exp"], 1)
                attention(units_causal(0) + units_causal(1))
                rwkv()
                slots.at += 4
                act.wait_ge(sem["x_ready"], w.next("x_ready"))
                square_sum(mem, (None, None))
                finish_h(lambda c: col2("mem", c))
                for k in range(4):
                    s = slots.next()
                    if k < 2:
                        two(k, xk[:, 2 * k, :], xk[:, 2 * k + 1, :], s)
                    else:
                        two(k, xv[:, 0, (k - 2) * CH:(k - 2) * CH + CH], xv[:, 1, (k - 2) * CH:(k - 2) * CH + CH], s)
                square_sum(x, (None, None))
                finish_h(lambda c: col2("xat", c))
                for k in range(2):
                    s = slots.next()
                    two(k, xq[:, 2 * k, :], xq[:, 2 * k + 1, :], s)
                head_norms([xk[:, 2 * i:2 * i + 2, :] for i in range(2)]
                           + [xq[:, 2 * i:2 * i + 2, :] for i in range(2)], 1.0 / P)
                attention(units_mem())
                slots.at += 2
                act.wait_ge(sem["x_ready"], w.next("x_ready"))
                square_sum(x, (None, None))
                finish_h(lambda c: col2("ffn2", c))
                ffn(FFN_DIM // CH, TT)
                slots.at += SKIP2

            def rwkv():
                s = slots.next()
                act.wait_ge(sem["tail_shifted"], w.next("tail_shifted"))
                f(zr[0:64, 12, 1:S + 1], zr[0:64, 12, 1:S + 1], ACT.Tanh)
                f(zr[:, 13, 1:S + 1], zr[:, 13, 1:S + 1], ACT.Sigmoid)
                f(zr[0:32, 14, 1:S + 1], zr[0:32, 14, 1:S + 1], ACT.Sigmoid).then_inc(sem["lora_ready"], 1)
                for j in range(3):
                    for p in range(4):
                        act.wait_ge(sem["lora_psum"], w.next("lora_psum"))
                        b = gu[(4 * j + p) % 2][:, 0:S]
                        if j == 0:
                            ins = f(lw[:, p, :], b, ACT.Sigmoid, bias=col2("w0", p))
                        elif j == 1:
                            ins = f(ra[:, p, :], b, ACT.Sigmoid, bias=col2("a0", p))
                        elif p < 3:
                            ins = f(rg[:, p, :], b, ACT.Copy)
                        else:
                            f(rg[:, p, 0:P], b[:, 0:P], ACT.Copy).then_inc(sem[f"slot{s}_free"], 1)
                            ins = f(rg[:, p, P:S], b[:, P:S], ACT.Copy)
                        ins.then_inc(sem["proj_copied"], w.mark("proj_copied"))
                act.wait_ge(sem["removal_keys"], w.next("removal_keys"))
                for i in range(2):
                    f(sqb[i].rearrange("p (a b) -> p a b", a=2), kk[:, 2 * i:2 * i + 2, :], ACT.Square).then_inc(sem["squares_ready"], 1)
                for i in range(2):
                    act.wait_ge(sem["sumsq_psum"], w.next("sumsq_psum"))
                    f(rtb[i], tr[i][:, :], ACT.Sqrt).then_inc(sem["root_ready"], 1)
                act.wait_ge(sem["sums_ready"], w.next("sums_ready"))
                f(ew[:, :, :], cw[:, :, :], ACT.Exp).then_inc(sem["decays_ready"], 1)
                f(ei[:, :, :], cw[:, :, :], ACT.Exp, scale=-1.0).then_inc(sem["decays_ready"], 1)
                f(ep[:, :, :], ep[:, :, :], ACT.Exp).then_inc(sem["decays_ready"], 1)
                f(et[:, :, :], et[:, :, :], ACT.Exp).then_inc(sem["decays_ready"], 1)
                for dst in (Vt, Bt, Kt):
                    for t in range(TT):
                        act.wait_ge(sem["tokens_psum"], w.next("tokens_psum"))
                        f(dst[:, t, :], tr[t][:, :], ACT.Copy).then_inc(sem["tokens_copied"], 1)
                for t in range(TT):
                    act.wait_ge(sem["akv_psum"], w.next("akv_psum"))
                    f(AkV[:, t, :], tr[t][:, :], ACT.Copy).then_inc(sem["akv_ready"], 1)
                for k in range(4 * (len(LEVELS) - 1)):
                    act.wait_ge(sem["inv_x_psum"], w.next("inv_x_psum"))
                    f(Xb[:, k % 2, :], gu[k % 2][:, :], ACT.Copy).then_inc(sem["inv_x_ready"], 1)
                for c in range(NRW):
                    t, r = c // 2, slice(RW * (c % 2), RW * (c % 2) + RW)
                    if c:
                        act.wait_ge(sem["carry_y_psum"], w.next("carry_y_psum"))
                        f(yS[r, t, :], gu[1][r, :], ACT.Copy).then_inc(sem["carry_y_ready"], 1)
                    act.wait_ge(sem["removal_psum"], w.next("removal_psum"))
                    f(SA[r, t, :], tr[0][r, :], ACT.Copy).then_inc(sem["removal_ready"], 1)
                for t in range(TT):
                    act.wait_ge(sem["y_var"], w.next("y_var"))
                    f(gnst[:, 2, :], gnst[:, 1, :], ACT.Sqrt, scale=1.0 / HD, bias=epsc[:, 1:2]).then_inc(sem["y_root"], 1)
                for t in range(TT):
                    act.wait_ge(sem["yT_psum"], w.next("yT_psum"))
                    for p in range(4):
                        ins = f(mixT[:, 2 + p, t * P:t * P + P], acc[2 + t][:, p * P:p * P + P], ACT.Identity,
                                scale=col2("ln_w", p), bias=col2("ln_b", p))
                    ins.then_inc(sem["yT_ready"], 1)

            act.wait_ge(sem["mem_loaded"], w.next("mem_loaded", 16))
            run_layers(w, layer, LAYER_ACT)

        @block.vector
        def _(dve):
            w = Turns(dve, sem)
            slots = Slots()
            v = nc.vector

            def log1p(out, e, z, z2):
                v.tensor_scalar(z, e, 2.0, None, ALU.add).then_inc(sem["dve_done"], w.mark("dve_done"))
                dve.wait_ge(sem["dve_done"], w.now("dve_done"))
                v.reciprocal(z, z).then_inc(sem["dve_done"], w.mark("dve_done"))
                dve.wait_ge(sem["dve_done"], w.now("dve_done"))
                v.tensor_tensor(z, z, e, ALU.mult).then_inc(sem["dve_done"], w.mark("dve_done"))
                dve.wait_ge(sem["dve_done"], w.now("dve_done"))
                v.tensor_tensor(z2, z, z, ALU.mult).then_inc(sem["dve_done"], w.mark("dve_done"))
                dve.wait_ge(sem["dve_done"], w.now("dve_done"))
                v.tensor_scalar(out, z2, 1.0 / 13, None, ALU.mult).then_inc(sem["dve_done"], w.mark("dve_done"))
                dve.wait_ge(sem["dve_done"], w.now("dve_done"))
                for d in (11, 9, 7, 5, 3):
                    v.scalar_tensor_tensor(out, out, 1.0 / d, z2, ALU.add, ALU.mult).then_inc(sem["dve_done"], w.mark("dve_done"))
                    dve.wait_ge(sem["dve_done"], w.now("dve_done"))
                v.scalar_tensor_tensor(out, out, 1.0, z, ALU.add, ALU.mult).then_inc(sem["dve_done"], w.mark("dve_done"))
                dve.wait_ge(sem["dve_done"], w.now("dve_done"))
                v.tensor_scalar(out, out, 2.0, None, ALU.mult).then_inc(sem["dve_done"], w.mark("dve_done"))
                dve.wait_ge(sem["dve_done"], w.now("dve_done"))

            def norm(src):
                dve.wait_ge(sem["rms_ready"], w.next("rms_ready"))
                v.reciprocal(ss[:, 1, :], ss[:, 1, :]).then_inc(sem["dve_done"], w.mark("dve_done"))
                dve.wait_ge(sem["dve_done"], w.now("dve_done"))
                for t in range(TT):
                    v.tensor_scalar(xn[:, t, :], src[:, t, :], ss[:, 1, t:t + 1], None, ALU.mult).then_inc(sem["xn_ready"], 1)

            def finish_h(gain):
                for cp in (1, 3):
                    dve.wait_ge(sem["hT_psum_dve"], w.next("hT_psum_dve"))
                    for i in range(2):
                        c = 2 * cp + i
                        ins = v.tensor_scalar(hT[:, c, :], tr[1][:, i * S:i * S + S], gain(c), None, ALU.mult)
                    ins.then_inc(sem["hT_dve"], 1)

            def head_norms(pairs, gains):
                for i, (pair, gain) in enumerate(zip(pairs, gains)):
                    dve.wait_ge(sem["root_ready"], w.next("root_ready"))
                    v.reciprocal(rtb[i % 2], rtb[i % 2]).then_inc(sem["dve_done"], w.mark("dve_done"))
                    dve.wait_ge(sem["dve_done"], w.now("dve_done"))
                    v.scalar_tensor_tensor(pair, pair, gain, rtb[i % 2].rearrange("p (a b) -> p a b", a=2),
                                                 ALU.mult, ALU.mult).then_inc(sem["qk_ready"], 1)

            def attention(units, between=()):
                n = len(units)

                def maxima(i):
                    u, b = units[i], i % 2
                    nk = u["nk"]
                    src = sbank[b][:, :, 0:nk]
                    dst = sc[:, b, :, 0:nk]
                    dve.wait_ge(sem["scores_psum"], w.next("scores_psum"))
                    if "slope" in u:
                        for h in range(2):
                            ins = v.scalar_tensor_tensor(sc[:, b, h, 0:nk], awin[:, S - nk:S], u["slope"][h],
                                                         sbank[b][:, h, 0:nk], ALU.mult, ALU.add)
                        ins.then_inc(sem["dve_done"], w.mark("dve_done"))
                        dve.wait_ge(sem["dve_done"], w.now("dve_done"))
                        src = dst
                    elif "causal" in u:
                        v.tensor_tensor(dst, src, cmask[:, None, S - nk:S].to_broadcast([P, 2, nk]), ALU.add).then_inc(sem["dve_done"], w.mark("dve_done"))
                        dve.wait_ge(sem["dve_done"], w.now("dve_done"))
                        src = dst
                    ins = v.tensor_reduce(negmx[:, b, :], src, AX.X, ALU.max, negate=True)
                    if "sink" in u:
                        k = u["sink"]
                        ins.then_inc(sem["dve_done"], w.mark("dve_done"))
                        dve.wait_ge(sem["dve_done"], w.now("dve_done"))
                        v.tensor_tensor(negmx[:, b, :], negmx[:, b, :], sinks[:, 8 + k:10 + k], ALU.min).then_inc(sem["dve_done"], w.mark("dve_done"))
                        dve.wait_ge(sem["dve_done"], w.now("dve_done"))
                        ins = v.tensor_tensor(snk[:, b, :], negmx[:, b, :], sinks[:, k:k + 2], ALU.add)
                    ins.then_inc(sem["maxima_ready"], 1)

                def normalise(i):
                    u, b = units[i], i % 2
                    nk = u["nk"]
                    dve.wait_ge(sem["exp_ready"], w.next("exp_ready"))
                    if "sink" in u:
                        v.tensor_tensor(rsum[:, b, :], rsum[:, b, :], snk[:, b, :], ALU.add).then_inc(sem["dve_done"], w.mark("dve_done"))
                        dve.wait_ge(sem["dve_done"], w.now("dve_done"))
                    v.reciprocal(rsum[:, b, :], rsum[:, b, :]).then_inc(sem["dve_done"], w.mark("dve_done"))
                    dve.wait_ge(sem["dve_done"], w.now("dve_done"))
                    v.tensor_tensor(sc[:, b, :, 0:nk], sc[:, b, :, 0:nk],
                                          rsum[:, b, :, None].to_broadcast([P, 2, nk]), ALU.mult).then_inc(sem["probs_ready"], 1)

                for i in range(n + 1):
                    if i < n:
                        maxima(i)
                    if i:
                        normalise(i - 1)
                    if i < len(between):
                        between[i]()

            def add_x(scale, freed):
                for i in range(2 * TT):
                    o = x[:, i // 2, (i % 2) * HALF:(i % 2) * HALF + HALF]
                    if scale == 1.0:
                        ins = v.tensor_tensor(o, o, acc[i][:, :], ALU.add)
                    else:
                        ins = v.scalar_tensor_tensor(o, acc[i][:, :], scale, o, ALU.mult, ALU.add)
                    if i == 0:
                        ins.then_inc(sem[f"slot{freed}_free"], 1)
                ins.then_inc(sem["x_ready"], 1)

            def out_proj(nslots):
                slots.at += nslots
                dve.wait_ge(sem["out_psum"], w.next("out_psum"))
                add_x(1.0, (slots.at - 1) % NSLOT)

            def hidden(n, nt, w=w, slots=slots):
                N = nt * P
                slots.at += 3 * n
                with w.loop(n, {"silu_ready": 2}):
                    for j in range(2):
                        dve.wait_ge(w.sem["silu_ready"], w.next("silu_ready"))
                        v.tensor_tensor(hid[:, j, 0:N], sg[:, j, 0:N], gu[j][:, S:S + N], ALU.mult).then_inc(w.sem["hidden_ready"], 1)

            def ffn(n, scale):
                hidden(n, TT)
                dve.wait_ge(sem["ffn_psum"], w.next("ffn_psum"))
                add_x(scale, (slots.at - 1) % NSLOT)

            dve.wait_ge(sem["consts_ready"], w.next("consts_ready"))
            for k in range(len(LEVELS)):
                for m, (a, b) in enumerate(((part_i, col_i), (col_i, part_i))):
                    v.tensor_scalar(lv_a[:, :], a[:, :], k, None, ALU.logical_shift_right).then_inc(sem["dve_done"], w.mark("dve_done"))
                    dve.wait_ge(sem["dve_done"], w.now("dve_done"))
                    v.tensor_scalar(lv_b[:, :], b[:, :], k, 1, ALU.logical_shift_right, ALU.bitwise_xor).then_inc(sem["dve_done"], w.mark("dve_done"))
                    dve.wait_ge(sem["dve_done"], w.now("dve_done"))
                    v.tensor_tensor(lv_c[:, :], lv_a[:, :], lv_b[:, :], ALU.is_equal).then_inc(sem["dve_done"], w.mark("dve_done"))
                    dve.wait_ge(sem["dve_done"], w.now("dve_done"))
                    v.tensor_scalar(lv_a[:, :], lv_a[:, :], 1, None, ALU.bitwise_and).then_inc(sem["dve_done"], w.mark("dve_done"))
                    dve.wait_ge(sem["dve_done"], w.now("dve_done"))
                    v.tensor_tensor(lvl[:, m, k, :], lv_a[:, :], lv_c[:, :], ALU.mult).then_inc(sem["dve_done"], w.mark("dve_done"))
                    dve.wait_ge(sem["dve_done"], w.now("dve_done"))
            dve.wait_ge(sem["cols_psum"], w.next("cols_psum"))
            v.tensor_copy(pv1[:, :], tr[0][:, 0:N1])
            for l in range(DEPTH2):
                v.tensor_copy(pv2[:, l, :], tr[0][:, P + l * N2:P + l * N2 + N2])
            v.tensor_copy(fcol[:, :], tr[1][:, 0:1]).then_inc(sem["cols_ready"], w.mark("cols_ready"))
            dve.wait_ge(sem["cols_ready"], w.now("cols_ready"))
            v.tensor_scalar(col("qg"), col("qg"), HD ** -0.5, None, ALU.mult)
            for name, dim in (("fqg", HD), ("mqg", HD), ("xqg", P)):
                c = pv2[:, :, V2[name][0]]
                v.tensor_scalar(c, c, dim ** -0.5, None, ALU.mult)
            dve.wait_ge(sem["sinks_loaded"], w.next("sinks_loaded", 16))
            v.tensor_scalar(sinks[:, 8:16], sinks[:, 0:8], -1.0, None, ALU.mult).then_inc(sem["dve_done"], w.mark("dve_done"))
            dve.wait_ge(sem["dve_done"], w.now("dve_done"))
            dve.wait_ge(sem["pos_loaded"], w.next("pos_loaded", 16))
            v.tensor_copy(ang[:, 0, :], pos_i[:, :]).then_inc(sem["dve_done"], w.mark("dve_done"))
            dve.wait_ge(sem["dve_done"], w.now("dve_done"))
            v.tensor_scalar(ang[:, 0, :], ang[:, 0, :], fcol[:, 0:1], None, ALU.mult).then_inc(sem["dve_done"], w.mark("dve_done"))
            dve.wait_ge(sem["dve_done"], w.now("dve_done"))
            v.tensor_scalar(ang[:, 1, :], ang[:, 0, :], 0.15915494309189535, 12582912.0, ALU.mult, ALU.add).then_inc(sem["dve_done"], w.mark("dve_done"))
            dve.wait_ge(sem["dve_done"], w.now("dve_done"))
            v.tensor_scalar(ang[:, 1, :], ang[:, 1, :], -12582912.0, None, ALU.add).then_inc(sem["dve_done"], w.mark("dve_done"))
            dve.wait_ge(sem["dve_done"], w.now("dve_done"))
            for part in (6.28125, 0.0019350051879882812, 3.0199159819e-07):
                v.scalar_tensor_tensor(ang[:, 0, :], ang[:, 1, :], -part, ang[:, 0, :], ALU.mult, ALU.add).then_inc(sem["dve_done"], w.mark("dve_done"))
                dve.wait_ge(sem["dve_done"], w.now("dve_done"))
            v.tensor_scalar(ang[:, 0, :], ang[:, 0, :], 3.1415925, -3.1415925, ALU.min, ALU.max).then_inc(sem["dve_done"], w.mark("dve_done"))
            dve.wait_ge(sem["dve_done"], w.now("dve_done"))
            v.tensor_scalar(ang[:, 2, :], ang[:, 0, :], -1.0, None, ALU.mult).then_inc(sem["dve_done"], w.mark("dve_done"))
            dve.wait_ge(sem["dve_done"], w.now("dve_done"))
            v.tensor_tensor(ang[:, 1, :], ang[:, 0, :], ang[:, 2, :], ALU.min).then_inc(sem["dve_done"], w.mark("dve_done"))
            dve.wait_ge(sem["dve_done"], w.now("dve_done"))
            v.tensor_scalar(ang[:, 1, :], ang[:, 1, :], 1.5707963267948966, None, ALU.add).then_inc(sem["angles_ready"], 1)
            lam = pv1[:, V1["lam"][0]:V1["lam"][1]]
            v.tensor_scalar(lamb[:, 0, :], lam, -1.0, None, ALU.mult).then_inc(sem["dve_done"], w.mark("dve_done"))
            dve.wait_ge(sem["dve_done"], w.now("dve_done"))
            v.tensor_tensor(lamb[:, 1, :], lamb[:, 0, :], lam, ALU.max).then_inc(sem["lam_abs"], 1)
            dve.wait_ge(sem["lam_exp"], w.next("lam_exp"))
            v.tensor_scalar(lamb[:, 4, :], lam, -1.0, 0.0, ALU.mult, ALU.max).then_inc(sem["dve_done"], w.mark("dve_done"))
            dve.wait_ge(sem["dve_done"], w.now("dve_done"))
            log1p(lamb[:, 0, :], lamb[:, 1, :], lamb[:, 2, :], lamb[:, 3, :])
            v.tensor_tensor(lamb[:, 4, :], lamb[:, 4, :], lamb[:, 0, :], ALU.add).then_inc(sem["dve_done"], w.mark("dve_done"))
            dve.wait_ge(sem["dve_done"], w.now("dve_done"))
            v.tensor_scalar(lamb[:, 4, :], lamb[:, 4, :], -8.0, None, ALU.mult).then_inc(sem["dve_done"], w.mark("dve_done"))
            dve.wait_ge(sem["dve_done"], w.now("dve_done"))

            norm(x)
            finish_h(lambda c: col("mix", c))
            v.memset(gcu[:, :, 0:2], 0.0)
            dve.wait_ge(sem["proj_copied"], w.next("proj_copied", 10))
            head_norms([z0[:, 2 * i:2 * i + 2, :] for i in range(3)], [col("qg"), col("qg"), col("kg")])

            def conv(c):
                v.tensor_tensor(gcu[:, c, 2:S + 2], z0[:, 11 + c, :], z0[:, 15 + c, :], ALU.mult).then_inc(sem["dve_done"], w.mark("dve_done"))
                dve.wait_ge(sem["dve_done"], w.now("dve_done"))
                v.tensor_scalar(cv[:, c, :], gcu[:, c, 0:S], col("hconv", c), None, ALU.mult).then_inc(sem["dve_done"], w.mark("dve_done"))
                dve.wait_ge(sem["dve_done"], w.now("dve_done"))
                for k in (1, 2):
                    v.scalar_tensor_tensor(cv[:, c, :], gcu[:, c, k:k + S], col("hconv", 4 * k + c),
                                                cv[:, c, :], ALU.mult, ALU.add).then_inc(sem["dve_done"], w.mark("dve_done"))
                    dve.wait_ge(sem["dve_done"], w.now("dve_done"))
                ins = v.tensor_tensor(mixT[:, 4 + c, :], cv[:, c, :], z0[:, 7 + c, :], ALU.mult)
                if c == 3:
                    ins.then_inc(sem["conv_ready"], 1)

            attention(units_mix0(), [lambda c=c: conv(c) for c in range(4)])
            out_proj(4 + len(MIX0_LOADS))
            norm(x)
            finish_h(lambda c: col("ffn", c))
            ffn(D_FF // CH, 1.0)

            norm(x)
            finish_h(lambda c: col("mix", DC + c))
            v.memset(g_x[:, :, 0:3], 0.0).then_inc(sem["dve_done"], w.mark("dve_done"))
            dve.wait_ge(sem["dve_done"], w.now("dve_done"))
            dve.wait_ge(sem["proj_copied"], w.next("proj_copied", 8))
            for c in range(DC):
                dve.wait_ge(sem["xc_started"], w.next("xc_started"))
                for k in range(3):
                    ins = v.scalar_tensor_tensor(g_xc[:, c, :], g_x[:, c, k:k + S], col("rconv", k * DC + c),
                                                 g_xc[:, c, :], ALU.mult, ALU.add)
                    if k < 2:
                        ins.then_inc(sem["dve_done"], w.mark("dve_done"))
                        dve.wait_ge(sem["dve_done"], w.now("dve_done"))
                ins.then_inc(sem["xc_ready"], 1)
            for h in range(DC):
                dve.wait_ge(sem["proj_copied"], w.next("proj_copied"))
                ins = v.tensor_scalar(g_r[:, h, :], g_r[:, h, :], lamb[:, 4, h:h + 1], None, ALU.mult)
            ins.then_inc(sem["log_a_ready"], 1)
            v.tensor_tensor(g_i[:, :, :], g_i[:, :, :], g_xc[:, :, :], ALU.mult).then_inc(sem["dve_done"], w.mark("dve_done"))
            dve.wait_ge(sem["dve_done"], w.now("dve_done"))
            dve.wait_ge(sem["tanh_ready"], w.next("tanh_ready"))
            v.tensor_scalar(g_m[:, :, :], g_t[:, :, :], -1.0, 1.0, ALU.mult, ALU.add).then_inc(sem["dve_done"], w.mark("dve_done"))
            dve.wait_ge(sem["dve_done"], w.now("dve_done"))
            v.reciprocal(g_m[:, :, :], g_m[:, :, :]).then_inc(sem["dve_done"], w.mark("dve_done"))
            dve.wait_ge(sem["dve_done"], w.now("dve_done"))
            v.tensor_tensor(g_m[:, :, :], g_m[:, :, :], g_t[:, :, :], ALU.mult).then_inc(sem["mult_sq_ready"], 1)
            dve.wait_ge(sem["decay_ready"], w.next("decay_ready"))
            v.memset(g_r[:, :, 0:1], 0.0)
            dve.wait_ge(sem["mult_ready"], w.next("mult_ready"))
            v.memset(g_m[:, :, 0:1], 1.0).then_inc(sem["dve_done"], w.mark("dve_done"))
            dve.wait_ge(sem["dve_done"], w.now("dve_done"))
            v.tensor_tensor(g_m[:, :, :], g_m[:, :, :], g_i[:, :, :], ALU.mult).then_inc(sem["dve_done"], w.mark("dve_done"))
            dve.wait_ge(sem["dve_done"], w.now("dve_done"))
            flat = [r[:, :, :].rearrange("p c s -> p (c s)") for r in (g_t, g_r, g_m)]
            v.tensor_tensor_scan(flat[0], flat[1], flat[2], 0.0, ALU.mult, ALU.add).then_inc(sem["dve_done"], w.mark("dve_done"))
            dve.wait_ge(sem["dve_done"], w.now("dve_done"))
            v.tensor_tensor(mixT[:, :, :], g_t[:, :, :], g_y[:, :, :], ALU.mult).then_inc(sem["lru_ready"], 1)
            out_proj(4 + len(MIX1_LOADS) + 1)

            norm(x)
            finish_h(lambda c: col("ffn", DC + c))
            dve.wait_ge(sem["logits_psum"], w.next("logits_psum"))
            v.tensor_copy(lg[:, :, :], tr[0][:, 0:TT * N_EXP].rearrange("p (t e) -> p t e", t=TT)).then_inc(sem["dve_done"], w.mark("dve_done"))
            dve.wait_ge(sem["dve_done"], w.now("dve_done"))
            for t in range(TT):
                v.max(top[:, t, :], lg[:, t, :]).then_inc(sem["dve_done"], w.mark("dve_done"))
                dve.wait_ge(sem["dve_done"], w.now("dve_done"))
                v.max_index(topi[:, t, :], top[:, t, :], lg[:, t, :]).then_inc(sem["dve_done"], w.mark("dve_done"))
                dve.wait_ge(sem["dve_done"], w.now("dve_done"))
            v.tensor_tensor(gt[:, :, 0:1], top[:, :, 1:2], top[:, :, 0:1], ALU.subtract).then_inc(sem["top_ready"], 1)
            v.tensor_copy(topf[:, :, :], topi[:, :, :]).then_inc(sem["dve_done"], w.mark("dve_done"))
            dve.wait_ge(sem["dve_done"], w.now("dve_done"))
            for j in range(2):
                for t in range(TT):
                    v.tensor_scalar(hot[:, j, t, :], iota_s[:, 0:N_EXP], topf[:, t, j:j + 1], None,
                                         ALU.is_equal).then_inc(sem["dve_done"], w.mark("dve_done"))
                    dve.wait_ge(sem["dve_done"], w.now("dve_done"))
            dve.wait_ge(sem["gate_exp"], w.next("gate_exp"))
            v.tensor_scalar(gt[:, :, 2:3], gt[:, :, 1:2], 1.0, None, ALU.add).then_inc(sem["dve_done"], w.mark("dve_done"))
            dve.wait_ge(sem["dve_done"], w.now("dve_done"))
            v.reciprocal(gt[:, :, 2:3], gt[:, :, 2:3]).then_inc(sem["dve_done"], w.mark("dve_done"))
            dve.wait_ge(sem["dve_done"], w.now("dve_done"))
            v.tensor_tensor(gt[:, :, 3:4], gt[:, :, 1:2], gt[:, :, 2:3], ALU.mult).then_inc(sem["dve_done"], w.mark("dve_done"))
            dve.wait_ge(sem["dve_done"], w.now("dve_done"))
            for t in range(TT):
                v.tensor_scalar(route[:, 1, t, :], hot[:, 0, t, :], gt[:, t, 2:3], None, ALU.mult).then_inc(sem["dve_done"], w.mark("dve_done"))
                dve.wait_ge(sem["dve_done"], w.now("dve_done"))
                v.scalar_tensor_tensor(route[:, 1, t, :], hot[:, 1, t, :], gt[:, t, 3:4], route[:, 1, t, :],
                                            ALU.mult, ALU.add).then_inc(sem["dve_done"], w.mark("dve_done"))
                dve.wait_ge(sem["dve_done"], w.now("dve_done"))
            v.tensor_tensor(route[:, 2, :, :], hot[:, 0, :, :], hot[:, 1, :, :], ALU.add).then_inc(sem["chosen_ready"], 1)
            dve.wait_ge(sem["ranks_psum"], w.next("ranks_psum"))
            v.tensor_copy(route[:, 0, :, :], tr[1][:, 0:TT * N_EXP].rearrange("p (t e) -> p t e", t=TT))
            v.tensor_reduce(cnt_f[:, 0:1], tr[1][:, 32:32 + N_EXP], AX.X, ALU.max).then_inc(sem["ranks_ready"], w.mark("ranks_ready"))
            dve.wait_ge(sem["ranks_ready"], w.now("ranks_ready"))
            v.tensor_copy(cnt[:, :], cnt_f[:, 0:1]).then_inc(sem["count_ready"], w.mark("count_ready"))
            dve.wait_ge(sem["count_ready"], w.now("count_ready"))

            def experts(w, slots):
                per = {"dve_done": 1, "chosen_h_psum": 2, "silu_ready": 28, "expert_psum": 1}
                with w.loop(N_EXP, per) as e:
                    v.tensor_copy(cur[:, :, :, None], route[:, :, :, bass.ds(e, 1)]).then_inc(sem["dve_done"], w.mark("dve_done"))
                    dve.wait_ge(sem["dve_done"], w.now("dve_done"))
                    for t in range(TT):
                        v.tensor_scalar(sel[:, t, :], iota_s[:, :], cur[:, 0, t:t + 1], cur[:, 2, t:t + 1],
                                        ALU.is_equal, ALU.mult)
                        ins = v.tensor_scalar(selg[:, t, :], iota_s[:, :], cur[:, 0, t:t + 1], cur[:, 1, t:t + 1],
                                              ALU.is_equal, ALU.mult)
                    ins.then_inc(w.sem["sel_ready"], 1)
                    for i in range(2):
                        dve.wait_ge(w.sem["chosen_h_psum"], w.next("chosen_h_psum"))
                        for j in range(4):
                            c = 4 * i + j
                            ins = v.tensor_scalar(hTe[:, c, :], tr[i][:, j * P:j * P + P], col("ffn", DC + c), None,
                                                  ALU.mult)
                        ins.then_inc(w.sem["chosen_h_ready"], 1)
                    hidden(D_FF // CH, 1, w, slots)
                    dve.wait_ge(w.sem["expert_psum"], w.next("expert_psum"))
                    for i, b in enumerate((acc[2], acc[3], tr[0], tr[1])):
                        o = x[:, i // 2, (i % 2) * HALF:(i % 2) * HALF + HALF]
                        ins = v.tensor_tensor(o, o, b[:, :], ALU.add)
                    ins.then_inc(w.sem["expert_added"], 1)

            experts(w, slots)
            n_max = dve.value_load(cnt[0:1, 0:1], min_val=0, max_val=S)
            with dve.If(n_max > CAP):
                over = Turns(dve, sem_over)
                v.tensor_scalar(route[:, 0, :, :], route[:, 0, :, :], float(CAP), None, ALU.subtract).then_inc(over.sem["dve_done"], over.mark("dve_done"))
                dve.wait_ge(over.sem["dve_done"], over.now("dve_done"))
                experts(over, Slots())
            v.memset(cnt_f[:, 1:2], 0.0).then_inc(sem["x_ready"], 1)

            def layer(l):
                v.tensor_copy(pv[:, None, :], pv2[:, bass.ds(l, 1), :]).then_inc(sem["dve_done"], w.mark("dve_done"))
                dve.wait_ge(sem["dve_done"], w.now("dve_done"))
                norm(x)
                finish_h(lambda c: col2("ffn1", c))
                ffn(FFN_DIM // CH, 0.5)
                norm(x)
                v.memset(zr[:, :, 0:1], 0.0)
                v.memset(zf, 0.0)
                finish_h(lambda c: col2("mix", c))
                dve.wait_ge(sem["proj_copied"], w.next("proj_copied", 15))
                head_norms([q2[:, 2 * i:2 * i + 2, :] for i in range(4)],
                           [col2(n) for n in ("fqg", "fkg", "mqg", "mkg")])
                f0, f1, f2, f3, f4, f5 = (fsc[:, i, :] for i in range(6))
                v.tensor_scalar(f0, zf, col2("fb"), None, ALU.add).then_inc(sem["dve_done"], w.mark("dve_done"))
                dve.wait_ge(sem["dve_done"], w.now("dve_done"))
                v.tensor_scalar(f1, f0, -1.0, None, ALU.mult).then_inc(sem["dve_done"], w.mark("dve_done"))
                dve.wait_ge(sem["dve_done"], w.now("dve_done"))
                v.tensor_tensor(f1, f1, f0, ALU.max).then_inc(sem["forget_abs"], 1)
                for i in range(2):
                    dve.wait_ge(sem["rope_psum"], w.next("rope_psum"))
                    q, turned = q2[:, 4 + 2 * i:6 + 2 * i, :], rtb[i].rearrange("p (a b) -> p a b", a=2)
                    v.tensor_tensor(turned, gu[i][:, :].rearrange("p (a b) -> p a b", a=2),
                                    sinT[:, None, :].to_broadcast([P, 2, S]), ALU.mult)
                    v.tensor_tensor(q, q, cosT[:, None, :].to_broadcast([P, 2, S]), ALU.mult).then_inc(sem["dve_done"], w.mark("dve_done"))
                    dve.wait_ge(sem["dve_done"], w.now("dve_done"))
                    v.tensor_tensor(q, q, turned, ALU.add).then_inc(sem["rope_ready"], 1)
                dve.wait_ge(sem["forget_exp"], w.next("forget_exp"))
                log1p(f5, f2, f1, f3)
                v.memset(f3, 1.0)
                v.scalar_tensor_tensor(f0, f0, 0.0, f5, ALU.min, ALU.subtract).then_inc(sem["dve_done"], w.mark("dve_done"))
                dve.wait_ge(sem["dve_done"], w.now("dve_done"))
                v.tensor_tensor_scan(f4, f3, f0, 0.0, ALU.mult, ALU.add).then_inc(sem["dve_done"], w.mark("dve_done"))
                dve.wait_ge(sem["dve_done"], w.now("dve_done"))
                v.tensor_scalar(f5, f4, -1.0, None, ALU.mult).then_inc(sem["forget_ready"], 1)

                def shift(tiles, rows_=P, name="dve_done"):
                    a, n = tiles[0], len(tiles)
                    d = zd[0:rows_, 0:n, :]
                    v.tensor_tensor(d, zr[0:rows_, a:a + n, 0:S], zr[0:rows_, a:a + n, 1:S + 1], ALU.subtract).then_inc(sem["dve_done"], w.mark("dve_done"))
                    dve.wait_ge(sem["dve_done"], w.now("dve_done"))
                    for i, c in enumerate(tiles):
                        o = zr[0:rows_, c, 1:S + 1]
                        ins = v.scalar_tensor_tensor(o, zd[0:rows_, i, :], col2("mu", c)[0:rows_, :], o,
                                                     ALU.mult, ALU.add)
                    ins.then_inc(sem[name], w.mark(name))
                    dve.wait_ge(sem[name], w.now(name))

                def shift_tail():
                    shift((12, 13))
                    shift((14,), 32, "tail_shifted")

                attention(units_causal(0) + units_causal(1),
                          [shift_tail, lambda: shift((0, 1, 2, 3)), lambda: shift((4, 5, 6, 7)),
                           lambda: shift((8, 9, 10, 11), name="tokens_in")])
                rwkv()
                out_proj(4 + len(MIX2_LOADS) + 1)
                norm(mem)
                finish_h(lambda c: col2("mem", c))
                norm(x)
                finish_h(lambda c: col2("xat", c))
                dve.wait_ge(sem["proj_copied"], w.next("proj_copied", 6))
                head_norms([xk[:, 2 * i:2 * i + 2, :] for i in range(2)] + [xq[:, 2 * i:2 * i + 2, :] for i in range(2)],
                           [col2("xkg"), col2("xkg"), col2("xqg"), col2("xqg")])
                attention(units_mem())
                out_proj(2 + len(XKV_LOADS) + len(XQ_LOADS))
                norm(x)
                finish_h(lambda c: col2("ffn2", c))
                ffn(FFN_DIM // CH, 0.5)
                slots.at += SKIP2

            def rwkv():
                r_, k_, v_ = (zr[:, 4 * i:4 * i + 4, 1:S + 1] for i in range(3))

                def flat(a):
                    return a[:, :, :].rearrange("p a b -> p (a b)")

                def chunks(a):
                    return flat(a).rearrange("p (c s) -> p c s", s=RW)

                dve.wait_ge(sem["proj_copied"], w.next("proj_copied", 4))
                v.tensor_scalar(lw[:, :, :], lw[:, :, :], -(2.718281828459045 ** -0.5), None, ALU.mult).then_inc(sem["dve_done"], w.mark("dve_done"))
                dve.wait_ge(sem["dve_done"], w.now("dve_done"))
                v.tensor_tensor_scan(flat(cw), keep[:, :], flat(lw), 0.0, ALU.mult, ALU.add).then_inc(sem["dve_done"], w.mark("dve_done"))
                dve.wait_ge(sem["dve_done"], w.now("dve_done"))
                v.tensor_tensor(ep[:, :, :], cw[:, :, :], lw[:, :, :], ALU.subtract)
                v.tensor_tensor(chunks(et), chunks(cw)[:, :, RW - 1:RW].to_broadcast([P, S * 4 // RW, RW]),
                                      chunks(cw), ALU.subtract).then_inc(sem["sums_ready"], 1)
                for p in range(4):
                    ins = v.tensor_scalar(kk[:, p, :], k_[:, p, :], col2("k_k", p), None, ALU.mult)
                ins.then_inc(sem["removal_keys"], 1)
                v.tensor_copy(Tm, ident[:, None, :].to_broadcast([P, 2 * 8, P]))
                v.tensor_copy(Um, ident[:, None, :].to_broadcast([P, 2 * 8, P]))
                dve.wait_ge(sem["proj_copied"], w.next("proj_copied", 4))
                for p in range(4):
                    ins = v.tensor_scalar(Kb[:, p, :], ra[:, p, :], 1.0, col2("k_a", p), ALU.subtract, ALU.mult)
                ins.then_inc(sem["dve_done"], w.mark("dve_done"))
                dve.wait_ge(sem["dve_done"], w.now("dve_done"))
                v.scalar_tensor_tensor(k_, Kb[:, :, :], 1.0, k_, ALU.add, ALU.mult).then_inc(sem["dve_done"], w.mark("dve_done"))
                dve.wait_ge(sem["dve_done"], w.now("dve_done"))
                for i in range(2):
                    dve.wait_ge(sem["root_ready"], w.next("root_ready"))
                    v.tensor_scalar(rtb[i], rtb[i], 1e-12, None, ALU.max).then_inc(sem["dve_done"], w.mark("dve_done"))
                    dve.wait_ge(sem["dve_done"], w.now("dve_done"))
                    v.reciprocal(rtb[i], rtb[i]).then_inc(sem["sumsq_read"], w.mark("sumsq_read"))
                    dve.wait_ge(sem["sumsq_read"], w.now("sumsq_read"))
                    o = kk[:, 2 * i:2 * i + 2, :]
                    v.tensor_tensor(o, o, rtb[i].rearrange("p (a b) -> p a b", a=2), ALU.mult).then_inc(sem["dve_done"], w.mark("dve_done"))
                    dve.wait_ge(sem["dve_done"], w.now("dve_done"))
                v.tensor_tensor(ra[:, :, :], ra[:, :, :], kk[:, :, :], ALU.mult).then_inc(sem["dve_done"], w.mark("dve_done"))
                dve.wait_ge(sem["dve_done"], w.now("dve_done"))
                dve.wait_ge(sem["proj_copied"], w.next("proj_copied", 4))
                for p in range(4):
                    o = rtb[p // 2][:, (p % 2) * S:(p % 2) * S + S]
                    ins = v.scalar_tensor_tensor(o, r_[:, p, :], col2("r_k", p), k_[:, p, :], ALU.mult, ALU.mult)
                    if p % 2:
                        ins.then_inc(sem["bonus_in"], 1)
                dve.wait_ge(sem["decays_ready"], w.next("decays_ready", 4))
                v.tensor_tensor(Bb[:, :, :], ra[:, :, :], et[:, :, :], ALU.mult).then_inc(sem["tokens_in"], w.mark("tokens_in"))
                v.tensor_tensor(Kb[:, :, :], k_, et[:, :, :], ALU.mult).then_inc(sem["tokens_in"], w.mark("tokens_in"))
                v.tensor_tensor(Bh[:, :, :], ra[:, :, :], ei[:, :, :], ALU.mult)
                v.tensor_tensor(Kh[:, :, :], k_, ei[:, :, :], ALU.mult)
                for t in range(TT):
                    ts = slice(t * P, t * P + P)
                    v.scalar_tensor_tensor(AR[:, :, t, 0, :], kk[:, :, ts], -1.0, ep[:, :, ts], ALU.mult, ALU.mult)
                    ins = v.tensor_tensor(AR[:, :, t, 1, :], r_[:, :, ts], ew[:, :, ts], ALU.mult)
                ins.then_inc(sem["gram_in"], 1)
                for i in range(2):
                    dve.wait_ge(sem["bonus_psum"], w.next("bonus_psum"))
                    ins = v.tensor_tensor(bon[:, 2 * i:2 * i + 2, :], gu[i][:, :].rearrange("p (a b) -> p a b", a=2),
                                          v_[:, 2 * i:2 * i + 2, :], ALU.mult)
                ins.then_inc(sem["bonus_ready"], 1)
                for u in range(2 * 8):
                    dve.wait_ge(sem["gram_psum"], w.next("gram_psum"))
                    if u == 0:
                        v.tensor_copy(sdec[:, :, 0:NRW], ew[:, :, :].rearrange("p a (c s) -> p a c s", s=RW)[:, :, :, RW - 1])
                        v.memset(Sbd[:, :, :], 0.0)
                        v.memset(yS[0:RW, 0, :], 0.0)
                    v.tensor_tensor(G[:, u // 8, u % 8, :, :], gu[u % 2][:, :].rearrange("p (k s) -> p k s", k=4),
                                          rmask[:, :, :], ALU.mult).then_inc(sem["gram_ready"], 1)
                def put(M, q, m, k, src):
                    return v.copy_predicated(M[:, 4 * q:4 * q + 4, :], lvl[:, m, k:k + 1, :].to_broadcast([P, 4, P]), src)

                def quad(b):
                    return b[:, :].rearrange("p (j s) -> p j s", j=4)

                for q in range(4):
                    dve.wait_ge(sem["inv_a_psum"], w.next("inv_a_psum"))
                    v.tensor_copy(took[:, q:q + 1], epsc[:, 0:1])
                    put(Tm, q, 0, 0, quad(gu[q % 2]))
                    put(Um, q, 1, 0, G[:, q // 2, 4 * (q % 2):4 * (q % 2) + 4, 0, :]).then_inc(sem["inv_ready"], 1)
                steps = 4 * (len(LEVELS) - 1)
                for k in range(steps):
                    dve.wait_ge(sem["inv_y_psum"], w.next("inv_y_psum"))
                    v.tensor_copy(took[:, 4 + k:5 + k], epsc[:, 0:1])
                    if k < steps - 4:
                        put(Tm, k % 4, 0, 1 + k // 4, quad(tr[k % 2]))
                    put(Um, k % 4, 1, 1 + k // 4, quad(acc[k % 2])).then_inc(sem["inv_ready"], 1)
                for c in range(NRW):
                    t, r = c // 2, slice(RW * (c % 2), RW * (c % 2) + RW)
                    if c:
                        dve.wait_ge(sem["carry_psum"], w.next("carry_psum"))
                        if c == 1:
                            dve.wait_ge(sem["akv_ready"], w.next("akv_ready", TT))
                        v.tensor_tensor(AkV[r, t, :], AkV[r, t, :], gu[0][r, :], ALU.add).then_inc(sem["removal_in"], 1)
                    if c < NRW - 1:
                        dve.wait_ge(sem["state_psum"], w.next("state_psum"))
                        for h in range(2):
                            d = slice(64 * h, 64 * h + 64)
                            new = tr[1][d, :].rearrange("p (a b) -> p a b", a=4)[:, :, d]
                            if c == 0:
                                ins = v.tensor_copy(Sbd[d, :, d], new)
                            else:
                                v.tensor_tensor(Sbd[d, :, d], Sbd[d, :, d],
                                                     sdec[d, :, c:c + 1].to_broadcast([64, 4, 64]), ALU.mult).then_inc(sem["dve_done"], w.mark("dve_done"))
                                dve.wait_ge(sem["dve_done"], w.now("dve_done"))
                                ins = v.tensor_tensor(Sbd[d, :, d], Sbd[d, :, d], new, ALU.add)
                        ins.then_inc(sem["state_ready"], 1)
                for t in range(TT):
                    y = yS[:, t, :].rearrange("p (h d) -> p h d", h=8)

                    def head(i):
                        return gnst[:, i, :, None].to_broadcast([P, 8, HD])

                    dve.wait_ge(sem["y_psum"], w.next("y_psum"))
                    dve.wait_ge(sem["carry_y_ready"], w.next("carry_y_ready", t + 1))
                    v.tensor_tensor(yS[:, t, :], yS[:, t, :], acc[t][:, :], ALU.add).then_inc(sem["dve_done"], w.mark("dve_done"))
                    dve.wait_ge(sem["dve_done"], w.now("dve_done"))
                    v.tensor_reduce(gnst[:, 0, :], y, AX.X, ALU.add).then_inc(sem["dve_done"], w.mark("dve_done"))
                    dve.wait_ge(sem["dve_done"], w.now("dve_done"))
                    v.tensor_scalar(gnst[:, 0, :], gnst[:, 0, :], 1.0 / HD, None, ALU.mult).then_inc(sem["dve_done"], w.mark("dve_done"))
                    dve.wait_ge(sem["dve_done"], w.now("dve_done"))
                    v.tensor_tensor(y, y, head(0), ALU.subtract).then_inc(sem["dve_done"], w.mark("dve_done"))
                    dve.wait_ge(sem["dve_done"], w.now("dve_done"))
                    v.tensor_tensor(sqb[0], yS[:, t, :], yS[:, t, :], ALU.mult).then_inc(sem["dve_done"], w.mark("dve_done"))
                    dve.wait_ge(sem["dve_done"], w.now("dve_done"))
                    v.tensor_reduce(gnst[:, 1, :], sqb[0].rearrange("p (h d) -> p h d", h=8), AX.X, ALU.add).then_inc(sem["y_var"], 1)
                    dve.wait_ge(sem["y_root"], w.next("y_root"))
                    v.reciprocal(gnst[:, 3, :], gnst[:, 2, :]).then_inc(sem["dve_done"], w.mark("dve_done"))
                    dve.wait_ge(sem["dve_done"], w.now("dve_done"))
                    v.tensor_tensor(y, y, head(3), ALU.mult).then_inc(sem["y_normed"], 1)
                for t in range(TT):
                    dve.wait_ge(sem["yT_ready"], w.next("yT_ready"))
                    o, ts = mixT[:, 2:6, t * P:t * P + P], slice(t * P, t * P + P)
                    v.tensor_tensor(o, o, bon[:, :, ts], ALU.add).then_inc(sem["dve_done"], w.mark("dve_done"))
                    dve.wait_ge(sem["dve_done"], w.now("dve_done"))
                    ins = v.tensor_tensor(o, o, rg[:, :, ts], ALU.mult)
                ins.then_inc(sem["rwkv_ready"], 1)

            run_layers(w, layer, LAYER_DVE)
            v.memset(cnt_f[:, 1:2], 0.0).then_inc(sem["out_ready"], 1)

        @block.gpsimd
        def _(pool):
            w = Turns(pool, sem)
            g = nc.gpsimd

            def select(out_, pattern, op, fill, base, p):
                return g.affine_select(out_, out_, pattern, op, fill, base=base, channel_multiplier=p)

            g.memset(rows[:, :, :], 0.0).then_inc(sem["rows_zeroed"], 1)
            g.memset(epsc[:, 0:1], EPS).then_inc(sem["pool_done"], w.mark("pool_done"))
            pool.wait_ge(sem["pool_done"], w.now("pool_done"))
            g.memset(epsc[:, 1:2], GN_EPS).then_inc(sem["eps_ready"], 1)
            for m in (ident, blk64, rope):
                g.memset(m[:, :], 0.0).then_inc(sem["pool_done"], w.mark("pool_done"))
                pool.wait_ge(sem["pool_done"], w.now("pool_done"))
            for m in (ones, upper):
                g.memset(m[:, :], 1.0).then_inc(sem["pool_done"], w.mark("pool_done"))
                pool.wait_ge(sem["pool_done"], w.now("pool_done"))
            g.memset(sel4[:, :, :], 0.0).then_inc(sem["pool_done"], w.mark("pool_done"))
            pool.wait_ge(sem["pool_done"], w.now("pool_done"))
            g.memset(cmask[:, :], 0.0).then_inc(sem["pool_done"], w.mark("pool_done"))
            pool.wait_ge(sem["pool_done"], w.now("pool_done"))
            g.memset(rmask[:, :, :], 1.0).then_inc(sem["pool_done"], w.mark("pool_done"))
            pool.wait_ge(sem["pool_done"], w.now("pool_done"))
            g.memset(keep[:, :], 1.0).then_inc(sem["pool_done"], w.mark("pool_done"))
            pool.wait_ge(sem["pool_done"], w.now("pool_done"))
            g.memset(frow[:, :], 0.0).then_inc(sem["pool_done"], w.mark("pool_done"))
            pool.wait_ge(sem["pool_done"], w.now("pool_done"))
            for h in range(2):
                g.memset(blk64[64 * h:64 * h + 64, 64 * h:64 * h + 64], 1.0).then_inc(sem["pool_done"], w.mark("pool_done"))
                pool.wait_ge(sem["pool_done"], w.now("pool_done"))
            g.memset(keep[:, :].rearrange("p (c s) -> p c s", s=RW)[:, :, 0:1], 0.0).then_inc(sem["pool_done"], w.mark("pool_done"))
            pool.wait_ge(sem["pool_done"], w.now("pool_done"))
            f4 = frow[:, :].rearrange("p (h o i) -> p h o i", h=2, o=8)
            for i in range(8):
                g.memset(f4[:, :, 0:2, i:i + 1], float(500000.0 ** (-2 * i / 16))).then_inc(sem["pool_done"], w.mark("pool_done"))
                pool.wait_ge(sem["pool_done"], w.now("pool_done"))
            select(ident[:, :], [[-1, P]], ALU.not_equal, 1.0, 0, 1).then_inc(sem["pool_done"], w.mark("pool_done"))
            pool.wait_ge(sem["pool_done"], w.now("pool_done"))
            select(upper[:, :], [[1, P]], ALU.is_gt, 0.0, 0, -1).then_inc(sem["pool_done"], w.mark("pool_done"))
            pool.wait_ge(sem["pool_done"], w.now("pool_done"))
            for h in range(2):
                select(sel4[:, :, :], [[-1, 4], [0, P]], ALU.not_equal, 1.0, -64 * h, 1).then_inc(sem["pool_done"], w.mark("pool_done"))
                pool.wait_ge(sem["pool_done"], w.now("pool_done"))
            select(cmask[:, :], [[-1, S]], ALU.is_ge, -BIG, P, 1).then_inc(sem["pool_done"], w.mark("pool_done"))
            pool.wait_ge(sem["pool_done"], w.now("pool_done"))
            for k in range(4):
                select(rmask[:, k, :], [[1, P]], ALU.is_ge if k % 2 else ALU.is_gt, 0.0, 0, -1).then_inc(sem["pool_done"], w.mark("pool_done"))
                pool.wait_ge(sem["pool_done"], w.now("pool_done"))
            g.memset(rmask[0:RW, :, RW:P], 0.0).then_inc(sem["pool_done"], w.mark("pool_done"))
            pool.wait_ge(sem["pool_done"], w.now("pool_done"))
            for h in range(2):
                select(rope[:, 64 * h:64 * h + 8], [[-1, 8]], ALU.not_equal, -1.0, -(64 * h + 8), 1).then_inc(sem["pool_done"], w.mark("pool_done"))
                pool.wait_ge(sem["pool_done"], w.now("pool_done"))
                select(rope[:, 64 * h + 8:64 * h + 16], [[-1, 8]], ALU.not_equal, 1.0, -64 * h, 1).then_inc(sem["pool_done"], w.mark("pool_done"))
                pool.wait_ge(sem["pool_done"], w.now("pool_done"))
            g.iota(part_i[:, :], [[0, P]], base=0, channel_multiplier=1).then_inc(sem["pool_done"], w.mark("pool_done"))
            pool.wait_ge(sem["pool_done"], w.now("pool_done"))
            g.iota(col_i[:, :], [[1, P]], base=0, channel_multiplier=0).then_inc(sem["pool_done"], w.mark("pool_done"))
            pool.wait_ge(sem["pool_done"], w.now("pool_done"))
            g.iota(awin_i[:, :], [[1, S]], base=-P, channel_multiplier=-1).then_inc(sem["pool_done"], w.mark("pool_done"))
            pool.wait_ge(sem["pool_done"], w.now("pool_done"))
            g.tensor_copy(iota_s[:, :], col_i[:, :]).then_inc(sem["pool_done"], w.mark("pool_done"))
            pool.wait_ge(sem["pool_done"], w.now("pool_done"))
            g.tensor_copy(awin[:, :], awin_i[:, :]).then_inc(sem["pool_done"], w.mark("pool_done"))
            pool.wait_ge(sem["pool_done"], w.now("pool_done"))
            select(awin[:, :], [[-1, S]], ALU.is_ge, -BIG, P, 1).then_inc(sem["pool_done"], w.mark("pool_done"))
            pool.wait_ge(sem["pool_done"], w.now("pool_done"))
            select(awin[:, :], [[1, S]], ALU.is_ge, -BIG, -1, -1).then_inc(sem["consts_ready"], 1)


def kernel(**inputs):
    import numpy as np
    import concourse.bacc as bacc
    from concourse.bass_utils import run_bass_kernel_spmd

    nc = bacc.Bacc("TRN2", target_bir_lowering=False, num_devices=1)
    arrays, A = {}, {}
    for name, value in inputs.items():
        a = np.ascontiguousarray(value)
        arrays[f"in_{name}_dram"] = a
        A[name] = nc.dram_tensor(f"in_{name}_dram", a.shape, mybir.dt.from_np(a.dtype), kind="ExternalInput").ap()
    out = nc.dram_tensor("out_0_dram", (1, S, D), F32, kind="ExternalOutput").ap()
    build(nc, A, out)
    r = run_bass_kernel_spmd(nc, [arrays], core_ids=[0])
    return r.results[0]["out_0_dram"]
```

```python
from contextlib import ExitStack, contextmanager

import concourse.bass as bass
from concourse import mybir

F32 = mybir.dt.float32
FR = mybir.dt.float32r
I32 = mybir.dt.int32
U32 = mybir.dt.uint32
ALU = mybir.AluOpType
ACT = mybir.ActivationFunctionType
AX = mybir.AxisListType

P = 128
D = 1024
DC = D // P
S = 256
TT = S // P
HALF = 512
BIG = 1e30
EPS = 1e-6
GN_EPS = 64e-5
NSLOT = 6
NLOW = 3
CH = 256
D_FF = 3584
FFN_DIM = 2816
N_EXP = 8
CAP = 128
HD = 64
RW = 64
NRW = S // RW
LEVELS = (1, 2, 4, 8, 16, 32)
DEPTH2 = 2


class Turns:

    def __init__(self, eng, sem):
        self.eng, self.sem = eng, sem
        self.n, self.loops = {}, []

    def branch(self, sem):
        w = Turns(self.eng, sem)
        w.n = {k: c for k, c in self.n.items() if sem[k] is self.sem[k]}
        return w

    def now(self, name):
        v = self.n[name]
        for i, per in self.loops:
            if per.get(name):
                v = i * per[name] + v
        return v

    def next(self, name, count=1):
        self.n[name] = self.n.get(name, 0) + count
        return self.now(name)

    def mark(self, name):
        self.n[name] = self.n.get(name, 0) + 1
        return 1

    @contextmanager
    def loop(self, n, per):
        with self.eng.Fori(0, n) as i:
            start = dict(self.n)
            self.loops.append((i, per))
            yield i
            self.loops.pop()
        got = {k: v - start.get(k, 0) for k, v in self.n.items() if v != start.get(k, 0)}
        assert got == {k: v for k, v in per.items() if v}, got
        for k, v in got.items():
            self.n[k] = start.get(k, 0) + n * v


class Slots:

    def __init__(self):
        self.at, self.used = 0, set()

    def next(self):
        s = self.at % NSLOT
        self.at += 1
        return s


def expert_loads(k):
    n = D_FF // CH
    if k < 2:
        return 2 * k, 2
    return (4 + 3 * (k - 2), 3) if k < n else (4 + 3 * (n - 2) + k - n, 1)

def seq(*sizes):
    out, at = [], 0
    for n in sizes:
        out.append((at, at + n))
        at += n
    return out


V1 = dict(zip(
    ("mix", "ffn", "rconv", "rconvb", "gab", "gxb", "lam", "hconv", "qg", "kg"),
    seq(2 * DC, 2 * DC, 4 * DC, DC, DC, DC, DC, 12, 1, 1)))
N1 = V1["kg"][1]
V2 = dict(zip(
    ("ffn1", "mix", "xat", "mem", "ffn2", "w0", "a0", "k_k", "k_a", "r_k", "ln_w", "ln_b", "mu",
     "fqg", "fkg", "mqg", "mkg", "xqg", "xkg", "fb"),
    seq(DC, DC, DC, DC, DC, 4, 4, 4, 4, 4, 4, 4, 15, 1, 1, 1, 1, 1, 1, 1)))
N2 = V2["fb"][1]

FOX_IN, MOBA_IN = 772, 768
RW0 = FOX_IN + MOBA_IN
MIX0_LOADS = [(k * CH, CH) for k in range(9)]
MIX1_LOADS = [(k * CH, CH) for k in range(8)]
MIX2_LOADS = ([(0, CH), (CH, CH), (2 * CH, CH), (3 * CH, 4)]
              + [(FOX_IN + k * CH, CH) for k in range(3)]
              + [(RW0 + k * CH, CH) for k in range(7)] + [(RW0 + 7 * CH, 32)])
XKV_LOADS = [(k * CH, CH) for k in range(4)]
XQ_LOADS = [(k * CH, CH) for k in range(2)]
SKIP2 = 2


SEMAPHORES = (
    "x_loaded", "out_stored",
    "hT_psum_act", "hT_psum_dve", "proj_psum", "out_psum", "scores_psum", "probsT_psum", "attn_psum",
    "sumsq_psum", "cols_psum", "gates_psum", "logits_psum", "ranks_psum", "rope_psum", "lora_psum",
    "bonus_psum", "tokens_psum", "gram_psum", "akv_psum", "inv_a_psum", "inv_x_psum", "inv_y_psum",
    "removal_psum", "state_psum", "y_psum", "yT_psum", "ffn_psum", "carry_psum", "carry_y_psum",
    "rows_loaded", "inputs_loaded", "mem_loaded", "act_done", "rms_ready", "hT_act",
    "proj_copied", "root_ready", "squares_ready", "exp_ready", "probsT_ready", "attn_copied",
    "lam_exp", "xc_started", "tanh_ready", "decay_ready", "mult_ready", "gate_exp", "forget_exp",
    "lora_ready", "decays_ready", "tokens_copied", "akv_ready", "inv_x_ready", "carry_y_ready",
    "removal_ready", "y_root", "yT_ready",
    "xn_ready", "hT_dve", "qk_ready", "maxima_ready", "probs_ready", "x_ready", "cols_ready",
    "angles_ready", "lam_abs", "conv_ready", "xc_ready", "log_a_ready", "mult_sq_ready", "lru_ready",
    "tail_shifted", "top_ready", "chosen_ready", "ranks_ready", "count_ready", "forget_abs", "rope_ready", "forget_ready",
    "sums_ready", "removal_keys", "sumsq_read", "bonus_in", "tokens_in", "gram_in", "bonus_ready",
    "gram_ready", "inv_ready", "removal_in", "state_ready", "y_var", "y_normed", "rwkv_ready", "out_ready",
    "selT_psum", "chosen_h_psum", "hidT_psum", "expert_ffn_psum", "expert_psum",
    "selT_ready", "chosen_h_up", "hidT_up", "expert_out",
    "sel_ready", "chosen_h_ready", "hidT_ready", "expert_added",
    "rows_zeroed", "pool_done", "eps_ready", "consts_ready",
) + tuple(f"slot{s}_full" for s in range(NSLOT))
PASS_SEMAPHORES = ("gate_up_psum", "hidden_ready", "silu_ready", "dve_done", "hi_ready", "lo_ready", "lo_used") + tuple(
    f"slot{s}_{what}" for s in range(NSLOT) for what in ("raw", "free"))


ROW_DMAS = 8 + 4 + DEPTH2 * 25
LAYER_SP = {
    "slot0_free": 15, "slot1_free": 15, "slot2_free": 16, "slot3_free": 16, "slot4_free": 16,
    "slot5_free": 16}
LAYER_PE = {
    "xn_ready": 10, "hT_act": 10, "hT_dve": 14, "slot0_full": 80, "slot1_full": 80, "slot2_full":
    128, "proj_copied": 33, "slot3_full": 64, "slot4_full": 64, "slot5_full": 80, "squares_ready":
    10, "qk_ready": 8, "probs_ready": 12, "probsT_ready": 12, "attn_copied": 12, "lo_ready": 66,
    "hidden_ready": 44, "forget_ready": 1, "rope_ready": 2, "lora_ready": 1, "bonus_in": 2,
    "tokens_in": 3, "sumsq_read": 2, "tokens_copied": 6, "gram_in": 1, "bonus_ready": 1,
    "gram_ready": 16, "inv_ready": 24, "inv_x_ready": 20, "akv_ready": 2, "removal_ready": 4,
    "state_ready": 3, "removal_in": 3, "y_normed": 2, "rwkv_ready": 1}
LAYER_ACT = {
    "act_done": 10, "hT_psum_act": 10, "proj_psum": 21, "proj_copied": 33, "sumsq_psum": 10,
    "qk_ready": 8, "maxima_ready": 12, "probsT_psum": 12, "attn_psum": 12, "x_ready": 8,
    "slot1_raw": 160, "slot2_raw": 176, "slot3_raw": 192, "gate_up_psum": 44, "slot4_raw": 192,
    "slot5_raw": 176, "slot0_raw": 160, "forget_abs": 1, "tail_shifted": 1, "lora_psum": 12,
    "removal_keys": 1, "sums_ready": 1, "tokens_psum": 6, "akv_psum": 2, "inv_x_psum": 20,
    "removal_psum": 4, "carry_y_psum": 3, "y_var": 2, "yT_psum": 2}
LAYER_DVE = {
    "dve_done": 184, "rms_ready": 10, "hT_act": 10, "hT_psum_dve": 10, "proj_copied": 33,
    "root_ready": 10, "scores_psum": 12, "exp_ready": 12, "out_psum": 2, "hi_ready": 66,
    "silu_ready": 44, "lo_used": 66, "ffn_psum": 2, "rope_psum": 2, "forget_exp": 1, "tail_shifted":
    1, "tokens_in": 3, "sumsq_read": 2, "decays_ready": 4, "bonus_psum": 2, "gram_psum": 16,
    "inv_a_psum": 4, "inv_y_psum": 20, "state_psum": 3, "carry_psum": 3, "akv_ready": 2, "y_psum":
    2, "carry_y_ready": 3, "y_root": 2, "yT_ready": 2}


def run_layers(w, layer, per):
    if per is None:
        for l in range(DEPTH2):
            layer(l)
        return
    with w.loop(DEPTH2, per) as l:
        layer(l)


def build(nc, A, out):
    ctx = ExitStack()

    def sb(name, shape, dt=F32):
        return ctx.enter_context(nc.sbuf_tensor(name, shape, dt))

    with ctx:
        sem = {name: ctx.enter_context(nc.semaphore(name)) for name in SEMAPHORES + PASS_SEMAPHORES}
        sem_over = sem | {name: ctx.enter_context(nc.semaphore(name + "_over")) for name in PASS_SEMAPHORES}

        banks = ctx.enter_context(nc.psum_tensor("banks", [P, 8, HALF], F32))
        gu = [banks[:, i, :] for i in range(2)]
        tr = [banks[:, 2 + i, :] for i in range(2)]
        acc = [banks[:, 4 + i, :] for i in range(4)]
        ebank = (acc[2], acc[3], acc[0], acc[1])
        sbank = [banks[:, 0:2, :], banks[:, 6:8, :]]

        hbank = (tr[0], tr[1], acc[0], acc[1])

        ring = sb("ring", [P, NSLOT, DC * CH])
        x = sb("x", [P, TT, D])
        xn = sb("xn", [P, TT, D])
        with nc.sbuf_tensor("hT_up", [P, DC, S], FR) as hT_up:
            pass
        hT = sb("hT", [P, DC, S])
        mixT = sb("mixT", [P, DC, S])
        hid_up = sb("hid_up", [P, 2, S], FR)
        sg = sb("sg", [P, 2, S])
        sc = sb("sc", [P, 2, 2, S])
        pT = sb("pT", [P, 2, 2, S])
        negmx = sb("negmx", [P, 2, 2])
        rsum = sb("rsum", [P, 2, 2])
        snk = sb("snk", [P, 2, 2])
        ident = sb("ident", [P, P])
        blk64 = sb("blk64", [P, P])
        ones = sb("ones", [P, P])
        upper = sb("upper", [P, P])
        iota_s = sb("iota_s", [P, P])
        cmask = sb("cmask", [P, S])
        awin = sb("awin", [P, S])
        rmask = sb("rmask", [P, 4, P])
        lvl = sb("lvl", [P, 2, len(LEVELS), P], mybir.dt.uint8)
        sel4 = sb("sel4", [P, 4, P])
        rope = sb("rope", [P, P])
        cosT = sb("cosT", [P, S])
        sinT = sb("sinT", [P, S])
        rows = sb("rows", [P, 3, P])
        frow = sb("frow", [1, P])
        fcol = sb("fcol", [P, 1])
        epsc = sb("epsc", [P, 4])
        keep = sb("keep", [P, 4 * S], mybir.dt.bfloat16)
        pv1 = sb("pv1", [P, N1])
        pv2 = sb("pv2", [P, DEPTH2, N2])
        pv = sb("pv", [P, N2])
        sinks = sb("sinks", [P, 16])
        ss = sb("ss", [P, 2, 2])
        rt = sb("rt", [P, DC, N_EXP])
        lg = sb("lg", [P, TT, N_EXP])
        top = sb("top", [P, TT, 8])
        topi = sb("topi", [P, TT, 8], U32)
        topf = sb("topf", [P, TT, 8])
        gt = sb("gt", [P, TT, 4])
        hot = sb("hot", [P, 2, TT, N_EXP])
        route = sb("route", [P, 3, TT, N_EXP])
        cur = sb("cur", [P, 3, TT])
        cnt_f = sb("cnt_f", [P, 2])
        took = sb("took", [P, 24])
        cnt = sb("cnt", [P, 1], I32)
        lamb = sb("lamb", [P, 5, DC])
        gnst = sb("gnst", [P, 4, 8])
        mem = sb("mem", [P, TT, D])
        with (nc.sbuf_tensor("w_up", [P, NSLOT, DC * CH], FR) as w_up,
              nc.sbuf_tensor("w_low", [P, NLOW, DC * CH], FR) as w_low,
              nc.sbuf_tensor("hT_low", [P, DC, S], FR) as hT_low,
              nc.sbuf_tensor("hid_low", [P, 2, S], FR) as hid_low):
            pass
        arena = sb("arena", [P, 22528])

        def region(at, *shape, dt=None):
            n = 1
            for k in shape:
                n *= k
            v = arena[:, at:at + n]
            if dt is not None:
                v = v.bitcast(dt)
            if len(shape) == 2:
                return v.rearrange("p (a b) -> p a b", a=shape[0])
            if len(shape) == 3:
                return v.rearrange("p (a b c) -> p a b c", a=shape[0], b=shape[1])
            if len(shape) == 4:
                return v.rearrange("p (a b c d) -> p a b c d", a=shape[0], b=shape[1], c=shape[2])
            return v

        part_i, col_i = region(512, P, dt=I32), region(640, P, dt=I32)
        lv_a, lv_b, lv_c = (region(768 + P * i, P, dt=I32) for i in range(3))
        awin_i = region(1280, S, dt=I32)
        pos_i = region(1536, S, dt=I32)
        ang = region(1792, 4, S)
        z0 = region(0, 19, S)
        gcu = region(19 * S, 4, S + 2)
        cv = region(19 * S + 4 * (S + 2), 4, S)
        g_y, g_x, g_xc = region(0, DC, S), region(2048, DC, S + 3), region(4128, DC, S)
        g_r, g_i, g_t = region(6176, DC, S), region(8224, DC, S), region(10272, DC, S)
        g_m = region(12320, DC, S)
        mflat = mixT[:, :, :].rearrange("p c s -> p (c s)")
        sel, selg, selT = (mflat[:, TT * P * i:TT * P * i + TT * P].rearrange("p (t s) -> p t s", t=TT) for i in range(3))
        ye = mflat[:, D:2 * D]
        rg, bon = region(0, 4, S), region(1024, 4, S)
        Bh, Kh, AR = region(2048, 4, S), region(3072, 4, S), region(4096, 4, TT, 2, P)
        Bt, Kt, Vt = (region(6144 + 1024 * i, TT, HALF) for i in range(3))
        q2, v2 = region(4096, 8, S), region(6144, 2, TT, S)
        zf, fsc = region(7168, S), region(7424, 6, S)
        zr, zd = region(9216, 15, S + 1), region(13072, 4, S)
        lw, ra, kk = (region(14096 + 1024 * i, 4, S) for i in range(3))
        cw, ew, et = (region(17168 + 1024 * i, 4, S) for i in range(3))
        Bb, Kb = region(20240, 4, S), region(21264, 4, S)
        ep, ei = lw, zd
        G = arena[:, 9216:17408].rearrange("p (t h k s) -> p t h k s", t=TT, h=8, k=4)
        Xb = region(17408, 2, HALF)
        SA, AkV, yS = (region(18432 + 1024 * i, TT, HALF) for i in range(3))
        Sbd, sdec = region(21504, 4, P), region(22016, 4, P)
        Tm = xn[:, :, :].rearrange("p t (u s) -> p (t u) s", s=P)
        Um = hT[:, :, :].rearrange("p c (u s) -> p (c u) s", s=P)
        xk, xv, xq = region(2048, 4, S), region(3072, TT, HALF), region(4096, 4, S)

        sqb = [sc[:, i, :, :].rearrange("p a b -> p (a b)") for i in range(2)]
        rtb = [pT[:, i, :, :].rearrange("p a b -> p (a b)") for i in range(2)]

        def col(name, i=0):
            return pv1[:, V1[name][0] + i:V1[name][0] + i + 1]

        def col2(name, i=0):
            return pv[:, V2[name][0] + i:V2[name][0] + i + 1]

        def wcols(s, w):
            return ring[:, s, 0:DC * w].rearrange("p (c n) -> p c n", c=DC)

        def halves_of(s, low, by_rows=False):
            return [a.rearrange("p (c n) -> p c n", c=2 if by_rows else DC) for a in (w_up[:, s, :], w_low[:, low, :])]

        def wrows(s):
            return ring[:, s, :].rearrange("p (k n) -> p k n", k=2)

        def units_mix0():
            return [dict(q=[z0[64 * h:64 * h + 64, hp, t * P:t * P + P] for h in range(2)],
                         k=[z0[64 * h:64 * h + 64, 4 + hp // 2, 0:P * (t + 1)] for h in range(2)],
                         nk=P * (t + 1),
                         slope=[2.0 ** -(2 * hp + h + 1) for h in range(2)], t=t,
                         sink=2 * hp,
                         v=[[z0[:, 6, kt * P + 64 * (hp // 2):kt * P + 64 * (hp // 2) + 64]
                             for kt in range(t + 1)] for h in range(2)],
                         dst=mixT[:, hp, t * P:t * P + P], wide=False)
                    for t in range(TT) for hp in range(4)]

        def units_causal(m):
            return [dict(q=[q2[64 * h:64 * h + 64, 4 * m + hp, t * P:t * P + P] for h in range(2)],
                         k=[q2[64 * h:64 * h + 64, 4 * m + 2 + hp, 0:P * (t + 1)] for h in range(2)],
                         nk=P * (t + 1), t=t, causal=True,
                         forget=[2 * hp + h for h in range(2)] if m == 0 else None,
                         v=[[v2[:, m, kt, (2 * hp + h) * 64:(2 * hp + h) * 64 + 64]
                             for kt in range(t + 1)] for h in range(2)],
                         dst=mixT[:, (0 if m == 0 else 6) + hp, t * P:t * P + P], wide=False)
                    for t in range(TT) for hp in range(2)]

        def units_mem():
            return [dict(q=[xq[:, 2 * hp + h, t * P:t * P + P] for h in range(2)],
                         k=[xk[:, 2 * hp + h, :] for h in range(2)], nk=S, t=t,
                         v=[[xv[:, kt, (2 * hp + h) * P:(2 * hp + h) * P + P]
                             for kt in range(TT)] for h in range(2)],
                         dst=mixT[:, 2 * hp:2 * hp + 2, t * P:t * P + P], wide=True)
                    for t in range(TT) for hp in range(2)]

        block = ctx.enter_context(nc.Block())

        @block.sync
        def _(sp):
            w = Turns(sp, sem)
            slots = Slots()

            def load(parts, w=w, slots=slots, what="full"):
                s = slots.next()
                if s in slots.used:
                    sp.wait_ge(w.sem[f"slot{s}_free"], w.next(f"slot{s}_free"))
                slots.used.add(s)
                for dst, src in parts(s):
                    sp.dma_start(dst, src).then_inc(w.sem[f"slot{s}_{what}"], 16)

            def load_cols(W, l, c0, n, w=w, slots=slots, what="full"):
                load(lambda s: [(wcols(s, n), W[bass.ds(l, 1), :, bass.ds(c0, n)].rearrange(
                    "o (c p) n -> p (o c) n", p=P))], w, slots, what)

            def load_rows(W, l, r0, w=w, slots=slots, what="full"):
                load(lambda s: [(wrows(s), W[bass.ds(l, 1), bass.ds(r0, 2 * P), :].rearrange(
                    "o (k p) n -> p (o k) n", p=P))], w, slots, what)

            def load_chunk(Wg, Wu, up0, Wd, l, k, w, slots, what):
                load_cols(Wg, l, k * CH, CH, w, slots, what)
                load_cols(Wu, l, k * CH + up0, CH, w, slots, what)
                load_rows(Wd, l, k * CH, w, slots, what)

            def load_ffn(Wg, Wu, up0, Wd, l, n, w=w, slots=slots, what="raw"):
                if n % 2:
                    load_chunk(Wg, Wu, up0, Wd, l, 0, w, slots, what)
                with w.loop(n // 2, {f"slot{s}_free": 1 for s in range(NSLOT)}) as i:
                    for j in range(2):
                        load_chunk(Wg, Wu, up0, Wd, l, i * 2 + (n % 2 + j), w, slots, what)

            def load_experts(w, slots):
                Wg, Wu, Wd = (A[n][0] for n in ("moe_w_gate", "moe_w_up", "moe_w_down"))
                with w.loop(N_EXP, {f"slot{s}_free": 7 for s in range(NSLOT)}) as e:
                    def gate_up(k):
                        load_cols(Wg, e, k * CH, CH, w, slots, "raw")
                        load_cols(Wu, e, k * CH, CH, w, slots, "raw")

                    n = D_FF // CH
                    gate_up(0)
                    gate_up(1)
                    with w.loop(n // 2 - 1, {f"slot{s}_free": 1 for s in range(NSLOT)}) as i:
                        for j in range(2):
                            gate_up(i * 2 + (2 + j))
                            load_rows(Wd, e, (i * 2 + j) * CH, w, slots, "raw")
                    for k in (n - 2, n - 1):
                        load_rows(Wd, e, k * CH, w, slots, "raw")

            sp.dma_start(x[:, :, :], A["x"][0].rearrange("(t p) d -> p t d", p=P)).then_inc(sem["x_loaded"], 16)
            for c0, n in MIX0_LOADS:
                load_cols(A["hy_w_in"], 0, c0, n)
            for k in range(4):
                load_rows(A["hy_w_out"], 0, k * CH)
            load_ffn(A["ffn_w_gate"], A["ffn_w_up"], 0, A["ffn_w_down"], 0, D_FF // CH)
            for c0, n in MIX1_LOADS:
                load_cols(A["rg_w_in"], 0, c0, n)
            load(lambda s: [(ring[:, s, g * D:g * D + D].rearrange("p (h j) -> p h j", h=DC),
                             A[n][0].rearrange("h i j -> i h j"))
                            for g, n in enumerate(("rg_gate_a_w", "rg_gate_x_w"))])
            for k in range(4):
                load_rows(A["rg_w_out"], 0, k * CH)
            load_experts(w, slots)
            sp.wait_ge(sem["count_ready"], 1)
            n_max = sp.value_load(cnt[0:1, 0:1], min_val=0, max_val=S)
            with sp.If(n_max > CAP):
                w_over = w.branch(sem_over)
                over = Slots()
                over.used = set(range(NSLOT))
                for s in range(NSLOT):
                    sp.wait_ge(sem[f"slot{s}_free"], w.n[f"slot{s}_free"] + 1)
                    sp.sem_inc(w_over.sem[f"slot{s}_free"], 1)
                load_experts(w_over, over)
                for s in range(NSLOT):
                    sp.wait_ge(w_over.sem[f"slot{s}_free"], w_over.next(f"slot{s}_free"))

            def layer(l):
                load_ffn(A["ffn1_w_in_2"], A["ffn1_w_in_2"], FFN_DIM, A["ffn1_w_out_2"], l, FFN_DIM // CH)
                for c0, n in MIX2_LOADS:
                    load_cols(A["mix_w_in_2"], l, c0, n)
                load(lambda s: [
                    (ring[0:64, s, 0:HALF], A["rwkv_w2_2"][bass.ds(l, 1), :, :].rearrange("o k n -> (o k) n")),
                    (ring[64:P, s, 0:HALF], A["rwkv_a2_2"][bass.ds(l, 1), :, :].rearrange("o k n -> (o k) n")),
                    (ring[:, s, HALF:D], A["rwkv_g2_2"][bass.ds(l, 1), 0:P, :].rearrange("o k n -> (o k) n")),
                    (ring[0:32, s, D:D + HALF],
                     A["rwkv_g2_2"][bass.ds(l, 1), P:P + 32, :].rearrange("o k n -> (o k) n"))])
                for k in range(4):
                    load_rows(A["mix_w_out_2"], l, k * CH)
                for c0, n in XKV_LOADS:
                    load_cols(A["xattn_w_kv_2"], l, c0, n)
                for c0, n in XQ_LOADS:
                    load_cols(A["xattn_w_q_2"], l, c0, n)
                for k in range(2):
                    load_rows(A["xattn_w_out_2"], l, k * CH)
                load_ffn(A["ffn2_w_in_2"], A["ffn2_w_in_2"], FFN_DIM, A["ffn2_w_out_2"], l, FFN_DIM // CH)
                slots.at += SKIP2

            run_layers(w, layer, LAYER_SP)
            sp.wait_ge(sem["out_ready"], 1)
            sp.dma_start(out[0].rearrange("(t p) d -> p t d", p=P), x[:, :, :]).then_inc(sem["out_stored"], 16)
            sp.wait_ge(sem["out_stored"], 16)

        @block.tensor
        def _(pe):
            w = Turns(pe, sem)
            slots = Slots()
            mm = nc.tensor.matmul

            def take(ndma=1, w=w, slots=slots):
                s = slots.next()
                pe.wait_ge(w.sem[f"slot{s}_full"], w.next(f"slot{s}_full", 16 * ndma))
                return s

            def turn(dst, src):
                return nc.tensor.transpose(dst, src, ident[0:src.shape[0], 0:src.shape[0]])

            def transpose_h(split=False):
                for t in range(TT):
                    pe.wait_ge(sem["xn_ready"], w.next("xn_ready"))
                    for cp in range(DC // 2):
                        for i in range(2):
                            c = 2 * cp + i
                            ins = turn(hbank[cp][:, i * S + t * P:i * S + t * P + P], xn[:, t, c * P:c * P + P])
                        if t == TT - 1:
                            ins.then_inc(sem["hT_psum_act" if cp % 2 == 0 else "hT_psum_dve"], 1)
                pe.wait_ge(sem["hT_act"], w.next("hT_act", 2))
                pe.wait_ge(sem["hT_dve"], w.next("hT_dve", 4 if split else 2))

            fills = [0]

            def begin_fill():
                n = fills[0]
                fills[0] += 1
                if n >= 2:
                    pe.wait_ge(sem["proj_copied"], w.next("proj_copied"))
                return gu[n % 2]

            def end_fills():
                pe.wait_ge(sem["proj_copied"], w.next("proj_copied", min(2, fills[0])))
                fills[0] = 0

            def tiles_out(s, width, tiles):
                b = begin_fill()
                wv = wcols(s, width)
                for co, m, oc, po in tiles:
                    for c in range(DC):
                        ins = mm(b[po:po + m, oc:oc + S], wv[:, c, co:co + m], hT[:, c, :],
                                 start=(c == 0), stop=(c == DC - 1))
                ins.then_inc(sem["proj_psum"], 1)

            def tokens_out(s, width, co, n):
                b = begin_fill()
                wv = wcols(s, width)
                for t in range(TT):
                    for c in range(DC):
                        ins = mm(b[:, t * n:t * n + n], hT[:, c, t * P:t * P + P], wv[:, c, co:co + n],
                                 start=(c == 0), stop=(c == DC - 1))
                ins.then_inc(sem["proj_psum"], 1)

            def two_tiles(width=CH):
                s = take()
                tiles_out(s, width, [(0, P, 0, 0), (P, P, S, 0)])

            def out_proj(nslots):
                for k in range(nslots):
                    s = take()
                    wv = wrows(s)
                    for j in range(2):
                        c = 2 * k + j
                        for t in range(TT):
                            for h in range(2):
                                ins = mm(acc[2 * t + h][:, :], mixT[:, c, t * P:t * P + P],
                                         wv[:, j, h * HALF:h * HALF + HALF],
                                         start=(c == 0), stop=(c == 2 * nslots - 1))
                    ins.then_inc(sem["out_psum" if k == nslots - 1 else f"slot{s}_free"], 1)


            def ffn(n):
                base = slots.at
                slots.at += 3 * n

                def slot(k, j):
                    return (base + 3 * k + j) % NSLOT

                def project(s, j, f, o):
                    if f == 0:
                        pe.wait_ge(sem["lo_ready"], w.next("lo_ready"))
                    up, low = halves_of(s, j)
                    products = [(up, hT_up), (low, hT_up), (up, hT_low)] if f else [
                        (up, hT_up), (up, hT_low), (low, hT_up)]
                    for i, (wv, r) in enumerate(products):
                        for c in range(DC):
                            ins = mm(o, wv[:, c, f * P:f * P + P], r[:, c, :], start=(i == 0 and c == 0),
                                     stop=(i == len(products) - 1 and c == DC - 1))
                        if f and i == 1:
                            ins.then_inc(sem["lo_used"], 1)
                    return ins

                def gate_up(k, f):
                    g, u = slot(k, 0), slot(k, 1)
                    ins = project(g, 0, f, gu[f][:, 0:S])
                    if f == 1:
                        ins.then_inc(sem[f"slot{g}_free"], 1)
                    project(u, 1, f, gu[f][:, S:2 * S]).then_inc(sem["gate_up_psum"], 1)

                def down(k, f, first=False, last=False):
                    u, d = slot(k, 1), slot(k, 2)
                    if f == 0:
                        pe.wait_ge(sem["lo_ready"], w.next("lo_ready"))
                    pe.wait_ge(sem["hidden_ready"], w.next("hidden_ready"))
                    up, low = halves_of(d, 2, True)
                    for i in range(2 * TT):
                        t, h = i // 2, i % 2
                        for j, (hv, wv) in enumerate([(hid_up, up), (hid_up, low), (hid_low, up)]):
                            ins = mm(acc[i][:, :], hv[:, f, t * P:t * P + P], wv[:, f, h * HALF:h * HALF + HALF],
                                     start=first and j == 0, stop=last and j == 2)
                            if f == 0 and i == 0 and j == 0:
                                ins.then_inc(sem[f"slot{u}_free"], 1)
                            if f == 1 and i == 2 * TT - 1 and j == 1:
                                ins.then_inc(sem["lo_used"], 1)
                    if f == 1:
                        ins.then_inc(sem["ffn_psum" if last else f"slot{d}_free"], 1)

                def step(k):
                    gate_up(k, 0)
                    down(k - 1, 1)
                    gate_up(k, 1)
                    down(k, 0)

                gate_up(0, 0)
                gate_up(0, 1)
                down(0, 0, first=True)
                with w.loop((n - 1) // 2, {"hidden_ready": 4, "lo_ready": 6}):
                    step(1)
                    step(2)
                if n % 2 == 0:
                    step(n - 1)
                down(n - 1, 1, last=True)

            def expert_ffn(w, slots):
                base, n = slots.at, D_FF // CH
                slots.at += 3 * n

                def gate_up(k, freed=None):
                    first = expert_loads(k)[0]
                    for j in range(2):
                        s = (base + first + j) % NSLOT
                        pe.wait_ge(w.sem["lo_ready"], w.next("lo_ready"))
                        up, low = halves_of(s, (first + j) % NLOW)
                        for i, (r, wv) in enumerate([(hT_up, up), (hT_up, low), (hT_low, up)]):
                            for c in range(DC):
                                ins = mm(gu[k % 2][:, j * S:j * S + S], r[:, c, 0:P], wv[:, c, :],
                                         start=(i == 0 and c == 0), stop=(i == 2 and c == DC - 1))
                                if freed is not None and j == 0 and i == 0 and c == 0:
                                    ins.then_inc(w.sem[f"slot{freed}_free"], 1)
                            if i == 1:
                                ins.then_inc(w.sem["lo_used"], 1)
                        ins.then_inc(w.sem["gate_up_psum" if j else f"slot{s}_free"], 1)

                def up_slot(k):
                    return (base + expert_loads(k)[0] + 1) % NSLOT

                def turn_hidden(k, freed=None):
                    pe.wait_ge(w.sem["hidden_ready"], w.next("hidden_ready"))
                    for f in range(2):
                        ins = turn(tr[k % 2][:, f * P:f * P + P], sg[:, k % 2, f * P:f * P + P])
                        if f == 0 and freed is not None:
                            ins.then_inc(w.sem[f"slot{freed}_free"], 1)
                    ins.then_inc(w.sem["hidT_psum"], 1)

                def down(k, first=False, last=False):
                    i = sum(expert_loads(k + 2)) - 1
                    s = (base + i) % NSLOT
                    pe.wait_ge(w.sem["lo_ready"], w.next("lo_ready"))
                    pe.wait_ge(w.sem["hidT_ready"], w.next("hidT_ready"))
                    up, low = halves_of(s, i % NLOW, True)
                    cs = slice(k % 2 * P, k % 2 * P + P)
                    for f in range(2):
                        for j, (hv, wv) in enumerate([(hid_up, up), (hid_up, low), (hid_low, up)]):
                            for h in range(2):
                                ins = mm(acc[h][:, :], hv[:, f, cs], wv[:, f, h * HALF:h * HALF + HALF],
                                         start=(first and f == 0 and j == 0), stop=(last and f == 1 and j == 2))
                            if f == 1 and j == 1:
                                ins.then_inc(w.sem["lo_used"], 1)
                    ins.then_inc(w.sem["expert_ffn_psum" if last else f"slot{s}_free"], 1)

                def step(k):
                    gate_up(k)
                    turn_hidden(k - 1, up_slot(k))
                    down(k - 2, first=(k == 2))

                gate_up(0)
                gate_up(1, up_slot(0))
                turn_hidden(0, up_slot(1))
                pe.wait_ge(sem["expert_added"], w.next("expert_added"))
                for t in range(TT):
                    ins = turn(acc[2][:, t * P:t * P + P], selg[:, t, :])
                ins.then_inc(sem["selT_psum"], 1)
                step(2)
                step(3)
                with w.loop(n // 2 - 2, {"lo_ready": 6, "hidden_ready": 2, "hidT_ready": 2}):
                    step(4)
                    step(5)
                turn_hidden(n - 1)
                down(n - 2)
                down(n - 1, last=True)

            def attention(units):
                n = len(units)
                for i in range(n + 2):
                    if i < n:
                        u = units[i]
                        for h in range(2):
                            o = sbank[i % 2][:, h, 0:u["nk"]]
                            fg = u.get("forget")
                            ins = mm(o, u["q"][h], u["k"][h], start=True, stop=fg is None)
                            if fg is not None:
                                t0, nk, r = u["t"] * P, u["nk"], slice(64 * h, 64 * h + 4)
                                mm(o, fsc[r, 4, t0:t0 + P],
                                   sel4[r, fg[h]:fg[h] + 1, :].to_broadcast([4, nk // P, P]),
                                   start=False, stop=False)
                                ins = mm(o, sel4[r, fg[h], :], fsc[r, 5, 0:nk], start=False, stop=True)
                        ins.then_inc(sem["scores_psum"], 1)
                    if 1 <= i <= n:
                        u = units[i - 1]
                        pe.wait_ge(sem["probs_ready"], w.next("probs_ready"))
                        for h in range(2):
                            for kt in range(u["nk"] // P):
                                o = h * S + kt * P
                                ins = turn(tr[(i - 1) % 2][:, o:o + P],
                                           sc[:, (i - 1) % 2, h, kt * P:kt * P + P])
                        ins.then_inc(sem["probsT_psum"], 1)
                    if i >= 2:
                        u = units[i - 2]
                        pe.wait_ge(sem["probsT_ready"], w.next("probsT_ready"))
                        b = acc[i % 2]
                        for h in range(2):
                            o = b[:, h * P:h * P + P] if u["wide"] else b[64 * h:64 * h + 64, 0:P]
                            kts = u["nk"] // P
                            for kt in range(kts):
                                ins = mm(o, u["v"][h][kt], pT[:, i % 2, h, kt * P:kt * P + P],
                                         start=(kt == 0), stop=(kt == kts - 1))
                        ins.then_inc(sem["attn_psum"], 1)
                pe.wait_ge(sem["attn_copied"], w.next("attn_copied", n))

            def head_norms(n, block):
                for i in range(n):
                    pe.wait_ge(sem["squares_ready"], w.next("squares_ready"))
                    mm(tr[i % 2][:, :], block[:, :], sqb[i % 2], start=True,
                       stop=True).then_inc(sem["sumsq_psum"], 1)

            pe.wait_ge(sem["consts_ready"], w.next("consts_ready"))
            pe.wait_ge(sem["rows_loaded"], w.next("rows_loaded", 16 * ROW_DMAS))
            turn(tr[0][:, 0:N1], rows[0:N1, 0, :])
            for l in range(DEPTH2):
                turn(tr[0][:, P + l * N2:P + l * N2 + N2], rows[0:N2, 1 + l, :])
            ins = mm(tr[1][:, 0:1], frow[0:1, :], ones[0:1, 0:1], start=True, stop=True)
            ins.then_inc(sem["cols_psum"], 1)
            pe.wait_ge(sem["cols_ready"], w.next("cols_ready"))

            transpose_h()
            for k in range(9):
                if k == 2:
                    s = take()
                    tiles_out(s, CH, [(64 * g, 64, g * S, po) for g in range(2) for po in (0, 64)])
                    tokens_out(s, CH, P, P)
                else:
                    two_tiles()
            end_fills()
            head_norms(3, blk64)
            pe.wait_ge(sem["qk_ready"], w.next("qk_ready", 3))
            attention(units_mix0())
            pe.wait_ge(sem["conv_ready"], w.next("conv_ready"))
            out_proj(4)
            transpose_h(split=True)
            ffn(D_FF // CH)

            transpose_h()
            for k in range(8):
                two_tiles()
            end_fills()
            s = take(2)
            for h in range(DC):
                pe.wait_ge(sem["xc_ready"], w.next("xc_ready"))
                b = begin_fill()
                for g in range(2):
                    ins = mm(b[:, g * S:g * S + S], ring[:, s, g * D + h * P:g * D + h * P + P],
                             g_xc[:, h, :], start=True, stop=True)
                ins.then_inc(sem["gates_psum"], 1)
            end_fills()
            pe.wait_ge(sem["lru_ready"], w.next("lru_ready"))
            out_proj(4)

            transpose_h()
            pe.wait_ge(sem["inputs_loaded"], w.next("inputs_loaded", 48))
            for t in range(TT):
                for c in range(DC):
                    ins = mm(tr[0][:, t * N_EXP:t * N_EXP + N_EXP], hT[:, c, t * P:t * P + P],
                             rt[:, c, :], start=(c == 0), stop=(c == DC - 1))
            ins.then_inc(sem["logits_psum"], 1)
            pe.wait_ge(sem["chosen_ready"], w.next("chosen_ready"))
            for t in range(TT):
                for tt in range(t + 1):
                    mm(tr[1][:, t * N_EXP:t * N_EXP + N_EXP], (upper if tt == t else ones)[:, :],
                       route[:, 2, tt, :], start=(tt == 0), stop=(tt == t))
            for t in range(TT):
                ins = mm(tr[1][:, 32:32 + N_EXP], ones[:, :], route[:, 2, t, :],
                         start=(t == 0), stop=(t == TT - 1))
            ins.then_inc(sem["ranks_psum"], 1)

            def experts(w, slots):
                def gather():
                    pe.wait_ge(sem["sel_ready"], w.next("sel_ready"))
                    for c in range(DC):
                        for t in range(TT):
                            ins = mm(tr[c // 4][:, (c % 4) * P:(c % 4) * P + P],
                                     xn[:, t, c * P:c * P + P], sel[:, t, :],
                                     start=(t == 0), stop=(t == TT - 1))
                        if c % 4 == 3:
                            ins.then_inc(sem["chosen_h_psum"], 1)

                def expert(last=False):
                    pe.wait_ge(sem["chosen_h_ready"], w.next("chosen_h_ready", 2))
                    expert_ffn(w, slots)
                    if not last:
                        gather()
                    pe.wait_ge(sem["selT_ready"], w.next("selT_ready"))
                    pe.wait_ge(sem["expert_out"], w.next("expert_out"))
                    for t in range(TT):
                        for h in range(2):
                            ins = mm(ebank[2 * t + h][:, :], selT[:, t, :],
                                     ye[:, h * HALF:h * HALF + HALF], start=True, stop=True)
                    ins.then_inc(sem["expert_psum"], 1)

                gather()
                per = {"lo_ready": 42, "hidden_ready": 14, "hidT_ready": 14, "sel_ready": 1, "selT_ready": 1,
                       "chosen_h_ready": 2, "expert_out": 1, "expert_added": 1}
                with w.loop(N_EXP - 1, per):
                    expert()
                expert(last=True)
                w.next("expert_added")

            pe.wait_ge(sem["ranks_ready"], w.next("ranks_ready"))
            experts(w, slots)
            pe.wait_ge(sem["count_ready"], w.next("count_ready"))
            n_max = pe.value_load(cnt[0:1, 0:1], min_val=0, max_val=S)
            with pe.If(n_max > CAP):
                experts(w.branch(sem_over), Slots())

            def layer(l):
                transpose_h(split=True)
                ffn(FFN_DIM // CH)
                transpose_h()
                for m in range(2):
                    two_tiles()
                    two_tiles()
                    s = take()
                    tokens_out(s, CH, 0, CH)
                    if m == 0:
                        s = take()
                        tiles_out(s, 4, [(0, 4, 0, 0), (0, 4, 0, 64)])
                for k in range(7):
                    two_tiles()
                s = take()
                tiles_out(s, 32, [(0, 32, 0, 0)])
                end_fills()
                head_norms(4, blk64)
                pe.wait_ge(sem["qk_ready"], w.next("qk_ready", 4))
                for i in range(2):
                    for j in range(2):
                        ins = mm(gu[i][:, j * S:j * S + S], rope[:, :], q2[:, 4 + 2 * i + j, :],
                                 start=True, stop=True)
                    ins.then_inc(sem["rope_psum"], 1)
                pe.wait_ge(sem["forget_ready"], w.next("forget_ready"))
                pe.wait_ge(sem["rope_ready"], w.next("rope_ready", 2))
                attention(units_causal(0) + units_causal(1))
                rwkv()
                out_proj(4)
                transpose_h()
                for k in range(2):
                    two_tiles()
                for k in range(2):
                    s = take()
                    tokens_out(s, CH, 0, CH)
                transpose_h()
                for k in range(2):
                    two_tiles()
                end_fills()
                head_norms(4, ones)
                pe.wait_ge(sem["qk_ready"], w.next("qk_ready", 4))
                attention(units_mem())
                out_proj(2)
                transpose_h(split=True)
                ffn(FFN_DIM // CH)
                slots.at += SKIP2

            def rwkv():
                s = take(4)
                pe.wait_ge(sem["lora_ready"], w.next("lora_ready"))
                for j in range(3):
                    for p in range(4):
                        b = begin_fill()
                        cs = slice(p * P, p * P + P)
                        if j == 0:
                            ins = mm(b[:, 0:S], ring[0:64, s, cs], zr[0:64, 12, 1:S + 1], start=True, stop=True)
                        elif j == 1:
                            ins = mm(b[:, 0:S], ring[64:P, s, cs], zr[64:P, 12, 1:S + 1], start=True, stop=True)
                        else:
                            mm(b[:, 0:S], ring[:, s, HALF + p * P:HALF + p * P + P], zr[:, 13, 1:S + 1],
                               start=True, stop=False)
                            ins = mm(b[:, 0:S], ring[0:32, s, D + p * P:D + p * P + P],
                                     zr[0:32, 14, 1:S + 1], start=False, stop=True)
                        ins.then_inc(sem["lora_psum"], 1)
                end_fills()
                for i in range(2):
                    pe.wait_ge(sem["squares_ready"], w.next("squares_ready"))
                    mm(tr[i][:, :], blk64[:, :], sqb[i], start=True, stop=True).then_inc(sem["sumsq_psum"], 1)
                for i in range(2):
                    pe.wait_ge(sem["bonus_in"], w.next("bonus_in"))
                    mm(gu[i][:, :], blk64[:, :], rtb[i], start=True, stop=True).then_inc(sem["bonus_psum"], 1)
                for n, (src, off) in enumerate(((zr, 1), (Bb, 0), (Kb, 0))):
                    pe.wait_ge(sem["tokens_in"], w.next("tokens_in"))
                    for t in range(TT):
                        b = tr[t]
                        if n:
                            pe.wait_ge(sem["tokens_copied"], w.next("tokens_copied"))
                        else:
                            pe.wait_ge(sem["sumsq_read"], w.next("sumsq_read"))
                        for p in range(4):
                            v = src[:, 8 + p, off + t * P:off + t * P + P] if n == 0 else src[:, p, t * P:t * P + P]
                            ins = turn(b[:, p * P:p * P + P], v)
                        ins.then_inc(sem["tokens_psum"], 1)
                pe.wait_ge(sem["gram_in"], w.next("gram_in"))
                pe.wait_ge(sem["bonus_ready"], w.next("bonus_ready"))
                for u in range(2 * 8):
                    t, h = u // 8, u % 8
                    p, r = h // 2, slice(64 * (h % 2), 64 * (h % 2) + 64)
                    if u >= 2:
                        pe.wait_ge(sem["gram_ready"], w.next("gram_ready"))
                    b = gu[u % 2]
                    mm(b[:, 0:S], Bh[r, p, t * P:t * P + P], AR[r, p, t, :, :].rearrange("p a s -> p (a s)"),
                       start=True, stop=True)
                    mm(b[:, S:2 * S], Kh[r, p, t * P:t * P + P], AR[r, p, t, :, :].rearrange("p a s -> p (a s)"),
                       start=True, stop=True).then_inc(sem["gram_psum"], 1)
                pe.wait_ge(sem["gram_ready"], w.next("gram_ready", 2))
                pe.wait_ge(sem["tokens_copied"], w.next("tokens_copied", 2))
                for t in range(TT):
                    for h in range(8):
                        ins = mm(tr[t][:, h * 64:h * 64 + 64], G[:, t, h, 2, :], Vt[:, t, h * 64:h * 64 + 64],
                                 start=True, stop=True)
                    ins.then_inc(sem["akv_psum"], 1)
                for q in range(4):
                    if q >= 2:
                        pe.wait_ge(sem["inv_ready"], w.next("inv_ready"))
                    for j in range(4):
                        ins = mm(gu[q % 2][:, j * P:j * P + P], G[:, q // 2, 4 * (q % 2) + j, 0, :],
                                 ident[:, :], start=True, stop=True)
                    ins.then_inc(sem["inv_a_psum"], 1)
                steps = 4 * (len(LEVELS) - 1)
                for i in range(steps + 1):
                    if i < steps:
                        q = i % 4
                        if i < 2:
                            pe.wait_ge(sem["inv_ready"], w.next("inv_ready"))
                        for j in range(4):
                            ins = mm(gu[i % 2][:, j * P:j * P + P], G[:, q // 2, 4 * (q % 2) + j, 0, :],
                                     Tm[:, 4 * q + j, :], start=True, stop=True)
                        ins.then_inc(sem["inv_x_psum"], 1)
                    if i >= 1:
                        k = i - 1
                        q = k % 4
                        pe.wait_ge(sem["inv_x_ready"], w.next("inv_x_ready"))
                        if k >= 2:
                            pe.wait_ge(sem["inv_ready"], w.next("inv_ready"))
                        for j in range(4):
                            o = slice(j * P, j * P + P)
                            if k < steps - 4:
                                mm(tr[k % 2][:, o], Um[:, 4 * q + j, :], Xb[:, k % 2, o], start=True, stop=True)
                            ins = mm(acc[k % 2][:, o], Xb[:, k % 2, o], Um[:, 4 * q + j, :],
                                     start=True, stop=True)
                        ins.then_inc(sem["inv_y_psum"], 1)
                pe.wait_ge(sem["inv_ready"], w.next("inv_ready", 2))
                pe.wait_ge(sem["akv_ready"], w.next("akv_ready", TT))
                for c in range(NRW):
                    t, r = c // 2, slice(RW * (c % 2), RW * (c % 2) + RW)
                    if c:
                        pe.wait_ge(sem["state_ready"], w.next("state_ready"))
                        for k, name in enumerate(("carry_psum", "carry_y_psum")):
                            for p in range(4):
                                ins = mm(gu[k][:, p * P:p * P + P], AR[:, p, t, k, :], Sbd[:, p, :],
                                         start=True, stop=True)
                            ins.then_inc(sem[name], 1)
                        pe.wait_ge(sem["removal_in"], w.next("removal_in"))
                    for h in range(8):
                        ins = mm(tr[0][:, h * 64:h * 64 + 64], Um[:, 8 * t + h, :],
                                 AkV[:, t, h * 64:h * 64 + 64], start=True, stop=True)
                    ins.then_inc(sem["removal_psum"], 1)
                    pe.wait_ge(sem["removal_ready"], w.next("removal_ready"))
                    if c < NRW - 1:
                        for p in range(4):
                            o = slice(p * P, p * P + P)
                            mm(tr[1][:, o], Bt[r, t, o], SA[r, t, o], start=True, stop=False)
                            ins = mm(tr[1][:, o], Kt[r, t, o], Vt[r, t, o], start=False, stop=True)
                        ins.then_inc(sem["state_psum"], 1)
                    if c % 2:
                        for h in range(8):
                            o = slice(h * 64, h * 64 + 64)
                            mm(acc[t][:, o], G[:, t, h, 1, :], SA[:, t, o], start=True, stop=False)
                            ins = mm(acc[t][:, o], G[:, t, h, 3, :], Vt[:, t, o], start=False, stop=True)
                        ins.then_inc(sem["y_psum"], 1)
                for t in range(TT):
                    pe.wait_ge(sem["y_normed"], w.next("y_normed"))
                    for p in range(4):
                        ins = turn(acc[2 + t][:, p * P:p * P + P], yS[:, t, p * P:p * P + P])
                    ins.then_inc(sem["yT_psum"], 1)
                pe.wait_ge(sem["rwkv_ready"], w.next("rwkv_ready"))

            run_layers(w, layer, LAYER_PE)

        @block.scalar
        def _(act):
            w = Turns(act, sem)
            slots = Slots()
            f = nc.scalar.activation

            def load_rows_table(i, name, at, src, n, last=P):
                full = n if last == P else n - 1
                if full:
                    act.dma_start(rows[at:at + full, i, :], src[0:full * P].rearrange(
                        "(r k) -> r k", k=P)).then_inc(sem["rows_loaded"], 16)
                if last != P:
                    act.dma_start(rows[at + full:at + n, i, 0:last],
                                  src[full * P:full * P + last].rearrange("(r k) -> r k", r=1)
                                  ).then_inc(sem["rows_loaded"], 16)

            act.wait_ge(sem["rows_zeroed"], w.next("rows_zeroed"))
            flat1 = [("mix", A["norm_mix"].rearrange("l d -> (l d)"), 16),
                     ("ffn", A["norm_ffn"].rearrange("l d -> (l d)"), 16),
                     ("rconv", A["rg_conv_w"][0].rearrange("k d -> (k d)"), 32),
                     ("rconvb", A["rg_conv_b"][0], 8), ("gab", A["rg_gate_a_b"][0], 8),
                     ("gxb", A["rg_gate_x_b"][0], 8), ("lam", A["rg_lambda"][0], 8),
                     ("hconv", A["hy_conv_w"][0].rearrange("k d -> (k d)"), 12)]
            for name, src, n in flat1:
                load_rows_table(0, name, V1[name][0], src, n)
            for name, src in (("qg", A["hy_q_gain"][0]), ("kg", A["hy_k_gain"][0])):
                for h in range(2):
                    act.dma_start(rows[V1[name][0]:V1[name][1], 0, h * HD:h * HD + HD],
                                  src.rearrange("(r k) -> r k", r=1)).then_inc(sem["rows_loaded"], 16)
            for l in range(DEPTH2):
                for name, key, n, last in (
                        ("ffn1", "ffn1_norm_2", 8, P), ("mix", "mix_norm_2", 8, P), ("xat", "xattn_norm_2", 8, P),
                        ("mem", "xattn_mem_norm_2", 8, P), ("ffn2", "ffn2_norm_2", 8, P),
                        ("w0", "rwkv_w0_2", 4, P), ("a0", "rwkv_a0_2", 4, P), ("k_k", "rwkv_k_k_2", 4, P),
                        ("k_a", "rwkv_k_a_2", 4, P), ("ln_w", "rwkv_ln_w_2", 4, P), ("ln_b", "rwkv_ln_b_2", 4, P),
                        ("mu", "rwkv_mu_2", 15, 32), ("xqg", "xattn_q_gain_2", 1, P),
                        ("xkg", "xattn_k_gain_2", 1, P)):
                    load_rows_table(1 + l, name, V2[name][0], A[key][l], n, last)
                act.dma_start(rows[V2["fb"][0]:V2["fb"][1], 1 + l, :].rearrange("o (r k) -> o r k", k=4),
                              A["fox_f_bias_2"][l:l + 1, None, :].to_broadcast([1, P // 4, 4])
                              ).then_inc(sem["rows_loaded"], 16)
                load_rows_table(1 + l, "r_k", V2["r_k"][0], A["rwkv_r_k_2"][l].rearrange("h k -> (h k)"), 4)
                for name, key in (("fqg", "fox_q_gain_2"), ("fkg", "fox_k_gain_2"),
                                  ("mqg", "moba_q_gain_2"), ("mkg", "moba_k_gain_2")):
                    for h in range(2):
                        act.dma_start(rows[V2[name][0]:V2[name][1], 1 + l, h * HD:h * HD + HD],
                                      A[key][l].rearrange("(r k) -> r k", r=1)).then_inc(sem["rows_loaded"], 16)
            act.dma_start(sinks[:, 0:8], A["hy_sinks"][0:1, :].to_broadcast([P, 8])).then_inc(sem["inputs_loaded"], 16)
            act.dma_start(pos_i[:, :], A["positions_2"][0:1, :].to_broadcast([P, S])).then_inc(sem["inputs_loaded"], 16)
            act.dma_start(rt[:, :, :], A["moe_router"][0].rearrange("(c p) e -> p c e", p=P)
                          ).then_inc(sem["inputs_loaded"], 16)

            act.dma_start(mem[:, :, :], A["mem_2"][0].rearrange("(t p) d -> p t d", p=P)
                          ).then_inc(sem["mem_loaded"], 16)

            def square_sum(src, wait=True):
                for t in range(TT):
                    if wait:
                        act.wait_ge(sem["x_ready"], w.next("x_ready"))
                    f(xn[:, t, :], src[:, t, :], ACT.Square,
                      accum_out=ss[:, 0, t:t + 1]).then_inc(sem["act_done"], w.mark("act_done"))
                    act.wait_ge(sem["act_done"], w.now("act_done"))
                    f(ss[:, 1, t:t + 1], ss[:, 0, t:t + 1], ACT.Sqrt, scale=1.0 / D,
                      bias=epsc[:, 0:1]).then_inc(sem["rms_ready"], 1)

            def finish_h(gain, split=False):
                dst = hT_up if split else hT
                for cp in (0, 2):
                    act.wait_ge(sem["hT_psum_act"], w.next("hT_psum_act"))
                    for i in range(2):
                        c = 2 * cp + i
                        ins = f(dst[:, c, :], hbank[cp][:, i * S:i * S + S], ACT.Copy, scale=gain(c))
                    ins.then_inc(sem["hT_act"], 1)

            def copy_fill(n, parts, freed=None):
                act.wait_ge(sem["proj_psum"], w.next("proj_psum"))
                for j, (dst, src, fn, kw) in enumerate(parts):
                    ins = f(dst, src, fn, **kw)
                    if j == 0 and freed is not None:
                        ins.then_inc(sem[f"slot{freed}_free"], 1)
                    elif j == len(parts) - 1:
                        ins.then_inc(sem["proj_copied"], w.mark("proj_copied"))

            def two(n, d0, d1, freed, fn=ACT.Copy, rows_=P):
                b = gu[n % 2]
                copy_fill(n, [(d0, b[0:rows_, 0:S], fn, {}), (d1, b[0:rows_, S:2 * S], fn, {})], freed)

            def halves(n, dst, rows_, freed):
                b = gu[n % 2]
                copy_fill(n, [(dst[0:rows_, i * P:i * P + P], b[0:rows_, i * P:i * P + P], ACT.Copy, {})
                              for i in range(2)], freed)

            def norm_ffn(n, gain):
                base = slots.at
                slots.at += 3 * n

                def upper(k, j):
                    s = (base + 3 * k + j) % NSLOT
                    act.wait_ge(sem[f"slot{s}_raw"], w.next(f"slot{s}_raw", 16))
                    f(w_up[:, s, :], ring[:, s, :], ACT.Copy).then_inc(sem["hi_ready"], 1)

                def silu(j):
                    act.wait_ge(sem["gate_up_psum"], w.next("gate_up_psum"))
                    f(sg[:, j, :], gu[j][:, 0:S], ACT.Silu).then_inc(sem["silu_ready"], 1)

                def step(k):
                    silu(0)
                    upper(k + 1, 0)
                    upper(k + 1, 1)
                    silu(1)
                    upper(k + 1, 2)

                square_sum(x)
                upper(0, 0)
                finish_h(gain, split=True)
                upper(0, 1)
                upper(0, 2)
                with w.loop((n - 1) // 2, {"gate_up_psum": 4} | {f"slot{s}_raw": 16 for s in range(NSLOT)}):
                    step(0)
                    step(1)
                if n % 2 == 0:
                    step(n - 2)
                silu(0)
                silu(1)

            def head_norms(pairs, inv):
                n = len(pairs)

                def root(i):
                    act.wait_ge(sem["sumsq_psum"], w.next("sumsq_psum"))
                    if i >= 2:
                        act.wait_ge(sem["qk_ready"], w.next("qk_ready"))
                    f(rtb[i % 2], tr[i % 2][:, :], ACT.Sqrt, scale=inv, bias=epsc[:, 0:1]).then_inc(sem["root_ready"], 1)

                for i in range(n):
                    if i >= 2:
                        root(i - 2)
                    f(sqb[i % 2].rearrange("p (a b) -> p a b", a=2), pairs[i], ACT.Square).then_inc(sem["squares_ready"], 1)
                for i in range(max(0, n - 2), n):
                    root(i)
                act.wait_ge(sem["qk_ready"], w.next("qk_ready", min(2, n)))

            def attention(units):
                n = len(units)
                for i in range(n + 2):
                    if i < n:
                        u, b = units[i], i % 2
                        act.wait_ge(sem["maxima_ready"], w.next("maxima_ready"))
                        src = sc[:, b, :, :] if ("slope" in u or "causal" in u) else sbank[b][:, :, 0:S]
                        nk = u["nk"]
                        if "sink" in u:
                            f(snk[:, b, :], snk[:, b, :], ACT.Exp)
                        for h in range(2):
                            ins = f(sc[:, b, h, 0:nk], src[:, h, 0:nk], ACT.Exp, bias=negmx[:, b, h:h + 1],
                                    accum_out=rsum[:, b, h:h + 1])
                        ins.then_inc(sem["exp_ready"], 1)
                    if 1 <= i <= n:
                        u, b = units[i - 1], (i - 1) % 2
                        act.wait_ge(sem["probsT_psum"], w.next("probsT_psum"))
                        nk = u["nk"]
                        f(pT[:, b, :, 0:nk], tr[b][:, :].rearrange("p (h k) -> p h k", h=2)[:, :, 0:nk],
                                ACT.Copy).then_inc(sem["probsT_ready"], 1)
                    if i >= 2:
                        u, b = units[i - 2], acc[i % 2]
                        act.wait_ge(sem["attn_psum"], w.next("attn_psum"))
                        src = b[:, 0:2 * P].rearrange("p (h s) -> p h s", h=2) if u["wide"] else b[:, 0:P]
                        f(u["dst"], src, ACT.Copy).then_inc(sem["attn_copied"], 1)

            act.wait_ge(sem["angles_ready"], w.next("angles_ready"))
            f(sinT[:, :], ang[:, 0, :], ACT.Sin)
            f(cosT[:, :], ang[:, 1, :], ACT.Sin)
            act.wait_ge(sem["lam_abs"], w.next("lam_abs"))
            f(lamb[:, 1, :], lamb[:, 1, :], ACT.Exp, scale=-1.0).then_inc(sem["lam_exp"], 1)

            act.wait_ge(sem["x_loaded"], w.next("x_loaded", 16))
            act.wait_ge(sem["eps_ready"], w.next("eps_ready"))
            square_sum(x, wait=False)
            finish_h(lambda c: col("mix", c))
            n = 0
            for k in range(9):
                s = slots.next()
                if k == 2:
                    two(n, z0[:, 4, :], z0[:, 5, :], None)
                    halves(n + 1, z0[:, 6, :], P, s)
                    n += 2
                else:
                    j = (0, 2, None, 7, 9, 11, 13, 15, 17)[k]
                    two(n, z0[:, j, :], z0[:, j + 1, :], s)
                    n += 1
            head_norms([z0[:, 2 * i:2 * i + 2, :] for i in range(3)], 1.0 / HD)
            attention(units_mix0())
            slots.at += 4
            norm_ffn(D_FF // CH, lambda c: col("ffn", c))

            square_sum(x)
            finish_h(lambda c: col("mix", DC + c))
            for k in range(8):
                s = slots.next()
                if k < 4:
                    two(k, g_y[:, 2 * k, :], g_y[:, 2 * k + 1, :], s, ACT.Gelu_apprx_tanh)
                else:
                    j = 2 * (k - 4)
                    two(k, g_x[:, j, 3:S + 3], g_x[:, j + 1, 3:S + 3], s)
            act.wait_ge(sem["proj_copied"], w.now("proj_copied"))
            for c in range(DC):
                f(g_xc[:, c, :], g_x[:, c, 3:S + 3], ACT.Identity, scale=col("rconv", 3 * DC + c),
                        bias=col("rconvb", c)).then_inc(sem["xc_started"], 1)
            s = slots.next()
            for h in range(DC):
                act.wait_ge(sem["gates_psum"], w.next("gates_psum"))
                b = gu[h % 2]
                ins = f(g_r[:, h, :], b[:, 0:S], ACT.Sigmoid, bias=col("gab", h))
                if h == DC - 1:
                    ins.then_inc(sem[f"slot{s}_free"], 1)
                f(g_i[:, h, :], b[:, S:2 * S], ACT.Sigmoid, bias=col("gxb", h)).then_inc(sem["proj_copied"], w.mark("proj_copied"))
            act.wait_ge(sem["log_a_ready"], w.next("log_a_ready"))
            f(g_t[:, :, :], g_r[:, :, :], ACT.Tanh).then_inc(sem["tanh_ready"], 1)
            f(g_r[:, :, :], g_r[:, :, :], ACT.Exp).then_inc(sem["decay_ready"], 1)
            act.wait_ge(sem["mult_sq_ready"], w.next("mult_sq_ready"))
            f(g_m[:, :, :], g_m[:, :, :], ACT.Sqrt, scale=-2.0).then_inc(sem["mult_ready"], 1)
            slots.at += 4
            square_sum(x)
            finish_h(lambda c: col("ffn", DC + c))
            act.wait_ge(sem["top_ready"], w.next("top_ready"))
            f(gt[:, :, 1], gt[:, :, 0], ACT.Exp).then_inc(sem["gate_exp"], 1)

            def expert_ffn(w, slots):
                base, n = slots.at, D_FF // CH
                slots.at += 3 * n

                def upper(i):
                    s = (base + i) % NSLOT
                    act.wait_ge(w.sem[f"slot{s}_raw"], w.next(f"slot{s}_raw", 16))
                    f(w_up[:, s, :], ring[:, s, :], ACT.Copy).then_inc(w.sem["hi_ready"], 1)

                def silu(k):
                    act.wait_ge(w.sem["gate_up_psum"], w.next("gate_up_psum"))
                    f(sg[:, k % 2, :], gu[k % 2][:, 0:S], ACT.Silu).then_inc(w.sem["silu_ready"], 1)

                def hidden_upper(k):
                    act.wait_ge(w.sem["hidT_psum"], w.next("hidT_psum"))
                    f(hid_up[:, :, k % 2 * P:k % 2 * P + P], tr[k % 2][:, 0:S].rearrange("p (f s) -> p f s", f=2),
                      ACT.Copy).then_inc(w.sem["hidT_up"], 1)

                def step(k):
                    first, m = expert_loads(k + 1)
                    upper(first)
                    if m > 1:
                        upper(first + 1)
                    silu(k)
                    if k:
                        hidden_upper(k - 1)
                    if m > 2:
                        upper(first + 2)

                def start():
                    upper(0)
                    upper(1)
                    for i in range(2):
                        act.wait_ge(sem["chosen_h_psum"], w.next("chosen_h_psum"))
                        for c in range(4 * i, 4 * i + 4):
                            ins = f(hT_up[:, c, 0:P], tr[i][:, c % 4 * P:c % 4 * P + P], ACT.Copy, scale=col("ffn", DC + c))
                        ins.then_inc(sem["chosen_h_up"], 1)

                def rest():
                    step(0)
                    with w.loop(n // 2 - 1, {"gate_up_psum": 2, "hidT_psum": 2}
                                | {f"slot{s}_raw": 16 for s in range(NSLOT)}):
                        step(1)
                        step(2)
                    step(n - 1)
                    upper(expert_loads(n + 1)[0])
                    hidden_upper(n - 1)

                return start, rest

            def experts(w, slots):
                start, rest = expert_ffn(w, slots)

                def expert(last=False):
                    rest()
                    act.wait_ge(sem["selT_psum"], w.next("selT_psum"))
                    f(selT[:, :, :], acc[2][:, 0:S].rearrange("p (t s) -> p t s", t=TT), ACT.Copy).then_inc(sem["selT_ready"], 1)
                    act.wait_ge(sem["expert_ffn_psum"], w.next("expert_ffn_psum"))
                    f(ye[:, 0:HALF], acc[0][:, :], ACT.Copy).then_inc(w.sem[f"slot{(slots.at - 1) % NSLOT}_free"], 1)
                    f(ye[:, HALF:D], acc[1][:, :], ACT.Copy).then_inc(sem["expert_out"], 1)
                    if not last:
                        start()

                start()
                per = ({"selT_psum": 1, "chosen_h_psum": 2, "gate_up_psum": 14, "hidT_psum": 14, "expert_ffn_psum": 1}
                       | {f"slot{s}_raw": 16 * 7 for s in range(NSLOT)})
                with w.loop(N_EXP - 1, per):
                    expert()
                expert(last=True)

            experts(w, slots)
            act.wait_ge(sem["count_ready"], w.next("count_ready"))
            n_max = act.value_load(cnt[0:1, 0:1], min_val=0, max_val=S)
            with act.If(n_max > CAP):
                experts(w.branch(sem_over), Slots())

            def layer(l):
                norm_ffn(FFN_DIM // CH, lambda c: col2("ffn1", c))
                square_sum(x)
                finish_h(lambda c: col2("mix", c))
                n = 0
                for m in range(2):
                    for j in (0, 2):
                        s = slots.next()
                        two(n, q2[:, 4 * m + j, :], q2[:, 4 * m + j + 1, :], s)
                        n += 1
                    s = slots.next()
                    two(n, v2[:, m, 0, :], v2[:, m, 1, :], s)
                    n += 1
                    if m == 0:
                        s = slots.next()
                        copy_fill(n, [(zf[r:r + 4, :], gu[n % 2][r:r + 4, 0:S], ACT.Copy, {}) for r in (0, 64)], s)
                        n += 1
                for k in range(7):
                    s = slots.next()
                    two(n, zr[:, 2 * k, 1:S + 1], zr[:, 2 * k + 1, 1:S + 1], s)
                    n += 1
                s = slots.next()
                halves(n, zr[:, 14, 1:S + 1], 32, s)
                head_norms([q2[:, 2 * i:2 * i + 2, :] for i in range(4)], 1.0 / HD)
                act.wait_ge(sem["forget_abs"], w.next("forget_abs"))
                f(fsc[:, 2, :], fsc[:, 1, :], ACT.Exp, scale=-1.0).then_inc(sem["forget_exp"], 1)
                attention(units_causal(0) + units_causal(1))
                rwkv()
                slots.at += 4
                square_sum(mem, wait=False)
                finish_h(lambda c: col2("mem", c))
                for k in range(4):
                    s = slots.next()
                    if k < 2:
                        two(k, xk[:, 2 * k, :], xk[:, 2 * k + 1, :], s)
                    else:
                        two(k, xv[:, 0, (k - 2) * CH:(k - 2) * CH + CH], xv[:, 1, (k - 2) * CH:(k - 2) * CH + CH], s)
                square_sum(x)
                finish_h(lambda c: col2("xat", c))
                for k in range(2):
                    s = slots.next()
                    two(k, xq[:, 2 * k, :], xq[:, 2 * k + 1, :], s)
                head_norms([xk[:, 2 * i:2 * i + 2, :] for i in range(2)]
                           + [xq[:, 2 * i:2 * i + 2, :] for i in range(2)], 1.0 / P)
                attention(units_mem())
                slots.at += 2
                norm_ffn(FFN_DIM // CH, lambda c: col2("ffn2", c))
                slots.at += SKIP2

            def rwkv():
                s = slots.next()
                act.wait_ge(sem["tail_shifted"], w.next("tail_shifted"))
                f(zr[0:64, 12, 1:S + 1], zr[0:64, 12, 1:S + 1], ACT.Tanh)
                f(zr[:, 13, 1:S + 1], zr[:, 13, 1:S + 1], ACT.Sigmoid)
                f(zr[0:32, 14, 1:S + 1], zr[0:32, 14, 1:S + 1], ACT.Sigmoid).then_inc(sem["lora_ready"], 1)
                for j in range(3):
                    for p in range(4):
                        act.wait_ge(sem["lora_psum"], w.next("lora_psum"))
                        b = gu[(4 * j + p) % 2][:, 0:S]
                        if j == 0:
                            ins = f(lw[:, p, :], b, ACT.Sigmoid, bias=col2("w0", p))
                        elif j == 1:
                            ins = f(ra[:, p, :], b, ACT.Sigmoid, bias=col2("a0", p))
                        elif p < 3:
                            ins = f(rg[:, p, :], b, ACT.Copy)
                        else:
                            f(rg[:, p, 0:P], b[:, 0:P], ACT.Copy).then_inc(sem[f"slot{s}_free"], 1)
                            ins = f(rg[:, p, P:S], b[:, P:S], ACT.Copy)
                        ins.then_inc(sem["proj_copied"], w.mark("proj_copied"))
                act.wait_ge(sem["removal_keys"], w.next("removal_keys"))
                for i in range(2):
                    f(sqb[i].rearrange("p (a b) -> p a b", a=2), kk[:, 2 * i:2 * i + 2, :], ACT.Square).then_inc(sem["squares_ready"], 1)
                for i in range(2):
                    act.wait_ge(sem["sumsq_psum"], w.next("sumsq_psum"))
                    f(rtb[i], tr[i][:, :], ACT.Sqrt).then_inc(sem["root_ready"], 1)
                act.wait_ge(sem["sums_ready"], w.next("sums_ready"))
                f(ew[:, :, :], cw[:, :, :], ACT.Exp).then_inc(sem["decays_ready"], 1)
                f(ei[:, :, :], cw[:, :, :], ACT.Exp, scale=-1.0).then_inc(sem["decays_ready"], 1)
                f(ep[:, :, :], ep[:, :, :], ACT.Exp).then_inc(sem["decays_ready"], 1)
                f(et[:, :, :], et[:, :, :], ACT.Exp).then_inc(sem["decays_ready"], 1)
                for dst in (Vt, Bt, Kt):
                    for t in range(TT):
                        act.wait_ge(sem["tokens_psum"], w.next("tokens_psum"))
                        f(dst[:, t, :], tr[t][:, :], ACT.Copy).then_inc(sem["tokens_copied"], 1)
                for t in range(TT):
                    act.wait_ge(sem["akv_psum"], w.next("akv_psum"))
                    f(AkV[:, t, :], tr[t][:, :], ACT.Copy).then_inc(sem["akv_ready"], 1)
                for k in range(4 * (len(LEVELS) - 1)):
                    act.wait_ge(sem["inv_x_psum"], w.next("inv_x_psum"))
                    f(Xb[:, k % 2, :], gu[k % 2][:, :], ACT.Copy).then_inc(sem["inv_x_ready"], 1)
                for c in range(NRW):
                    t, r = c // 2, slice(RW * (c % 2), RW * (c % 2) + RW)
                    if c:
                        act.wait_ge(sem["carry_y_psum"], w.next("carry_y_psum"))
                        f(yS[r, t, :], gu[1][r, :], ACT.Copy).then_inc(sem["carry_y_ready"], 1)
                    act.wait_ge(sem["removal_psum"], w.next("removal_psum"))
                    f(SA[r, t, :], tr[0][r, :], ACT.Copy).then_inc(sem["removal_ready"], 1)
                for t in range(TT):
                    act.wait_ge(sem["y_var"], w.next("y_var"))
                    f(gnst[:, 2, :], gnst[:, 1, :], ACT.Sqrt, scale=1.0 / HD, bias=epsc[:, 1:2]).then_inc(sem["y_root"], 1)
                for t in range(TT):
                    act.wait_ge(sem["yT_psum"], w.next("yT_psum"))
                    for p in range(4):
                        ins = f(mixT[:, 2 + p, t * P:t * P + P], acc[2 + t][:, p * P:p * P + P], ACT.Identity,
                                scale=col2("ln_w", p), bias=col2("ln_b", p))
                    ins.then_inc(sem["yT_ready"], 1)

            act.wait_ge(sem["mem_loaded"], w.next("mem_loaded", 16))
            run_layers(w, layer, LAYER_ACT)

        @block.vector
        def _(dve):
            w = Turns(dve, sem)
            slots = Slots()
            v = nc.vector

            def log1p(out, e, z, z2):
                v.tensor_scalar(z, e, 2.0, None, ALU.add).then_inc(sem["dve_done"], w.mark("dve_done"))
                dve.wait_ge(sem["dve_done"], w.now("dve_done"))
                v.reciprocal(z, z).then_inc(sem["dve_done"], w.mark("dve_done"))
                dve.wait_ge(sem["dve_done"], w.now("dve_done"))
                v.tensor_tensor(z, z, e, ALU.mult).then_inc(sem["dve_done"], w.mark("dve_done"))
                dve.wait_ge(sem["dve_done"], w.now("dve_done"))
                v.tensor_tensor(z2, z, z, ALU.mult).then_inc(sem["dve_done"], w.mark("dve_done"))
                dve.wait_ge(sem["dve_done"], w.now("dve_done"))
                v.tensor_scalar(out, z2, 1.0 / 13, None, ALU.mult).then_inc(sem["dve_done"], w.mark("dve_done"))
                dve.wait_ge(sem["dve_done"], w.now("dve_done"))
                for d in (11, 9, 7, 5, 3):
                    v.scalar_tensor_tensor(out, out, 1.0 / d, z2, ALU.add, ALU.mult).then_inc(sem["dve_done"], w.mark("dve_done"))
                    dve.wait_ge(sem["dve_done"], w.now("dve_done"))
                v.scalar_tensor_tensor(out, out, 1.0, z, ALU.add, ALU.mult).then_inc(sem["dve_done"], w.mark("dve_done"))
                dve.wait_ge(sem["dve_done"], w.now("dve_done"))
                v.tensor_scalar(out, out, 2.0, None, ALU.mult).then_inc(sem["dve_done"], w.mark("dve_done"))
                dve.wait_ge(sem["dve_done"], w.now("dve_done"))

            def norm(src):
                for t in range(TT):
                    dve.wait_ge(sem["rms_ready"], w.next("rms_ready"))
                    v.reciprocal(ss[:, 1, t:t + 1], ss[:, 1, t:t + 1]).then_inc(sem["dve_done"], w.mark("dve_done"))
                    dve.wait_ge(sem["dve_done"], w.now("dve_done"))
                    v.tensor_scalar(xn[:, t, :], src[:, t, :], ss[:, 1, t:t + 1], None, ALU.mult).then_inc(sem["xn_ready"], 1)

            def finish_h(gain):
                w.next("hT_act", 2)
                for cp in (1, 3):
                    dve.wait_ge(sem["hT_psum_dve"], w.next("hT_psum_dve"))
                    for i in range(2):
                        c = 2 * cp + i
                        ins = v.tensor_scalar(hT[:, c, :], hbank[cp][:, i * S:i * S + S], gain(c), None, ALU.mult)
                    ins.then_inc(sem["hT_dve"], 1)

            def finish_h_split(gain):
                for cp in range(DC // 2):
                    cs = (2 * cp, 2 * cp + 1)
                    if cp % 2 == 0:
                        dve.wait_ge(sem["hT_act"], w.next("hT_act"))
                    else:
                        dve.wait_ge(sem["hT_psum_dve"], w.next("hT_psum_dve"))
                        for i, c in enumerate(cs):
                            ins = v.tensor_scalar(hT_up[:, c, :], hbank[cp][:, i * S:i * S + S], gain(c), None, ALU.mult)
                        ins.then_inc(sem["dve_done"], w.mark("dve_done"))
                        dve.wait_ge(sem["dve_done"], w.now("dve_done"))
                    for i, c in enumerate(cs):
                        ins = v.scalar_tensor_tensor(hT_low[:, c, :], hbank[cp][:, i * S:i * S + S], gain(c),
                                                     hT_up[:, c, :].bitcast(F32), ALU.mult, ALU.subtract)
                    ins.then_inc(sem["hT_dve"], 1)

            def head_norms(pairs, gains):
                for i, (pair, gain) in enumerate(zip(pairs, gains)):
                    dve.wait_ge(sem["root_ready"], w.next("root_ready"))
                    v.reciprocal(rtb[i % 2], rtb[i % 2]).then_inc(sem["dve_done"], w.mark("dve_done"))
                    dve.wait_ge(sem["dve_done"], w.now("dve_done"))
                    v.scalar_tensor_tensor(pair, pair, gain, rtb[i % 2].rearrange("p (a b) -> p a b", a=2),
                                                 ALU.mult, ALU.mult).then_inc(sem["qk_ready"], 1)

            def attention(units, between=()):
                n = len(units)

                def maxima(i):
                    u, b = units[i], i % 2
                    nk = u["nk"]
                    src = sbank[b][:, :, 0:nk]
                    dst = sc[:, b, :, 0:nk]
                    dve.wait_ge(sem["scores_psum"], w.next("scores_psum"))
                    if "slope" in u:
                        for h in range(2):
                            ins = v.scalar_tensor_tensor(sc[:, b, h, 0:nk], awin[:, S - nk:S], u["slope"][h],
                                                         sbank[b][:, h, 0:nk], ALU.mult, ALU.add)
                        ins.then_inc(sem["dve_done"], w.mark("dve_done"))
                        dve.wait_ge(sem["dve_done"], w.now("dve_done"))
                        src = dst
                    elif "causal" in u:
                        v.tensor_tensor(dst, src, cmask[:, None, S - nk:S].to_broadcast([P, 2, nk]), ALU.add).then_inc(sem["dve_done"], w.mark("dve_done"))
                        dve.wait_ge(sem["dve_done"], w.now("dve_done"))
                        src = dst
                    ins = v.tensor_reduce(negmx[:, b, :], src, AX.X, ALU.max, negate=True)
                    if "sink" in u:
                        k = u["sink"]
                        ins.then_inc(sem["dve_done"], w.mark("dve_done"))
                        dve.wait_ge(sem["dve_done"], w.now("dve_done"))
                        v.tensor_tensor(negmx[:, b, :], negmx[:, b, :], sinks[:, 8 + k:10 + k], ALU.min).then_inc(sem["dve_done"], w.mark("dve_done"))
                        dve.wait_ge(sem["dve_done"], w.now("dve_done"))
                        ins = v.tensor_tensor(snk[:, b, :], negmx[:, b, :], sinks[:, k:k + 2], ALU.add)
                    ins.then_inc(sem["maxima_ready"], 1)

                def normalise(i):
                    u, b = units[i], i % 2
                    nk = u["nk"]
                    dve.wait_ge(sem["exp_ready"], w.next("exp_ready"))
                    if "sink" in u:
                        v.tensor_tensor(rsum[:, b, :], rsum[:, b, :], snk[:, b, :], ALU.add).then_inc(sem["dve_done"], w.mark("dve_done"))
                        dve.wait_ge(sem["dve_done"], w.now("dve_done"))
                    v.reciprocal(rsum[:, b, :], rsum[:, b, :]).then_inc(sem["dve_done"], w.mark("dve_done"))
                    dve.wait_ge(sem["dve_done"], w.now("dve_done"))
                    v.tensor_tensor(sc[:, b, :, 0:nk], sc[:, b, :, 0:nk],
                                          rsum[:, b, :, None].to_broadcast([P, 2, nk]), ALU.mult).then_inc(sem["probs_ready"], 1)

                for i in range(n + 1):
                    if i < n:
                        maxima(i)
                    if i:
                        normalise(i - 1)
                    if i < len(between):
                        between[i]()

            def add_x(scale, freed):
                for i in range(2 * TT):
                    o = x[:, i // 2, (i % 2) * HALF:(i % 2) * HALF + HALF]
                    if scale == 1.0:
                        ins = v.tensor_tensor(o, o, acc[i][:, :], ALU.add)
                    else:
                        ins = v.scalar_tensor_tensor(o, acc[i][:, :], scale, o, ALU.mult, ALU.add)
                    if i == 0:
                        ins.then_inc(sem[f"slot{freed}_free"], 1)
                    if i % 2:
                        ins.then_inc(sem["x_ready"], 1)

            def out_proj(nslots):
                slots.at += nslots
                dve.wait_ge(sem["out_psum"], w.next("out_psum"))
                add_x(1.0, (slots.at - 1) % NSLOT)

            def norm_ffn(n, gain, scale, first=False):
                base = slots.at
                slots.at += 3 * n

                def lower(k, j):
                    s = (base + 3 * k + j) % NSLOT
                    dve.wait_ge(sem["hi_ready"], w.next("hi_ready"))
                    if k or not first:
                        dve.wait_ge(sem["lo_used"], w.next("lo_used"))
                    v.tensor_tensor(w_low[:, j, :], ring[:, s, :], w_up[:, s, :].bitcast(F32), ALU.subtract).then_inc(sem["lo_ready"], 1)

                def hidden_rows(j):
                    dve.wait_ge(sem["silu_ready"], w.next("silu_ready"))
                    v.tensor_tensor(sg[:, j, :], sg[:, j, :], gu[j][:, S:2 * S], ALU.mult).then_inc(sem["dve_done"], w.mark("dve_done"))
                    dve.wait_ge(sem["dve_done"], w.now("dve_done"))
                    v.tensor_copy(hid_up[:, j, :], sg[:, j, :]).then_inc(sem["dve_done"], w.mark("dve_done"))
                    dve.wait_ge(sem["dve_done"], w.now("dve_done"))
                    v.tensor_tensor(hid_low[:, j, :], sg[:, j, :], hid_up[:, j, :].bitcast(F32), ALU.subtract).then_inc(sem["hidden_ready"], 1)

                def step(k):
                    hidden_rows(0)
                    lower(k + 1, 0)
                    lower(k + 1, 1)
                    hidden_rows(1)
                    lower(k + 1, 2)

                norm(x)
                lower(0, 0)
                finish_h_split(gain)
                lower(0, 1)
                lower(0, 2)
                with w.loop((n - 1) // 2, {"silu_ready": 4, "hi_ready": 6, "lo_used": 6, "dve_done": 8}):
                    step(0)
                    step(1)
                if n % 2 == 0:
                    step(n - 2)
                hidden_rows(0)
                hidden_rows(1)
                dve.wait_ge(sem["ffn_psum"], w.next("ffn_psum"))
                add_x(scale, (slots.at - 1) % NSLOT)

            dve.wait_ge(sem["consts_ready"], w.next("consts_ready"))
            for k in range(len(LEVELS)):
                for m, (a, b) in enumerate(((part_i, col_i), (col_i, part_i))):
                    v.tensor_scalar(lv_a[:, :], a[:, :], k, None, ALU.logical_shift_right).then_inc(sem["dve_done"], w.mark("dve_done"))
                    dve.wait_ge(sem["dve_done"], w.now("dve_done"))
                    v.tensor_scalar(lv_b[:, :], b[:, :], k, 1, ALU.logical_shift_right, ALU.bitwise_xor).then_inc(sem["dve_done"], w.mark("dve_done"))
                    dve.wait_ge(sem["dve_done"], w.now("dve_done"))
                    v.tensor_tensor(lv_c[:, :], lv_a[:, :], lv_b[:, :], ALU.is_equal).then_inc(sem["dve_done"], w.mark("dve_done"))
                    dve.wait_ge(sem["dve_done"], w.now("dve_done"))
                    v.tensor_scalar(lv_a[:, :], lv_a[:, :], 1, None, ALU.bitwise_and).then_inc(sem["dve_done"], w.mark("dve_done"))
                    dve.wait_ge(sem["dve_done"], w.now("dve_done"))
                    v.tensor_tensor(lvl[:, m, k, :], lv_a[:, :], lv_c[:, :], ALU.mult).then_inc(sem["dve_done"], w.mark("dve_done"))
                    dve.wait_ge(sem["dve_done"], w.now("dve_done"))
            dve.wait_ge(sem["cols_psum"], w.next("cols_psum"))
            v.tensor_copy(pv1[:, :], tr[0][:, 0:N1])
            for l in range(DEPTH2):
                v.tensor_copy(pv2[:, l, :], tr[0][:, P + l * N2:P + l * N2 + N2])
            v.tensor_copy(fcol[:, :], tr[1][:, 0:1]).then_inc(sem["cols_ready"], w.mark("cols_ready"))
            dve.wait_ge(sem["cols_ready"], w.now("cols_ready"))
            v.tensor_scalar(col("qg"), col("qg"), HD ** -0.5, None, ALU.mult)
            for name, dim in (("fqg", HD), ("mqg", HD), ("xqg", P)):
                c = pv2[:, :, V2[name][0]]
                v.tensor_scalar(c, c, dim ** -0.5, None, ALU.mult)
            dve.wait_ge(sem["inputs_loaded"], w.next("inputs_loaded", 48))
            v.tensor_scalar(sinks[:, 8:16], sinks[:, 0:8], -1.0, None, ALU.mult).then_inc(sem["dve_done"], w.mark("dve_done"))
            dve.wait_ge(sem["dve_done"], w.now("dve_done"))
            v.tensor_copy(ang[:, 0, :], pos_i[:, :]).then_inc(sem["dve_done"], w.mark("dve_done"))
            dve.wait_ge(sem["dve_done"], w.now("dve_done"))
            v.tensor_scalar(ang[:, 0, :], ang[:, 0, :], fcol[:, 0:1], None, ALU.mult).then_inc(sem["dve_done"], w.mark("dve_done"))
            dve.wait_ge(sem["dve_done"], w.now("dve_done"))
            v.tensor_scalar(ang[:, 1, :], ang[:, 0, :], 0.15915494309189535, 12582912.0, ALU.mult, ALU.add).then_inc(sem["dve_done"], w.mark("dve_done"))
            dve.wait_ge(sem["dve_done"], w.now("dve_done"))
            v.tensor_scalar(ang[:, 1, :], ang[:, 1, :], -12582912.0, None, ALU.add).then_inc(sem["dve_done"], w.mark("dve_done"))
            dve.wait_ge(sem["dve_done"], w.now("dve_done"))
            for part in (6.28125, 0.0019350051879882812, 3.0199159819e-07):
                v.scalar_tensor_tensor(ang[:, 0, :], ang[:, 1, :], -part, ang[:, 0, :], ALU.mult, ALU.add).then_inc(sem["dve_done"], w.mark("dve_done"))
                dve.wait_ge(sem["dve_done"], w.now("dve_done"))
            v.tensor_scalar(ang[:, 0, :], ang[:, 0, :], 3.1415925, -3.1415925, ALU.min, ALU.max).then_inc(sem["dve_done"], w.mark("dve_done"))
            dve.wait_ge(sem["dve_done"], w.now("dve_done"))
            v.tensor_scalar(ang[:, 2, :], ang[:, 0, :], -1.0, None, ALU.mult).then_inc(sem["dve_done"], w.mark("dve_done"))
            dve.wait_ge(sem["dve_done"], w.now("dve_done"))
            v.tensor_tensor(ang[:, 1, :], ang[:, 0, :], ang[:, 2, :], ALU.min).then_inc(sem["dve_done"], w.mark("dve_done"))
            dve.wait_ge(sem["dve_done"], w.now("dve_done"))
            v.tensor_scalar(ang[:, 1, :], ang[:, 1, :], 1.5707963267948966, None, ALU.add).then_inc(sem["angles_ready"], 1)
            lam = pv1[:, V1["lam"][0]:V1["lam"][1]]
            v.tensor_scalar(lamb[:, 0, :], lam, -1.0, None, ALU.mult).then_inc(sem["dve_done"], w.mark("dve_done"))
            dve.wait_ge(sem["dve_done"], w.now("dve_done"))
            v.tensor_tensor(lamb[:, 1, :], lamb[:, 0, :], lam, ALU.max).then_inc(sem["lam_abs"], 1)
            dve.wait_ge(sem["lam_exp"], w.next("lam_exp"))
            v.tensor_scalar(lamb[:, 4, :], lam, -1.0, 0.0, ALU.mult, ALU.max).then_inc(sem["dve_done"], w.mark("dve_done"))
            dve.wait_ge(sem["dve_done"], w.now("dve_done"))
            log1p(lamb[:, 0, :], lamb[:, 1, :], lamb[:, 2, :], lamb[:, 3, :])
            v.tensor_tensor(lamb[:, 4, :], lamb[:, 4, :], lamb[:, 0, :], ALU.add).then_inc(sem["dve_done"], w.mark("dve_done"))
            dve.wait_ge(sem["dve_done"], w.now("dve_done"))
            v.tensor_scalar(lamb[:, 4, :], lamb[:, 4, :], -8.0, None, ALU.mult).then_inc(sem["dve_done"], w.mark("dve_done"))
            dve.wait_ge(sem["dve_done"], w.now("dve_done"))

            norm(x)
            finish_h(lambda c: col("mix", c))
            v.memset(gcu[:, :, 0:2], 0.0)
            dve.wait_ge(sem["proj_copied"], w.next("proj_copied", 10))
            head_norms([z0[:, 2 * i:2 * i + 2, :] for i in range(3)], [col("qg"), col("qg"), col("kg")])

            def conv(c):
                v.tensor_tensor(gcu[:, c, 2:S + 2], z0[:, 11 + c, :], z0[:, 15 + c, :], ALU.mult).then_inc(sem["dve_done"], w.mark("dve_done"))
                dve.wait_ge(sem["dve_done"], w.now("dve_done"))
                v.tensor_scalar(cv[:, c, :], gcu[:, c, 0:S], col("hconv", c), None, ALU.mult).then_inc(sem["dve_done"], w.mark("dve_done"))
                dve.wait_ge(sem["dve_done"], w.now("dve_done"))
                for k in (1, 2):
                    v.scalar_tensor_tensor(cv[:, c, :], gcu[:, c, k:k + S], col("hconv", 4 * k + c),
                                                cv[:, c, :], ALU.mult, ALU.add).then_inc(sem["dve_done"], w.mark("dve_done"))
                    dve.wait_ge(sem["dve_done"], w.now("dve_done"))
                ins = v.tensor_tensor(mixT[:, 4 + c, :], cv[:, c, :], z0[:, 7 + c, :], ALU.mult)
                if c == 3:
                    ins.then_inc(sem["conv_ready"], 1)

            attention(units_mix0(), [lambda c=c: conv(c) for c in range(4)])
            out_proj(4 + len(MIX0_LOADS))
            norm_ffn(D_FF // CH, lambda c: col("ffn", c), 1.0, first=True)

            norm(x)
            finish_h(lambda c: col("mix", DC + c))
            v.memset(g_x[:, :, 0:3], 0.0).then_inc(sem["dve_done"], w.mark("dve_done"))
            dve.wait_ge(sem["dve_done"], w.now("dve_done"))
            dve.wait_ge(sem["proj_copied"], w.next("proj_copied", 8))
            for c in range(DC):
                dve.wait_ge(sem["xc_started"], w.next("xc_started"))
                for k in range(3):
                    ins = v.scalar_tensor_tensor(g_xc[:, c, :], g_x[:, c, k:k + S], col("rconv", k * DC + c),
                                                 g_xc[:, c, :], ALU.mult, ALU.add)
                    if k < 2:
                        ins.then_inc(sem["dve_done"], w.mark("dve_done"))
                        dve.wait_ge(sem["dve_done"], w.now("dve_done"))
                ins.then_inc(sem["xc_ready"], 1)
            for h in range(DC):
                dve.wait_ge(sem["proj_copied"], w.next("proj_copied"))
                ins = v.tensor_scalar(g_r[:, h, :], g_r[:, h, :], lamb[:, 4, h:h + 1], None, ALU.mult)
            ins.then_inc(sem["log_a_ready"], 1)
            v.tensor_tensor(g_i[:, :, :], g_i[:, :, :], g_xc[:, :, :], ALU.mult).then_inc(sem["dve_done"], w.mark("dve_done"))
            dve.wait_ge(sem["dve_done"], w.now("dve_done"))
            dve.wait_ge(sem["tanh_ready"], w.next("tanh_ready"))
            v.tensor_scalar(g_m[:, :, :], g_t[:, :, :], -1.0, 1.0, ALU.mult, ALU.add).then_inc(sem["dve_done"], w.mark("dve_done"))
            dve.wait_ge(sem["dve_done"], w.now("dve_done"))
            v.reciprocal(g_m[:, :, :], g_m[:, :, :]).then_inc(sem["dve_done"], w.mark("dve_done"))
            dve.wait_ge(sem["dve_done"], w.now("dve_done"))
            v.tensor_tensor(g_m[:, :, :], g_m[:, :, :], g_t[:, :, :], ALU.mult).then_inc(sem["mult_sq_ready"], 1)
            dve.wait_ge(sem["decay_ready"], w.next("decay_ready"))
            v.memset(g_r[:, :, 0:1], 0.0)
            dve.wait_ge(sem["mult_ready"], w.next("mult_ready"))
            v.memset(g_m[:, :, 0:1], 1.0).then_inc(sem["dve_done"], w.mark("dve_done"))
            dve.wait_ge(sem["dve_done"], w.now("dve_done"))
            v.tensor_tensor(g_m[:, :, :], g_m[:, :, :], g_i[:, :, :], ALU.mult).then_inc(sem["dve_done"], w.mark("dve_done"))
            dve.wait_ge(sem["dve_done"], w.now("dve_done"))
            flat = [r[:, :, :].rearrange("p c s -> p (c s)") for r in (g_t, g_r, g_m)]
            v.tensor_tensor_scan(flat[0], flat[1], flat[2], 0.0, ALU.mult, ALU.add).then_inc(sem["dve_done"], w.mark("dve_done"))
            dve.wait_ge(sem["dve_done"], w.now("dve_done"))
            v.tensor_tensor(mixT[:, :, :], g_t[:, :, :], g_y[:, :, :], ALU.mult).then_inc(sem["lru_ready"], 1)
            out_proj(4 + len(MIX1_LOADS) + 1)

            norm(x)
            finish_h(lambda c: col("ffn", DC + c))
            dve.wait_ge(sem["logits_psum"], w.next("logits_psum"))
            v.tensor_copy(lg[:, :, :], tr[0][:, 0:TT * N_EXP].rearrange("p (t e) -> p t e", t=TT)).then_inc(sem["dve_done"], w.mark("dve_done"))
            dve.wait_ge(sem["dve_done"], w.now("dve_done"))
            for t in range(TT):
                v.max(top[:, t, :], lg[:, t, :]).then_inc(sem["dve_done"], w.mark("dve_done"))
                dve.wait_ge(sem["dve_done"], w.now("dve_done"))
                v.max_index(topi[:, t, :], top[:, t, :], lg[:, t, :]).then_inc(sem["dve_done"], w.mark("dve_done"))
                dve.wait_ge(sem["dve_done"], w.now("dve_done"))
            v.tensor_tensor(gt[:, :, 0:1], top[:, :, 1:2], top[:, :, 0:1], ALU.subtract).then_inc(sem["top_ready"], 1)
            v.tensor_copy(topf[:, :, :], topi[:, :, :]).then_inc(sem["dve_done"], w.mark("dve_done"))
            dve.wait_ge(sem["dve_done"], w.now("dve_done"))
            for j in range(2):
                for t in range(TT):
                    v.tensor_scalar(hot[:, j, t, :], iota_s[:, 0:N_EXP], topf[:, t, j:j + 1], None,
                                         ALU.is_equal).then_inc(sem["dve_done"], w.mark("dve_done"))
                    dve.wait_ge(sem["dve_done"], w.now("dve_done"))
            dve.wait_ge(sem["gate_exp"], w.next("gate_exp"))
            v.tensor_scalar(gt[:, :, 2:3], gt[:, :, 1:2], 1.0, None, ALU.add).then_inc(sem["dve_done"], w.mark("dve_done"))
            dve.wait_ge(sem["dve_done"], w.now("dve_done"))
            v.reciprocal(gt[:, :, 2:3], gt[:, :, 2:3]).then_inc(sem["dve_done"], w.mark("dve_done"))
            dve.wait_ge(sem["dve_done"], w.now("dve_done"))
            v.tensor_tensor(gt[:, :, 3:4], gt[:, :, 1:2], gt[:, :, 2:3], ALU.mult).then_inc(sem["dve_done"], w.mark("dve_done"))
            dve.wait_ge(sem["dve_done"], w.now("dve_done"))
            for t in range(TT):
                v.tensor_scalar(route[:, 1, t, :], hot[:, 0, t, :], gt[:, t, 2:3], None, ALU.mult).then_inc(sem["dve_done"], w.mark("dve_done"))
                dve.wait_ge(sem["dve_done"], w.now("dve_done"))
                v.scalar_tensor_tensor(route[:, 1, t, :], hot[:, 1, t, :], gt[:, t, 3:4], route[:, 1, t, :],
                                            ALU.mult, ALU.add).then_inc(sem["dve_done"], w.mark("dve_done"))
                dve.wait_ge(sem["dve_done"], w.now("dve_done"))
            v.tensor_tensor(route[:, 2, :, :], hot[:, 0, :, :], hot[:, 1, :, :], ALU.add).then_inc(sem["chosen_ready"], 1)
            dve.wait_ge(sem["ranks_psum"], w.next("ranks_psum"))
            v.tensor_copy(route[:, 0, :, :], tr[1][:, 0:TT * N_EXP].rearrange("p (t e) -> p t e", t=TT))
            v.tensor_reduce(cnt_f[:, 0:1], tr[1][:, 32:32 + N_EXP], AX.X, ALU.max).then_inc(sem["ranks_ready"], w.mark("ranks_ready"))
            dve.wait_ge(sem["ranks_ready"], w.now("ranks_ready"))
            v.tensor_copy(cnt[:, :], cnt_f[:, 0:1]).then_inc(sem["count_ready"], w.mark("count_ready"))
            dve.wait_ge(sem["count_ready"], w.now("count_ready"))

            def expert_ffn(w, slots):
                base, n = slots.at, D_FF // CH
                slots.at += 3 * n

                def lower(i):
                    s = (base + i) % NSLOT
                    dve.wait_ge(w.sem["hi_ready"], w.next("hi_ready"))
                    dve.wait_ge(w.sem["lo_used"], w.next("lo_used"))
                    v.tensor_tensor(w_low[:, i % NLOW, :], ring[:, s, :], w_up[:, s, :].bitcast(F32),
                                    ALU.subtract).then_inc(w.sem["lo_ready"], 1)

                def hidden_rows(k):
                    dve.wait_ge(w.sem["silu_ready"], w.next("silu_ready"))
                    v.tensor_tensor(sg[:, k % 2, :], sg[:, k % 2, :], gu[k % 2][:, S:2 * S],
                                    ALU.mult).then_inc(w.sem["hidden_ready"], 1)

                def hidden_lower(k):
                    dve.wait_ge(w.sem["hidT_up"], w.next("hidT_up"))
                    cs = slice(k % 2 * P, k % 2 * P + P)
                    v.tensor_tensor(hid_low[:, :, cs], tr[k % 2][:, 0:S].rearrange("p (f s) -> p f s", f=2),
                                    hid_up[:, :, cs].bitcast(F32), ALU.subtract).then_inc(w.sem["hidT_ready"], 1)

                def step(k):
                    first, m = expert_loads(k + 1)
                    lower(first)
                    if m > 1:
                        lower(first + 1)
                    hidden_rows(k)
                    if k:
                        hidden_lower(k - 1)
                    if m > 2:
                        lower(first + 2)

                def start():
                    lower(0)
                    lower(1)
                    for i in range(2):
                        dve.wait_ge(sem["chosen_h_up"], w.next("chosen_h_up"))
                        for c in range(4 * i, 4 * i + 4):
                            ins = v.scalar_tensor_tensor(hT_low[:, c, 0:P], tr[i][:, c % 4 * P:c % 4 * P + P],
                                                         col("ffn", DC + c), hT_up[:, c, 0:P].bitcast(F32),
                                                         ALU.mult, ALU.subtract)
                        ins.then_inc(sem["chosen_h_ready"], 1)

                def rest():
                    step(0)
                    with w.loop(n // 2 - 1, {"hi_ready": 6, "lo_used": 6, "silu_ready": 2, "hidT_up": 2}):
                        step(1)
                        step(2)
                    step(n - 1)
                    lower(expert_loads(n + 1)[0])
                    hidden_lower(n - 1)

                return start, rest

            def experts(w, slots):
                start, rest = expert_ffn(w, slots)

                def select(e):
                    v.tensor_copy(cur[:, :, :, None], route[:, :, :, bass.ds(e, 1)]).then_inc(w.sem["dve_done"], w.mark("dve_done"))
                    dve.wait_ge(w.sem["dve_done"], w.now("dve_done"))
                    for t in range(TT):
                        v.tensor_scalar(sel[:, t, :], iota_s[:, :], cur[:, 0, t:t + 1], cur[:, 2, t:t + 1],
                                        ALU.is_equal, ALU.mult)
                        ins = v.tensor_scalar(selg[:, t, :], iota_s[:, :], cur[:, 0, t:t + 1], cur[:, 1, t:t + 1],
                                              ALU.is_equal, ALU.mult)
                    ins.then_inc(sem["sel_ready"], 1)

                def add():
                    dve.wait_ge(sem["expert_psum"], w.next("expert_psum"))
                    for i, b in enumerate(ebank):
                        o = x[:, i // 2, (i % 2) * HALF:(i % 2) * HALF + HALF]
                        ins = v.tensor_tensor(o, o, b[:, :], ALU.add)
                    ins.then_inc(sem["expert_added"], 1)

                select(0)
                v.memset(cnt_f[:, 1:2], 0.0).then_inc(sem["expert_added"], 1)
                start()
                per = {"dve_done": 1, "chosen_h_up": 2, "hi_ready": 42, "lo_used": 42, "silu_ready": 14,
                       "hidT_up": 14, "expert_psum": 1}
                with w.loop(N_EXP - 1, per) as e:
                    rest()
                    select(e + 1)
                    start()
                    add()
                rest()
                add()

            experts(w, slots)
            n_max = dve.value_load(cnt[0:1, 0:1], min_val=0, max_val=S)
            with dve.If(n_max > CAP):
                over = w.branch(sem_over)
                v.tensor_scalar(route[:, 0, :, :], route[:, 0, :, :], float(CAP), None, ALU.subtract).then_inc(over.sem["dve_done"], over.mark("dve_done"))
                dve.wait_ge(over.sem["dve_done"], over.now("dve_done"))
                dve.sem_inc(over.sem["lo_used"], NLOW)
                experts(over, Slots())
            for t in range(TT):
                v.memset(took[:, t:t + 1], 0.0).then_inc(sem["x_ready"], 1)

            def layer(l):
                v.tensor_copy(pv[:, None, :], pv2[:, bass.ds(l, 1), :]).then_inc(sem["dve_done"], w.mark("dve_done"))
                dve.wait_ge(sem["dve_done"], w.now("dve_done"))
                norm_ffn(FFN_DIM // CH, lambda c: col2("ffn1", c), 0.5)
                norm(x)
                v.memset(zr[:, :, 0:1], 0.0)
                v.memset(zf, 0.0)
                finish_h(lambda c: col2("mix", c))
                dve.wait_ge(sem["proj_copied"], w.next("proj_copied", 15))
                head_norms([q2[:, 2 * i:2 * i + 2, :] for i in range(4)],
                           [col2(n) for n in ("fqg", "fkg", "mqg", "mkg")])
                f0, f1, f2, f3, f4, f5 = (fsc[:, i, :] for i in range(6))
                v.tensor_scalar(f0, zf, col2("fb"), None, ALU.add).then_inc(sem["dve_done"], w.mark("dve_done"))
                dve.wait_ge(sem["dve_done"], w.now("dve_done"))
                v.tensor_scalar(f1, f0, -1.0, None, ALU.mult).then_inc(sem["dve_done"], w.mark("dve_done"))
                dve.wait_ge(sem["dve_done"], w.now("dve_done"))
                v.tensor_tensor(f1, f1, f0, ALU.max).then_inc(sem["forget_abs"], 1)
                for i in range(2):
                    dve.wait_ge(sem["rope_psum"], w.next("rope_psum"))
                    q, turned = q2[:, 4 + 2 * i:6 + 2 * i, :], rtb[i].rearrange("p (a b) -> p a b", a=2)
                    v.tensor_tensor(turned, gu[i][:, :].rearrange("p (a b) -> p a b", a=2),
                                    sinT[:, None, :].to_broadcast([P, 2, S]), ALU.mult)
                    v.tensor_tensor(q, q, cosT[:, None, :].to_broadcast([P, 2, S]), ALU.mult).then_inc(sem["dve_done"], w.mark("dve_done"))
                    dve.wait_ge(sem["dve_done"], w.now("dve_done"))
                    v.tensor_tensor(q, q, turned, ALU.add).then_inc(sem["rope_ready"], 1)
                dve.wait_ge(sem["forget_exp"], w.next("forget_exp"))
                log1p(f5, f2, f1, f3)
                v.memset(f3, 1.0)
                v.scalar_tensor_tensor(f0, f0, 0.0, f5, ALU.min, ALU.subtract).then_inc(sem["dve_done"], w.mark("dve_done"))
                dve.wait_ge(sem["dve_done"], w.now("dve_done"))
                v.tensor_tensor_scan(f4, f3, f0, 0.0, ALU.mult, ALU.add).then_inc(sem["dve_done"], w.mark("dve_done"))
                dve.wait_ge(sem["dve_done"], w.now("dve_done"))
                v.tensor_scalar(f5, f4, -1.0, None, ALU.mult).then_inc(sem["forget_ready"], 1)

                def shift(tiles, rows_=P, name="dve_done"):
                    a, n = tiles[0], len(tiles)
                    d = zd[0:rows_, 0:n, :]
                    v.tensor_tensor(d, zr[0:rows_, a:a + n, 0:S], zr[0:rows_, a:a + n, 1:S + 1], ALU.subtract).then_inc(sem["dve_done"], w.mark("dve_done"))
                    dve.wait_ge(sem["dve_done"], w.now("dve_done"))
                    for i, c in enumerate(tiles):
                        o = zr[0:rows_, c, 1:S + 1]
                        ins = v.scalar_tensor_tensor(o, zd[0:rows_, i, :], col2("mu", c)[0:rows_, :], o,
                                                     ALU.mult, ALU.add)
                    ins.then_inc(sem[name], w.mark(name))
                    dve.wait_ge(sem[name], w.now(name))

                def shift_tail():
                    shift((12, 13))
                    shift((14,), 32, "tail_shifted")

                attention(units_causal(0) + units_causal(1),
                          [shift_tail, lambda: shift((0, 1, 2, 3)), lambda: shift((4, 5, 6, 7)),
                           lambda: shift((8, 9, 10, 11), name="tokens_in")])
                rwkv()
                out_proj(4 + len(MIX2_LOADS) + 1)
                norm(mem)
                finish_h(lambda c: col2("mem", c))
                norm(x)
                finish_h(lambda c: col2("xat", c))
                dve.wait_ge(sem["proj_copied"], w.next("proj_copied", 6))
                head_norms([xk[:, 2 * i:2 * i + 2, :] for i in range(2)] + [xq[:, 2 * i:2 * i + 2, :] for i in range(2)],
                           [col2("xkg"), col2("xkg"), col2("xqg"), col2("xqg")])
                attention(units_mem())
                out_proj(2 + len(XKV_LOADS) + len(XQ_LOADS))
                norm_ffn(FFN_DIM // CH, lambda c: col2("ffn2", c), 0.5)
                slots.at += SKIP2

            def rwkv():
                r_, k_, v_ = (zr[:, 4 * i:4 * i + 4, 1:S + 1] for i in range(3))

                def flat(a):
                    return a[:, :, :].rearrange("p a b -> p (a b)")

                def chunks(a):
                    return flat(a).rearrange("p (c s) -> p c s", s=RW)

                dve.wait_ge(sem["proj_copied"], w.next("proj_copied", 4))
                v.tensor_scalar(lw[:, :, :], lw[:, :, :], -(2.718281828459045 ** -0.5), None, ALU.mult).then_inc(sem["dve_done"], w.mark("dve_done"))
                dve.wait_ge(sem["dve_done"], w.now("dve_done"))
                v.tensor_tensor_scan(flat(cw), keep[:, :], flat(lw), 0.0, ALU.mult, ALU.add).then_inc(sem["dve_done"], w.mark("dve_done"))
                dve.wait_ge(sem["dve_done"], w.now("dve_done"))
                v.tensor_tensor(ep[:, :, :], cw[:, :, :], lw[:, :, :], ALU.subtract)
                v.tensor_tensor(chunks(et), chunks(cw)[:, :, RW - 1:RW].to_broadcast([P, S * 4 // RW, RW]),
                                      chunks(cw), ALU.subtract).then_inc(sem["sums_ready"], 1)
                for p in range(4):
                    ins = v.tensor_scalar(kk[:, p, :], k_[:, p, :], col2("k_k", p), None, ALU.mult)
                ins.then_inc(sem["removal_keys"], 1)
                v.tensor_copy(Tm, ident[:, None, :].to_broadcast([P, 2 * 8, P]))
                v.tensor_copy(Um, ident[:, None, :].to_broadcast([P, 2 * 8, P]))
                dve.wait_ge(sem["proj_copied"], w.next("proj_copied", 4))
                for p in range(4):
                    ins = v.tensor_scalar(Kb[:, p, :], ra[:, p, :], 1.0, col2("k_a", p), ALU.subtract, ALU.mult)
                ins.then_inc(sem["dve_done"], w.mark("dve_done"))
                dve.wait_ge(sem["dve_done"], w.now("dve_done"))
                v.scalar_tensor_tensor(k_, Kb[:, :, :], 1.0, k_, ALU.add, ALU.mult).then_inc(sem["dve_done"], w.mark("dve_done"))
                dve.wait_ge(sem["dve_done"], w.now("dve_done"))
                for i in range(2):
                    dve.wait_ge(sem["root_ready"], w.next("root_ready"))
                    v.tensor_scalar(rtb[i], rtb[i], 1e-12, None, ALU.max).then_inc(sem["dve_done"], w.mark("dve_done"))
                    dve.wait_ge(sem["dve_done"], w.now("dve_done"))
                    v.reciprocal(rtb[i], rtb[i]).then_inc(sem["sumsq_read"], w.mark("sumsq_read"))
                    dve.wait_ge(sem["sumsq_read"], w.now("sumsq_read"))
                    o = kk[:, 2 * i:2 * i + 2, :]
                    v.tensor_tensor(o, o, rtb[i].rearrange("p (a b) -> p a b", a=2), ALU.mult).then_inc(sem["dve_done"], w.mark("dve_done"))
                    dve.wait_ge(sem["dve_done"], w.now("dve_done"))
                v.tensor_tensor(ra[:, :, :], ra[:, :, :], kk[:, :, :], ALU.mult).then_inc(sem["dve_done"], w.mark("dve_done"))
                dve.wait_ge(sem["dve_done"], w.now("dve_done"))
                dve.wait_ge(sem["proj_copied"], w.next("proj_copied", 4))
                for p in range(4):
                    o = rtb[p // 2][:, (p % 2) * S:(p % 2) * S + S]
                    ins = v.scalar_tensor_tensor(o, r_[:, p, :], col2("r_k", p), k_[:, p, :], ALU.mult, ALU.mult)
                    if p % 2:
                        ins.then_inc(sem["bonus_in"], 1)
                dve.wait_ge(sem["decays_ready"], w.next("decays_ready", 4))
                v.tensor_tensor(Bb[:, :, :], ra[:, :, :], et[:, :, :], ALU.mult).then_inc(sem["tokens_in"], w.mark("tokens_in"))
                v.tensor_tensor(Kb[:, :, :], k_, et[:, :, :], ALU.mult).then_inc(sem["tokens_in"], w.mark("tokens_in"))
                v.tensor_tensor(Bh[:, :, :], ra[:, :, :], ei[:, :, :], ALU.mult)
                v.tensor_tensor(Kh[:, :, :], k_, ei[:, :, :], ALU.mult)
                for t in range(TT):
                    ts = slice(t * P, t * P + P)
                    v.scalar_tensor_tensor(AR[:, :, t, 0, :], kk[:, :, ts], -1.0, ep[:, :, ts], ALU.mult, ALU.mult)
                    ins = v.tensor_tensor(AR[:, :, t, 1, :], r_[:, :, ts], ew[:, :, ts], ALU.mult)
                ins.then_inc(sem["gram_in"], 1)
                for i in range(2):
                    dve.wait_ge(sem["bonus_psum"], w.next("bonus_psum"))
                    ins = v.tensor_tensor(bon[:, 2 * i:2 * i + 2, :], gu[i][:, :].rearrange("p (a b) -> p a b", a=2),
                                          v_[:, 2 * i:2 * i + 2, :], ALU.mult)
                ins.then_inc(sem["bonus_ready"], 1)
                for u in range(2 * 8):
                    dve.wait_ge(sem["gram_psum"], w.next("gram_psum"))
                    if u == 0:
                        v.tensor_copy(sdec[:, :, 0:NRW], ew[:, :, :].rearrange("p a (c s) -> p a c s", s=RW)[:, :, :, RW - 1])
                        v.memset(Sbd[:, :, :], 0.0)
                        v.memset(yS[0:RW, 0, :], 0.0)
                    v.tensor_tensor(G[:, u // 8, u % 8, :, :], gu[u % 2][:, :].rearrange("p (k s) -> p k s", k=4),
                                          rmask[:, :, :], ALU.mult).then_inc(sem["gram_ready"], 1)
                def put(M, q, m, k, src):
                    return v.copy_predicated(M[:, 4 * q:4 * q + 4, :], lvl[:, m, k:k + 1, :].to_broadcast([P, 4, P]), src)

                def quad(b):
                    return b[:, :].rearrange("p (j s) -> p j s", j=4)

                for q in range(4):
                    dve.wait_ge(sem["inv_a_psum"], w.next("inv_a_psum"))
                    v.tensor_copy(took[:, q:q + 1], epsc[:, 0:1])
                    put(Tm, q, 0, 0, quad(gu[q % 2]))
                    put(Um, q, 1, 0, G[:, q // 2, 4 * (q % 2):4 * (q % 2) + 4, 0, :]).then_inc(sem["inv_ready"], 1)
                steps = 4 * (len(LEVELS) - 1)
                for k in range(steps):
                    dve.wait_ge(sem["inv_y_psum"], w.next("inv_y_psum"))
                    v.tensor_copy(took[:, 4 + k:5 + k], epsc[:, 0:1])
                    if k < steps - 4:
                        put(Tm, k % 4, 0, 1 + k // 4, quad(tr[k % 2]))
                    put(Um, k % 4, 1, 1 + k // 4, quad(acc[k % 2])).then_inc(sem["inv_ready"], 1)
                for c in range(NRW):
                    t, r = c // 2, slice(RW * (c % 2), RW * (c % 2) + RW)
                    if c:
                        dve.wait_ge(sem["carry_psum"], w.next("carry_psum"))
                        if c == 1:
                            dve.wait_ge(sem["akv_ready"], w.next("akv_ready", TT))
                        v.tensor_tensor(AkV[r, t, :], AkV[r, t, :], gu[0][r, :], ALU.add).then_inc(sem["removal_in"], 1)
                    if c < NRW - 1:
                        dve.wait_ge(sem["state_psum"], w.next("state_psum"))
                        for h in range(2):
                            d = slice(64 * h, 64 * h + 64)
                            new = tr[1][d, :].rearrange("p (a b) -> p a b", a=4)[:, :, d]
                            if c == 0:
                                ins = v.tensor_copy(Sbd[d, :, d], new)
                            else:
                                v.tensor_tensor(Sbd[d, :, d], Sbd[d, :, d],
                                                     sdec[d, :, c:c + 1].to_broadcast([64, 4, 64]), ALU.mult).then_inc(sem["dve_done"], w.mark("dve_done"))
                                dve.wait_ge(sem["dve_done"], w.now("dve_done"))
                                ins = v.tensor_tensor(Sbd[d, :, d], Sbd[d, :, d], new, ALU.add)
                        ins.then_inc(sem["state_ready"], 1)
                for t in range(TT):
                    y = yS[:, t, :].rearrange("p (h d) -> p h d", h=8)

                    def head(i):
                        return gnst[:, i, :, None].to_broadcast([P, 8, HD])

                    dve.wait_ge(sem["y_psum"], w.next("y_psum"))
                    dve.wait_ge(sem["carry_y_ready"], w.next("carry_y_ready", t + 1))
                    v.tensor_tensor(yS[:, t, :], yS[:, t, :], acc[t][:, :], ALU.add).then_inc(sem["dve_done"], w.mark("dve_done"))
                    dve.wait_ge(sem["dve_done"], w.now("dve_done"))
                    v.tensor_reduce(gnst[:, 0, :], y, AX.X, ALU.add).then_inc(sem["dve_done"], w.mark("dve_done"))
                    dve.wait_ge(sem["dve_done"], w.now("dve_done"))
                    v.tensor_scalar(gnst[:, 0, :], gnst[:, 0, :], 1.0 / HD, None, ALU.mult).then_inc(sem["dve_done"], w.mark("dve_done"))
                    dve.wait_ge(sem["dve_done"], w.now("dve_done"))
                    v.tensor_tensor(y, y, head(0), ALU.subtract).then_inc(sem["dve_done"], w.mark("dve_done"))
                    dve.wait_ge(sem["dve_done"], w.now("dve_done"))
                    v.tensor_tensor(sqb[0], yS[:, t, :], yS[:, t, :], ALU.mult).then_inc(sem["dve_done"], w.mark("dve_done"))
                    dve.wait_ge(sem["dve_done"], w.now("dve_done"))
                    v.tensor_reduce(gnst[:, 1, :], sqb[0].rearrange("p (h d) -> p h d", h=8), AX.X, ALU.add).then_inc(sem["y_var"], 1)
                    dve.wait_ge(sem["y_root"], w.next("y_root"))
                    v.reciprocal(gnst[:, 3, :], gnst[:, 2, :]).then_inc(sem["dve_done"], w.mark("dve_done"))
                    dve.wait_ge(sem["dve_done"], w.now("dve_done"))
                    v.tensor_tensor(y, y, head(3), ALU.mult).then_inc(sem["y_normed"], 1)
                for t in range(TT):
                    dve.wait_ge(sem["yT_ready"], w.next("yT_ready"))
                    o, ts = mixT[:, 2:6, t * P:t * P + P], slice(t * P, t * P + P)
                    v.tensor_tensor(o, o, bon[:, :, ts], ALU.add).then_inc(sem["dve_done"], w.mark("dve_done"))
                    dve.wait_ge(sem["dve_done"], w.now("dve_done"))
                    ins = v.tensor_tensor(o, o, rg[:, :, ts], ALU.mult)
                ins.then_inc(sem["rwkv_ready"], 1)

            run_layers(w, layer, LAYER_DVE)
            v.memset(cnt_f[:, 1:2], 0.0).then_inc(sem["out_ready"], 1)

        @block.gpsimd
        def _(pool):
            w = Turns(pool, sem)
            g = nc.gpsimd

            def select(out_, pattern, op, fill, base, p):
                return g.affine_select(out_, out_, pattern, op, fill, base=base, channel_multiplier=p)

            g.memset(rows[:, :, :], 0.0).then_inc(sem["rows_zeroed"], 1)
            g.memset(epsc[:, 0:1], EPS).then_inc(sem["pool_done"], w.mark("pool_done"))
            pool.wait_ge(sem["pool_done"], w.now("pool_done"))
            g.memset(epsc[:, 1:2], GN_EPS).then_inc(sem["eps_ready"], 1)
            for m in (ident, blk64, rope):
                g.memset(m[:, :], 0.0).then_inc(sem["pool_done"], w.mark("pool_done"))
                pool.wait_ge(sem["pool_done"], w.now("pool_done"))
            for m in (ones, upper):
                g.memset(m[:, :], 1.0).then_inc(sem["pool_done"], w.mark("pool_done"))
                pool.wait_ge(sem["pool_done"], w.now("pool_done"))
            g.memset(sel4[:, :, :], 0.0).then_inc(sem["pool_done"], w.mark("pool_done"))
            pool.wait_ge(sem["pool_done"], w.now("pool_done"))
            g.memset(cmask[:, :], 0.0).then_inc(sem["pool_done"], w.mark("pool_done"))
            pool.wait_ge(sem["pool_done"], w.now("pool_done"))
            g.memset(rmask[:, :, :], 1.0).then_inc(sem["pool_done"], w.mark("pool_done"))
            pool.wait_ge(sem["pool_done"], w.now("pool_done"))
            g.memset(keep[:, :], 1.0).then_inc(sem["pool_done"], w.mark("pool_done"))
            pool.wait_ge(sem["pool_done"], w.now("pool_done"))
            g.memset(frow[:, :], 0.0).then_inc(sem["pool_done"], w.mark("pool_done"))
            pool.wait_ge(sem["pool_done"], w.now("pool_done"))
            for h in range(2):
                g.memset(blk64[64 * h:64 * h + 64, 64 * h:64 * h + 64], 1.0).then_inc(sem["pool_done"], w.mark("pool_done"))
                pool.wait_ge(sem["pool_done"], w.now("pool_done"))
            g.memset(keep[:, :].rearrange("p (c s) -> p c s", s=RW)[:, :, 0:1], 0.0).then_inc(sem["pool_done"], w.mark("pool_done"))
            pool.wait_ge(sem["pool_done"], w.now("pool_done"))
            f4 = frow[:, :].rearrange("p (h o i) -> p h o i", h=2, o=8)
            for i in range(8):
                g.memset(f4[:, :, 0:2, i:i + 1], float(500000.0 ** (-2 * i / 16))).then_inc(sem["pool_done"], w.mark("pool_done"))
                pool.wait_ge(sem["pool_done"], w.now("pool_done"))
            select(ident[:, :], [[-1, P]], ALU.not_equal, 1.0, 0, 1).then_inc(sem["pool_done"], w.mark("pool_done"))
            pool.wait_ge(sem["pool_done"], w.now("pool_done"))
            select(upper[:, :], [[1, P]], ALU.is_gt, 0.0, 0, -1).then_inc(sem["pool_done"], w.mark("pool_done"))
            pool.wait_ge(sem["pool_done"], w.now("pool_done"))
            for h in range(2):
                select(sel4[:, :, :], [[-1, 4], [0, P]], ALU.not_equal, 1.0, -64 * h, 1).then_inc(sem["pool_done"], w.mark("pool_done"))
                pool.wait_ge(sem["pool_done"], w.now("pool_done"))
            select(cmask[:, :], [[-1, S]], ALU.is_ge, -BIG, P, 1).then_inc(sem["pool_done"], w.mark("pool_done"))
            pool.wait_ge(sem["pool_done"], w.now("pool_done"))
            for k in range(4):
                select(rmask[:, k, :], [[1, P]], ALU.is_ge if k % 2 else ALU.is_gt, 0.0, 0, -1).then_inc(sem["pool_done"], w.mark("pool_done"))
                pool.wait_ge(sem["pool_done"], w.now("pool_done"))
            g.memset(rmask[0:RW, :, RW:P], 0.0).then_inc(sem["pool_done"], w.mark("pool_done"))
            pool.wait_ge(sem["pool_done"], w.now("pool_done"))
            for h in range(2):
                select(rope[:, 64 * h:64 * h + 8], [[-1, 8]], ALU.not_equal, -1.0, -(64 * h + 8), 1).then_inc(sem["pool_done"], w.mark("pool_done"))
                pool.wait_ge(sem["pool_done"], w.now("pool_done"))
                select(rope[:, 64 * h + 8:64 * h + 16], [[-1, 8]], ALU.not_equal, 1.0, -64 * h, 1).then_inc(sem["pool_done"], w.mark("pool_done"))
                pool.wait_ge(sem["pool_done"], w.now("pool_done"))
            g.iota(part_i[:, :], [[0, P]], base=0, channel_multiplier=1).then_inc(sem["pool_done"], w.mark("pool_done"))
            pool.wait_ge(sem["pool_done"], w.now("pool_done"))
            g.iota(col_i[:, :], [[1, P]], base=0, channel_multiplier=0).then_inc(sem["pool_done"], w.mark("pool_done"))
            pool.wait_ge(sem["pool_done"], w.now("pool_done"))
            g.iota(awin_i[:, :], [[1, S]], base=-P, channel_multiplier=-1).then_inc(sem["pool_done"], w.mark("pool_done"))
            pool.wait_ge(sem["pool_done"], w.now("pool_done"))
            g.tensor_copy(iota_s[:, :], col_i[:, :]).then_inc(sem["pool_done"], w.mark("pool_done"))
            pool.wait_ge(sem["pool_done"], w.now("pool_done"))
            g.tensor_copy(awin[:, :], awin_i[:, :]).then_inc(sem["pool_done"], w.mark("pool_done"))
            pool.wait_ge(sem["pool_done"], w.now("pool_done"))
            select(awin[:, :], [[-1, S]], ALU.is_ge, -BIG, P, 1).then_inc(sem["pool_done"], w.mark("pool_done"))
            pool.wait_ge(sem["pool_done"], w.now("pool_done"))
            select(awin[:, :], [[1, S]], ALU.is_ge, -BIG, -1, -1).then_inc(sem["consts_ready"], 1)


def kernel(**inputs):
    import numpy as np
    import concourse.bacc as bacc
    from concourse.bass_utils import run_bass_kernel_spmd

    nc = bacc.Bacc("TRN2", target_bir_lowering=False, num_devices=1)
    arrays, A = {}, {}
    for name, value in inputs.items():
        a = np.ascontiguousarray(value)
        arrays[f"in_{name}_dram"] = a
        A[name] = nc.dram_tensor(f"in_{name}_dram", a.shape, mybir.dt.from_np(a.dtype), kind="ExternalInput").ap()
    out = nc.dram_tensor("out_0_dram", (1, S, D), F32, kind="ExternalOutput").ap()
    build(nc, A, out)
    r = run_bass_kernel_spmd(nc, [arrays], core_ids=[0])
    return r.results[0]["out_0_dram"]
```

```python
from contextlib import ExitStack, contextmanager

import concourse.bass as bass
from concourse import mybir

F32 = mybir.dt.float32
FR = mybir.dt.float32r
I32 = mybir.dt.int32
U32 = mybir.dt.uint32
ALU = mybir.AluOpType
ACT = mybir.ActivationFunctionType
AX = mybir.AxisListType

P = 128
D = 1024
DC = D // P
S = 256
TT = S // P
HALF = 512
BIG = 1e30
EPS = 1e-6
GN_EPS = 64e-5
NSLOT = 6
NLOW = 3
CH = 256
D_FF = 3584
FFN_DIM = 2816
N_EXP = 8
CAP = 128
HD = 64
RW = 64
NRW = S // RW
LEVELS = (1, 2, 4, 8, 16, 32)
DEPTH2 = 2


class Turns:

    def __init__(self, eng, sem):
        self.eng, self.sem = eng, sem
        self.n, self.loops = {}, []

    def branch(self, sem):
        w = Turns(self.eng, sem)
        w.n = {k: c for k, c in self.n.items() if sem[k] is self.sem[k]}
        return w

    def now(self, name):
        v = self.n[name]
        for i, per in self.loops:
            if per.get(name):
                v = i * per[name] + v
        return v

    def next(self, name, count=1):
        self.n[name] = self.n.get(name, 0) + count
        return self.now(name)

    def mark(self, name):
        self.n[name] = self.n.get(name, 0) + 1
        return 1

    @contextmanager
    def loop(self, n, per):
        with self.eng.Fori(0, n) as i:
            start = dict(self.n)
            self.loops.append((i, per))
            yield i
            self.loops.pop()
        got = {k: v - start.get(k, 0) for k, v in self.n.items() if v != start.get(k, 0)}
        assert got == {k: v for k, v in per.items() if v}, got
        for k, v in got.items():
            self.n[k] = start.get(k, 0) + n * v


class Slots:

    def __init__(self):
        self.at, self.used = 0, set()

    def next(self):
        s = self.at % NSLOT
        self.at += 1
        return s


def expert_loads(k):
    n = D_FF // CH
    if k < 2:
        return 2 * k, 2
    return (4 + 3 * (k - 2), 3) if k < n else (4 + 3 * (n - 2) + k - n, 1)

def seq(*sizes):
    out, at = [], 0
    for n in sizes:
        out.append((at, at + n))
        at += n
    return out


V1 = dict(zip(
    ("mix", "ffn", "rconv", "rconvb", "gab", "gxb", "lam", "hconv", "qg", "kg"),
    seq(2 * DC, 2 * DC, 4 * DC, DC, DC, DC, DC, 12, 1, 1)))
N1 = V1["kg"][1]
V2 = dict(zip(
    ("ffn1", "mix", "xat", "mem", "ffn2", "w0", "a0", "k_k", "k_a", "r_k", "ln_w", "ln_b", "mu",
     "fqg", "fkg", "mqg", "mkg", "xqg", "xkg", "fb"),
    seq(DC, DC, DC, DC, DC, 4, 4, 4, 4, 4, 4, 4, 15, 1, 1, 1, 1, 1, 1, 1)))
N2 = V2["fb"][1]

FOX_IN, MOBA_IN = 772, 768
RW0 = FOX_IN + MOBA_IN
MIX0_LOADS = [(0, CH), (CH, CH), (2 * CH, P, 2, 2), (2 * CH + P, P)] + [(k * CH, CH) for k in range(3, 9)]
MIX1_LOADS = [(k * CH, CH) for k in (4, 5, 6, 7, 0, 1, 2, 3)]
MIX2_LOADS = ([(0, CH), (CH, CH), (2 * CH, CH), (3 * CH, 4, 1, P // 4)]
              + [(FOX_IN + k * CH, CH) for k in range(3)]
              + [(RW0 + k * CH, CH) for k in range(7)] + [(RW0 + 7 * CH, 32)])
XKV_LOADS = [(k * CH, CH) for k in range(4)]
XQ_LOADS = [(k * CH, CH) for k in range(2)]
UP1, UP2, LOW = 4, 0, 1
def repeats(load):
    return load[1:] if len(load) == 4 else (load[1], 1, 1)


SKIP2 = 2


SEMAPHORES = (
    "x_loaded", "out_stored",
    "hT_psum_act", "hT_psum_dve", "proj_psum", "out_psum", "scores_psum", "probsT_psum", "attn_psum",
    "sumsq_psum", "cols_psum", "gates_psum", "logits_psum", "ranks_psum", "rope_psum", "lora_psum",
    "bonus_psum", "tokens_psum", "gram_psum", "akv_psum", "inv_a_psum", "inv_x_psum", "inv_y_psum",
    "removal_psum", "state_psum", "y_psum", "yT_psum", "ffn_psum", "carry_psum", "carry_y_psum",
    "rows_loaded", "inputs_loaded", "mem_loaded", "act_done", "rms_ready", "hT_act",
    "proj_copied", "root_ready", "squares_ready", "exp_ready", "probsT_ready", "attn_copied",
    "lam_exp", "xc_started", "tanh_ready", "decay_ready", "mult_ready", "gate_exp", "forget_exp",
    "lora_ready", "decays_ready", "tokens_copied", "akv_ready", "inv_x_ready", "carry_y_ready",
    "removal_ready", "y_root", "yT_ready",
    "xn_ready", "hT_dve", "qk_ready", "maxima_ready", "probs_ready", "x_ready", "cols_ready",
    "angles_ready", "lam_abs", "conv_ready", "xc_ready", "log_a_ready", "mult_sq_ready", "lru_ready",
    "tail_shifted", "top_ready", "chosen_ready", "ranks_ready", "count_ready", "forget_abs", "rope_ready", "forget_ready",
    "sums_ready", "removal_keys", "sumsq_read", "bonus_in", "tokens_in", "gram_in", "bonus_ready",
    "gram_ready", "inv_ready", "removal_in", "state_ready", "y_var", "y_normed", "rwkv_ready", "out_ready",
    "selT_psum", "chosen_h_psum", "hidT_psum", "expert_ffn_psum", "expert_psum",
    "selT_ready", "chosen_h_up", "hidT_up", "expert_out",
    "sel_ready", "chosen_h_ready", "hidT_ready", "expert_added",
    "rows_zeroed", "pool_done", "first_consts_ready", "consts_ready", "rows2_loaded",
) + tuple(f"slot{s}_full" for s in range(NSLOT))
PASS_SEMAPHORES = ("gate_up_psum", "hidden_ready", "silu_ready", "dve_done", "hi_ready", "lo_ready", "lo_used") + tuple(
    f"slot{s}_{what}" for s in range(NSLOT) for what in ("raw", "free"))


ROW_DMAS, ROW_DMAS2 = 8 + 4, 25
LAYER_SP = {
    "slot0_free": 16, "slot1_free": 15, "slot2_free": 15, "slot3_free": 16, "slot4_free": 16,
    "slot5_free": 16}
LAYER_PE = {
    "xn_ready": 10, "lo_ready": 87, "hT_act": 20, "hT_dve": 20, "proj_copied": 33, "squares_ready":
    10, "qk_ready": 8, "probs_ready": 12, "probsT_ready": 12, "attn_copied": 12, "slot4_full": 16,
    "slot5_full": 16, "slot1_full": 64, "hidden_ready": 44, "slot2_full": 32, "forget_ready": 1,
    "rope_ready": 2, "lora_ready": 1, "bonus_in": 2, "tokens_in": 3, "sumsq_read": 2,
    "tokens_copied": 6, "gram_in": 1, "bonus_ready": 1, "gram_ready": 16, "inv_ready": 24,
    "inv_x_ready": 20, "akv_ready": 2, "removal_ready": 4, "state_ready": 3, "removal_in": 3,
    "y_normed": 2, "rwkv_ready": 1, "slot3_full": 32}
LAYER_ACT = {
    "act_done": 10, "slot0_raw": 256, "hT_psum_act": 20, "slot1_raw": 224, "proj_psum": 21,
    "proj_copied": 33, "slot2_raw": 208, "slot3_raw": 224, "slot4_raw": 240, "slot5_raw": 240,
    "sumsq_psum": 10, "qk_ready": 8, "maxima_ready": 12, "probsT_psum": 12, "attn_psum": 12,
    "x_ready": 8, "gate_up_psum": 44, "mem_loaded": 16, "forget_abs": 1, "tail_shifted": 1,
    "lora_psum": 12, "removal_keys": 1, "sums_ready": 1, "tokens_psum": 6, "akv_psum": 2,
    "inv_x_psum": 20, "removal_psum": 4, "carry_y_psum": 3, "y_var": 2, "yT_psum": 2}
LAYER_DVE = {
    "rms_ready": 10, "dve_done": 180, "hi_ready": 87, "hT_act": 20, "proj_copied": 33, "root_ready":
    10, "scores_psum": 12, "exp_ready": 12, "out_psum": 2, "silu_ready": 44, "lo_used": 66,
    "ffn_psum": 2, "forget_exp": 1, "rope_psum": 2, "tail_shifted": 1, "tokens_in": 3, "sumsq_read":
    2, "decays_ready": 4, "bonus_psum": 2, "gram_psum": 16, "inv_a_psum": 4, "inv_y_psum": 20,
    "state_psum": 3, "carry_psum": 3, "akv_ready": 2, "y_psum": 2, "carry_y_ready": 3, "y_root": 2,
    "yT_ready": 2}


def run_layers(w, layer, per):
    if per is None:
        for l in range(DEPTH2):
            layer(l)
        return
    with w.loop(DEPTH2, per) as l:
        layer(l)


def build(nc, A, out):
    ctx = ExitStack()

    def sb(name, shape, dt=F32):
        return ctx.enter_context(nc.sbuf_tensor(name, shape, dt))

    with ctx:
        sem = {name: ctx.enter_context(nc.semaphore(name)) for name in SEMAPHORES + PASS_SEMAPHORES}
        sem_over = sem | {name: ctx.enter_context(nc.semaphore(name + "_over")) for name in PASS_SEMAPHORES}

        banks = ctx.enter_context(nc.psum_tensor("banks", [P, 8, HALF], F32))
        gu = [banks[:, i, :] for i in range(2)]
        tr = [banks[:, 2 + i, :] for i in range(2)]
        acc = [banks[:, 4 + i, :] for i in range(4)]
        ebank = (acc[2], acc[3], acc[0], acc[1])
        sbank = [banks[:, 0:2, :], banks[:, 6:8, :]]

        hbank = acc

        ring = sb("ring", [P, NSLOT, DC * CH])
        x = sb("x", [P, TT, D])
        xn = sb("xn", [P, TT, D])
        with nc.sbuf_tensor("hT_up", [P, DC, S], FR) as hT_up:
            pass
        hT = sb("hT", [P, DC, S])
        mixT = sb("mixT", [P, DC, S])
        hid_up = sb("hid_up", [P, 2, S], FR)
        sg = sb("sg", [P, 2, S])
        sc = sb("sc", [P, 2, 2, S])
        pT = sb("pT", [P, 2, 2, S])
        negmx = sb("negmx", [P, 2, 2])
        rsum = sb("rsum", [P, 2, 2])
        snk = sb("snk", [P, 2, 2])
        ident = sb("ident", [P, P])
        blk64 = sb("blk64", [P, P])
        ones = sb("ones", [P, P])
        upper = sb("upper", [P, P])
        iota_s = sb("iota_s", [P, P])
        cmask = sb("cmask", [P, S])
        awin = sb("awin", [P, S])
        rmask = sb("rmask", [P, 4, P])
        lvl = sb("lvl", [P, 2, len(LEVELS), P], mybir.dt.uint8)
        sel4 = sb("sel4", [P, 4, P])
        rope = sb("rope", [P, P])
        cosT = sb("cosT", [P, S])
        sinT = sb("sinT", [P, S])
        rows = sb("rows", [P, 3, P])
        frow = sb("frow", [1, P])
        fcol = sb("fcol", [P, 1])
        epsc = sb("epsc", [P, 4])
        keep = sb("keep", [P, 4 * S], mybir.dt.bfloat16)
        pv1 = sb("pv1", [P, N1])
        pv2 = sb("pv2", [P, DEPTH2, N2])
        pv = sb("pv", [P, N2])
        sinks = sb("sinks", [P, 16])
        ss = sb("ss", [P, 2, 2])
        rt = sb("rt", [P, DC, N_EXP])
        lg = sb("lg", [P, TT, N_EXP])
        top = sb("top", [P, TT, 8])
        topi = sb("topi", [P, TT, 8], U32)
        topf = sb("topf", [P, TT, 8])
        gt = sb("gt", [P, TT, 4])
        hot = sb("hot", [P, 2, TT, N_EXP])
        route = sb("route", [P, 3, TT, N_EXP])
        cur = sb("cur", [P, 3, TT])
        cnt_f = sb("cnt_f", [P, 2])
        took = sb("took", [P, 24])
        cnt = sb("cnt", [P, 1], I32)
        lamb = sb("lamb", [P, 5, DC])
        gnst = sb("gnst", [P, 4, 8])
        mem = sb("mem", [P, TT, D])
        with (nc.sbuf_tensor("w_up", [P, NSLOT, DC * CH], FR) as w_up,
              nc.sbuf_tensor("w_low", [P, NLOW, DC * CH], FR) as w_low,
              nc.sbuf_tensor("hT_low", [P, DC, S], FR) as hT_low,
              nc.sbuf_tensor("hid_low", [P, 2, S], FR) as hid_low):
            pass
        arena = sb("arena", [P, 22528])

        def region(at, *shape, dt=None):
            n = 1
            for k in shape:
                n *= k
            v = arena[:, at:at + n]
            if dt is not None:
                v = v.bitcast(dt)
            if len(shape) == 2:
                return v.rearrange("p (a b) -> p a b", a=shape[0])
            if len(shape) == 3:
                return v.rearrange("p (a b c) -> p a b c", a=shape[0], b=shape[1])
            if len(shape) == 4:
                return v.rearrange("p (a b c d) -> p a b c d", a=shape[0], b=shape[1], c=shape[2])
            return v

        part_i, col_i = region(20480, P, dt=I32), region(20608, P, dt=I32)
        lv_a, lv_b, lv_c = (region(20736 + P * i, P, dt=I32) for i in range(3))
        awin_i = region(21120, S, dt=I32)
        pos_i = region(21376, S, dt=I32)
        ang = region(21632, 3, S)
        z0 = region(0, 19, S)
        gcu = region(19 * S, 4, S + 2)
        cv = region(19 * S + 4 * (S + 2), 4, S)
        g_y, g_x, g_xc = region(0, DC, S), region(2048, DC, S + 3), region(4128, DC, S)
        g_r, g_i, g_t = region(6176, DC, S), region(8224, DC, S), region(10272, DC, S)
        g_m = region(12320, DC, S)
        mflat = mixT[:, :, :].rearrange("p c s -> p (c s)")
        sel, selg, selT = (mflat[:, TT * P * i:TT * P * i + TT * P].rearrange("p (t s) -> p t s", t=TT) for i in range(3))
        ye = mflat[:, D:2 * D]
        rg, bon = region(0, 4, S), region(1024, 4, S)
        Bh, Kh, AR = region(2048, 4, S), region(3072, 4, S), region(4096, 4, TT, 2, P)
        Bt, Kt, Vt = (region(6144 + 1024 * i, TT, HALF) for i in range(3))
        q2, v2 = region(4096, 8, S), region(6144, 2, TT, S)
        zf, fsc = region(7168, S), region(7424, 6, S)
        zr, zd = region(9216, 15, S + 1), region(13072, 4, S)
        lw, ra, kk = (region(14096 + 1024 * i, 4, S) for i in range(3))
        cw, ew, et = (region(17168 + 1024 * i, 4, S) for i in range(3))
        Bb, Kb = region(20240, 4, S), region(21264, 4, S)
        ep, ei = lw, zd
        G = arena[:, 9216:17408].rearrange("p (t h k s) -> p t h k s", t=TT, h=8, k=4)
        Xb = region(17408, 2, HALF)
        SA, AkV, yS = (region(18432 + 1024 * i, TT, HALF) for i in range(3))
        Sbd, sdec = region(21504, 4, P), region(22016, 4, P)
        Tm = xn[:, :, :].rearrange("p t (u s) -> p (t u) s", s=P)
        Um = hT[:, :, :].rearrange("p c (u s) -> p (c u) s", s=P)
        xk, xv, xq = (mem[:, 0, :].rearrange("p (h s) -> p h s", h=4), mem[:, 1, :].rearrange("p (t n) -> p t n", t=TT),
                      region(4096, 4, S))

        sqb = [sc[:, i, :, :].rearrange("p a b -> p (a b)") for i in range(2)]
        rtb = [pT[:, i, :, :].rearrange("p a b -> p (a b)") for i in range(2)]

        def col(name, i=0):
            return pv1[:, V1[name][0] + i:V1[name][0] + i + 1]

        def col2(name, i=0):
            return pv[:, V2[name][0] + i:V2[name][0] + i + 1]

        def wcols(s, w):
            return ring[:, s, 0:DC * w].rearrange("p (c n) -> p c n", c=DC)

        def halves_of(s, low, by_rows=False):
            return [a.rearrange("p (c n) -> p c n", c=2 if by_rows else DC) for a in (w_up[:, s, :], w_low[:, low, :])]

        def split_views(load, *flat):
            width, groups, copies = repeats(load)
            if copies == 1:
                return [a[:, 0:DC * width] for a in flat]
            m = width // groups
            return ([flat[0][:, 0:DC * width].rearrange("p (q o m) -> p q o m", o=1, m=m).to_broadcast(
                        [P, DC * groups, copies, m])]
                    + [a[:, 0:DC * width * copies].rearrange("p (q r m) -> p q r m", r=copies, m=m) for a in flat[1:]])

        def proj_halves(k, up, width):
            return [a.rearrange("p (c n) -> p c n", c=DC) for a in (
                w_up[:, up + k % 2, 0:DC * width], w_low[:, LOW + k % 2, 0:DC * width])]

        def wrows(s):
            return ring[:, s, :].rearrange("p (k n) -> p k n", k=2)

        def units_mix0():
            return [dict(q=[z0[64 * h:64 * h + 64, hp, t * P:t * P + P] for h in range(2)],
                         k=[z0[64 * h:64 * h + 64, 4 + hp // 2, 0:P * (t + 1)] for h in range(2)],
                         nk=P * (t + 1),
                         slope=[2.0 ** -(2 * hp + h + 1) for h in range(2)], t=t,
                         sink=2 * hp,
                         v=[[z0[:, 6, kt * P + 64 * (hp // 2):kt * P + 64 * (hp // 2) + 64]
                             for kt in range(t + 1)] for h in range(2)],
                         dst=mixT[:, hp, t * P:t * P + P], wide=False)
                    for t in range(TT) for hp in range(4)]

        def units_causal(m):
            return [dict(q=[q2[64 * h:64 * h + 64, 4 * m + hp, t * P:t * P + P] for h in range(2)],
                         k=[q2[64 * h:64 * h + 64, 4 * m + 2 + hp, 0:P * (t + 1)] for h in range(2)],
                         nk=P * (t + 1), t=t, causal=True,
                         forget=[2 * hp + h for h in range(2)] if m == 0 else None,
                         v=[[v2[:, m, kt, (2 * hp + h) * 64:(2 * hp + h) * 64 + 64]
                             for kt in range(t + 1)] for h in range(2)],
                         dst=mixT[:, (0 if m == 0 else 6) + hp, t * P:t * P + P], wide=False)
                    for t in range(TT) for hp in range(2)]

        def units_mem():
            return [dict(q=[xq[:, 2 * hp + h, t * P:t * P + P] for h in range(2)],
                         k=[xk[:, 2 * hp + h, :] for h in range(2)], nk=S, t=t,
                         v=[[xv[:, kt, (2 * hp + h) * P:(2 * hp + h) * P + P]
                             for kt in range(TT)] for h in range(2)],
                         dst=mixT[:, 2 * hp:2 * hp + 2, t * P:t * P + P], wide=True)
                    for t in range(TT) for hp in range(2)]

        block = ctx.enter_context(nc.Block())

        @block.sync
        def _(sp):
            w = Turns(sp, sem)
            slots = Slots()

            def load(parts, w=w, slots=slots, what="full"):
                s = slots.next()
                if s in slots.used:
                    sp.wait_ge(w.sem[f"slot{s}_free"], w.next(f"slot{s}_free"))
                slots.used.add(s)
                for dst, src in parts(s):
                    sp.dma_start(dst, src).then_inc(w.sem[f"slot{s}_{what}"], 16)

            def load_cols(W, l, c0, n, w=w, slots=slots, what="full"):
                load(lambda s: [(wcols(s, n), W[bass.ds(l, 1), :, bass.ds(c0, n)].rearrange(
                    "o (c p) n -> p (o c) n", p=P))], w, slots, what)

            def load_rows(W, l, r0, w=w, slots=slots, what="full"):
                load(lambda s: [(wrows(s), W[bass.ds(l, 1), bass.ds(r0, 2 * P), :].rearrange(
                    "o (k p) n -> p (o k) n", p=P))], w, slots, what)

            def load_chunk(Wg, Wu, up0, Wd, l, k, w, slots, what):
                load_cols(Wg, l, k * CH, CH, w, slots, what)
                load_cols(Wu, l, k * CH + up0, CH, w, slots, what)
                load_rows(Wd, l, k * CH, w, slots, what)

            def load_ffn(Wg, Wu, up0, Wd, l, n, w=w, slots=slots, what="raw"):
                if n % 2:
                    load_chunk(Wg, Wu, up0, Wd, l, 0, w, slots, what)
                with w.loop(n // 2, {f"slot{s}_free": 1 for s in range(NSLOT)}) as i:
                    for j in range(2):
                        load_chunk(Wg, Wu, up0, Wd, l, i * 2 + (n % 2 + j), w, slots, what)

            def load_experts(w, slots):
                Wg, Wu, Wd = (A[n][0] for n in ("moe_w_gate", "moe_w_up", "moe_w_down"))
                with w.loop(N_EXP, {f"slot{s}_free": 7 for s in range(NSLOT)}) as e:
                    def gate_up(k):
                        load_cols(Wg, e, k * CH, CH, w, slots, "raw")
                        load_cols(Wu, e, k * CH, CH, w, slots, "raw")

                    n = D_FF // CH
                    gate_up(0)
                    gate_up(1)
                    with w.loop(n // 2 - 1, {f"slot{s}_free": 1 for s in range(NSLOT)}) as i:
                        for j in range(2):
                            gate_up(i * 2 + (2 + j))
                            load_rows(Wd, e, (i * 2 + j) * CH, w, slots, "raw")
                    for k in (n - 2, n - 1):
                        load_rows(Wd, e, k * CH, w, slots, "raw")

            sp.dma_start(x[:, :, :], A["x"][0].rearrange("(t p) d -> p t d", p=P)).then_inc(sem["x_loaded"], 16)
            for k, (c0, n, *_) in enumerate(MIX0_LOADS):
                if k == 2:
                    sp.wait_ge(sem["rows_loaded"], 16 * ROW_DMAS)
                load_cols(A["hy_w_in"], 0, c0, n, what="raw")
            for k in range(4):
                load_rows(A["hy_w_out"], 0, k * CH)
            load_ffn(A["ffn_w_gate"], A["ffn_w_up"], 0, A["ffn_w_down"], 0, D_FF // CH)
            for c0, n, *_ in MIX1_LOADS:
                load_cols(A["rg_w_in"], 0, c0, n, what="raw")
            load(lambda s: [(ring[:, s, g * D:g * D + D].rearrange("p (h j) -> p h j", h=DC),
                             A[n][0].rearrange("h i j -> i h j"))
                            for g, n in enumerate(("rg_gate_a_w", "rg_gate_x_w"))])
            for k in range(4):
                load_rows(A["rg_w_out"], 0, k * CH)
            load_experts(w, slots)
            sp.wait_ge(sem["count_ready"], 1)
            n_max = sp.value_load(cnt[0:1, 0:1], min_val=0, max_val=S)
            with sp.If(n_max > CAP):
                w_over = w.branch(sem_over)
                over = Slots()
                over.used = set(range(NSLOT))
                for s in range(NSLOT):
                    sp.wait_ge(sem[f"slot{s}_free"], w.n[f"slot{s}_free"] + 1)
                    sp.sem_inc(w_over.sem[f"slot{s}_free"], 1)
                load_experts(w_over, over)
                for s in range(NSLOT):
                    sp.wait_ge(w_over.sem[f"slot{s}_free"], w_over.next(f"slot{s}_free"))

            def layer(l):
                load_ffn(A["ffn1_w_in_2"], A["ffn1_w_in_2"], FFN_DIM, A["ffn1_w_out_2"], l, FFN_DIM // CH)
                for c0, n, *_ in MIX2_LOADS:
                    load_cols(A["mix_w_in_2"], l, c0, n, what="raw")
                for c0, n, *_ in XKV_LOADS:
                    load_cols(A["xattn_w_kv_2"], l, c0, n, what="raw")
                load(lambda s: [
                    (ring[0:64, s, 0:HALF], A["rwkv_w2_2"][bass.ds(l, 1), :, :].rearrange("o k n -> (o k) n")),
                    (ring[64:P, s, 0:HALF], A["rwkv_a2_2"][bass.ds(l, 1), :, :].rearrange("o k n -> (o k) n")),
                    (ring[:, s, HALF:D], A["rwkv_g2_2"][bass.ds(l, 1), 0:P, :].rearrange("o k n -> (o k) n")),
                    (ring[0:32, s, D:D + HALF],
                     A["rwkv_g2_2"][bass.ds(l, 1), P:P + 32, :].rearrange("o k n -> (o k) n"))])
                for k in range(4):
                    load_rows(A["mix_w_out_2"], l, k * CH)
                for c0, n, *_ in XQ_LOADS:
                    load_cols(A["xattn_w_q_2"], l, c0, n, what="raw")
                for k in range(2):
                    load_rows(A["xattn_w_out_2"], l, k * CH)
                load_ffn(A["ffn2_w_in_2"], A["ffn2_w_in_2"], FFN_DIM, A["ffn2_w_out_2"], l, FFN_DIM // CH)
                slots.at += SKIP2

            run_layers(w, layer, LAYER_SP)
            sp.wait_ge(sem["out_ready"], 1)
            sp.dma_start(out[0].rearrange("(t p) d -> p t d", p=P), x[:, :, :]).then_inc(sem["out_stored"], 16)
            sp.wait_ge(sem["out_stored"], 16)

        @block.tensor
        def _(pe):
            w = Turns(pe, sem)
            slots = Slots()
            mm = nc.tensor.matmul

            def take(ndma=1, w=w, slots=slots):
                s = slots.next()
                pe.wait_ge(w.sem[f"slot{s}_full"], w.next(f"slot{s}_full", 16 * ndma))
                return s

            def turn(dst, src):
                return nc.tensor.transpose(dst, src, ident[0:src.shape[0], 0:src.shape[0]])

            awaited = {"up": 0, "low": 0}

            def h_ready(half, c):
                if awaited[half] and c % 2 == 0:
                    name = "hT_act" if half == "up" else "hT_dve"
                    pe.wait_ge(sem[name], w.next(name))
                    awaited[half] -= 1

            def transpose_h(split=False):
                for t in range(TT):
                    pe.wait_ge(sem["xn_ready"], w.next("xn_ready"))
                    for cp in range(DC // 2):
                        for i in range(2):
                            c = 2 * cp + i
                            ins = turn(hbank[cp][:, i * S + t * P:i * S + t * P + P], xn[:, t, c * P:c * P + P])
                        if t == TT - 1:
                            ins.then_inc(sem["hT_psum_act" if split or cp % 2 == 0 else "hT_psum_dve"], 1)
                if split:
                    awaited.update(up=DC // 2, low=DC // 2)
                else:
                    pe.wait_ge(sem["hT_act"], w.next("hT_act", 2))
                    pe.wait_ge(sem["hT_dve"], w.next("hT_dve", 2))

            fills = [0]

            def begin_fill():
                n = fills[0]
                fills[0] += 1
                if n >= 2:
                    pe.wait_ge(sem["proj_copied"], w.next("proj_copied"))
                return gu[n % 2]

            def end_fills():
                pe.wait_ge(sem["proj_copied"], w.next("proj_copied", min(2, fills[0])))
                fills[0] = 0


            def take_halves(k, up, width=CH):
                slots.next()
                pe.wait_ge(sem["lo_ready"], w.next("lo_ready"))
                return proj_halves(k, up, width)

            def tiles_out(weights, tiles):
                b = begin_fill()
                up, low = weights
                for co, m, oc in tiles:
                    for i, (wv, r) in enumerate([(up, hT_up), (low, hT_up), (up, hT_low)]):
                        for c in range(DC):
                            h_ready("low" if r is hT_low else "up", c)
                            ins = mm(b[0:m, oc:oc + S], wv[:, c, co:co + m], r[:, c, :],
                                     start=(i == 0 and c == 0), stop=(i == 2 and c == DC - 1))
                ins.then_inc(sem["proj_psum"], 1)

            def tokens_out(weights, co, n):
                b = begin_fill()
                up, low = weights
                for t in range(TT):
                    for i, (r, wv) in enumerate([(hT_up, up), (hT_up, low), (hT_low, up)]):
                        for c in range(DC):
                            ins = mm(b[:, t * n:t * n + n], r[:, c, t * P:t * P + P], wv[:, c, co:co + n],
                                     start=(i == 0 and c == 0), stop=(i == 2 and c == DC - 1))
                ins.then_inc(sem["proj_psum"], 1)

            def two_tiles(k, up):
                tiles_out(take_halves(k, up), [(0, P, 0), (P, P, S)])

            def out_proj(nslots, second_half=None):
                for k in range(nslots):
                    if second_half and k == nslots // 2:
                        pe.wait_ge(sem[second_half], w.next(second_half))
                    s = take()
                    wv = wrows(s)
                    for j in range(2):
                        c = 2 * k + j
                        for t in range(TT):
                            for h in range(2):
                                ins = mm(acc[2 * t + h][:, :], mixT[:, c, t * P:t * P + P],
                                         wv[:, j, h * HALF:h * HALF + HALF],
                                         start=(c == 0), stop=(c == 2 * nslots - 1))
                    ins.then_inc(sem["out_psum" if k == nslots - 1 else f"slot{s}_free"], 1)

            def ffn(n):
                base = slots.at
                slots.at += 3 * n

                def slot(k, j):
                    return (base + 3 * k + j) % NSLOT

                def project(s, j, f, o, first=False):
                    if f == 0:
                        pe.wait_ge(sem["lo_ready"], w.next("lo_ready"))
                    up, low = halves_of(s, j)
                    products = [(up, hT_up), (low, hT_up), (up, hT_low)] if f or first else [
                        (up, hT_up), (up, hT_low), (low, hT_up)]
                    for i, (wv, r) in enumerate(products):
                        for c in range(DC):
                            h_ready("low" if r is hT_low else "up", c)
                            ins = mm(o, wv[:, c, f * P:f * P + P], r[:, c, :], start=(i == 0 and c == 0),
                                     stop=(i == len(products) - 1 and c == DC - 1))
                        if f and i == 1:
                            ins.then_inc(sem["lo_used"], 1)
                    return ins

                def gate_up(k, f):
                    g, u = slot(k, 0), slot(k, 1)
                    ins = project(g, 0, f, gu[f][:, 0:S], first=(k == 0 and f == 0))
                    if f == 1:
                        ins.then_inc(sem[f"slot{g}_free"], 1)
                    project(u, 1, f, gu[f][:, S:2 * S]).then_inc(sem["gate_up_psum"], 1)

                def down(k, f, first=False, last=False):
                    u, d = slot(k, 1), slot(k, 2)
                    if f == 0:
                        pe.wait_ge(sem["lo_ready"], w.next("lo_ready"))
                    pe.wait_ge(sem["hidden_ready"], w.next("hidden_ready"))
                    up, low = halves_of(d, 2, True)
                    for i in range(2 * TT):
                        t, h = i // 2, i % 2
                        for j, (hv, wv) in enumerate([(hid_up, up), (hid_up, low), (hid_low, up)]):
                            ins = mm(acc[i][:, :], hv[:, f, t * P:t * P + P], wv[:, f, h * HALF:h * HALF + HALF],
                                     start=first and j == 0, stop=last and j == 2)
                            if f == 0 and i == 0 and j == 0:
                                ins.then_inc(sem[f"slot{u}_free"], 1)
                            if f == 1 and i == 2 * TT - 1 and j == 1:
                                ins.then_inc(sem["lo_used"], 1)
                    if f == 1:
                        ins.then_inc(sem["ffn_psum" if last else f"slot{d}_free"], 1)

                def step(k):
                    gate_up(k, 0)
                    down(k - 1, 1)
                    gate_up(k, 1)
                    down(k, 0)

                gate_up(0, 0)
                gate_up(0, 1)
                down(0, 0, first=True)
                with w.loop((n - 1) // 2, {"hidden_ready": 4, "lo_ready": 6}):
                    step(1)
                    step(2)
                if n % 2 == 0:
                    step(n - 1)
                down(n - 1, 1, last=True)

            def expert_ffn(w, slots):
                base, n = slots.at, D_FF // CH
                slots.at += 3 * n

                def gate_up(k, freed=None):
                    first = expert_loads(k)[0]
                    for j in range(2):
                        s = (base + first + j) % NSLOT
                        pe.wait_ge(w.sem["lo_ready"], w.next("lo_ready"))
                        up, low = halves_of(s, (first + j) % NLOW)
                        for i, (r, wv) in enumerate([(hT_up, up), (hT_up, low), (hT_low, up)]):
                            for c in range(DC):
                                ins = mm(gu[k % 2][:, j * S:j * S + S], r[:, c, 0:P], wv[:, c, :],
                                         start=(i == 0 and c == 0), stop=(i == 2 and c == DC - 1))
                                if freed is not None and j == 0 and i == 0 and c == 0:
                                    ins.then_inc(w.sem[f"slot{freed}_free"], 1)
                            if i == 1:
                                ins.then_inc(w.sem["lo_used"], 1)
                        ins.then_inc(w.sem["gate_up_psum" if j else f"slot{s}_free"], 1)

                def up_slot(k):
                    return (base + expert_loads(k)[0] + 1) % NSLOT

                def turn_hidden(k, freed=None):
                    pe.wait_ge(w.sem["hidden_ready"], w.next("hidden_ready"))
                    for f in range(2):
                        ins = turn(tr[k % 2][:, f * P:f * P + P], sg[:, k % 2, f * P:f * P + P])
                        if f == 0 and freed is not None:
                            ins.then_inc(w.sem[f"slot{freed}_free"], 1)
                    ins.then_inc(w.sem["hidT_psum"], 1)

                def down(k, first=False, last=False):
                    i = sum(expert_loads(k + 2)) - 1
                    s = (base + i) % NSLOT
                    pe.wait_ge(w.sem["lo_ready"], w.next("lo_ready"))
                    pe.wait_ge(w.sem["hidT_ready"], w.next("hidT_ready"))
                    up, low = halves_of(s, i % NLOW, True)
                    cs = slice(k % 2 * P, k % 2 * P + P)
                    for f in range(2):
                        for j, (hv, wv) in enumerate([(hid_up, up), (hid_up, low), (hid_low, up)]):
                            for h in range(2):
                                ins = mm(acc[h][:, :], hv[:, f, cs], wv[:, f, h * HALF:h * HALF + HALF],
                                         start=(first and f == 0 and j == 0), stop=(last and f == 1 and j == 2))
                            if f == 1 and j == 1:
                                ins.then_inc(w.sem["lo_used"], 1)
                    ins.then_inc(w.sem["expert_ffn_psum" if last else f"slot{s}_free"], 1)

                def step(k):
                    gate_up(k)
                    turn_hidden(k - 1, up_slot(k))
                    down(k - 2, first=(k == 2))

                gate_up(0)
                gate_up(1, up_slot(0))
                turn_hidden(0, up_slot(1))
                pe.wait_ge(sem["expert_added"], w.next("expert_added"))
                for t in range(TT):
                    ins = turn(acc[2][:, t * P:t * P + P], selg[:, t, :])
                ins.then_inc(sem["selT_psum"], 1)
                step(2)
                step(3)
                with w.loop(n // 2 - 2, {"lo_ready": 6, "hidden_ready": 2, "hidT_ready": 2}):
                    step(4)
                    step(5)
                turn_hidden(n - 1)
                down(n - 2)
                down(n - 1, last=True)

            def attention(units):
                n = len(units)
                for i in range(n + 2):
                    if i < n:
                        u = units[i]
                        for h in range(2):
                            o = sbank[i % 2][:, h, 0:u["nk"]]
                            fg = u.get("forget")
                            ins = mm(o, u["q"][h], u["k"][h], start=True, stop=fg is None)
                            if fg is not None:
                                t0, nk, r = u["t"] * P, u["nk"], slice(64 * h, 64 * h + 4)
                                mm(o, fsc[r, 4, t0:t0 + P],
                                   sel4[r, fg[h]:fg[h] + 1, :].to_broadcast([4, nk // P, P]),
                                   start=False, stop=False)
                                ins = mm(o, sel4[r, fg[h], :], fsc[r, 5, 0:nk], start=False, stop=True)
                        ins.then_inc(sem["scores_psum"], 1)
                    if 1 <= i <= n:
                        u = units[i - 1]
                        pe.wait_ge(sem["probs_ready"], w.next("probs_ready"))
                        for h in range(2):
                            for kt in range(u["nk"] // P):
                                o = h * S + kt * P
                                ins = turn(tr[(i - 1) % 2][:, o:o + P],
                                           sc[:, (i - 1) % 2, h, kt * P:kt * P + P])
                        ins.then_inc(sem["probsT_psum"], 1)
                    if i >= 2:
                        u = units[i - 2]
                        pe.wait_ge(sem["probsT_ready"], w.next("probsT_ready"))
                        b = acc[i % 2]
                        for h in range(2):
                            o = b[:, h * P:h * P + P] if u["wide"] else b[64 * h:64 * h + 64, 0:P]
                            kts = u["nk"] // P
                            for kt in range(kts):
                                ins = mm(o, u["v"][h][kt], pT[:, i % 2, h, kt * P:kt * P + P],
                                         start=(kt == 0), stop=(kt == kts - 1))
                        ins.then_inc(sem["attn_psum"], 1)
                pe.wait_ge(sem["attn_copied"], w.next("attn_copied", n))

            def head_norms(n, block):
                for i in range(n):
                    pe.wait_ge(sem["squares_ready"], w.next("squares_ready"))
                    mm(tr[i % 2][:, :], block[:, :], sqb[i % 2], start=True,
                       stop=True).then_inc(sem["sumsq_psum"], 1)

            pe.wait_ge(sem["first_consts_ready"], w.next("first_consts_ready"))
            pe.wait_ge(sem["rows_loaded"], w.next("rows_loaded", 16 * ROW_DMAS))
            turn(tr[0][:, 0:N1], rows[0:N1, 0, :])
            mm(tr[0][:, P:P + 1], frow[0:1, :], ones[0:1, 0:1], start=True, stop=True).then_inc(sem["cols_psum"], 1)
            pe.wait_ge(sem["cols_ready"], w.next("cols_ready"))

            transpose_h(split=True)
            for k in range(len(MIX0_LOADS)):
                if k == 3:
                    tokens_out(take_halves(k, UP1, P), 0, P)
                else:
                    two_tiles(k, UP1)
                if k == 4:
                    pe.wait_ge(sem["consts_ready"], w.next("consts_ready"))
                    head_norms(2, blk64)
                elif k == 7:
                    head_norms(1, blk64)
            end_fills()
            pe.wait_ge(sem["qk_ready"], w.next("qk_ready", 3))
            attention(units_mix0())
            pe.wait_ge(sem["conv_ready"], w.next("conv_ready"))
            out_proj(4)
            transpose_h(split=True)
            ffn(D_FF // CH)

            transpose_h(split=True)
            for k in range(len(MIX1_LOADS)):
                two_tiles(k, UP1)
            end_fills()
            s = take(2)
            for h in range(DC):
                pe.wait_ge(sem["xc_ready"], w.next("xc_ready"))
                b = begin_fill()
                for g in range(2):
                    ins = mm(b[:, g * S:g * S + S], ring[:, s, g * D + h * P:g * D + h * P + P],
                             g_xc[:, h, :], start=True, stop=True)
                ins.then_inc(sem["gates_psum"], 1)
            end_fills()
            pe.wait_ge(sem["lru_ready"], w.next("lru_ready"))
            out_proj(4, second_half="lru_ready")

            transpose_h()
            pe.wait_ge(sem["inputs_loaded"], w.next("inputs_loaded", 48))
            for t in range(TT):
                for c in range(DC):
                    ins = mm(tr[0][:, t * N_EXP:t * N_EXP + N_EXP], hT[:, c, t * P:t * P + P],
                             rt[:, c, :], start=(c == 0), stop=(c == DC - 1))
            ins.then_inc(sem["logits_psum"], 1)
            pe.wait_ge(sem["chosen_ready"], w.next("chosen_ready"))
            for t in range(TT):
                for tt in range(t + 1):
                    mm(tr[1][:, t * N_EXP:t * N_EXP + N_EXP], (upper if tt == t else ones)[:, :],
                       route[:, 2, tt, :], start=(tt == 0), stop=(tt == t))
            for t in range(TT):
                ins = mm(tr[1][:, 32:32 + N_EXP], ones[:, :], route[:, 2, t, :],
                         start=(t == 0), stop=(t == TT - 1))
            ins.then_inc(sem["ranks_psum"], 1)

            def experts(w, slots):
                def gather():
                    pe.wait_ge(sem["sel_ready"], w.next("sel_ready"))
                    for c in range(DC):
                        for t in range(TT):
                            ins = mm(tr[c // 4][:, (c % 4) * P:(c % 4) * P + P],
                                     xn[:, t, c * P:c * P + P], sel[:, t, :],
                                     start=(t == 0), stop=(t == TT - 1))
                        if c % 4 == 3:
                            ins.then_inc(sem["chosen_h_psum"], 1)

                def expert(last=False):
                    pe.wait_ge(sem["chosen_h_ready"], w.next("chosen_h_ready", 2))
                    expert_ffn(w, slots)
                    if not last:
                        gather()
                    pe.wait_ge(sem["selT_ready"], w.next("selT_ready"))
                    pe.wait_ge(sem["expert_out"], w.next("expert_out"))
                    for t in range(TT):
                        for h in range(2):
                            ins = mm(ebank[2 * t + h][:, :], selT[:, t, :],
                                     ye[:, h * HALF:h * HALF + HALF], start=True, stop=True)
                    ins.then_inc(sem["expert_psum"], 1)

                gather()
                per = {"lo_ready": 42, "hidden_ready": 14, "hidT_ready": 14, "sel_ready": 1, "selT_ready": 1,
                       "chosen_h_ready": 2, "expert_out": 1, "expert_added": 1}
                with w.loop(N_EXP - 1, per):
                    expert()
                expert(last=True)
                w.next("expert_added")

            pe.wait_ge(sem["ranks_ready"], w.next("ranks_ready"))
            experts(w, slots)
            pe.wait_ge(sem["count_ready"], w.next("count_ready"))
            n_max = pe.value_load(cnt[0:1, 0:1], min_val=0, max_val=S)
            with pe.If(n_max > CAP):
                experts(w.branch(sem_over), Slots())

            def layer(l):
                transpose_h(split=True)
                ffn(FFN_DIM // CH)
                transpose_h(split=True)
                for k, (c0, n, *_) in enumerate(MIX2_LOADS):
                    if k in (2, 6):
                        tokens_out(take_halves(k, UP2), 0, CH)
                    elif n == 4:
                        tiles_out(take_halves(k, UP2, P), [(0, P, 0)])
                    elif n == 32:
                        tiles_out(take_halves(k, UP2, n), [(0, n, 0)])
                    else:
                        two_tiles(k, UP2)
                k = len(MIX2_LOADS)
                transpose_h(split=True)
                head_norms(2, blk64)
                two_tiles(k, UP2)
                two_tiles(k + 1, UP2)
                head_norms(2, blk64)
                tokens_out(take_halves(k + 2, UP2), 0, CH)
                tokens_out(take_halves(k + 3, UP2), 0, CH)
                end_fills()
                pe.wait_ge(sem["qk_ready"], w.next("qk_ready", 4))
                for i in range(2):
                    for j in range(2):
                        ins = mm(gu[i][:, j * S:j * S + S], rope[:, :], q2[:, 4 + 2 * i + j, :],
                                 start=True, stop=True)
                    ins.then_inc(sem["rope_psum"], 1)
                pe.wait_ge(sem["forget_ready"], w.next("forget_ready"))
                pe.wait_ge(sem["rope_ready"], w.next("rope_ready", 2))
                attention(units_causal(0) + units_causal(1))
                rwkv()
                out_proj(4)
                head_norms(2, ones)
                transpose_h(split=True)
                for k in range(len(XQ_LOADS)):
                    two_tiles(k, UP2)
                end_fills()
                head_norms(2, ones)
                pe.wait_ge(sem["qk_ready"], w.next("qk_ready", 4))
                attention(units_mem())
                out_proj(2)
                transpose_h(split=True)
                ffn(FFN_DIM // CH)
                slots.at += SKIP2

            def rwkv():
                s = take(4)
                pe.wait_ge(sem["lora_ready"], w.next("lora_ready"))
                for j in range(3):
                    for p in range(4):
                        b = begin_fill()
                        cs = slice(p * P, p * P + P)
                        if j == 0:
                            ins = mm(b[:, 0:S], ring[0:64, s, cs], zr[0:64, 12, 1:S + 1], start=True, stop=True)
                        elif j == 1:
                            ins = mm(b[:, 0:S], ring[64:P, s, cs], zr[64:P, 12, 1:S + 1], start=True, stop=True)
                        else:
                            mm(b[:, 0:S], ring[:, s, HALF + p * P:HALF + p * P + P], zr[:, 13, 1:S + 1],
                               start=True, stop=False)
                            ins = mm(b[:, 0:S], ring[0:32, s, D + p * P:D + p * P + P],
                                     zr[0:32, 14, 1:S + 1], start=False, stop=True)
                        ins.then_inc(sem["lora_psum"], 1)
                end_fills()
                for i in range(2):
                    pe.wait_ge(sem["squares_ready"], w.next("squares_ready"))
                    mm(tr[i][:, :], blk64[:, :], sqb[i], start=True, stop=True).then_inc(sem["sumsq_psum"], 1)
                for i in range(2):
                    pe.wait_ge(sem["bonus_in"], w.next("bonus_in"))
                    mm(gu[i][:, :], blk64[:, :], rtb[i], start=True, stop=True).then_inc(sem["bonus_psum"], 1)
                for n, (src, off) in enumerate(((zr, 1), (Bb, 0), (Kb, 0))):
                    pe.wait_ge(sem["tokens_in"], w.next("tokens_in"))
                    for t in range(TT):
                        b = tr[t]
                        if n:
                            pe.wait_ge(sem["tokens_copied"], w.next("tokens_copied"))
                        else:
                            pe.wait_ge(sem["sumsq_read"], w.next("sumsq_read"))
                        for p in range(4):
                            v = src[:, 8 + p, off + t * P:off + t * P + P] if n == 0 else src[:, p, t * P:t * P + P]
                            ins = turn(b[:, p * P:p * P + P], v)
                        ins.then_inc(sem["tokens_psum"], 1)
                pe.wait_ge(sem["gram_in"], w.next("gram_in"))
                pe.wait_ge(sem["bonus_ready"], w.next("bonus_ready"))
                for u in range(2 * 8):
                    t, h = u // 8, u % 8
                    p, r = h // 2, slice(64 * (h % 2), 64 * (h % 2) + 64)
                    if u >= 2:
                        pe.wait_ge(sem["gram_ready"], w.next("gram_ready"))
                    b = gu[u % 2]
                    mm(b[:, 0:S], Bh[r, p, t * P:t * P + P], AR[r, p, t, :, :].rearrange("p a s -> p (a s)"),
                       start=True, stop=True)
                    mm(b[:, S:2 * S], Kh[r, p, t * P:t * P + P], AR[r, p, t, :, :].rearrange("p a s -> p (a s)"),
                       start=True, stop=True).then_inc(sem["gram_psum"], 1)
                pe.wait_ge(sem["gram_ready"], w.next("gram_ready", 2))
                pe.wait_ge(sem["tokens_copied"], w.next("tokens_copied", 2))
                for t in range(TT):
                    for h in range(8):
                        ins = mm(tr[t][:, h * 64:h * 64 + 64], G[:, t, h, 2, :], Vt[:, t, h * 64:h * 64 + 64],
                                 start=True, stop=True)
                    ins.then_inc(sem["akv_psum"], 1)
                for q in range(4):
                    if q >= 2:
                        pe.wait_ge(sem["inv_ready"], w.next("inv_ready"))
                    for j in range(4):
                        ins = mm(gu[q % 2][:, j * P:j * P + P], G[:, q // 2, 4 * (q % 2) + j, 0, :],
                                 ident[:, :], start=True, stop=True)
                    ins.then_inc(sem["inv_a_psum"], 1)
                steps = 4 * (len(LEVELS) - 1)
                for i in range(steps + 1):
                    if i < steps:
                        q = i % 4
                        if i < 2:
                            pe.wait_ge(sem["inv_ready"], w.next("inv_ready"))
                        for j in range(4):
                            ins = mm(gu[i % 2][:, j * P:j * P + P], G[:, q // 2, 4 * (q % 2) + j, 0, :],
                                     Tm[:, 4 * q + j, :], start=True, stop=True)
                        ins.then_inc(sem["inv_x_psum"], 1)
                    if i >= 1:
                        k = i - 1
                        q = k % 4
                        pe.wait_ge(sem["inv_x_ready"], w.next("inv_x_ready"))
                        if k >= 2:
                            pe.wait_ge(sem["inv_ready"], w.next("inv_ready"))
                        for j in range(4):
                            o = slice(j * P, j * P + P)
                            if k < steps - 4:
                                mm(tr[k % 2][:, o], Um[:, 4 * q + j, :], Xb[:, k % 2, o], start=True, stop=True)
                            ins = mm(acc[k % 2][:, o], Xb[:, k % 2, o], Um[:, 4 * q + j, :],
                                     start=True, stop=True)
                        ins.then_inc(sem["inv_y_psum"], 1)
                pe.wait_ge(sem["inv_ready"], w.next("inv_ready", 2))
                pe.wait_ge(sem["akv_ready"], w.next("akv_ready", TT))
                for c in range(NRW):
                    t, r = c // 2, slice(RW * (c % 2), RW * (c % 2) + RW)
                    if c:
                        pe.wait_ge(sem["state_ready"], w.next("state_ready"))
                        for k, name in enumerate(("carry_psum", "carry_y_psum")):
                            for p in range(4):
                                ins = mm(gu[k][:, p * P:p * P + P], AR[:, p, t, k, :], Sbd[:, p, :],
                                         start=True, stop=True)
                            ins.then_inc(sem[name], 1)
                        pe.wait_ge(sem["removal_in"], w.next("removal_in"))
                    for h in range(8):
                        ins = mm(tr[0][:, h * 64:h * 64 + 64], Um[:, 8 * t + h, :],
                                 AkV[:, t, h * 64:h * 64 + 64], start=True, stop=True)
                    ins.then_inc(sem["removal_psum"], 1)
                    pe.wait_ge(sem["removal_ready"], w.next("removal_ready"))
                    if c < NRW - 1:
                        for p in range(4):
                            o = slice(p * P, p * P + P)
                            mm(tr[1][:, o], Bt[r, t, o], SA[r, t, o], start=True, stop=False)
                            ins = mm(tr[1][:, o], Kt[r, t, o], Vt[r, t, o], start=False, stop=True)
                        ins.then_inc(sem["state_psum"], 1)
                    if c % 2:
                        for h in range(8):
                            o = slice(h * 64, h * 64 + 64)
                            mm(acc[t][:, o], G[:, t, h, 1, :], SA[:, t, o], start=True, stop=False)
                            ins = mm(acc[t][:, o], G[:, t, h, 3, :], Vt[:, t, o], start=False, stop=True)
                        ins.then_inc(sem["y_psum"], 1)
                for t in range(TT):
                    pe.wait_ge(sem["y_normed"], w.next("y_normed"))
                    for p in range(4):
                        ins = turn(acc[2 + t][:, p * P:p * P + P], yS[:, t, p * P:p * P + P])
                    ins.then_inc(sem["yT_psum"], 1)
                pe.wait_ge(sem["rwkv_ready"], w.next("rwkv_ready"))

            pe.wait_ge(sem["rows2_loaded"], w.next("rows2_loaded", 16 * ROW_DMAS2 * DEPTH2))
            for l in range(DEPTH2):
                ins = turn(tr[0][:, l * N2:l * N2 + N2], rows[0:N2, 1 + l, :])
            ins.then_inc(sem["cols_psum"], 1)
            run_layers(w, layer, LAYER_PE)

        @block.scalar
        def _(act):
            w = Turns(act, sem)
            slots = Slots()
            f = nc.scalar.activation

            act.wait_ge(sem["rows_zeroed"], w.next("rows_zeroed"))
            flat1 = [("mix", A["norm_mix"].rearrange("l d -> (l d)"), 16),
                     ("ffn", A["norm_ffn"].rearrange("l d -> (l d)"), 16),
                     ("rconv", A["rg_conv_w"][0].rearrange("k d -> (k d)"), 32),
                     ("rconvb", A["rg_conv_b"][0], 8), ("gab", A["rg_gate_a_b"][0], 8),
                     ("gxb", A["rg_gate_x_b"][0], 8), ("lam", A["rg_lambda"][0], 8),
                     ("hconv", A["hy_conv_w"][0].rearrange("k d -> (k d)"), 12)]
            for name, src, n in flat1:
                act.dma_start(rows[V1[name][0]:V1[name][1], 0, :],
                              src.rearrange("(r k) -> r k", k=P)).then_inc(sem["rows_loaded"], 16)
            for name, src in (("qg", A["hy_q_gain"][0]), ("kg", A["hy_k_gain"][0])):
                for h in range(2):
                    act.dma_start(rows[V1[name][0]:V1[name][1], 0, h * HD:h * HD + HD],
                                  src.rearrange("(r k) -> r k", r=1)).then_inc(sem["rows_loaded"], 16)
            def square_sum(src, wait=True):
                for t in range(TT):
                    if wait:
                        act.wait_ge(sem["x_ready"], w.next("x_ready"))
                    f(xn[:, t, :], src[:, t, :], ACT.Square,
                      accum_out=ss[:, 0, t:t + 1]).then_inc(sem["act_done"], w.mark("act_done"))
                    act.wait_ge(sem["act_done"], w.now("act_done"))
                    f(ss[:, 1, t:t + 1], ss[:, 0, t:t + 1], ACT.Sqrt, scale=1.0 / D,
                      bias=epsc[:, 0:1]).then_inc(sem["rms_ready"], 1)

            def finish_h(gain, split=False):
                dst = hT_up if split else hT
                for cp in range(DC // 2) if split else (0, 2):
                    act.wait_ge(sem["hT_psum_act"], w.next("hT_psum_act"))
                    for i in range(2):
                        c = 2 * cp + i
                        ins = f(dst[:, c, :], hbank[cp][:, i * S:i * S + S], ACT.Copy, scale=gain(c))
                    ins.then_inc(sem["hT_act"], 1)

            def copy_fill(n, parts, freed=None):
                act.wait_ge(sem["proj_psum"], w.next("proj_psum"))
                for j, (dst, src, fn, kw) in enumerate(parts):
                    ins = f(dst, src, fn, **kw)
                    if j == 0 and freed is not None:
                        ins.then_inc(sem[f"slot{freed}_free"], 1)
                    elif j == len(parts) - 1:
                        ins.then_inc(sem["proj_copied"], w.mark("proj_copied"))

            def two(n, d0, d1, freed, fn=ACT.Copy, rows_=P):
                b = gu[n % 2]
                copy_fill(n, [(d0, b[0:rows_, 0:S], fn, {}), (d1, b[0:rows_, S:2 * S], fn, {})], freed)

            def halves(n, dst, rows_, freed):
                b = gu[n % 2]
                copy_fill(n, [(dst[0:rows_, i * P:i * P + P], b[0:rows_, i * P:i * P + P], ACT.Copy, {})
                              for i in range(2)], freed)

            def proj_upper(up, loads):
                base = slots.at

                def upper(k):
                    if k < len(loads):
                        s = (base + k) % NSLOT
                        slot, half = split_views(loads[k], ring[:, s, :], w_up[:, up + k % 2, :])
                        act.wait_ge(sem[f"slot{s}_raw"], w.next(f"slot{s}_raw", 16))
                        f(half, slot, ACT.Copy).then_inc(sem["hi_ready"], 1)

                return upper

            def norm_ffn(n, gain):
                base = slots.at
                slots.at += 3 * n

                def upper(k, j):
                    s = (base + 3 * k + j) % NSLOT
                    act.wait_ge(sem[f"slot{s}_raw"], w.next(f"slot{s}_raw", 16))
                    f(w_up[:, s, :], ring[:, s, :], ACT.Copy).then_inc(sem["hi_ready"], 1)

                def silu(j):
                    act.wait_ge(sem["gate_up_psum"], w.next("gate_up_psum"))
                    f(sg[:, j, :], gu[j][:, 0:S], ACT.Silu).then_inc(sem["silu_ready"], 1)

                def step(k):
                    silu(0)
                    upper(k + 1, 0)
                    upper(k + 1, 1)
                    silu(1)
                    upper(k + 1, 2)

                square_sum(x)
                upper(0, 0)
                upper(0, 1)
                finish_h(gain, split=True)
                upper(0, 2)
                with w.loop((n - 1) // 2, {"gate_up_psum": 4} | {f"slot{s}_raw": 16 for s in range(NSLOT)}):
                    step(0)
                    step(1)
                if n % 2 == 0:
                    step(n - 2)
                silu(0)
                silu(1)

            def head_square(i, pair):
                f(sqb[i % 2].rearrange("p (a b) -> p a b", a=2), pair, ACT.Square).then_inc(sem["squares_ready"], 1)

            def head_root(i, inv):
                act.wait_ge(sem["sumsq_psum"], w.next("sumsq_psum"))
                if i >= 2:
                    act.wait_ge(sem["qk_ready"], w.next("qk_ready"))
                f(rtb[i % 2], tr[i % 2][:, :], ACT.Sqrt, scale=inv, bias=epsc[:, 0:1]).then_inc(sem["root_ready"], 1)

            def head_norms(pairs, inv, then=None, later=None):
                n = len(pairs)
                for i in range(n):
                    if i >= 2:
                        head_root(i - 2, inv)
                    head_square(i, pairs[i])
                    if i == 1 and then is not None:
                        then()
                if later is not None:
                    later()
                for i in range(max(0, n - 2), n):
                    head_root(i, inv)

            def norms_used(n=2):
                act.wait_ge(sem["qk_ready"], w.next("qk_ready", n))

            def attention(units):
                n = len(units)
                for i in range(n + 2):
                    if i < n:
                        u, b = units[i], i % 2
                        act.wait_ge(sem["maxima_ready"], w.next("maxima_ready"))
                        src = sc[:, b, :, :] if ("slope" in u or "causal" in u) else sbank[b][:, :, 0:S]
                        nk = u["nk"]
                        if "sink" in u:
                            f(snk[:, b, :], snk[:, b, :], ACT.Exp)
                        for h in range(2):
                            ins = f(sc[:, b, h, 0:nk], src[:, h, 0:nk], ACT.Exp, bias=negmx[:, b, h:h + 1],
                                    accum_out=rsum[:, b, h:h + 1])
                        ins.then_inc(sem["exp_ready"], 1)
                    if 1 <= i <= n:
                        u, b = units[i - 1], (i - 1) % 2
                        act.wait_ge(sem["probsT_psum"], w.next("probsT_psum"))
                        nk = u["nk"]
                        f(pT[:, b, :, 0:nk], tr[b][:, :].rearrange("p (h k) -> p h k", h=2)[:, :, 0:nk],
                                ACT.Copy).then_inc(sem["probsT_ready"], 1)
                    if i >= 2:
                        u, b = units[i - 2], acc[i % 2]
                        act.wait_ge(sem["attn_psum"], w.next("attn_psum"))
                        src = b[:, 0:2 * P].rearrange("p (h s) -> p h s", h=2) if u["wide"] else b[:, 0:P]
                        f(u["dst"], src, ACT.Copy).then_inc(sem["attn_copied"], 1)

            act.wait_ge(sem["x_loaded"], w.next("x_loaded", 16))
            act.wait_ge(sem["first_consts_ready"], w.next("first_consts_ready"))
            square_sum(x, wait=False)
            upper = proj_upper(UP1, MIX0_LOADS)
            upper(0)
            finish_h(lambda c: col("mix", c), split=True)
            upper(1)
            act.dma_start(sinks[:, 0:8], A["hy_sinks"][0:1, :].to_broadcast([P, 8])).then_inc(sem["inputs_loaded"], 16)
            act.dma_start(pos_i[:, :], A["positions_2"][0:1, :].to_broadcast([P, S])).then_inc(sem["inputs_loaded"], 16)
            act.dma_start(rt[:, :, :], A["moe_router"][0].rearrange("(c p) e -> p c e", p=P)
                          ).then_inc(sem["inputs_loaded"], 16)

            act.dma_start(mem[:, :, :], A["mem_2"][0].rearrange("(t p) d -> p t d", p=P)
                          ).then_inc(sem["mem_loaded"], 16)
            for k in range(len(MIX0_LOADS)):
                s = slots.next()
                if k == 3:
                    halves(k, z0[:, 6, :], P, s)
                else:
                    j = 2 * k - (k > 3)
                    two(k, z0[:, j, :], z0[:, j + 1, :], s)
                upper(k + 2)
                if k == 2:
                    act.wait_ge(sem["proj_copied"], w.now("proj_copied"))
                    head_square(0, z0[:, 0:2, :])
                    head_square(1, z0[:, 2:4, :])
                elif k == 5:
                    head_root(0, 1.0 / HD)
                    head_square(2, z0[:, 4:6, :])
                    head_root(1, 1.0 / HD)
                elif k == 8:
                    head_root(2, 1.0 / HD)
                if k == 3:
                    act.wait_ge(sem["angles_ready"], w.next("angles_ready"))
                    f(sinT[:, :], ang[:, 0, :], ACT.Sin)
                    f(cosT[:, :], ang[:, 1, :], ACT.Sin)
                    act.wait_ge(sem["lam_abs"], w.next("lam_abs"))
                    f(lamb[:, 1, :], lamb[:, 1, :], ACT.Exp, scale=-1.0).then_inc(sem["lam_exp"], 1)
            norms_used()
            attention(units_mix0())
            slots.at += 4
            norm_ffn(D_FF // CH, lambda c: col("ffn", c))

            square_sum(x)
            upper = proj_upper(UP1, MIX1_LOADS)
            upper(0)
            finish_h(lambda c: col("mix", DC + c), split=True)
            upper(1)
            for k in range(len(MIX1_LOADS)):
                s = slots.next()
                if k < 4:
                    two(k, g_x[:, 2 * k, 3:S + 3], g_x[:, 2 * k + 1, 3:S + 3], s)
                else:
                    j = 2 * (k - 4)
                    two(k, g_y[:, j, :], g_y[:, j + 1, :], s, ACT.Gelu_apprx_tanh)
                upper(k + 2)
                if k >= 4:
                    act.wait_ge(sem["proj_copied"], w.now("proj_copied"))
                    for c in (j, j + 1):
                        f(g_xc[:, c, :], g_x[:, c, 3:S + 3], ACT.Identity, scale=col("rconv", 3 * DC + c),
                          bias=col("rconvb", c)).then_inc(sem["xc_started"], 1)
            s = slots.next()
            for h in range(DC):
                act.wait_ge(sem["gates_psum"], w.next("gates_psum"))
                b = gu[h % 2]
                ins = f(g_r[:, h, :], b[:, 0:S], ACT.Sigmoid, bias=col("gab", h))
                if h == DC - 1:
                    ins.then_inc(sem[f"slot{s}_free"], 1)
                f(g_i[:, h, :], b[:, S:2 * S], ACT.Sigmoid, bias=col("gxb", h)).then_inc(sem["proj_copied"], w.mark("proj_copied"))
            act.wait_ge(sem["log_a_ready"], w.next("log_a_ready"))
            f(g_t[:, :, :], g_r[:, :, :], ACT.Tanh).then_inc(sem["tanh_ready"], w.mark("tanh_ready"))
            act.wait_ge(sem["tanh_ready"], w.now("tanh_ready"))
            for i in range(2):
                cs = slice(4 * i, 4 * i + 4)
                f(g_r[:, cs, :], g_r[:, cs, :], ACT.Exp).then_inc(sem["decay_ready"], 1)
            for i in range(2):
                cs = slice(4 * i, 4 * i + 4)
                act.wait_ge(sem["mult_sq_ready"], w.next("mult_sq_ready"))
                f(g_m[:, cs, :], g_m[:, cs, :], ACT.Sqrt, scale=-1.0).then_inc(sem["mult_ready"], 1)
            slots.at += 4
            square_sum(x)
            finish_h(lambda c: col("ffn", DC + c))
            act.wait_ge(sem["top_ready"], w.next("top_ready"))
            f(gt[:, :, 1], gt[:, :, 0], ACT.Exp).then_inc(sem["gate_exp"], 1)

            def expert_ffn(w, slots):
                base, n = slots.at, D_FF // CH
                slots.at += 3 * n

                def upper(i):
                    s = (base + i) % NSLOT
                    act.wait_ge(w.sem[f"slot{s}_raw"], w.next(f"slot{s}_raw", 16))
                    f(w_up[:, s, :], ring[:, s, :], ACT.Copy).then_inc(w.sem["hi_ready"], 1)

                def silu(k):
                    act.wait_ge(w.sem["gate_up_psum"], w.next("gate_up_psum"))
                    f(sg[:, k % 2, :], gu[k % 2][:, 0:S], ACT.Silu).then_inc(w.sem["silu_ready"], 1)

                def hidden_upper(k):
                    act.wait_ge(w.sem["hidT_psum"], w.next("hidT_psum"))
                    f(hid_up[:, :, k % 2 * P:k % 2 * P + P], tr[k % 2][:, 0:S].rearrange("p (f s) -> p f s", f=2),
                      ACT.Copy).then_inc(w.sem["hidT_up"], 1)

                def step(k):
                    first, m = expert_loads(k + 1)
                    upper(first)
                    if m > 1:
                        upper(first + 1)
                    silu(k)
                    if k:
                        hidden_upper(k - 1)
                    if m > 2:
                        upper(first + 2)

                def start():
                    upper(0)
                    upper(1)
                    for i in range(2):
                        act.wait_ge(sem["chosen_h_psum"], w.next("chosen_h_psum"))
                        for c in range(4 * i, 4 * i + 4):
                            ins = f(hT_up[:, c, 0:P], tr[i][:, c % 4 * P:c % 4 * P + P], ACT.Copy, scale=col("ffn", DC + c))
                        ins.then_inc(sem["chosen_h_up"], 1)

                def rest():
                    step(0)
                    with w.loop(n // 2 - 1, {"gate_up_psum": 2, "hidT_psum": 2}
                                | {f"slot{s}_raw": 16 for s in range(NSLOT)}):
                        step(1)
                        step(2)
                    step(n - 1)
                    upper(expert_loads(n + 1)[0])
                    hidden_upper(n - 1)

                return start, rest

            def experts(w, slots):
                start, rest = expert_ffn(w, slots)

                def expert(last=False):
                    rest()
                    act.wait_ge(sem["selT_psum"], w.next("selT_psum"))
                    f(selT[:, :, :], acc[2][:, 0:S].rearrange("p (t s) -> p t s", t=TT), ACT.Copy).then_inc(sem["selT_ready"], 1)
                    act.wait_ge(sem["expert_ffn_psum"], w.next("expert_ffn_psum"))
                    f(ye[:, 0:HALF], acc[0][:, :], ACT.Copy).then_inc(w.sem[f"slot{(slots.at - 1) % NSLOT}_free"], 1)
                    f(ye[:, HALF:D], acc[1][:, :], ACT.Copy).then_inc(sem["expert_out"], 1)
                    if not last:
                        start()

                start()
                per = ({"selT_psum": 1, "chosen_h_psum": 2, "gate_up_psum": 14, "hidT_psum": 14, "expert_ffn_psum": 1}
                       | {f"slot{s}_raw": 16 * 7 for s in range(NSLOT)})
                with w.loop(N_EXP - 1, per):
                    expert()
                expert(last=True)

            experts(w, slots)
            act.wait_ge(sem["count_ready"], w.next("count_ready"))
            n_max = act.value_load(cnt[0:1, 0:1], min_val=0, max_val=S)
            with act.If(n_max > CAP):
                experts(w.branch(sem_over), Slots())

            def layer(l):
                norm_ffn(FFN_DIM // CH, lambda c: col2("ffn1", c))
                square_sum(x)
                upper = proj_upper(UP2, MIX2_LOADS + XKV_LOADS)
                upper(0)
                finish_h(lambda c: col2("mix", c), split=True)
                upper(1)
                n = 0
                for m in range(2):
                    for j in (0, 2):
                        s = slots.next()
                        two(n, q2[:, 4 * m + j, :], q2[:, 4 * m + j + 1, :], s)
                        n += 1
                        upper(n + 1)
                        if n == 1:
                            act.wait_ge(sem["mem_loaded"], w.next("mem_loaded", 16))
                            square_sum(mem, wait=False)
                    s = slots.next()
                    two(n, v2[:, m, 0, :], v2[:, m, 1, :], s)
                    n += 1
                    upper(n + 1)
                    if m == 0:
                        s = slots.next()
                        copy_fill(n, [(zf[r:r + 4, :], gu[n % 2][r:r + 4, 0:S], ACT.Copy, {}) for r in (0, 64)], s)
                        n += 1
                        upper(n + 1)
                for k in range(7):
                    s = slots.next()
                    two(n, zr[:, 2 * k, 1:S + 1], zr[:, 2 * k + 1, 1:S + 1], s)
                    n += 1
                    upper(n + 1)
                s = slots.next()
                halves(n, zr[:, 14, 1:S + 1], 32, s)
                n += 1
                upper(n + 1)

                def memory_keys():
                    act.wait_ge(sem["forget_abs"], w.next("forget_abs"))
                    f(fsc[:, 2, :], fsc[:, 1, :], ACT.Exp, scale=-1.0).then_inc(sem["forget_exp"], 1)
                    for k in range(2):
                        s = slots.next()
                        two(n + k, xk[:, 2 * k, :], xk[:, 2 * k + 1, :], s)
                        upper(n + k + 2)

                head_norms([q2[:, 2 * i:2 * i + 2, :] for i in range(4)], 1.0 / HD,
                           then=lambda: finish_h(lambda c: col2("mem", c), split=True), later=memory_keys)
                for k in range(2):
                    s = slots.next()
                    two(n + 2 + k, xv[:, 0, k * CH:k * CH + CH], xv[:, 1, k * CH:k * CH + CH], s)
                norms_used()
                attention(units_causal(0) + units_causal(1))
                rwkv()
                slots.at += 4

                def queries():
                    square_sum(x)
                    upper = proj_upper(UP2, XQ_LOADS)
                    upper(0)
                    finish_h(lambda c: col2("xat", c), split=True)
                    upper(1)
                    for k in range(2):
                        s = slots.next()
                        two(k, xq[:, 2 * k, :], xq[:, 2 * k + 1, :], s)
                    act.wait_ge(sem["proj_copied"], w.now("proj_copied"))

                head_norms([xk[:, 2 * i:2 * i + 2, :] for i in range(2)]
                           + [xq[:, 2 * i:2 * i + 2, :] for i in range(2)], 1.0 / P, then=queries)
                norms_used()
                attention(units_mem())
                act.dma_start(mem[:, :, :], A["mem_2"][0].rearrange("(t p) d -> p t d", p=P)
                              ).then_inc(sem["mem_loaded"], 16)
                slots.at += 2
                norm_ffn(FFN_DIM // CH, lambda c: col2("ffn2", c))
                slots.at += SKIP2

            def rwkv():
                s = slots.next()
                act.wait_ge(sem["tail_shifted"], w.next("tail_shifted"))
                f(zr[0:64, 12, 1:S + 1], zr[0:64, 12, 1:S + 1], ACT.Tanh)
                f(zr[:, 13, 1:S + 1], zr[:, 13, 1:S + 1], ACT.Sigmoid)
                f(zr[0:32, 14, 1:S + 1], zr[0:32, 14, 1:S + 1], ACT.Sigmoid).then_inc(sem["lora_ready"], 1)
                for j in range(3):
                    for p in range(4):
                        act.wait_ge(sem["lora_psum"], w.next("lora_psum"))
                        b = gu[(4 * j + p) % 2][:, 0:S]
                        if j == 0:
                            ins = f(lw[:, p, :], b, ACT.Sigmoid, bias=col2("w0", p))
                        elif j == 1:
                            ins = f(ra[:, p, :], b, ACT.Sigmoid, bias=col2("a0", p))
                        elif p < 3:
                            ins = f(rg[:, p, :], b, ACT.Copy)
                        else:
                            f(rg[:, p, 0:P], b[:, 0:P], ACT.Copy).then_inc(sem[f"slot{s}_free"], 1)
                            ins = f(rg[:, p, P:S], b[:, P:S], ACT.Copy)
                        ins.then_inc(sem["proj_copied"], w.mark("proj_copied"))
                act.wait_ge(sem["removal_keys"], w.next("removal_keys"))
                for i in range(2):
                    f(sqb[i].rearrange("p (a b) -> p a b", a=2), kk[:, 2 * i:2 * i + 2, :], ACT.Square).then_inc(sem["squares_ready"], 1)
                for i in range(2):
                    act.wait_ge(sem["sumsq_psum"], w.next("sumsq_psum"))
                    f(rtb[i], tr[i][:, :], ACT.Sqrt).then_inc(sem["root_ready"], 1)
                act.wait_ge(sem["sums_ready"], w.next("sums_ready"))
                f(ew[:, :, :], cw[:, :, :], ACT.Exp).then_inc(sem["decays_ready"], 1)
                f(ei[:, :, :], cw[:, :, :], ACT.Exp, scale=-1.0).then_inc(sem["decays_ready"], 1)
                f(ep[:, :, :], ep[:, :, :], ACT.Exp).then_inc(sem["decays_ready"], 1)
                f(et[:, :, :], et[:, :, :], ACT.Exp).then_inc(sem["decays_ready"], 1)
                for dst in (Vt, Bt, Kt):
                    for t in range(TT):
                        act.wait_ge(sem["tokens_psum"], w.next("tokens_psum"))
                        f(dst[:, t, :], tr[t][:, :], ACT.Copy).then_inc(sem["tokens_copied"], 1)
                for t in range(TT):
                    act.wait_ge(sem["akv_psum"], w.next("akv_psum"))
                    f(AkV[:, t, :], tr[t][:, :], ACT.Copy).then_inc(sem["akv_ready"], 1)
                for k in range(4 * (len(LEVELS) - 1)):
                    act.wait_ge(sem["inv_x_psum"], w.next("inv_x_psum"))
                    f(Xb[:, k % 2, :], gu[k % 2][:, :], ACT.Copy).then_inc(sem["inv_x_ready"], 1)
                for c in range(NRW):
                    t, r = c // 2, slice(RW * (c % 2), RW * (c % 2) + RW)
                    if c:
                        act.wait_ge(sem["carry_y_psum"], w.next("carry_y_psum"))
                        f(yS[r, t, :], gu[1][r, :], ACT.Copy).then_inc(sem["carry_y_ready"], 1)
                    act.wait_ge(sem["removal_psum"], w.next("removal_psum"))
                    f(SA[r, t, :], tr[0][r, :], ACT.Copy).then_inc(sem["removal_ready"], 1)
                for t in range(TT):
                    act.wait_ge(sem["y_var"], w.next("y_var"))
                    f(gnst[:, 2, :], gnst[:, 1, :], ACT.Sqrt, scale=1.0 / HD, bias=epsc[:, 1:2]).then_inc(sem["y_root"], 1)
                for t in range(TT):
                    act.wait_ge(sem["yT_psum"], w.next("yT_psum"))
                    for p in range(4):
                        ins = f(mixT[:, 2 + p, t * P:t * P + P], acc[2 + t][:, p * P:p * P + P], ACT.Identity,
                                scale=col2("ln_w", p), bias=col2("ln_b", p))
                    ins.then_inc(sem["yT_ready"], 1)

            run_layers(w, layer, LAYER_ACT)
            act.wait_ge(sem["mem_loaded"], w.next("mem_loaded", 16))

        @block.vector
        def _(dve):
            w = Turns(dve, sem)
            slots = Slots()
            v = nc.vector

            def log1p(out, e, z, z2):
                v.tensor_scalar(z, e, 2.0, None, ALU.add).then_inc(sem["dve_done"], w.mark("dve_done"))
                dve.wait_ge(sem["dve_done"], w.now("dve_done"))
                v.reciprocal(z, z).then_inc(sem["dve_done"], w.mark("dve_done"))
                dve.wait_ge(sem["dve_done"], w.now("dve_done"))
                v.tensor_tensor(z, z, e, ALU.mult).then_inc(sem["dve_done"], w.mark("dve_done"))
                dve.wait_ge(sem["dve_done"], w.now("dve_done"))
                v.tensor_tensor(z2, z, z, ALU.mult).then_inc(sem["dve_done"], w.mark("dve_done"))
                dve.wait_ge(sem["dve_done"], w.now("dve_done"))
                v.tensor_scalar(out, z2, 1.0 / 13, None, ALU.mult).then_inc(sem["dve_done"], w.mark("dve_done"))
                dve.wait_ge(sem["dve_done"], w.now("dve_done"))
                for d in (11, 9, 7, 5, 3):
                    v.scalar_tensor_tensor(out, out, 1.0 / d, z2, ALU.add, ALU.mult).then_inc(sem["dve_done"], w.mark("dve_done"))
                    dve.wait_ge(sem["dve_done"], w.now("dve_done"))
                v.scalar_tensor_tensor(out, out, 1.0, z, ALU.add, ALU.mult).then_inc(sem["dve_done"], w.mark("dve_done"))
                dve.wait_ge(sem["dve_done"], w.now("dve_done"))
                v.tensor_scalar(out, out, 2.0, None, ALU.mult).then_inc(sem["dve_done"], w.mark("dve_done"))
                dve.wait_ge(sem["dve_done"], w.now("dve_done"))

            def norm(src):
                for t in range(TT):
                    dve.wait_ge(sem["rms_ready"], w.next("rms_ready"))
                    v.reciprocal(ss[:, 1, t:t + 1], ss[:, 1, t:t + 1]).then_inc(sem["dve_done"], w.mark("dve_done"))
                    dve.wait_ge(sem["dve_done"], w.now("dve_done"))
                    v.tensor_scalar(xn[:, t, :], src[:, t, :], ss[:, 1, t:t + 1], None, ALU.mult).then_inc(sem["xn_ready"], 1)

            def finish_h(gain):
                w.next("hT_act", 2)
                for cp in (1, 3):
                    dve.wait_ge(sem["hT_psum_dve"], w.next("hT_psum_dve"))
                    for i in range(2):
                        c = 2 * cp + i
                        ins = v.tensor_scalar(hT[:, c, :], hbank[cp][:, i * S:i * S + S], gain(c), None, ALU.mult)
                    ins.then_inc(sem["hT_dve"], 1)

            def finish_h_split(gain):
                for cp in range(DC // 2):
                    dve.wait_ge(sem["hT_act"], w.next("hT_act"))
                    for c in (2 * cp, 2 * cp + 1):
                        ins = v.scalar_tensor_tensor(hT_low[:, c, :], hbank[cp][:, c % 2 * S:c % 2 * S + S], gain(c),
                                                     hT_up[:, c, :].bitcast(F32), ALU.mult, ALU.subtract)
                    ins.then_inc(sem["hT_dve"], 1)

            def head_norms(pairs, gains, then=None, start=0):
                for i, (pair, gain) in enumerate(zip(pairs, gains), start):
                    dve.wait_ge(sem["root_ready"], w.next("root_ready"))
                    v.reciprocal(rtb[i % 2], rtb[i % 2]).then_inc(sem["dve_done"], w.mark("dve_done"))
                    dve.wait_ge(sem["dve_done"], w.now("dve_done"))
                    v.scalar_tensor_tensor(pair, pair, gain, rtb[i % 2].rearrange("p (a b) -> p a b", a=2),
                                                 ALU.mult, ALU.mult).then_inc(sem["qk_ready"], 1)
                    if i == 1 and then is not None:
                        then()

            def attention(units, between=()):
                n = len(units)

                def maxima(i):
                    u, b = units[i], i % 2
                    nk = u["nk"]
                    src = sbank[b][:, :, 0:nk]
                    dst = sc[:, b, :, 0:nk]
                    dve.wait_ge(sem["scores_psum"], w.next("scores_psum"))
                    if "slope" in u:
                        for h in range(2):
                            ins = v.scalar_tensor_tensor(sc[:, b, h, 0:nk], awin[:, S - nk:S], u["slope"][h],
                                                         sbank[b][:, h, 0:nk], ALU.mult, ALU.add)
                        ins.then_inc(sem["dve_done"], w.mark("dve_done"))
                        dve.wait_ge(sem["dve_done"], w.now("dve_done"))
                        src = dst
                    elif "causal" in u:
                        v.tensor_tensor(dst, src, cmask[:, None, S - nk:S].to_broadcast([P, 2, nk]), ALU.add).then_inc(sem["dve_done"], w.mark("dve_done"))
                        dve.wait_ge(sem["dve_done"], w.now("dve_done"))
                        src = dst
                    ins = v.tensor_reduce(negmx[:, b, :], src, AX.X, ALU.max, negate=True)
                    if "sink" in u:
                        k = u["sink"]
                        ins.then_inc(sem["dve_done"], w.mark("dve_done"))
                        dve.wait_ge(sem["dve_done"], w.now("dve_done"))
                        v.tensor_tensor(negmx[:, b, :], negmx[:, b, :], sinks[:, 8 + k:10 + k], ALU.min).then_inc(sem["dve_done"], w.mark("dve_done"))
                        dve.wait_ge(sem["dve_done"], w.now("dve_done"))
                        ins = v.tensor_tensor(snk[:, b, :], negmx[:, b, :], sinks[:, k:k + 2], ALU.add)
                    ins.then_inc(sem["maxima_ready"], 1)

                def normalise(i):
                    u, b = units[i], i % 2
                    nk = u["nk"]
                    dve.wait_ge(sem["exp_ready"], w.next("exp_ready"))
                    if "sink" in u:
                        v.tensor_tensor(rsum[:, b, :], rsum[:, b, :], snk[:, b, :], ALU.add).then_inc(sem["dve_done"], w.mark("dve_done"))
                        dve.wait_ge(sem["dve_done"], w.now("dve_done"))
                    v.reciprocal(rsum[:, b, :], rsum[:, b, :]).then_inc(sem["dve_done"], w.mark("dve_done"))
                    dve.wait_ge(sem["dve_done"], w.now("dve_done"))
                    v.tensor_tensor(sc[:, b, :, 0:nk], sc[:, b, :, 0:nk],
                                          rsum[:, b, :, None].to_broadcast([P, 2, nk]), ALU.mult).then_inc(sem["probs_ready"], 1)

                for i in range(n + 1):
                    if i < n:
                        maxima(i)
                    if i:
                        normalise(i - 1)
                    if i < len(between):
                        between[i]()

            def add_x(scale, freed):
                for i in range(2 * TT):
                    o = x[:, i // 2, (i % 2) * HALF:(i % 2) * HALF + HALF]
                    if scale == 1.0:
                        ins = v.tensor_tensor(o, o, acc[i][:, :], ALU.add)
                    else:
                        ins = v.scalar_tensor_tensor(o, acc[i][:, :], scale, o, ALU.mult, ALU.add)
                    if i == 0:
                        ins.then_inc(sem[f"slot{freed}_free"], 1)
                    if i % 2:
                        ins.then_inc(sem["x_ready"], 1)

            def out_proj(nslots):
                slots.at += nslots
                dve.wait_ge(sem["out_psum"], w.next("out_psum"))
                add_x(1.0, (slots.at - 1) % NSLOT)

            def proj_lower(up, loads):
                base = slots.at
                slots.at += len(loads)

                def lower(k):
                    s = (base + k) % NSLOT
                    slot, half, rest = split_views(loads[k], ring[:, s, :], w_up[:, up + k % 2, :].bitcast(F32),
                                                   w_low[:, LOW + k % 2, :])
                    dve.wait_ge(sem["hi_ready"], w.next("hi_ready"))
                    v.tensor_tensor(rest, slot, half, ALU.subtract).then_inc(sem["lo_ready"], 1)

                return lower

            def norm_ffn(n, gain, scale, first=False):
                base = slots.at
                slots.at += 3 * n

                def lower(k, j):
                    s = (base + 3 * k + j) % NSLOT
                    dve.wait_ge(sem["hi_ready"], w.next("hi_ready"))
                    if k or not first:
                        dve.wait_ge(sem["lo_used"], w.next("lo_used"))
                    v.tensor_tensor(w_low[:, j, :], ring[:, s, :], w_up[:, s, :].bitcast(F32), ALU.subtract).then_inc(sem["lo_ready"], 1)

                def hidden_rows(j):
                    dve.wait_ge(sem["silu_ready"], w.next("silu_ready"))
                    v.tensor_tensor(sg[:, j, :], sg[:, j, :], gu[j][:, S:2 * S], ALU.mult).then_inc(sem["dve_done"], w.mark("dve_done"))
                    dve.wait_ge(sem["dve_done"], w.now("dve_done"))
                    v.tensor_copy(hid_up[:, j, :], sg[:, j, :]).then_inc(sem["dve_done"], w.mark("dve_done"))
                    dve.wait_ge(sem["dve_done"], w.now("dve_done"))
                    v.tensor_tensor(hid_low[:, j, :], sg[:, j, :], hid_up[:, j, :].bitcast(F32), ALU.subtract).then_inc(sem["hidden_ready"], 1)

                def step(k):
                    hidden_rows(0)
                    lower(k + 1, 0)
                    lower(k + 1, 1)
                    hidden_rows(1)
                    lower(k + 1, 2)

                norm(x)
                lower(0, 0)
                lower(0, 1)
                finish_h_split(gain)
                lower(0, 2)
                with w.loop((n - 1) // 2, {"silu_ready": 4, "hi_ready": 6, "lo_used": 6, "dve_done": 8}):
                    step(0)
                    step(1)
                if n % 2 == 0:
                    step(n - 2)
                hidden_rows(0)
                hidden_rows(1)
                dve.wait_ge(sem["ffn_psum"], w.next("ffn_psum"))
                add_x(scale, (slots.at - 1) % NSLOT)

            def setup_angles():
                dve.wait_ge(sem["inputs_loaded"], w.next("inputs_loaded", 48))
                v.tensor_scalar(sinks[:, 8:16], sinks[:, 0:8], -1.0, None, ALU.mult).then_inc(sem["dve_done"], w.mark("dve_done"))
                dve.wait_ge(sem["dve_done"], w.now("dve_done"))
                v.tensor_copy(ang[:, 0, :], pos_i[:, :]).then_inc(sem["dve_done"], w.mark("dve_done"))
                dve.wait_ge(sem["dve_done"], w.now("dve_done"))
                v.tensor_scalar(ang[:, 0, :], ang[:, 0, :], fcol[:, 0:1], None, ALU.mult).then_inc(sem["dve_done"], w.mark("dve_done"))
                dve.wait_ge(sem["dve_done"], w.now("dve_done"))
                v.tensor_scalar(ang[:, 1, :], ang[:, 0, :], 0.15915494309189535, 12582912.0, ALU.mult, ALU.add).then_inc(sem["dve_done"], w.mark("dve_done"))
                dve.wait_ge(sem["dve_done"], w.now("dve_done"))
                v.tensor_scalar(ang[:, 1, :], ang[:, 1, :], -12582912.0, None, ALU.add).then_inc(sem["dve_done"], w.mark("dve_done"))
                dve.wait_ge(sem["dve_done"], w.now("dve_done"))
                for part in (6.28125, 0.0019350051879882812, 3.0199159819e-07):
                    v.scalar_tensor_tensor(ang[:, 0, :], ang[:, 1, :], -part, ang[:, 0, :], ALU.mult, ALU.add).then_inc(sem["dve_done"], w.mark("dve_done"))
                    dve.wait_ge(sem["dve_done"], w.now("dve_done"))
                v.tensor_scalar(ang[:, 0, :], ang[:, 0, :], 3.1415925, -3.1415925, ALU.min, ALU.max).then_inc(sem["dve_done"], w.mark("dve_done"))
                dve.wait_ge(sem["dve_done"], w.now("dve_done"))
                v.tensor_scalar(ang[:, 2, :], ang[:, 0, :], -1.0, None, ALU.mult).then_inc(sem["dve_done"], w.mark("dve_done"))
                dve.wait_ge(sem["dve_done"], w.now("dve_done"))
                v.tensor_tensor(ang[:, 1, :], ang[:, 0, :], ang[:, 2, :], ALU.min).then_inc(sem["dve_done"], w.mark("dve_done"))
                dve.wait_ge(sem["dve_done"], w.now("dve_done"))
                v.tensor_scalar(ang[:, 1, :], ang[:, 1, :], 1.5707963267948966, None, ALU.add).then_inc(sem["angles_ready"], 1)
                lam = pv1[:, V1["lam"][0]:V1["lam"][1]]
                v.tensor_scalar(lamb[:, 0, :], lam, -1.0, None, ALU.mult).then_inc(sem["dve_done"], w.mark("dve_done"))
                dve.wait_ge(sem["dve_done"], w.now("dve_done"))
                v.tensor_tensor(lamb[:, 1, :], lamb[:, 0, :], lam, ALU.max).then_inc(sem["lam_abs"], 1)

            def setup_rates():
                lam = pv1[:, V1["lam"][0]:V1["lam"][1]]
                dve.wait_ge(sem["lam_exp"], w.next("lam_exp"))
                v.tensor_scalar(lamb[:, 4, :], lam, -1.0, 0.0, ALU.mult, ALU.max).then_inc(sem["dve_done"], w.mark("dve_done"))
                dve.wait_ge(sem["dve_done"], w.now("dve_done"))
                log1p(lamb[:, 0, :], lamb[:, 1, :], lamb[:, 2, :], lamb[:, 3, :])
                v.tensor_tensor(lamb[:, 4, :], lamb[:, 4, :], lamb[:, 0, :], ALU.add).then_inc(sem["dve_done"], w.mark("dve_done"))
                dve.wait_ge(sem["dve_done"], w.now("dve_done"))
                v.tensor_scalar(lamb[:, 4, :], lamb[:, 4, :], -8.0, None, ALU.mult).then_inc(sem["dve_done"], w.mark("dve_done"))
                dve.wait_ge(sem["dve_done"], w.now("dve_done"))

            def setup_masks(k):
                for m, (a, b) in enumerate(((part_i, col_i), (col_i, part_i))):
                    v.tensor_scalar(lv_a[:, :], a[:, :], k, None, ALU.logical_shift_right).then_inc(sem["dve_done"], w.mark("dve_done"))
                    dve.wait_ge(sem["dve_done"], w.now("dve_done"))
                    v.tensor_scalar(lv_b[:, :], b[:, :], k, 1, ALU.logical_shift_right, ALU.bitwise_xor).then_inc(sem["dve_done"], w.mark("dve_done"))
                    dve.wait_ge(sem["dve_done"], w.now("dve_done"))
                    v.tensor_tensor(lv_c[:, :], lv_a[:, :], lv_b[:, :], ALU.is_equal).then_inc(sem["dve_done"], w.mark("dve_done"))
                    dve.wait_ge(sem["dve_done"], w.now("dve_done"))
                    v.tensor_scalar(lv_a[:, :], lv_a[:, :], 1, None, ALU.bitwise_and).then_inc(sem["dve_done"], w.mark("dve_done"))
                    dve.wait_ge(sem["dve_done"], w.now("dve_done"))
                    v.tensor_tensor(lvl[:, m, k, :], lv_a[:, :], lv_c[:, :], ALU.mult).then_inc(sem["dve_done"], w.mark("dve_done"))
                    dve.wait_ge(sem["dve_done"], w.now("dve_done"))

            dve.wait_ge(sem["cols_psum"], w.next("cols_psum"))
            v.tensor_copy(pv1[:, :], tr[0][:, 0:N1])
            v.tensor_copy(fcol[:, :], tr[0][:, P:P + 1]).then_inc(sem["cols_ready"], w.mark("cols_ready"))
            dve.wait_ge(sem["cols_ready"], w.now("cols_ready"))
            v.tensor_scalar(col("qg"), col("qg"), HD ** -0.5, None, ALU.mult)

            norm(x)
            lower = proj_lower(UP1, MIX0_LOADS)
            lower(0)
            finish_h_split(lambda c: col("mix", c))
            for k in range(1, len(MIX0_LOADS)):
                lower(k)
                if k == 1:
                    dve.wait_ge(sem["consts_ready"], w.next("consts_ready"))
                if k == 2:
                    setup_angles()
                elif k == 6:
                    setup_rates()
                elif k >= 7:
                    i = k - 7
                    head_norms([z0[:, 2 * i:2 * i + 2, :]], [col("kg" if i == 2 else "qg")], start=i)
            v.memset(gcu[:, :, 0:2], 0.0)
            dve.wait_ge(sem["proj_copied"], w.next("proj_copied", 10))

            def conv(c):
                v.tensor_tensor(gcu[:, c, 2:S + 2], z0[:, 11 + c, :], z0[:, 15 + c, :], ALU.mult).then_inc(sem["dve_done"], w.mark("dve_done"))
                dve.wait_ge(sem["dve_done"], w.now("dve_done"))
                v.tensor_scalar(cv[:, c, :], gcu[:, c, 0:S], col("hconv", c), None, ALU.mult).then_inc(sem["dve_done"], w.mark("dve_done"))
                dve.wait_ge(sem["dve_done"], w.now("dve_done"))
                for k in (1, 2):
                    v.scalar_tensor_tensor(cv[:, c, :], gcu[:, c, k:k + S], col("hconv", 4 * k + c),
                                                cv[:, c, :], ALU.mult, ALU.add).then_inc(sem["dve_done"], w.mark("dve_done"))
                    dve.wait_ge(sem["dve_done"], w.now("dve_done"))
                ins = v.tensor_tensor(mixT[:, 4 + c, :], cv[:, c, :], z0[:, 7 + c, :], ALU.mult)
                if c == 3:
                    ins.then_inc(sem["conv_ready"], 1)

            attention(units_mix0(), [lambda c=c: conv(c) for c in range(4)])
            for k in range(len(LEVELS)):
                setup_masks(k)
            out_proj(4)
            norm_ffn(D_FF // CH, lambda c: col("ffn", c), 1.0, first=True)

            norm(x)
            lower = proj_lower(UP1, MIX1_LOADS)
            lower(0)
            finish_h_split(lambda c: col("mix", DC + c))
            v.memset(g_x[:, :, 0:3], 0.0).then_inc(sem["dve_done"], w.mark("dve_done"))
            dve.wait_ge(sem["dve_done"], w.now("dve_done"))

            def taps(c):
                dve.wait_ge(sem["xc_started"], w.next("xc_started"))
                for k in range(3):
                    ins = v.scalar_tensor_tensor(g_xc[:, c, :], g_x[:, c, k:k + S], col("rconv", k * DC + c),
                                                 g_xc[:, c, :], ALU.mult, ALU.add)
                    if k < 2:
                        ins.then_inc(sem["dve_done"], w.mark("dve_done"))
                        dve.wait_ge(sem["dve_done"], w.now("dve_done"))
                ins.then_inc(sem["xc_ready"], 1)

            for k in range(1, len(MIX1_LOADS)):
                lower(k)
                if k >= 6:
                    taps(2 * (k - 6))
                    taps(2 * (k - 6) + 1)
            for c in range(4, DC):
                taps(c)
            dve.wait_ge(sem["proj_copied"], w.next("proj_copied", len(MIX1_LOADS)))
            for h in range(DC):
                dve.wait_ge(sem["proj_copied"], w.next("proj_copied"))
                ins = v.tensor_scalar(g_r[:, h, :], g_r[:, h, :], lamb[:, 4, h:h + 1], None, ALU.mult)
            ins.then_inc(sem["log_a_ready"], 1)
            v.tensor_tensor(g_i[:, :, :], g_i[:, :, :], g_xc[:, :, :], ALU.mult)
            halves_ = [slice(0, 4), slice(4, 8)]
            for cs in halves_:
                dve.wait_ge(sem["decay_ready"], w.next("decay_ready"))
                v.tensor_tensor(g_m[:, cs, :], g_r[:, cs, :], g_r[:, cs, :], ALU.mult).then_inc(sem["dve_done"], w.mark("dve_done"))
                dve.wait_ge(sem["dve_done"], w.now("dve_done"))
                v.scalar_tensor_tensor(g_m[:, cs, :], g_m[:, cs, :], 1.0, g_t[:, cs, :], ALU.add,
                                       ALU.mult).then_inc(sem["mult_sq_ready"], 1)
                v.memset(g_r[:, cs, 0:1], 0.0)
            for cs in halves_:
                dve.wait_ge(sem["mult_ready"], w.next("mult_ready"))
                v.memset(g_m[:, cs, 0:1], 1.0).then_inc(sem["dve_done"], w.mark("dve_done"))
                dve.wait_ge(sem["dve_done"], w.now("dve_done"))
                v.tensor_tensor(g_m[:, cs, :], g_m[:, cs, :], g_i[:, cs, :], ALU.mult).then_inc(sem["dve_done"], w.mark("dve_done"))
                dve.wait_ge(sem["dve_done"], w.now("dve_done"))
                flat = [r[:, cs, :].rearrange("p c s -> p (c s)") for r in (g_t, g_r, g_m)]
                v.tensor_tensor_scan(flat[0], flat[1], flat[2], 0.0, ALU.mult, ALU.add).then_inc(sem["dve_done"], w.mark("dve_done"))
                dve.wait_ge(sem["dve_done"], w.now("dve_done"))
                v.tensor_tensor(mixT[:, cs, :], g_t[:, cs, :], g_y[:, cs, :], ALU.mult).then_inc(sem["lru_ready"], 1)
            out_proj(4 + 1)

            norm(x)
            finish_h(lambda c: col("ffn", DC + c))
            dve.wait_ge(sem["logits_psum"], w.next("logits_psum"))
            v.tensor_copy(lg[:, :, :], tr[0][:, 0:TT * N_EXP].rearrange("p (t e) -> p t e", t=TT)).then_inc(sem["dve_done"], w.mark("dve_done"))
            dve.wait_ge(sem["dve_done"], w.now("dve_done"))
            for t in range(TT):
                v.max(top[:, t, :], lg[:, t, :]).then_inc(sem["dve_done"], w.mark("dve_done"))
                dve.wait_ge(sem["dve_done"], w.now("dve_done"))
                v.max_index(topi[:, t, :], top[:, t, :], lg[:, t, :]).then_inc(sem["dve_done"], w.mark("dve_done"))
                dve.wait_ge(sem["dve_done"], w.now("dve_done"))
            v.tensor_tensor(gt[:, :, 0:1], top[:, :, 1:2], top[:, :, 0:1], ALU.subtract).then_inc(sem["top_ready"], 1)
            v.tensor_copy(topf[:, :, :], topi[:, :, :]).then_inc(sem["dve_done"], w.mark("dve_done"))
            dve.wait_ge(sem["dve_done"], w.now("dve_done"))
            for j in range(2):
                for t in range(TT):
                    v.tensor_scalar(hot[:, j, t, :], iota_s[:, 0:N_EXP], topf[:, t, j:j + 1], None,
                                         ALU.is_equal).then_inc(sem["dve_done"], w.mark("dve_done"))
                    dve.wait_ge(sem["dve_done"], w.now("dve_done"))
            dve.wait_ge(sem["gate_exp"], w.next("gate_exp"))
            v.tensor_scalar(gt[:, :, 2:3], gt[:, :, 1:2], 1.0, None, ALU.add).then_inc(sem["dve_done"], w.mark("dve_done"))
            dve.wait_ge(sem["dve_done"], w.now("dve_done"))
            v.reciprocal(gt[:, :, 2:3], gt[:, :, 2:3]).then_inc(sem["dve_done"], w.mark("dve_done"))
            dve.wait_ge(sem["dve_done"], w.now("dve_done"))
            v.tensor_tensor(gt[:, :, 3:4], gt[:, :, 1:2], gt[:, :, 2:3], ALU.mult).then_inc(sem["dve_done"], w.mark("dve_done"))
            dve.wait_ge(sem["dve_done"], w.now("dve_done"))
            for t in range(TT):
                v.tensor_scalar(route[:, 1, t, :], hot[:, 0, t, :], gt[:, t, 2:3], None, ALU.mult).then_inc(sem["dve_done"], w.mark("dve_done"))
                dve.wait_ge(sem["dve_done"], w.now("dve_done"))
                v.scalar_tensor_tensor(route[:, 1, t, :], hot[:, 1, t, :], gt[:, t, 3:4], route[:, 1, t, :],
                                            ALU.mult, ALU.add).then_inc(sem["dve_done"], w.mark("dve_done"))
                dve.wait_ge(sem["dve_done"], w.now("dve_done"))
            v.tensor_tensor(route[:, 2, :, :], hot[:, 0, :, :], hot[:, 1, :, :], ALU.add).then_inc(sem["chosen_ready"], 1)
            dve.wait_ge(sem["ranks_psum"], w.next("ranks_psum"))
            v.tensor_copy(route[:, 0, :, :], tr[1][:, 0:TT * N_EXP].rearrange("p (t e) -> p t e", t=TT))
            v.tensor_reduce(cnt_f[:, 0:1], tr[1][:, 32:32 + N_EXP], AX.X, ALU.max).then_inc(sem["ranks_ready"], w.mark("ranks_ready"))
            dve.wait_ge(sem["ranks_ready"], w.now("ranks_ready"))
            v.tensor_copy(cnt[:, :], cnt_f[:, 0:1]).then_inc(sem["count_ready"], w.mark("count_ready"))
            dve.wait_ge(sem["count_ready"], w.now("count_ready"))

            def expert_ffn(w, slots):
                base, n = slots.at, D_FF // CH
                slots.at += 3 * n

                def lower(i):
                    s = (base + i) % NSLOT
                    dve.wait_ge(w.sem["hi_ready"], w.next("hi_ready"))
                    dve.wait_ge(w.sem["lo_used"], w.next("lo_used"))
                    v.tensor_tensor(w_low[:, i % NLOW, :], ring[:, s, :], w_up[:, s, :].bitcast(F32),
                                    ALU.subtract).then_inc(w.sem["lo_ready"], 1)

                def hidden_rows(k):
                    dve.wait_ge(w.sem["silu_ready"], w.next("silu_ready"))
                    v.tensor_tensor(sg[:, k % 2, :], sg[:, k % 2, :], gu[k % 2][:, S:2 * S],
                                    ALU.mult).then_inc(w.sem["hidden_ready"], 1)

                def hidden_lower(k):
                    dve.wait_ge(w.sem["hidT_up"], w.next("hidT_up"))
                    cs = slice(k % 2 * P, k % 2 * P + P)
                    v.tensor_tensor(hid_low[:, :, cs], tr[k % 2][:, 0:S].rearrange("p (f s) -> p f s", f=2),
                                    hid_up[:, :, cs].bitcast(F32), ALU.subtract).then_inc(w.sem["hidT_ready"], 1)

                def step(k):
                    first, m = expert_loads(k + 1)
                    lower(first)
                    if m > 1:
                        lower(first + 1)
                    hidden_rows(k)
                    if k:
                        hidden_lower(k - 1)
                    if m > 2:
                        lower(first + 2)

                def start():
                    lower(0)
                    lower(1)
                    for i in range(2):
                        dve.wait_ge(sem["chosen_h_up"], w.next("chosen_h_up"))
                        for c in range(4 * i, 4 * i + 4):
                            ins = v.scalar_tensor_tensor(hT_low[:, c, 0:P], tr[i][:, c % 4 * P:c % 4 * P + P],
                                                         col("ffn", DC + c), hT_up[:, c, 0:P].bitcast(F32),
                                                         ALU.mult, ALU.subtract)
                        ins.then_inc(sem["chosen_h_ready"], 1)

                def rest():
                    step(0)
                    with w.loop(n // 2 - 1, {"hi_ready": 6, "lo_used": 6, "silu_ready": 2, "hidT_up": 2}):
                        step(1)
                        step(2)
                    step(n - 1)
                    lower(expert_loads(n + 1)[0])
                    hidden_lower(n - 1)

                return start, rest

            def experts(w, slots):
                start, rest = expert_ffn(w, slots)

                def select(e):
                    v.tensor_copy(cur[:, :, :, None], route[:, :, :, bass.ds(e, 1)]).then_inc(w.sem["dve_done"], w.mark("dve_done"))
                    dve.wait_ge(w.sem["dve_done"], w.now("dve_done"))
                    for t in range(TT):
                        v.tensor_scalar(sel[:, t, :], iota_s[:, :], cur[:, 0, t:t + 1], cur[:, 2, t:t + 1],
                                        ALU.is_equal, ALU.mult)
                        ins = v.tensor_scalar(selg[:, t, :], iota_s[:, :], cur[:, 0, t:t + 1], cur[:, 1, t:t + 1],
                                              ALU.is_equal, ALU.mult)
                    ins.then_inc(sem["sel_ready"], 1)

                def add():
                    dve.wait_ge(sem["expert_psum"], w.next("expert_psum"))
                    for i, b in enumerate(ebank):
                        o = x[:, i // 2, (i % 2) * HALF:(i % 2) * HALF + HALF]
                        ins = v.tensor_tensor(o, o, b[:, :], ALU.add)
                    ins.then_inc(sem["expert_added"], 1)

                select(0)
                v.memset(cnt_f[:, 1:2], 0.0).then_inc(sem["expert_added"], 1)
                start()
                per = {"dve_done": 1, "chosen_h_up": 2, "hi_ready": 42, "lo_used": 42, "silu_ready": 14,
                       "hidT_up": 14, "expert_psum": 1}
                with w.loop(N_EXP - 1, per) as e:
                    rest()
                    select(e + 1)
                    start()
                    add()
                rest()
                add()

            experts(w, slots)
            n_max = dve.value_load(cnt[0:1, 0:1], min_val=0, max_val=S)
            with dve.If(n_max > CAP):
                over = w.branch(sem_over)
                v.tensor_scalar(route[:, 0, :, :], route[:, 0, :, :], float(CAP), None, ALU.subtract).then_inc(over.sem["dve_done"], over.mark("dve_done"))
                dve.wait_ge(over.sem["dve_done"], over.now("dve_done"))
                dve.sem_inc(over.sem["lo_used"], NLOW)
                experts(over, Slots())
            for t in range(TT):
                v.memset(took[:, t:t + 1], 0.0).then_inc(sem["x_ready"], 1)

            def layer(l):
                v.tensor_copy(pv[:, None, :], pv2[:, bass.ds(l, 1), :]).then_inc(sem["dve_done"], w.mark("dve_done"))
                dve.wait_ge(sem["dve_done"], w.now("dve_done"))
                norm_ffn(FFN_DIM // CH, lambda c: col2("ffn1", c), 0.5)
                norm(x)
                v.memset(zr[:, :, 0:1], 0.0)
                v.memset(zf, 0.0)
                lower = proj_lower(UP2, MIX2_LOADS + XKV_LOADS)
                lower(0)
                finish_h_split(lambda c: col2("mix", c))
                lower(1)
                lower(2)
                norm(mem)
                for k in range(3, len(MIX2_LOADS) + 2):
                    lower(k)
                dve.wait_ge(sem["proj_copied"], w.next("proj_copied", len(MIX2_LOADS)))
                finish_h_split(lambda c: col2("mem", c))
                f0, f1, f2, f3, f4, f5 = (fsc[:, i, :] for i in range(6))
                v.tensor_scalar(f0, zf, col2("fb"), None, ALU.add).then_inc(sem["dve_done"], w.mark("dve_done"))
                dve.wait_ge(sem["dve_done"], w.now("dve_done"))
                v.tensor_scalar(f1, f0, -1.0, None, ALU.mult).then_inc(sem["dve_done"], w.mark("dve_done"))
                dve.wait_ge(sem["dve_done"], w.now("dve_done"))
                v.tensor_tensor(f1, f1, f0, ALU.max).then_inc(sem["forget_abs"], 1)

                def memory_values():
                    lower(len(MIX2_LOADS) + 2)
                    lower(len(MIX2_LOADS) + 3)

                head_norms([q2[:, 2 * i:2 * i + 2, :] for i in range(4)],
                           [col2(n) for n in ("fqg", "fkg", "mqg", "mkg")], then=memory_values)
                dve.wait_ge(sem["forget_exp"], w.next("forget_exp"))
                log1p(f5, f2, f1, f3)
                v.memset(f3, 1.0)
                v.scalar_tensor_tensor(f0, f0, 0.0, f5, ALU.min, ALU.subtract).then_inc(sem["dve_done"], w.mark("dve_done"))
                dve.wait_ge(sem["dve_done"], w.now("dve_done"))
                v.tensor_tensor_scan(f4, f3, f0, 0.0, ALU.mult, ALU.add).then_inc(sem["dve_done"], w.mark("dve_done"))
                dve.wait_ge(sem["dve_done"], w.now("dve_done"))
                v.tensor_scalar(f5, f4, -1.0, None, ALU.mult).then_inc(sem["forget_ready"], 1)

                for i in range(2):
                    dve.wait_ge(sem["rope_psum"], w.next("rope_psum"))
                    q, turned = q2[:, 4 + 2 * i:6 + 2 * i, :], rtb[i].rearrange("p (a b) -> p a b", a=2)
                    v.tensor_tensor(turned, gu[i][:, :].rearrange("p (a b) -> p a b", a=2),
                                    sinT[:, None, :].to_broadcast([P, 2, S]), ALU.mult)
                    v.tensor_tensor(q, q, cosT[:, None, :].to_broadcast([P, 2, S]), ALU.mult).then_inc(sem["dve_done"], w.mark("dve_done"))
                    dve.wait_ge(sem["dve_done"], w.now("dve_done"))
                    v.tensor_tensor(q, q, turned, ALU.add).then_inc(sem["rope_ready"], 1)
                dve.wait_ge(sem["proj_copied"], w.next("proj_copied", 4))
                def shift(tiles, rows_=P, name="dve_done"):
                    a, n = tiles[0], len(tiles)
                    d = zd[0:rows_, 0:n, :]
                    v.tensor_tensor(d, zr[0:rows_, a:a + n, 0:S], zr[0:rows_, a:a + n, 1:S + 1], ALU.subtract).then_inc(sem["dve_done"], w.mark("dve_done"))
                    dve.wait_ge(sem["dve_done"], w.now("dve_done"))
                    for i, c in enumerate(tiles):
                        o = zr[0:rows_, c, 1:S + 1]
                        ins = v.scalar_tensor_tensor(o, zd[0:rows_, i, :], col2("mu", c)[0:rows_, :], o,
                                                     ALU.mult, ALU.add)
                    ins.then_inc(sem[name], w.mark(name))
                    dve.wait_ge(sem[name], w.now(name))

                def shift_tail():
                    shift((12, 13))
                    shift((14,), 32, "tail_shifted")

                attention(units_causal(0) + units_causal(1),
                          [shift_tail, lambda: shift((0, 1, 2, 3)), lambda: shift((4, 5, 6, 7)),
                           lambda: shift((8, 9, 10, 11), name="tokens_in")])
                rwkv()
                out_proj(4 + 1)
                norm(x)
                lower = proj_lower(UP2, XQ_LOADS)
                lower(0)
                finish_h_split(lambda c: col2("xat", c))
                lower(1)
                head_norms([xk[:, 2 * i:2 * i + 2, :] for i in range(2)] + [xq[:, 2 * i:2 * i + 2, :] for i in range(2)],
                           [col2("xkg"), col2("xkg"), col2("xqg"), col2("xqg")])
                dve.wait_ge(sem["proj_copied"], w.next("proj_copied", 2))
                attention(units_mem())
                out_proj(2)
                norm_ffn(FFN_DIM // CH, lambda c: col2("ffn2", c), 0.5)
                slots.at += SKIP2

            def rwkv():
                r_, k_, v_ = (zr[:, 4 * i:4 * i + 4, 1:S + 1] for i in range(3))

                def flat(a):
                    return a[:, :, :].rearrange("p a b -> p (a b)")

                def chunks(a):
                    return flat(a).rearrange("p (c s) -> p c s", s=RW)

                dve.wait_ge(sem["proj_copied"], w.next("proj_copied", 4))
                v.tensor_scalar(lw[:, :, :], lw[:, :, :], -(2.718281828459045 ** -0.5), None, ALU.mult).then_inc(sem["dve_done"], w.mark("dve_done"))
                dve.wait_ge(sem["dve_done"], w.now("dve_done"))
                v.tensor_tensor_scan(flat(cw), keep[:, :], flat(lw), 0.0, ALU.mult, ALU.add).then_inc(sem["dve_done"], w.mark("dve_done"))
                dve.wait_ge(sem["dve_done"], w.now("dve_done"))
                v.tensor_tensor(ep[:, :, :], cw[:, :, :], lw[:, :, :], ALU.subtract)
                v.tensor_tensor(chunks(et), chunks(cw)[:, :, RW - 1:RW].to_broadcast([P, S * 4 // RW, RW]),
                                      chunks(cw), ALU.subtract).then_inc(sem["sums_ready"], 1)
                for p in range(4):
                    ins = v.tensor_scalar(kk[:, p, :], k_[:, p, :], col2("k_k", p), None, ALU.mult)
                ins.then_inc(sem["removal_keys"], 1)
                v.tensor_copy(Tm, ident[:, None, :].to_broadcast([P, 2 * 8, P]))
                v.tensor_copy(Um, ident[:, None, :].to_broadcast([P, 2 * 8, P]))
                dve.wait_ge(sem["proj_copied"], w.next("proj_copied", 4))
                for p in range(4):
                    ins = v.tensor_scalar(Kb[:, p, :], ra[:, p, :], 1.0, col2("k_a", p), ALU.subtract, ALU.mult)
                ins.then_inc(sem["dve_done"], w.mark("dve_done"))
                dve.wait_ge(sem["dve_done"], w.now("dve_done"))
                v.scalar_tensor_tensor(k_, Kb[:, :, :], 1.0, k_, ALU.add, ALU.mult).then_inc(sem["dve_done"], w.mark("dve_done"))
                dve.wait_ge(sem["dve_done"], w.now("dve_done"))
                for i in range(2):
                    dve.wait_ge(sem["root_ready"], w.next("root_ready"))
                    v.tensor_scalar(rtb[i], rtb[i], 1e-12, None, ALU.max).then_inc(sem["dve_done"], w.mark("dve_done"))
                    dve.wait_ge(sem["dve_done"], w.now("dve_done"))
                    v.reciprocal(rtb[i], rtb[i]).then_inc(sem["sumsq_read"], w.mark("sumsq_read"))
                    dve.wait_ge(sem["sumsq_read"], w.now("sumsq_read"))
                    o = kk[:, 2 * i:2 * i + 2, :]
                    v.tensor_tensor(o, o, rtb[i].rearrange("p (a b) -> p a b", a=2), ALU.mult).then_inc(sem["dve_done"], w.mark("dve_done"))
                    dve.wait_ge(sem["dve_done"], w.now("dve_done"))
                v.tensor_tensor(ra[:, :, :], ra[:, :, :], kk[:, :, :], ALU.mult).then_inc(sem["dve_done"], w.mark("dve_done"))
                dve.wait_ge(sem["dve_done"], w.now("dve_done"))
                dve.wait_ge(sem["proj_copied"], w.next("proj_copied", 4))
                for p in range(4):
                    o = rtb[p // 2][:, (p % 2) * S:(p % 2) * S + S]
                    ins = v.scalar_tensor_tensor(o, r_[:, p, :], col2("r_k", p), k_[:, p, :], ALU.mult, ALU.mult)
                    if p % 2:
                        ins.then_inc(sem["bonus_in"], 1)
                dve.wait_ge(sem["decays_ready"], w.next("decays_ready", 4))
                v.tensor_tensor(Bb[:, :, :], ra[:, :, :], et[:, :, :], ALU.mult).then_inc(sem["tokens_in"], w.mark("tokens_in"))
                v.tensor_tensor(Kb[:, :, :], k_, et[:, :, :], ALU.mult).then_inc(sem["tokens_in"], w.mark("tokens_in"))
                v.tensor_tensor(Bh[:, :, :], ra[:, :, :], ei[:, :, :], ALU.mult)
                v.tensor_tensor(Kh[:, :, :], k_, ei[:, :, :], ALU.mult)
                for t in range(TT):
                    ts = slice(t * P, t * P + P)
                    v.scalar_tensor_tensor(AR[:, :, t, 0, :], kk[:, :, ts], -1.0, ep[:, :, ts], ALU.mult, ALU.mult)
                    ins = v.tensor_tensor(AR[:, :, t, 1, :], r_[:, :, ts], ew[:, :, ts], ALU.mult)
                ins.then_inc(sem["gram_in"], 1)
                for i in range(2):
                    dve.wait_ge(sem["bonus_psum"], w.next("bonus_psum"))
                    ins = v.tensor_tensor(bon[:, 2 * i:2 * i + 2, :], gu[i][:, :].rearrange("p (a b) -> p a b", a=2),
                                          v_[:, 2 * i:2 * i + 2, :], ALU.mult)
                ins.then_inc(sem["bonus_ready"], 1)
                for u in range(2 * 8):
                    dve.wait_ge(sem["gram_psum"], w.next("gram_psum"))
                    if u == 0:
                        v.tensor_copy(sdec[:, :, 0:NRW], ew[:, :, :].rearrange("p a (c s) -> p a c s", s=RW)[:, :, :, RW - 1])
                        v.memset(Sbd[:, :, :], 0.0)
                        v.memset(yS[0:RW, 0, :], 0.0)
                    v.tensor_tensor(G[:, u // 8, u % 8, :, :], gu[u % 2][:, :].rearrange("p (k s) -> p k s", k=4),
                                          rmask[:, :, :], ALU.mult).then_inc(sem["gram_ready"], 1)
                def put(M, q, m, k, src):
                    return v.copy_predicated(M[:, 4 * q:4 * q + 4, :], lvl[:, m, k:k + 1, :].to_broadcast([P, 4, P]), src)

                def quad(b):
                    return b[:, :].rearrange("p (j s) -> p j s", j=4)

                for q in range(4):
                    dve.wait_ge(sem["inv_a_psum"], w.next("inv_a_psum"))
                    v.tensor_copy(took[:, q:q + 1], epsc[:, 0:1])
                    put(Tm, q, 0, 0, quad(gu[q % 2]))
                    put(Um, q, 1, 0, G[:, q // 2, 4 * (q % 2):4 * (q % 2) + 4, 0, :]).then_inc(sem["inv_ready"], 1)
                steps = 4 * (len(LEVELS) - 1)
                for k in range(steps):
                    dve.wait_ge(sem["inv_y_psum"], w.next("inv_y_psum"))
                    v.tensor_copy(took[:, 4 + k:5 + k], epsc[:, 0:1])
                    if k < steps - 4:
                        put(Tm, k % 4, 0, 1 + k // 4, quad(tr[k % 2]))
                    put(Um, k % 4, 1, 1 + k // 4, quad(acc[k % 2])).then_inc(sem["inv_ready"], 1)
                for c in range(NRW):
                    t, r = c // 2, slice(RW * (c % 2), RW * (c % 2) + RW)
                    if c:
                        dve.wait_ge(sem["carry_psum"], w.next("carry_psum"))
                        if c == 1:
                            dve.wait_ge(sem["akv_ready"], w.next("akv_ready", TT))
                        v.tensor_tensor(AkV[r, t, :], AkV[r, t, :], gu[0][r, :], ALU.add).then_inc(sem["removal_in"], 1)
                    if c < NRW - 1:
                        dve.wait_ge(sem["state_psum"], w.next("state_psum"))
                        for h in range(2):
                            d = slice(64 * h, 64 * h + 64)
                            new = tr[1][d, :].rearrange("p (a b) -> p a b", a=4)[:, :, d]
                            if c == 0:
                                ins = v.tensor_copy(Sbd[d, :, d], new)
                            else:
                                v.tensor_tensor(Sbd[d, :, d], Sbd[d, :, d],
                                                     sdec[d, :, c:c + 1].to_broadcast([64, 4, 64]), ALU.mult).then_inc(sem["dve_done"], w.mark("dve_done"))
                                dve.wait_ge(sem["dve_done"], w.now("dve_done"))
                                ins = v.tensor_tensor(Sbd[d, :, d], Sbd[d, :, d], new, ALU.add)
                        ins.then_inc(sem["state_ready"], 1)
                for t in range(TT):
                    y = yS[:, t, :].rearrange("p (h d) -> p h d", h=8)

                    def head(i):
                        return gnst[:, i, :, None].to_broadcast([P, 8, HD])

                    dve.wait_ge(sem["y_psum"], w.next("y_psum"))
                    dve.wait_ge(sem["carry_y_ready"], w.next("carry_y_ready", t + 1))
                    v.tensor_tensor(yS[:, t, :], yS[:, t, :], acc[t][:, :], ALU.add).then_inc(sem["dve_done"], w.mark("dve_done"))
                    dve.wait_ge(sem["dve_done"], w.now("dve_done"))
                    v.tensor_reduce(gnst[:, 0, :], y, AX.X, ALU.add).then_inc(sem["dve_done"], w.mark("dve_done"))
                    dve.wait_ge(sem["dve_done"], w.now("dve_done"))
                    v.tensor_scalar(gnst[:, 0, :], gnst[:, 0, :], 1.0 / HD, None, ALU.mult).then_inc(sem["dve_done"], w.mark("dve_done"))
                    dve.wait_ge(sem["dve_done"], w.now("dve_done"))
                    v.tensor_tensor(y, y, head(0), ALU.subtract).then_inc(sem["dve_done"], w.mark("dve_done"))
                    dve.wait_ge(sem["dve_done"], w.now("dve_done"))
                    v.tensor_tensor(sqb[0], yS[:, t, :], yS[:, t, :], ALU.mult).then_inc(sem["dve_done"], w.mark("dve_done"))
                    dve.wait_ge(sem["dve_done"], w.now("dve_done"))
                    v.tensor_reduce(gnst[:, 1, :], sqb[0].rearrange("p (h d) -> p h d", h=8), AX.X, ALU.add).then_inc(sem["y_var"], 1)
                    dve.wait_ge(sem["y_root"], w.next("y_root"))
                    v.reciprocal(gnst[:, 3, :], gnst[:, 2, :]).then_inc(sem["dve_done"], w.mark("dve_done"))
                    dve.wait_ge(sem["dve_done"], w.now("dve_done"))
                    v.tensor_tensor(y, y, head(3), ALU.mult).then_inc(sem["y_normed"], 1)
                for t in range(TT):
                    dve.wait_ge(sem["yT_ready"], w.next("yT_ready"))
                    o, ts = mixT[:, 2:6, t * P:t * P + P], slice(t * P, t * P + P)
                    v.tensor_tensor(o, o, bon[:, :, ts], ALU.add).then_inc(sem["dve_done"], w.mark("dve_done"))
                    dve.wait_ge(sem["dve_done"], w.now("dve_done"))
                    ins = v.tensor_tensor(o, o, rg[:, :, ts], ALU.mult)
                ins.then_inc(sem["rwkv_ready"], 1)

            dve.wait_ge(sem["cols_psum"], w.next("cols_psum"))
            for l in range(DEPTH2):
                v.tensor_copy(pv2[:, l, :], tr[0][:, l * N2:l * N2 + N2]).then_inc(sem["dve_done"], w.mark("dve_done"))
                dve.wait_ge(sem["dve_done"], w.now("dve_done"))
            for name, dim in (("fqg", HD), ("mqg", HD), ("xqg", P)):
                c = pv2[:, :, V2[name][0]]
                v.tensor_scalar(c, c, dim ** -0.5, None, ALU.mult).then_inc(sem["dve_done"], w.mark("dve_done"))
                dve.wait_ge(sem["dve_done"], w.now("dve_done"))
            run_layers(w, layer, LAYER_DVE)
            v.memset(cnt_f[:, 1:2], 0.0).then_inc(sem["out_ready"], 1)

        @block.gpsimd
        def _(pool):
            w = Turns(pool, sem)
            g = nc.gpsimd

            def select(out_, pattern, op, fill, base, p):
                return g.affine_select(out_, out_, pattern, op, fill, base=base, channel_multiplier=p)

            g.memset(rows[:, :, :], 0.0).then_inc(sem["rows_zeroed"], 1)
            g.memset(epsc[:, 0:1], EPS).then_inc(sem["pool_done"], w.mark("pool_done"))
            pool.wait_ge(sem["pool_done"], w.now("pool_done"))
            g.memset(ident[:, :], 0.0).then_inc(sem["pool_done"], w.mark("pool_done"))
            pool.wait_ge(sem["pool_done"], w.now("pool_done"))
            g.memset(ones[:, :], 1.0).then_inc(sem["pool_done"], w.mark("pool_done"))
            pool.wait_ge(sem["pool_done"], w.now("pool_done"))
            g.memset(frow[:, :], 0.0).then_inc(sem["pool_done"], w.mark("pool_done"))
            pool.wait_ge(sem["pool_done"], w.now("pool_done"))
            f4 = frow[:, :].rearrange("p (h o i) -> p h o i", h=2, o=8)
            for i in range(8):
                g.memset(f4[:, :, 0:2, i:i + 1], float(500000.0 ** (-2 * i / 16))).then_inc(sem["pool_done"], w.mark("pool_done"))
                pool.wait_ge(sem["pool_done"], w.now("pool_done"))
            select(ident[:, :], [[-1, P]], ALU.not_equal, 1.0, 0, 1).then_inc(sem["pool_done"], w.mark("pool_done"))
            pool.wait_ge(sem["pool_done"], w.now("pool_done"))
            g.memset(epsc[:, 1:2], GN_EPS).then_inc(sem["first_consts_ready"], 1)
            for m in (blk64, rope):
                g.memset(m[:, :], 0.0).then_inc(sem["pool_done"], w.mark("pool_done"))
                pool.wait_ge(sem["pool_done"], w.now("pool_done"))
            g.memset(upper[:, :], 1.0).then_inc(sem["pool_done"], w.mark("pool_done"))
            pool.wait_ge(sem["pool_done"], w.now("pool_done"))
            g.memset(sel4[:, :, :], 0.0).then_inc(sem["pool_done"], w.mark("pool_done"))
            pool.wait_ge(sem["pool_done"], w.now("pool_done"))
            g.memset(cmask[:, :], 0.0).then_inc(sem["pool_done"], w.mark("pool_done"))
            pool.wait_ge(sem["pool_done"], w.now("pool_done"))
            g.memset(rmask[:, :, :], 1.0).then_inc(sem["pool_done"], w.mark("pool_done"))
            pool.wait_ge(sem["pool_done"], w.now("pool_done"))
            g.memset(keep[:, :], 1.0).then_inc(sem["pool_done"], w.mark("pool_done"))
            pool.wait_ge(sem["pool_done"], w.now("pool_done"))
            for h in range(2):
                g.memset(blk64[64 * h:64 * h + 64, 64 * h:64 * h + 64], 1.0).then_inc(sem["pool_done"], w.mark("pool_done"))
                pool.wait_ge(sem["pool_done"], w.now("pool_done"))
            g.memset(keep[:, :].rearrange("p (c s) -> p c s", s=RW)[:, :, 0:1], 0.0).then_inc(sem["pool_done"], w.mark("pool_done"))
            pool.wait_ge(sem["pool_done"], w.now("pool_done"))
            select(upper[:, :], [[1, P]], ALU.is_gt, 0.0, 0, -1).then_inc(sem["pool_done"], w.mark("pool_done"))
            pool.wait_ge(sem["pool_done"], w.now("pool_done"))
            for h in range(2):
                select(sel4[:, :, :], [[-1, 4], [0, P]], ALU.not_equal, 1.0, -64 * h, 1).then_inc(sem["pool_done"], w.mark("pool_done"))
                pool.wait_ge(sem["pool_done"], w.now("pool_done"))
            select(cmask[:, :], [[-1, S]], ALU.is_ge, -BIG, P, 1).then_inc(sem["pool_done"], w.mark("pool_done"))
            pool.wait_ge(sem["pool_done"], w.now("pool_done"))
            for k in range(4):
                select(rmask[:, k, :], [[1, P]], ALU.is_ge if k % 2 else ALU.is_gt, 0.0, 0, -1).then_inc(sem["pool_done"], w.mark("pool_done"))
                pool.wait_ge(sem["pool_done"], w.now("pool_done"))
            g.memset(rmask[0:RW, :, RW:P], 0.0).then_inc(sem["pool_done"], w.mark("pool_done"))
            pool.wait_ge(sem["pool_done"], w.now("pool_done"))
            for h in range(2):
                select(rope[:, 64 * h:64 * h + 8], [[-1, 8]], ALU.not_equal, -1.0, -(64 * h + 8), 1).then_inc(sem["pool_done"], w.mark("pool_done"))
                pool.wait_ge(sem["pool_done"], w.now("pool_done"))
                select(rope[:, 64 * h + 8:64 * h + 16], [[-1, 8]], ALU.not_equal, 1.0, -64 * h, 1).then_inc(sem["pool_done"], w.mark("pool_done"))
                pool.wait_ge(sem["pool_done"], w.now("pool_done"))
            g.iota(part_i[:, :], [[0, P]], base=0, channel_multiplier=1).then_inc(sem["pool_done"], w.mark("pool_done"))
            pool.wait_ge(sem["pool_done"], w.now("pool_done"))
            g.iota(col_i[:, :], [[1, P]], base=0, channel_multiplier=0).then_inc(sem["pool_done"], w.mark("pool_done"))
            pool.wait_ge(sem["pool_done"], w.now("pool_done"))
            g.iota(awin_i[:, :], [[1, S]], base=-P, channel_multiplier=-1).then_inc(sem["pool_done"], w.mark("pool_done"))
            pool.wait_ge(sem["pool_done"], w.now("pool_done"))
            g.tensor_copy(iota_s[:, :], col_i[:, :]).then_inc(sem["pool_done"], w.mark("pool_done"))
            pool.wait_ge(sem["pool_done"], w.now("pool_done"))
            g.tensor_copy(awin[:, :], awin_i[:, :]).then_inc(sem["pool_done"], w.mark("pool_done"))
            pool.wait_ge(sem["pool_done"], w.now("pool_done"))
            select(awin[:, :], [[-1, S]], ALU.is_ge, -BIG, P, 1).then_inc(sem["pool_done"], w.mark("pool_done"))
            pool.wait_ge(sem["pool_done"], w.now("pool_done"))
            select(awin[:, :], [[1, S]], ALU.is_ge, -BIG, -1, -1).then_inc(sem["consts_ready"], 1)

            def load_rows_table(i, name, at, src, n, last=P):
                full = n if last == P else n - 1
                if full:
                    pool.dma_start(rows[at:at + full, i, :], src[0:full * P].rearrange(
                        "(r k) -> r k", k=P)).then_inc(sem["rows2_loaded"], 16)
                if last != P:
                    pool.dma_start(rows[at + full:at + n, i, 0:last],
                                  src[full * P:full * P + last].rearrange("(r k) -> r k", r=1)
                                  ).then_inc(sem["rows2_loaded"], 16)

            pool.wait_ge(sem["rows_zeroed"], w.next("rows_zeroed"))
            for l in range(DEPTH2):
                for name, key, n, last in (
                        ("ffn1", "ffn1_norm_2", 8, P), ("mix", "mix_norm_2", 8, P), ("xat", "xattn_norm_2", 8, P),
                        ("mem", "xattn_mem_norm_2", 8, P), ("ffn2", "ffn2_norm_2", 8, P),
                        ("w0", "rwkv_w0_2", 4, P), ("a0", "rwkv_a0_2", 4, P), ("k_k", "rwkv_k_k_2", 4, P),
                        ("k_a", "rwkv_k_a_2", 4, P), ("ln_w", "rwkv_ln_w_2", 4, P), ("ln_b", "rwkv_ln_b_2", 4, P),
                        ("mu", "rwkv_mu_2", 15, 32), ("xqg", "xattn_q_gain_2", 1, P),
                        ("xkg", "xattn_k_gain_2", 1, P)):
                    load_rows_table(1 + l, name, V2[name][0], A[key][l], n, last)
                pool.dma_start(rows[V2["fb"][0]:V2["fb"][1], 1 + l, :].rearrange("o (r k) -> o r k", k=4),
                              A["fox_f_bias_2"][l:l + 1, None, :].to_broadcast([1, P // 4, 4])
                              ).then_inc(sem["rows2_loaded"], 16)
                load_rows_table(1 + l, "r_k", V2["r_k"][0], A["rwkv_r_k_2"][l].rearrange("h k -> (h k)"), 4)
                for name, key in (("fqg", "fox_q_gain_2"), ("fkg", "fox_k_gain_2"),
                                  ("mqg", "moba_q_gain_2"), ("mkg", "moba_k_gain_2")):
                    for h in range(2):
                        pool.dma_start(rows[V2[name][0]:V2[name][1], 1 + l, h * HD:h * HD + HD],
                                      A[key][l].rearrange("(r k) -> r k", r=1)).then_inc(sem["rows2_loaded"], 16)


def kernel(**inputs):
    import numpy as np
    import concourse.bacc as bacc
    from concourse.bass_utils import run_bass_kernel_spmd

    nc = bacc.Bacc("TRN2", target_bir_lowering=False, num_devices=1)
    arrays, A = {}, {}
    for name, value in inputs.items():
        a = np.ascontiguousarray(value)
        arrays[f"in_{name}_dram"] = a
        A[name] = nc.dram_tensor(f"in_{name}_dram", a.shape, mybir.dt.from_np(a.dtype), kind="ExternalInput").ap()
    out = nc.dram_tensor("out_0_dram", (1, S, D), F32, kind="ExternalOutput").ap()
    build(nc, A, out)
    r = run_bass_kernel_spmd(nc, [arrays], core_ids=[0])
    return r.results[0]["out_0_dram"]
```
